# Optimizing a Trainium2 kernel written in Bass

```python
import math, functools
import jax
import jax.numpy as jnp
from jax import lax
import numpy as np

D_MODEL = 1024
BATCH = 1
SEQ = 512
DEPTH = 1
DEC_BATCH = 8
DEC_SEQ = 4
PAST_LEN = 2048
PAGE_SIZE = 128

MIX_WIDTH = D_MODEL
GROUP_WIDTH = MIX_WIDTH // 4
CONV_W = 4
MOBA_HEADS = 4
MOBA_DH = GROUP_WIDTH // MOBA_HEADS
MOBA_BLOCK = 256
MOBA_TOPK = 3
MOBA_QBLOCK = 128
SSM_HEADS = 4
SSM_HEADDIM = GROUP_WIDTH // SSM_HEADS
SSM_GROUPS = 2
SSM_DSTATE = 128
SSM_CHUNK = 128
SSM_CONV_DIM = GROUP_WIDTH + 2 * SSM_GROUPS * SSM_DSTATE
HGRN_HEADS = 4
HGRN_DK = GROUP_WIDTH // HGRN_HEADS
HGRN_DV = GROUP_WIDTH // HGRN_HEADS
GDN_HEADS = 4
GDN_DK = GROUP_WIDTH // GDN_HEADS
GDN_DV = GROUP_WIDTH // GDN_HEADS
GDN_CONV_DIM = 3 * GROUP_WIDTH
LIN_CHUNK = 64
N_MEM = 256
X_HEADS = 4
X_DH = D_MODEL // X_HEADS
FFN_HIDDEN = -(-8 * D_MODEL // (3 * 256)) * 256
IN_SIZES = (3 * GROUP_WIDTH,
            GROUP_WIDTH, SSM_CONV_DIM, SSM_HEADS,
            GROUP_WIDTH, GROUP_WIDTH, GROUP_WIDTH, GROUP_WIDTH,
            GDN_CONV_DIM, GROUP_WIDTH, GDN_HEADS, GDN_HEADS)
IN_COLS = sum(IN_SIZES)

kernel_name = 'hybrid_moba_ssd_hgrn2_gdn_decoder_step'

def rms_norm(x, w, eps=1e-6):
    xf = x.astype(jnp.float32)
    y = xf * lax.rsqrt(jnp.mean(xf * xf, axis=-1, keepdims=True) + eps)
    return (y * w.astype(jnp.float32)).astype(x.dtype)

def l2_norm(x, eps=1e-6):
    return x * lax.rsqrt(jnp.sum(x * x, axis=-1, keepdims=True) + eps)

def split_cols(t, sizes):
    points = [int(s) for s in np.cumsum(sizes)[:-1]]
    return jnp.split(t, points, axis=-1)

def to_chunks(t, cs):
    b, L = t.shape[:2]
    return jnp.moveaxis(t.reshape(b, L // cs, cs, *t.shape[2:]), 1, 0)

def from_chunks(t):
    nc, b, cs = t.shape[:3]
    return jnp.moveaxis(t, 0, 1).reshape(b, nc * cs, *t.shape[3:])

def causal_conv(u, prefix, w, bias):
    L = u.shape[1]
    up = jnp.concatenate([prefix.astype(u.dtype), u], axis=1)
    out = w[0] * up[:, 0:L]
    for j in range(1, CONV_W):
        out = out + w[j] * up[:, j:j + L]
    if bias is not None:
        out = out + bias
    return out, up[:, L:]

def moba_prompt(slopes, q, k, v):
    b, S, H, dh = q.shape
    nb = -(-S // MOBA_BLOCK)
    pad = nb * MOBA_BLOCK - S
    padw = ((0, 0), (0, pad), (0, 0), (0, 0))
    kb = jnp.pad(k, padw).reshape(b, nb, MOBA_BLOCK, H, dh).transpose(0, 3, 1, 2, 4)
    vb = jnp.pad(v, padw).reshape(b, nb, MOBA_BLOCK, H, dh).transpose(0, 3, 1, 2, 4)
    kmean = jnp.mean(kb, axis=3)
    n_sel = min(MOBA_TOPK, nb - 1)
    nq = S // MOBA_QBLOCK
    qb = q.reshape(b, nq, MOBA_QBLOCK, H, dh).transpose(1, 0, 3, 2, 4)
    scale = dh ** -0.5
    m = slopes[None, :, None, None]
    bi = jnp.arange(b)[:, None, None, None]
    hi = jnp.arange(H)[None, :, None, None]

    def one_block(args):
        qblk, qi = args
        start = qi * MOBA_QBLOCK
        t = start + jnp.arange(MOBA_QBLOCK)
        cb = start // MOBA_BLOCK
        own_k = lax.dynamic_index_in_dim(kb, cb, axis=2, keepdims=False)
        own_v = lax.dynamic_index_in_dim(vb, cb, axis=2, keepdims=False)
        dist = t[:, None] - (cb * MOBA_BLOCK + jnp.arange(MOBA_BLOCK))[None, :]
        sc_own = jnp.einsum('bhqd,bhkd->bhqk', qblk, own_k) * scale - m * dist
        sc_own = jnp.where(dist >= 0, sc_own, -jnp.inf)
        if n_sel == 0:
            p = jax.nn.softmax(sc_own, axis=-1)
            return jnp.einsum('bhqk,bhkd->bhqd', p, own_v)
        gate = jnp.einsum('bhqd,bhnd->bhqn', qblk, kmean)
        gate = jnp.where(jnp.arange(nb) < cb, gate, -jnp.inf)
        _, idx = lax.top_k(gate, n_sel)
        valid = idx < cb
        ks = kb[bi, hi, idx]
        vs = vb[bi, hi, idx]
        s_sel = idx[..., None] * MOBA_BLOCK + jnp.arange(MOBA_BLOCK)
        sc_sel = (jnp.einsum('bhqd,bhqnkd->bhqnk', qblk, ks) * scale
                  - m[..., None] * (t[None, None, :, None, None] - s_sel))
        sc_sel = jnp.where(valid[..., None], sc_sel, -jnp.inf)
        sc = jnp.concatenate([sc_sel.reshape(b, H, MOBA_QBLOCK, n_sel * MOBA_BLOCK), sc_own], axis=-1)
        p = jax.nn.softmax(sc, axis=-1)
        p_sel = p[..., :n_sel * MOBA_BLOCK].reshape(b, H, MOBA_QBLOCK, n_sel, MOBA_BLOCK)
        p_own = p[..., n_sel * MOBA_BLOCK:]
        return (jnp.einsum('bhqnk,bhqnkd->bhqd', p_sel, vs)
                + jnp.einsum('bhqk,bhkd->bhqd', p_own, own_v))

    o = lax.map(one_block, (qb, jnp.arange(nq)))
    return o.transpose(1, 0, 3, 2, 4).reshape(b, S, H * dh)

def moba_sample(k_cache, v_cache, layer, page_table, slopes, q, k_new, v_new):
    db, T, H, dh = q.shape
    n_pages = page_table.shape[1]
    past = n_pages * PAGE_SIZE
    ppb = MOBA_BLOCK // PAGE_SIZE
    nbp = past // MOBA_BLOCK
    r0 = nbp * MOBA_BLOCK
    scale = dh ** -0.5
    m = slopes[None, :, None, None]
    t = past + jnp.arange(T)
    k_past = k_cache[layer, page_table].reshape(db, past, H, dh)
    v_tail = v_cache[layer, page_table[:, nbp * ppb:]].reshape(db, past - r0, H, dh)
    own_k = jnp.concatenate([k_past[:, r0:], k_new.astype(k_past.dtype)], axis=1)
    own_v = jnp.concatenate([v_tail, v_new.astype(v_tail.dtype)], axis=1)
    dist = t[:, None] - (r0 + jnp.arange(past - r0 + T))[None, :]
    sc_own = jnp.einsum('bqhd,bkhd->bhqk', q, own_k) * scale - m * dist
    sc_own = jnp.where(dist >= 0, sc_own, -jnp.inf)
    n_sel = min(MOBA_TOPK, nbp)
    if n_sel == 0:
        p = jax.nn.softmax(sc_own.astype(jnp.float32), axis=-1)
        o = jnp.einsum('bhqk,bkhd->bhqd', p, own_v)
        return o.transpose(0, 2, 1, 3).reshape(db, T, H * dh)
    kblocks = k_past[:, :r0].reshape(db, nbp, MOBA_BLOCK, H, dh)
    kmean = jnp.mean(kblocks.astype(jnp.float32), axis=2)
    gate = jnp.einsum('bqhd,bnhd->bhqn', q, kmean)
    _, idx = lax.top_k(gate, n_sel)
    bi = jnp.arange(db)[:, None, None, None]
    hi = jnp.arange(H)[None, :, None, None]
    ks = kblocks[bi, idx, :, hi]
    logical = idx[..., None] * ppb + jnp.arange(ppb)
    phys = page_table[bi[..., None], logical]
    vs = v_cache[layer, phys, :, hi[..., None]].reshape(db, H, T, n_sel, MOBA_BLOCK, dh)
    s_sel = idx[..., None] * MOBA_BLOCK + jnp.arange(MOBA_BLOCK)
    sc_sel = (jnp.einsum('bqhd,bhqnkd->bhqnk', q, ks) * scale
              - m[..., None] * (t[None, None, :, None, None] - s_sel))
    sc = jnp.concatenate([sc_sel.reshape(db, H, T, n_sel * MOBA_BLOCK), sc_own], axis=-1)
    p = jax.nn.softmax(sc.astype(jnp.float32), axis=-1)
    p_sel = p[..., :n_sel * MOBA_BLOCK].reshape(db, H, T, n_sel, MOBA_BLOCK)
    p_own = p[..., n_sel * MOBA_BLOCK:]
    o = jnp.einsum('bhqnk,bhqnkd->bhqd', p_sel, vs) + jnp.einsum('bhqk,bkhd->bhqd', p_own, own_v)
    return o.transpose(0, 2, 1, 3).reshape(db, T, H * dh)

def ssd_scan(xdt, a, bm, cm, h0):
    cs = min(SSM_CHUNK, xdt.shape[1])
    mask = jnp.tril(jnp.ones((cs, cs), dtype=bool))[None, :, :, None]

    def step(h, inp):
        xc, ac, bc, cc = inp
        acum = jnp.cumsum(ac, axis=1)
        diff = acum[:, :, None] - acum[:, None, :]
        dec = jnp.exp(jnp.where(mask, diff, -jnp.inf))
        y = (jnp.einsum('blhn,bshn,blsh,bshp->blhp', cc, bc, dec, xc)
             + jnp.einsum('blhn,bhpn,blh->blhp', cc, h, jnp.exp(acum)))
        h = (jnp.exp(acum[:, -1])[..., None, None] * h
             + jnp.einsum('bshn,bsh,bshp->bhpn', bc, jnp.exp(acum[:, -1:] - acum), xc))
        return h, y

    h1, y = lax.scan(step, h0, (to_chunks(xdt, cs), to_chunks(a, cs), to_chunks(bm, cs), to_chunks(cm, cs)))
    return from_chunks(y), h1

def mamba2_mixer(z, xbc, dt_raw, conv0, h0, conv_w, conv_b, dt_bias, a_log, d_skip, norm_w):
    b, L, _ = xbc.shape
    xbc_c, conv1 = causal_conv(xbc, conv0, conv_w, conv_b)
    xbc_c = jax.nn.silu(xbc_c)
    xs, bm, cm = split_cols(xbc_c, (GROUP_WIDTH, SSM_GROUPS * SSM_DSTATE, SSM_GROUPS * SSM_DSTATE))
    xs = xs.reshape(b, L, SSM_HEADS, SSM_HEADDIM)
    rep = SSM_HEADS // SSM_GROUPS
    bm = jnp.repeat(bm.reshape(b, L, SSM_GROUPS, SSM_DSTATE), rep, axis=2)
    cm = jnp.repeat(cm.reshape(b, L, SSM_GROUPS, SSM_DSTATE), rep, axis=2)
    dt = jax.nn.softplus(dt_raw + dt_bias)
    a = -jnp.exp(a_log.astype(jnp.float32))
    y, h1 = ssd_scan(xs * dt[..., None], dt * a, bm, cm, h0)
    y = (y + d_skip[:, None] * xs).reshape(b, L, GROUP_WIDTH)
    return rms_norm(y * jax.nn.silu(z), norm_w), conv1, h1

def gla_chunked(q, k, v, log_f, s0):
    cs = min(LIN_CHUNK, q.shape[1])
    mask = jnp.tril(jnp.ones((cs, cs), dtype=bool))[None, :, :, None, None]

    def step(S, inp):
        qc, kc, vc, gc = inp
        bcum = jnp.cumsum(gc, axis=1)
        diff = bcum[:, :, None] - bcum[:, None, :]
        dec = jnp.exp(jnp.where(mask, diff, -jnp.inf))
        att = jnp.einsum('blhk,bshk,blshk->blsh', qc, kc, dec)
        o = (jnp.einsum('blsh,bshv->blhv', att, vc)
             + jnp.einsum('blhk,bhkv->blhv', qc * jnp.exp(bcum), S))
        b_last = bcum[:, -1:]
        S = (jnp.exp(b_last[:, 0])[..., None] * S
             + jnp.einsum('bshk,bshv->bhkv', kc * jnp.exp(b_last - bcum), vc))
        return S, o

    s1, o = lax.scan(step, s0, (to_chunks(q, cs), to_chunks(k, cs), to_chunks(v, cs), to_chunks(log_f, cs)))
    return from_chunks(o), s1

def hgrn2_mixer(q, fx, i, g, s0, lb, norm_w):
    b, L, _ = q.shape
    shp = (b, L, HGRN_HEADS, HGRN_DK)
    q = q.reshape(shp)
    fx = fx.reshape(shp)
    lb = lb.reshape(HGRN_HEADS, HGRN_DK)
    log_f = jnp.logaddexp(jnp.log(lb), jnp.log1p(-lb) + jax.nn.log_sigmoid(fx))
    k = (1.0 - lb) * jax.nn.sigmoid(-fx)
    v = i.reshape(b, L, HGRN_HEADS, HGRN_DV)
    o, s1 = gla_chunked(q, k, v, log_f, s0)
    o = rms_norm(o, norm_w) * jax.nn.silu(g.reshape(b, L, HGRN_HEADS, HGRN_DV))
    return o.reshape(b, L, GROUP_WIDTH), s1

def gated_delta_chunked(q, k, v, beta, log_g, s0):
    cs = min(LIN_CHUNK, q.shape[1])
    incl = jnp.tril(jnp.ones((cs, cs), dtype=bool))
    strict = jnp.tril(jnp.ones((cs, cs), dtype=bool), -1)
    eye = jnp.eye(cs, dtype=jnp.float32)

    def step(S, inp):
        qc, kc, vc, bc, gc = inp
        gam = jnp.cumsum(gc, axis=1)
        gam_h = jnp.moveaxis(gam, 2, 1)
        diff = gam_h[:, :, :, None] - gam_h[:, :, None, :]
        dec_incl = jnp.exp(jnp.where(incl, diff, -jnp.inf))
        dec_strict = jnp.where(strict, dec_incl, 0.0)
        kb = kc * bc[..., None]
        a_mat = jnp.einsum('blhk,bshk->bhls', kb, kc) * dec_strict
        t_mat = lax.linalg.triangular_solve(eye + a_mat, jnp.broadcast_to(eye, a_mat.shape),
                                            left_side=True, lower=True, unit_diagonal=True)
        u = jnp.einsum('bhls,bshv->bhlv', t_mat, vc * bc[..., None])
        w = jnp.einsum('bhls,bshk->bhlk', t_mat, kb * jnp.exp(gam)[..., None])
        v_new = u - jnp.einsum('bhlk,bhkv->bhlv', w, S)
        qk = jnp.einsum('blhk,bshk->bhls', qc, kc) * dec_incl
        o = (jnp.einsum('bhls,bhsv->blhv', qk, v_new)
             + jnp.einsum('blhk,bhkv->blhv', qc * jnp.exp(gam)[..., None], S))
        k_dec = kc * jnp.exp(gam[:, -1:] - gam)[..., None]
        S = jnp.exp(gam_h[:, :, -1])[..., None, None] * S + jnp.einsum('blhk,bhlv->bhkv', k_dec, v_new)
        return S, o

    s1, o = lax.scan(step, s0, (to_chunks(q, cs), to_chunks(k, cs), to_chunks(v, cs),
                                to_chunks(beta, cs), to_chunks(log_g, cs)))
    return from_chunks(o), s1

def gdn_mixer(qkv, z, beta_raw, a_raw, conv0, s0, conv_w, a_log, dt_bias, norm_w):
    b, L, _ = qkv.shape
    qkv_c, conv1 = causal_conv(qkv, conv0, conv_w, None)
    q, k, v = jnp.split(jax.nn.silu(qkv_c), 3, axis=-1)
    q = l2_norm(q.reshape(b, L, GDN_HEADS, GDN_DK)) * GDN_DK ** -0.5
    k = l2_norm(k.reshape(b, L, GDN_HEADS, GDN_DK))
    v = v.reshape(b, L, GDN_HEADS, GDN_DV)
    beta = jax.nn.sigmoid(beta_raw)
    log_g = -jnp.exp(a_log.astype(jnp.float32)) * jax.nn.softplus(a_raw + dt_bias)
    o, s1 = gated_delta_chunked(q, k, v, beta, log_g, s0)
    o = rms_norm(o, norm_w) * jax.nn.silu(z.reshape(b, L, GDN_HEADS, GDN_DV))
    return o.reshape(b, L, GROUP_WIDTH), conv1, s1

def memory_kv(mem, norm_w, w_kv):
    b, M, _ = mem.shape
    k, v = jnp.split(rms_norm(mem, norm_w) @ w_kv, 2, axis=-1)
    return k.reshape(b, M, X_HEADS, X_DH), v.reshape(b, M, X_HEADS, X_DH)

def memory_cross_attention(xn, w_q, k, v, w_o):
    b, L, _ = xn.shape
    q = (xn @ w_q).reshape(b, L, X_HEADS, X_DH).astype(jnp.float32)
    s = jnp.einsum('blhd,bmhd->bhlm', q, k.astype(jnp.float32)) * X_DH ** -0.5
    p = jax.nn.softmax(s, axis=-1)
    o = jnp.einsum('bhlm,bmhd->blhd', p, v.astype(jnp.float32)).reshape(b, L, X_HEADS * X_DH)
    return o.astype(xn.dtype) @ w_o

def swiglu(xn, w_gu, w_down):
    g, u = jnp.split(xn @ w_gu, 2, axis=-1)
    return (jax.nn.silu(g) * u) @ w_down

def hybrid_layer(x, attend, mem_k, mem_v, ssm_conv0, ssm0, hgrn0, gdn_conv0, gdn0, lb, lp):
    f32 = jnp.float32
    b, L, _ = x.shape
    xn = rms_norm(x, lp['n_mix_pre'])
    (m_qkv, s_z, s_xbc, s_dt, h_q, h_f, h_i, h_g,
     g_qkv, g_z, g_b, g_a) = split_cols((xn @ lp['w_in']).astype(f32), IN_SIZES)
    q, k, v = [t.reshape(b, L, MOBA_HEADS, MOBA_DH) for t in jnp.split(m_qkv, 3, axis=-1)]
    o_a = attend(q, k, v)
    o_b, ssm_conv1, ssm1 = mamba2_mixer(s_z, s_xbc, s_dt, ssm_conv0.astype(f32), ssm0.astype(f32),
                                        lp['ssm_conv_w'], lp['ssm_conv_b'], lp['ssm_dt_bias'],
                                        lp['ssm_a_log'], lp['ssm_d'], lp['ssm_norm'])
    o_c, hgrn1 = hgrn2_mixer(h_q, h_f, h_i, h_g, hgrn0.astype(f32), lb, lp['hgrn_norm'])
    o_d, gdn_conv1, gdn1 = gdn_mixer(g_qkv, g_z, g_b, g_a, gdn_conv0.astype(f32), gdn0.astype(f32),
                                     lp['gdn_conv_w'], lp['gdn_a_log'], lp['gdn_dt_bias'], lp['gdn_norm'])
    mixed = jnp.concatenate([o_a, o_b, o_c, o_d], axis=-1).astype(x.dtype) @ lp['w_out']
    x = x + rms_norm(mixed, lp['n_mix_post'])
    xn = rms_norm(x, lp['n_x_pre'])
    x = x + rms_norm(memory_cross_attention(xn, lp['w_xq'], mem_k, mem_v, lp['w_xo']), lp['n_x_post'])
    xn = rms_norm(x, lp['n_f_pre'])
    x = x + rms_norm(swiglu(xn, lp['w_gu'], lp['w_down']), lp['n_f_post'])
    return x, (k, v, ssm_conv1, ssm1, hgrn1, gdn_conv1, gdn1)

def stack_field(outs, i):
    return jnp.stack([o[i] for o in outs], axis=0)

def setup_inputs(seed: int = 0) -> dict:
    key = jax.random.key(seed)
    ks = iter(list(jax.random.split(key, 64)))
    f32 = jnp.float32
    n_pages = PAST_LEN // PAGE_SIZE
    n_pool = (DEC_BATCH * n_pages * 5) // 4

    def nrm(shape, scale=1.0):
        return scale * jax.random.normal(next(ks), shape, f32)

    def gain(shape):
        return 1.0 + 0.05 * jax.random.normal(next(ks), shape, f32)

    def a_log_init(shape):
        return jnp.log(jax.random.uniform(next(ks), shape, f32, 1.0, 16.0))

    def dt_bias_init(shape):
        dt = jnp.exp(jax.random.uniform(next(ks), shape, f32, math.log(1e-3), math.log(1e-1)))
        return dt + jnp.log(-jnp.expm1(-dt))

    page_table = jax.random.permutation(next(ks), n_pool)[:DEC_BATCH * n_pages]
    page_table = page_table.reshape(DEC_BATCH, n_pages).astype(jnp.int32)
    return {
        'x_prompt': nrm((BATCH, SEQ, D_MODEL)),
        'x_sample': nrm((DEC_BATCH, DEC_SEQ, D_MODEL)),
        'mem_prompt': nrm((BATCH, N_MEM, D_MODEL)),
        'cache_moba_k': nrm((DEPTH, n_pool, PAGE_SIZE, MOBA_HEADS, MOBA_DH)),
        'cache_moba_v': nrm((DEPTH, n_pool, PAGE_SIZE, MOBA_HEADS, MOBA_DH)),
        'page_table': page_table,
        'cache_mem_k': nrm((DEPTH, DEC_BATCH, N_MEM, X_HEADS, X_DH)),
        'cache_mem_v': nrm((DEPTH, DEC_BATCH, N_MEM, X_HEADS, X_DH)),
        'state_ssm_conv': nrm((DEPTH, DEC_BATCH, CONV_W - 1, SSM_CONV_DIM)),
        'state_ssm': nrm((DEPTH, DEC_BATCH, SSM_HEADS, SSM_HEADDIM, SSM_DSTATE), 0.1),
        'state_hgrn': nrm((DEPTH, DEC_BATCH, HGRN_HEADS, HGRN_DK, HGRN_DV), 0.5),
        'state_gdn_conv': nrm((DEPTH, DEC_BATCH, CONV_W - 1, GDN_CONV_DIM)),
        'state_gdn': nrm((DEPTH, DEC_BATCH, GDN_HEADS, GDN_DK, GDN_DV), 0.1),
        'n_mix_pre': gain((DEPTH, D_MODEL)),
        'n_mix_post': gain((DEPTH, D_MODEL)),
        'w_in': nrm((DEPTH, D_MODEL, IN_COLS), D_MODEL ** -0.5),
        'w_out': nrm((DEPTH, MIX_WIDTH, D_MODEL), MIX_WIDTH ** -0.5),
        'ssm_conv_w': nrm((DEPTH, CONV_W, SSM_CONV_DIM), CONV_W ** -0.5),
        'ssm_conv_b': nrm((DEPTH, SSM_CONV_DIM), 0.02),
        'ssm_dt_bias': dt_bias_init((DEPTH, SSM_HEADS)),
        'ssm_a_log': a_log_init((DEPTH, SSM_HEADS)),
        'ssm_d': gain((DEPTH, SSM_HEADS)),
        'ssm_norm': gain((DEPTH, GROUP_WIDTH)),
        'hgrn_lb_raw': nrm((DEPTH, HGRN_HEADS * HGRN_DK), 0.5),
        'hgrn_norm': gain((DEPTH, HGRN_DV)),
        'gdn_conv_w': nrm((DEPTH, CONV_W, GDN_CONV_DIM), CONV_W ** -0.5),
        'gdn_a_log': a_log_init((DEPTH, GDN_HEADS)),
        'gdn_dt_bias': dt_bias_init((DEPTH, GDN_HEADS)),
        'gdn_norm': gain((DEPTH, GDN_DV)),
        'n_x_pre': gain((DEPTH, D_MODEL)),
        'n_x_post': gain((DEPTH, D_MODEL)),
        'mem_norm': gain((DEPTH, D_MODEL)),
        'w_xq': nrm((DEPTH, D_MODEL, X_HEADS * X_DH), D_MODEL ** -0.5),
        'w_xkv': nrm((DEPTH, D_MODEL, 2 * X_HEADS * X_DH), D_MODEL ** -0.5),
        'w_xo': nrm((DEPTH, X_HEADS * X_DH, D_MODEL), D_MODEL ** -0.5),
        'n_f_pre': gain((DEPTH, D_MODEL)),
        'n_f_post': gain((DEPTH, D_MODEL)),
        'w_gu': nrm((DEPTH, D_MODEL, 2 * FFN_HIDDEN), D_MODEL ** -0.5),
        'w_down': nrm((DEPTH, FFN_HIDDEN, D_MODEL), FFN_HIDDEN ** -0.5),
    }

def reference(x_prompt, x_sample, mem_prompt, cache_moba_k, cache_moba_v, page_table,
              cache_mem_k, cache_mem_v, state_ssm_conv, state_ssm, state_hgrn, state_gdn_conv, state_gdn,
              n_mix_pre, n_mix_post, w_in, w_out, ssm_conv_w, ssm_conv_b, ssm_dt_bias, ssm_a_log, ssm_d,
              ssm_norm, hgrn_lb_raw, hgrn_norm, gdn_conv_w, gdn_a_log, gdn_dt_bias, gdn_norm,
              n_x_pre, n_x_post, mem_norm, w_xq, w_xkv, w_xo, n_f_pre, n_f_post, w_gu, w_down):
    f32 = jnp.float32
    slopes = jnp.exp2(-8.0 * jnp.arange(1, MOBA_HEADS + 1, dtype=f32) / MOBA_HEADS)
    lb_all = jnp.cumsum(jax.nn.softmax(hgrn_lb_raw.astype(f32), axis=0), axis=0)
    lb_all = lb_all - lb_all[:1]
    bp = x_prompt.shape[0]
    yp, ys = x_prompt, x_sample
    outs_p, outs_s, mem_ks, mem_vs = [], [], [], []
    for l in range(DEPTH):
        lp = {'n_mix_pre': n_mix_pre[l], 'n_mix_post': n_mix_post[l], 'w_in': w_in[l], 'w_out': w_out[l],
              'ssm_conv_w': ssm_conv_w[l], 'ssm_conv_b': ssm_conv_b[l], 'ssm_dt_bias': ssm_dt_bias[l],
              'ssm_a_log': ssm_a_log[l], 'ssm_d': ssm_d[l], 'ssm_norm': ssm_norm[l], 'hgrn_norm': hgrn_norm[l],
              'gdn_conv_w': gdn_conv_w[l], 'gdn_a_log': gdn_a_log[l], 'gdn_dt_bias': gdn_dt_bias[l],
              'gdn_norm': gdn_norm[l], 'n_x_pre': n_x_pre[l], 'n_x_post': n_x_post[l], 'w_xq': w_xq[l],
              'w_xo': w_xo[l], 'n_f_pre': n_f_pre[l], 'n_f_post': n_f_post[l], 'w_gu': w_gu[l],
              'w_down': w_down[l]}
        mk, mv = memory_kv(mem_prompt, mem_norm[l], w_xkv[l])
        yp, st_p = hybrid_layer(
            yp, functools.partial(moba_prompt, slopes), mk, mv,
            jnp.zeros((bp, CONV_W - 1, SSM_CONV_DIM), f32),
            jnp.zeros((bp, SSM_HEADS, SSM_HEADDIM, SSM_DSTATE), f32),
            jnp.zeros((bp, HGRN_HEADS, HGRN_DK, HGRN_DV), f32),
            jnp.zeros((bp, CONV_W - 1, GDN_CONV_DIM), f32),
            jnp.zeros((bp, GDN_HEADS, GDN_DK, GDN_DV), f32),
            lb_all[l], lp)
        outs_p.append(st_p)
        mem_ks.append(mk)
        mem_vs.append(mv)
        ys, st_s = hybrid_layer(
            ys, functools.partial(moba_sample, cache_moba_k, cache_moba_v, l, page_table, slopes),
            cache_mem_k[l], cache_mem_v[l], state_ssm_conv[l], state_ssm[l], state_hgrn[l],
            state_gdn_conv[l], state_gdn[l], lb_all[l], lp)
        outs_s.append(st_s)
    moba_k_prompt = stack_field(outs_p, 0)
    moba_v_prompt = stack_field(outs_p, 1)
    moba_k_sample = stack_field(outs_s, 0)
    moba_v_sample = stack_field(outs_s, 1)
    mem_k_prompt = jnp.stack(mem_ks, axis=0)
    mem_v_prompt = jnp.stack(mem_vs, axis=0)
    ssm_conv_prompt = stack_field(outs_p, 2)
    ssm_conv_sample = stack_field(outs_s, 2)
    ssm_prompt = stack_field(outs_p, 3)
    ssm_sample = stack_field(outs_s, 3)
    hgrn_prompt = stack_field(outs_p, 4)
    hgrn_sample = stack_field(outs_s, 4)
    gdn_conv_prompt = stack_field(outs_p, 5)
    gdn_conv_sample = stack_field(outs_s, 5)
    gdn_prompt = stack_field(outs_p, 6)
    gdn_sample = stack_field(outs_s, 6)
    return (yp, ys, moba_k_prompt, moba_k_sample, moba_v_prompt, moba_v_sample, mem_k_prompt, mem_v_prompt,
            ssm_conv_prompt, ssm_conv_sample, ssm_prompt, ssm_sample, hgrn_prompt, hgrn_sample,
            gdn_conv_prompt, gdn_conv_sample, gdn_prompt, gdn_sample)


_drawn_inputs = setup_inputs


def setup_inputs(seed=0):
    import zlib

    import numpy as np

    out = dict(_drawn_inputs(seed))
    spreads = {}
    factors = {'ssm_d': 8.0, 'hgrn_norm': 2.856, 'gdn_norm': 3.15}
    for name, (base, spread) in spreads.items():
        noise = np.random.default_rng([zlib.crc32(name.encode()), seed]).standard_normal(out[name].shape)
        drawn = base * np.exp(spread * noise) if base else spread * noise
        out[name] = jnp.asarray(drawn.astype(out[name].dtype))
    for name, factor in factors.items():
        out[name] = (out[name] * factor).astype(out[name].dtype)
    return out
```

```python
from contextlib import ExitStack

import concourse.bass as bass
from concourse import mybir

F32 = mybir.dt.float32
I32 = mybir.dt.int32
ALU = mybir.AluOpType
ACT = mybir.ActivationFunctionType
AXX = mybir.AxisListType.X

P = 128
D = 1024
KD = D // P
SEQ = 512
NB, TS = 8, 4
NS = NB * TS
T = SEQ + NS
HT = T // 2
GW = D // 4
H = 4
DH = GW // H
PAGE, NPAGE = 128, 16
MOBA_BLOCK = 256
NBLK = PAGE * NPAGE // MOBA_BLOCK
PAST = PAGE * NPAGE
MEM = 256
XDH = D // H
FF = 2816
KF = FF // P
NEG = -1.0e30
EPS = 1e-6
SCALE = DH ** -0.5
XSCALE = XDH ** -0.5
SLOPE = [2.0 ** (-8.0 * (h + 1) / H) for h in range(H)]

C_MQ, C_MK, C_MV, C_Z, C_XBC, C_HQ, C_HF, C_HI, C_HG, C_GQKV, C_GZ = 0, 2, 4, 6, 8, 14, 16, 18, 20, 22, 28
NPROJ = 30
WIN_COLS = [0, 256, 512, 768, 1024, 1280, 1536, 1796, 2052, 2308, 2564, 2820, 3076, 3332, 3588]
COL_DT, COL_B, COL_A = 1792, 3844, 3848

TILES = [(i * P, P, 7) for i in range(SEQ // P)] + [(SEQ, NS, 2)]
NT = len(TILES)

R_MIXPRE, R_MIXPOST, R_XPRE, R_XPOST, R_MEM, R_FPRE, R_FPOST = [8 * i for i in range(7)]
R_SCW, R_GCW, R_SCB, R_SNORM, R_HNORM, R_GNORM, R_SD = 56, 80, 104, 110, 112, 113, 114
NROWS = 116


def build(nc, a, o):
    ctx = ExitStack()
    sems = {}

    STAGES = ["inputs", "mixpre", "win", "moba_prompt", "moba_sample", "rows", "ssm", "hgrn", "gdn", "wout", "mixpost",
              "mem", "xpre", "xq", "cross_prompt", "cross_sample", "wxo", "xpost", "fpre", "ff", "wdn", "fpost", "result"]

    def S(name):
        if name not in sems:
            sems[name] = ctx.enter_context(nc.semaphore(name))
        return sems[name]

    with ctx:
        def sb(name, shape, dt=F32):
            return ctx.enter_context(nc.sbuf_tensor(name, shape, dt))

        XT = sb("XT", [P, KD, T])
        XN = sb("XN", [P, KD * T])
        OM = sb("OM", [P, KD, T])
        PROJ = sb("PROJ", [P, NPROJ * T])
        NW, WSZ = 4, 8 * 256
        W = sb("W", [P, NW, WSZ])
        SC = sb("SC", [P, 9200])
        CN = sb("CN", [P, 2900])
        SM = sb("SM", [P, 400])
        PTAB = sb("PTAB", [1, P], I32)
        PS = [ctx.enter_context(nc.psum_tensor(f"PS{i}", [P, 2, 512], F32)) for i in range(4)]

        def bank(i):
            return PS[i // 2][:, i % 2, :]

        def pair(i):
            return PS[i][:, :, 0:HT]

        def carve(buf, at, *shape):
            n = 1
            for s in shape:
                n *= s
            v = buf[:, at:at + n]
            if len(shape) == 2:
                v = v.rearrange("p (a b) -> p a b", b=shape[1])
            elif len(shape) == 3:
                v = v.rearrange("p (a b c) -> p a b c", b=shape[1], c=shape[2])
            return v

        class Carver:
            def __init__(self, buf, at=0, size=None):
                self.buf, self.at = buf, at

            def __call__(self, *shape):
                v = carve(self.buf, self.at, *shape)
                n = 1
                for s in shape:
                    n *= s
                self.at += n
                assert self.at <= self.buf.shape[1], (self.at, self.buf.shape)
                return v

        proj = PROJ[:, :].rearrange("p (c t) -> p c t", t=T)
        xn = XN[:, :].rearrange("p (c t) -> p c t", t=T)

        c = Carver(CN)
        ident = c(P)
        ones = c(P)
        blk64 = c(P)
        lev = c(8, P)
        negmask = c(P)
        negmask_s = c(NS)
        ind = c(NB)
        keep = c(T)
        onehot = c(H, P)
        pairsel = c(2, P)
        eps = c(1)
        prm = SM[:, 0:NROWS]
        sm = Carver(SM, NROWS)
        head4 = sm(8)

        def par(r):
            return prm[:, r:r + 1]

        chunks = []

        def add(w, k0, nk, c0, sem, count):
            src = w.rearrange("(k p) n -> p k n", p=P)[:, k0:k0 + nk, c0:c0 + 256]
            chunks.append((src, nk, sem, count))

        win = a["w_in"][0]
        first = {}

        def section(name):
            first[name] = len(chunks)

        BEFORE = {"wout": NPROJ + 3, "wkv": 0, "wxq": NPROJ + 3 + KD, "wxo": NPROJ + 3 + 2 * KD, "wdn": NPROJ + 3 + 3 * KD}
        section("win")
        for i, c0 in enumerate(WIN_COLS):
            add(win, 0, 8, c0, "gemm_mm", 2 * i + 2)
        for name, src in (("wout", a["w_out"][0]), ("wkv", a["w_xkv"][0]), ("wxq", a["w_xq"][0]), ("wxo", a["w_xo"][0])):
            section(name)
            for i in range(src.shape[1] // 256):
                add(src, 0, 8, 256 * i, "kvm_mm" if name == "wkv" else "gemm_mm", BEFORE[name] + 2 * i + 2)
        section("wgu")
        for i in range(KF // 2):
            add(a["w_gu"][0], 0, 8, 256 * i, "ff_mm", 4 * i + 3)
            add(a["w_gu"][0], 0, 8, FF + 256 * i, "ff_mm", 4 * i + 4)
        section("wdn")
        for i in range(4):
            add(a["w_down"][0], 0, 8, 256 * i, "gemm_part", 2 * i + 1)
            add(a["w_down"][0], 8, 8, 256 * i, "gemm_part", 2 * i + 2)
            add(a["w_down"][0], 16, 6, 256 * i, "gemm_mm", BEFORE["wdn"] + 2 * i + 2)

        def load_chunks(eng, n0, n1):
            for n in range(n0, n1):
                src, nk, _, _ = chunks[n]
                if n >= NW:
                    eng.wait_ge(S(chunks[n - NW][2]), chunks[n - NW][3])
                eng.dma_start(W[:, n % NW, 0:nk * 256].rearrange("p (k n) -> p k n", n=256), src)\
                   .then_inc(S(f"weights_in{n % NW}"), 16)

        def weights(eng, n):
            nk = chunks[n][1]
            eng.wait_ge(S(f"weights_in{n % NW}"), 16 * (n // NW + 1))
            return W[:, n % NW, 0:nk * 256].rearrange("p (k n) -> p k n", n=256)

        def mm(out, lhsT, rhs, start, stop):
            return nc.tensor.matmul(out, lhsT, rhs, start=start, stop=stop, skip_group_check=True)

        def tr(out, in_, k):
            return nc.tensor.transpose(out, in_, ident[0:k, 0:k])

        links = {"v": 0, "s": 0, "g": 0}
        chain_eng = {"v": nc.vector, "s": nc.scalar, "g": nc.gpsimd}
        chain_name = {"v": "vector_chain", "s": "scalar_chain", "g": "gpsimd_chain"}

        def link(ins, e="v"):
            links[e] += 1
            ins.then_inc(S(chain_name[e]), 1)
            chain_eng[e].wait_ge(S(chain_name[e]), links[e])

        def after(eng, name):
            eng.wait_ge(S("stage_ended"), 3 * (STAGES.index(name) + 1))

        V, A, G = nc.vector, nc.scalar, nc.gpsimd

        cumtok = sm(NT, 8)
        rsq = sb("RSQ", [P, T])
        ups = sb("UPS", [P, 12, NB, 7])
        w_small = sb("WSMALL", [P, 3, KD, H])

        x_tok = carve(PROJ, 0, 4, D)
        xs_tok = carve(PROJ, 4 * D, D)
        rows_in = carve(PROJ, 5 * D, P)
        cs_tok = carve(PROJ, 6 * D, 2, 768)
        raw = OM[0:H, 5:8, :]
        m = Carver(SC)
        kvs = m(2 * GW)
        kvtok = m(4, 2 * GW)
        mp_s = m(4, SEQ)
        mp_pt = m(2, SEQ)
        mp_stat = m(3, 16)
        mp_bias = carve(XN, 0, H, SEQ)
        m = Carver(SC, 2 * GW)
        NPG = 4
        pages = m(NPG, 4, 2 * P)
        ms_kt = m(2, 512)
        ms_q = m(2, P)
        st_all = m(NPAGE, P)
        ms_pown = m(P)
        ms_gate = m(8)
        ms_gt = m(8, 8)
        ms_eq = m(8, 8)
        ms_rank = m(8)
        ms_sel = m(8)
        ms_stat = m(4)
        ms_s = carve(XN, 0, PAST + NS)
        ms_bias = carve(XN, PAST + NS, PAST + NS)
        mr = sm(1)
        tr_ = sm(1)
        g8 = sm(NB)
        cr = sm(1)
        ltm = sm(8, 8)
        xc = carve(SC, 0, 6, T)
        pb = carve(PROJ, 0, 3, 2, T)
        rows = XN[0:H, 0:4 * T].rearrange("p (c t) -> p c t", t=T)
        rtmp = XN[0:H, 4 * T:8 * T].rearrange("p (c t) -> p c t", t=T)
        m = Carver(SC, 6 * T)
        xdt = m(2, T)
        s_m = m(H, P)
        s_er = m(H, P)
        s_c = m(H, P)
        s_tok = m(512)
        s_xd = m(2 * P)
        s_ht = m(2 * P)
        s_h0t = m(NB, 2 * P)
        s_dl = m(H)
        s_h0 = carve(XN, 4 * T, NB, 2, P)
        s_dec = sm(2, NB)
        m = Carver(SC)
        h_b = m(2, T)
        h_k = m(2, T)
        h_d = m(2, T)
        h_q1 = m(2, 2, T)
        h_k1 = m(2, 2, T)
        h_att = carve(PROJ, C_Z * T, 4 * 512 + H * NS)
        h_msk = carve(PROJ, C_Z * T + 2176, 4 * 512)
        m = Carver(SC, 6 * T)
        g_kb = m(2, T)
        g_kbg = m(2, T)
        g_qg = m(2, T)
        g_p1 = m(4, 512)
        base = C_Z * T
        g_T = carve(PROJ, base, 2176)
        g_N = carve(PROJ, base + 2176, 2176)
        g_A = carve(PROJ, base + 2 * 2176, 2176)
        g_QK = carve(PROJ, base + 3 * 2176, 2176)
        g_sq = carve(PROJ, C_HQ * T, 4, T)
        m = Carver(XN, 4 * T)
        t_tok = m(512)
        t_vn = m(2 * P)
        t_st = m(2, DH)
        t_last = m(2, NB)
        t_s0 = m(NB, 2, DH)
        t_kd = carve(PROJ, C_GQKV * T, 2, T)
        t_vm = carve(PROJ, (C_GQKV + 2) * T, H * NB * DH)
        memt = carve(SC, 0, KD, MEM)
        memn = carve(SC, KD * MEM, KD, MEM)
        mkv = carve(PROJ, 0, 2, 2 * D)
        mkt = carve(PROJ, 4 * D, KD, MEM)
        xq = carve(PROJ, 6 * D, KD, T)
        m = Carver(SC)
        cx_s = m(4, MEM)
        cx_pt = m(2, 2, SEQ)
        cx_stat = m(3, 16)
        cx_st = m(2, P)
        cx_ss = m(MEM)
        cx_pts = m(2, P)
        cx_kt = m(2, 8 * P)
        cx_ring = carve(PROJ, 6 * D + KD * T, 2, 2 * D)
        hT = PROJ[:, 0:KF * T].rearrange("p (c t) -> p c t", t=T)
        f_g = carve(SC, 0, 4, T)
        y_tok = carve(PROJ, 0, 5, D)

        block = ctx.enter_context(nc.Block())

        @block.sync
        def _(sp):
            def ld(dst, src, name):
                sp.dma_start(dst, src).then_inc(S(name), 16)

            for i in range(4):
                ld(x_tok[:, i, :], a["x_prompt"][0, i * P:(i + 1) * P, :], "x_in")
            ld(xs_tok[0:NS, :], a["x_sample"].rearrange("b t d -> (b t) d"), "params_in")
            for r, n in ((R_MIXPRE, "n_mix_pre"), (R_MIXPOST, "n_mix_post"), (R_XPRE, "n_x_pre"),
                         (R_XPOST, "n_x_post"), (R_MEM, "mem_norm"), (R_FPRE, "n_f_pre"), (R_FPOST, "n_f_post")):
                ld(rows_in[r:r + 8, :], a[n].rearrange("o (k p) -> (o k) p", p=P), "params_in")
            for w in range(4):
                ld(rows_in[R_SCW + 6 * w:R_SCW + 6 * w + 6, :], a["ssm_conv_w"][0, w].rearrange("(k p) -> k p", p=P), "params_in")
                ld(rows_in[R_GCW + 6 * w:R_GCW + 6 * w + 6, :], a["gdn_conv_w"][0, w].rearrange("(k p) -> k p", p=P), "params_in")
            ld(rows_in[R_SCB:R_SCB + 6, :], a["ssm_conv_b"].rearrange("o (k p) -> (o k) p", p=P), "params_in")
            ld(rows_in[R_SNORM:R_SNORM + 2, :], a["ssm_norm"].rearrange("o (k p) -> (o k) p", p=P), "params_in")
            for i in range(2):
                ld(rows_in[R_HNORM:R_HNORM + 1, i * DH:(i + 1) * DH], a["hgrn_norm"], "params_in")
                ld(rows_in[R_GNORM:R_GNORM + 1, i * DH:(i + 1) * DH], a["gdn_norm"], "params_in")
                for j in range(2):
                    ld(rows_in[R_SD + i:R_SD + i + 1, j * DH:(j + 1) * DH].rearrange("r (d o) -> r d o", o=1),
                       a["ssm_d"][:, 2 * i + j:2 * i + j + 1].rearrange("r (d o) -> r d o", o=1).to_broadcast((1, DH, 1)),
                       "params_in")
            for i, n in enumerate(("ssm_a_log", "ssm_dt_bias", "gdn_a_log", "gdn_dt_bias")):
                ld(head4[0:H, i:i + 1], a[n].rearrange("o h -> h o"), "params_in")
            ld(cs_tok[0:24, 0, :], a["state_ssm_conv"][0].rearrange("b w c -> (b w) c"), "params_in")
            ld(cs_tok[0:24, 1, :], a["state_gdn_conv"][0].rearrange("b w c -> (b w) c"), "params_in")
            ld(PTAB[0:1, :], a["page_table"].rearrange("b n -> (b n)").rearrange("(o n) -> o n", o=1), "pages_in")
            for i, c0 in enumerate((COL_DT, COL_B, COL_A)):
                ld(w_small[:, i, :, :], win.rearrange("(k p) n -> p k n", p=P)[:, :, c0:c0 + H], "params_in")
            load_chunks(sp, 0, first["wout"])
            sp.wait_ge(S("pages_in"), 16)
            after(sp, "moba_prompt")
            sp.wait_ge(S("moba_kv_out"), 16 * 10)
            for n in range(64):
                cache = a["cache_moba_k"] if n < 32 else a["cache_moba_v"]
                m_ = n - NPG
                if 0 <= m_ < 32:
                    sp.wait_ge(S("satt_turned"), 2 * m_ + 2)
                elif m_ >= 32:
                    sp.wait_ge(S("ms_values_used"), m_ - 31)
                for i in range(4):
                    page = sp.value_load(PTAB[0:1, (n % 32) * 4 + i:(n % 32) * 4 + i + 1], min_val=0,
                                         max_val=a["cache_moba_k"].shape[1] - 1)
                    sp.dma_start(pages[:, n % NPG, i, :],
                                 cache[0].rearrange("g p h d -> g p (h d)")[bass.ds(page, 1)].rearrange("g p n -> (g p) n"))\
                      .then_inc(S(f"pages{n % NPG}_in"), 16)
            after(sp, "rows")
            sp.dma_start(s_h0, a["state_ssm"][0].rearrange("b (c e) q n -> (e q) b c n", e=2)).then_inc(S("state_in"), 16)
            after(sp, "ssm")
            sp.wait_ge(S("states_out"), 32)
            sp.dma_start(t_s0, a["state_hgrn"][0].rearrange("b (c e) k v -> (e k) b c v", e=2)).then_inc(S("state_in"), 16)
            sp.wait_ge(S("g_inverted"), 1)
            sp.dma_start(t_s0, a["state_gdn"][0].rearrange("b (c e) k v -> (e k) b c v", e=2)).then_inc(S("state_in"), 16)
            load_chunks(sp, first["wout"], first["wkv"])
            after(sp, "mixpost")
            for i in range(2):
                ld(mkv[:, i, 0:D], a["mem_prompt"][0, i * P:(i + 1) * P, :], "mem_in")
            load_chunks(sp, first["wkv"], first["wxo"])
            after(sp, "xq")
            for n in range(16):
                src = a["cache_mem_k"] if n < 8 else a["cache_mem_v"]
                if n >= 2:
                    if n < 10:
                        sp.wait_ge(S("satt_turned"), 64 + 4 * (n - 1))
                    else:
                        sp.wait_ge(S("satt_pv"), 1 + n - 9)
                sp.dma_start(cx_ring[:, n % 2, :].rearrange("p (i n) -> p i n", n=D),
                             src[0, n % 8].rearrange("(i p) h d -> p i (h d)", p=P)).then_inc(S(f"cx_ring{n % 2}_in"), 16)
            load_chunks(sp, first["wxo"], len(chunks))

        def fill(view, pattern, base, mult, op, fillv):
            return G.affine_select(out=view, in_=view, compare_op=op, fill=fillv, base=base, pattern=pattern,
                                   channel_multiplier=mult)

        def g_constants(g):
            L = lambda ins: link(ins, "g")
            L(G.memset(CN[:, :], 0.0))
            L(G.memset(ones, 1.0))
            L(G.memset(keep, 1.0))
            L(G.memset(eps, EPS))
            L(G.memset(blk64[0:64, 0:64], 1.0))
            L(G.memset(blk64[64:128, 64:128], 1.0))
            L(fill(ident, [[-1, P]], 0, 1, ALU.not_equal, 1.0))
            L(G.memset(lev[:, 0, :], 0.0))
            L(fill(lev[:, 0, :], [[-1, P]], 0, 1, ALU.not_equal, 1.0))
            for j in range(1, 8):
                B = 1 << j
                r = lev[:, j, :].rearrange("p (n i) -> p n i", i=B)[:, :, B // 2:B]
                L(G.memset(r, 1.0))
                L(fill(r, [[-B, P // B], [0, B // 2]], 0, 1, ALU.is_ge, 0.0))
                L(fill(r, [[B, P // B], [0, B // 2]], B // 2 - 1, -1, ALU.is_ge, 0.0))
            L(fill(negmask, [[1, P]], 0, -1, ALU.is_ge, NEG))
            L(fill(negmask_s[0:NS, :], [[1, NS]], 0, -1, ALU.is_ge, NEG))
            v = negmask_s[0:NS, :].rearrange("p (b t) -> p b t", t=TS)
            L(fill(v, [[-TS, NB], [0, TS]], 0, 1, ALU.is_ge, NEG))
            L(G.memset(ind, 1.0))
            L(fill(ind, [[-TS, NB]], 0, 1, ALU.is_ge, 0.0))
            L(fill(ind, [[TS, NB]], TS - 1, -1, ALU.is_ge, 0.0))
            L(G.memset(keep[:, 0:SEQ].rearrange("p (n i) -> p n i", i=P)[:, :, 0:1], 0.0))
            L(G.memset(keep[:, SEQ:T].rearrange("p (n i) -> p n i", i=TS)[:, :, 0:1], 0.0))
            L(G.memset(onehot, 1.0))
            L(fill(onehot, [[-1, H], [0, P]], 0, 1, ALU.is_equal, 0.0))
            ps = pairsel.rearrange("p c (e d) -> p c e d", e=2)
            L(G.memset(pairsel, 1.0))
            L(fill(ps, [[-2, 2], [-1, 2], [0, DH]], 0, 1, ALU.is_equal, 0.0))
            L(G.memset(g8, 1.0))
            L(fill(g8, [[-16, NB]], 0, 1, ALU.is_ge, 0.0))
            L(fill(g8, [[16, NB]], 15, -1, ALU.is_ge, 0.0))
            L(G.memset(ltm, 1.0))
            G.affine_select(out=ltm, in_=ltm, compare_op=ALU.is_gt, fill=0.0, base=0, pattern=[[1, 8], [-1, 8]],
                            channel_multiplier=0).then_inc(S("consts"), 1)
            g.wait_ge(S("consts"), 1)

        ms_grp = XN[:, 2 * (PAST + NS):2 * (PAST + NS) + 96]
        ms_int = XN[:, 2 * (PAST + NS) + 96:2 * (PAST + NS) + 128].bitcast(I32)

        def g_moba_prompt_table(g):
            L = lambda ins: link(ins, "g")
            it = mp_s.rearrange("p a b -> p (a b)")[:, 0:SEQ].bitcast(I32)
            after(g, "win")
            L(G.iota(it, pattern=[[1, SEQ]], base=-384, channel_multiplier=-1))
            L(G.tensor_copy(mp_bias[:, 0, :], it))
            for h in range(H - 1, -1, -1):
                L(G.tensor_scalar(mp_bias[:, h, :], mp_bias[:, 0, :], SLOPE[h], None, ALU.mult))
            for h in range(H):
                L(fill(mp_bias[:, h, :], [[-1, SEQ]], 384, 1, ALU.is_ge, NEG))
            g.drain().then_inc(S("mp_tables"), 1)

        def g_moba_sample_table(g):
            L = lambda ins: link(ins, "g")
            after(g, "moba_prompt")
            grp, slope, gi = ms_grp[:, 0:32], ms_grp[:, 32:64], ms_grp[:, 64:96]
            L(G.memset(grp, 1.0))
            L(fill(grp, [[-4, 32]], 0, 1, ALU.is_ge, 0.0))
            L(fill(grp, [[4, 32]], 3, -1, ALU.is_ge, 0.0))
            for h in range(H):
                L(G.memset(slope.rearrange("p (b h) -> p b h", h=H)[:, :, h:h + 1], SLOPE[h]))
            L(G.iota(ms_int, pattern=[[-4, 32]], base=0, channel_multiplier=1))
            L(G.tensor_copy(gi, ms_int))
            L(G.tensor_tensor(slope, slope, grp, ALU.mult))
            L(G.tensor_tensor(gi, gi, grp, ALU.mult))
            L(G.iota(ms_s[:, 0:PAST].bitcast(I32), pattern=[[1, PAST]], base=-PAST, channel_multiplier=0))
            L(G.tensor_copy(ms_bias[:, 0:PAST], ms_s[:, 0:PAST].bitcast(I32)))
            L(G.iota(ms_s[:, 0:NS].bitcast(I32), pattern=[[0, NB], [1, TS]], base=0, channel_multiplier=0))
            L(G.tensor_copy(ms_bias[:, PAST:PAST + NS], ms_s[:, 0:NS].bitcast(I32)))
            g.drain().then_inc(S("ms_tables"), 1)

        def tt(out, x, y, op):
            return V.tensor_tensor(out, x, y, op)

        def bc(ap, shape):
            return ap.to_broadcast(shape)

        def norm_tensor(pe, name, sq, n):
            for k in range(KD):
                pe.wait_ge(S("norm_sq_s" if k % 2 == 0 else "norm_sq_v"), 4 * NPE[0] + k // 2 + 1)
                for j in range(2):
                    last = mm(bank(6 + j)[:, 0:n // 2], ones, sq[:, k, j * n // 2:(j + 1) * n // 2], k == 0, k == KD - 1)
            last.then_inc(S("norm_sum"), 1)
            NPE[0] += 1

        def norm_scalar(s, src, sq, n):
            for k in range(0, KD, 2):
                A.activation(sq[:, k, :], src[:, k, :], ACT.Square).then_inc(S("norm_sq_s"), 1)
            s.wait_ge(S("norm_sum"), NSC[0] + 1)
            A.activation(rsq[:, 0:n].rearrange("p (j t) -> p j t", j=2), PS[3][:, :, 0:n // 2], ACT.Sqrt,
                         bias=eps, scale=1.0 / D).then_inc(S("norm_root"), 1)
            NSC[0] += 1

        def norm_vector(v, src, sq, n, gain, dst, add=None):
            for k in range(1, KD, 2):
                tt(sq[:, k, :], src[:, k, :], src[:, k, :], ALU.mult).then_inc(S("norm_sq_v"), 1)
            v.wait_ge(S("norm_root"), NVE[0] + 1)
            NVE[0] += 1
            link(V.reciprocal(rsq[:, 0:n], rsq[:, 0:n]))
            for k in range(KD):
                last = V.scalar_tensor_tensor(dst[:, k, :], src[:, k, :], par(gain + k), rsq[:, 0:n], ALU.mult, ALU.mult)
                if add is not None:
                    link(last)
                    last = tt(add[:, k, :], add[:, k, :], dst[:, k, :], ALU.add)
            link(last)

        NPE, NSC, NVE = [0], [0], [0]

        GEMM_NAMES = ("win", "wout", "wxq", "wxo", "wdn")
        GEMM_MM = dict(zip(GEMM_NAMES, (0, NPROJ + 3, NPROJ + 3 + KD, NPROJ + 3 + 2 * KD, NPROJ + 3 + 3 * KD)))
        GEMM_OUT = {n: (0 if n == "win" else (NPROJ + (GEMM_NAMES.index(n) - 1) * KD) // 2) for n in GEMM_NAMES}

        def gemm_tensor(pe, name, n0, ntile, rhs, nparts=1):
            for i in range(0, ntile, 2):
                k0 = 0
                for part in range(nparts):
                    w = weights(pe, n0 + (i // 2) * nparts + part)
                    nk = w.shape[1]
                    for e in range(2):
                        if i + e >= 4 and part == 0:
                            pe.wait_ge(S("gemm_out_s" if e == 0 else "gemm_out_v"), GEMM_OUT[name] + (i - 4) // 2 + 1)
                        for k in range(nk):
                            for j in range(2):
                                last = mm(PS[(i + e) % 4][:, j, 0:HT], w[:, k, e * P:(e + 1) * P],
                                          rhs(k0 + k)[:, j * HT:(j + 1) * HT], part == 0 and k == 0,
                                          part == nparts - 1 and k == nk - 1)
                        if part == nparts - 1:
                            last.then_inc(S("gemm_mm"), 1)
                        elif e == 1:
                            last.then_inc(S("gemm_part"), 1)
                    k0 += nk

        def halves(ap):
            return ap.rearrange("p (j t) -> p j t", j=2)

        def gemm_scalar(s, name, ntile, dst):
            for i in range(0, ntile, 2):
                s.wait_ge(S("gemm_mm"), GEMM_MM[name] + i + 1)
                A.activation(halves(dst(i)), pair(i % 4), ACT.Copy).then_inc(S("gemm_out_s"), 1)

        def gemm_vector(v, name, ntile, dst):
            for i in range(1, ntile, 2):
                v.wait_ge(S("gemm_mm"), GEMM_MM[name] + i + 1)
                V.tensor_copy(halves(dst(i)), pair(i % 4)).then_inc(S("gemm_out_v"), 1)

        def inputs_tensor(pe):
            pe.wait_ge(S("consts"), 1)
            pe.wait_ge(S("params_in"), 16 * 35)
            tr(bank(0)[:, 0:NROWS], rows_in[0:NROWS, :], NROWS).then_inc(S("turned"), 1)
            for i in range(12):
                last = tr(bank(1)[:, i * 24:(i + 1) * 24], cs_tok[0:24, i // 6, (i % 6) * P:(i % 6 + 1) * P], 24)
            last.then_inc(S("turned"), 1)
            for i in range(4):
                pe.wait_ge(S("x_in"), 64)
                for hf in range(2):
                    job = 2 + 2 * i + hf
                    if job >= 8:
                        pe.wait_ge(S("turned_out_v" if job % 2 == 0 else "turned_out_s"), 1)
                    for k in range(4):
                        last = tr(bank(job % 8)[:, k * P:(k + 1) * P], x_tok[:, i, (4 * hf + k) * P:(4 * hf + k + 1) * P], P)
                    last.then_inc(S("turned"), 1)
            pe.wait_ge(S("turned_out_v"), 2)
            for k in range(8):
                last = tr(bank(2)[:, k * NS:(k + 1) * NS], xs_tok[0:NS, k * P:(k + 1) * P], NS)
            last.then_inc(S("turned"), 1)

        def inputs_evac(e, eng, copy, name, par_):
            for job in range(par_, 11, 2):
                eng.wait_ge(S("turned"), job + 1)
                if job == 0:
                    i = copy(prm, bank(0)[:, 0:NROWS])
                elif job == 1:
                    i = copy(ups[:, :, :, 0:3], bank(1)[:, 0:288].rearrange("p (c b w) -> p c b w", b=NB, w=3))
                elif job < 10:
                    i, hf = divmod(job - 2, 2)
                    i = copy(XT[:, 4 * hf:4 * hf + 4, i * P:(i + 1) * P], bank(job % 8).rearrange("p (k t) -> p k t", t=P))
                else:
                    i = copy(XT[:, :, SEQ:T], bank(2)[:, 0:8 * NS].rearrange("p (k t) -> p k t", t=NS))
                i.then_inc(S(name), 1)

        def vcopy(o_, i_):
            return V.tensor_copy(o_, i_)

        def scopy(o_, i_):
            return A.activation(o_, i_, ACT.Copy)

        def win_tensor(pe):
            gemm_tensor(pe, "win", 0, NPROJ, lambda k: xn[:, k, :])
            for i in range(3):
                ii = NPROJ + i
                pe.wait_ge(S("gemm_out_s" if ii % 2 == 0 else "gemm_out_v"), (ii - 4) // 2 + 1)
                for k in range(KD):
                    for j in range(2):
                        last = mm(PS[ii % 4][0:H, j, 0:HT], w_small[:, i, k, :], xn[:, k, j * HT:(j + 1) * HT], k == 0, k == KD - 1)
                last.then_inc(S("gemm_mm"), 1)

        def win_small_vector(v):
            for i in range(3):
                v.wait_ge(S("gemm_mm"), NPROJ + i + 1)
                link(V.tensor_copy(halves(raw[:, i, :]), PS[(NPROJ + i) % 4][0:H, :, 0:HT]))

        def kv_tensor(pe):
            for i, (t0, w, _) in enumerate(TILES):
                for k in range(4):
                    last = tr(bank(i)[0:w, k * P:(k + 1) * P], proj[:, C_MK + k, t0:t0 + w], P)
                last.then_inc(S("kv_turned"), 1)

        def kv_vector(v):
            for i, (t0, w, _) in enumerate(TILES):
                v.wait_ge(S("kv_turned"), i + 1)
                dst = kvtok[:, i, :] if i < 4 else kvs[0:NS, :]
                V.tensor_copy(dst, bank(i)[0:w, :]).then_inc(S("kv_out"), 1)

        def mp_scores(pe, j):
            i, h = divmod(j, H)
            if j >= 4:
                pe.wait_ge(S("mp_biased"), j - 3)
            r = slice((h % 2) * 64, (h % 2) * 64 + 64)
            nk = (i + 1) * P
            mm(bank(j % 4)[:, 0:nk], proj[r, C_MQ + h // 2, i * P:(i + 1) * P], proj[r, C_MK + h // 2, 0:nk], True, True)\
                .then_inc(S("att_scores"), 1)

        def mp_turn(pe, j):
            i = j // H
            pe.wait_ge(S("att_probs"), j + 1)
            if j >= 2:
                pe.wait_ge(S("att_pt"), j - 1)
            for k in range(i + 1):
                last = tr(bank(4 + j % 2)[:, k * P:(k + 1) * P], mp_s[:, j % 4, k * P:(k + 1) * P], P)
            last.then_inc(S("att_turned"), 1)

        def mp_pv(pe, j):
            i, h = divmod(j, H)
            pe.wait_ge(S("att_pt"), j + 1)
            if h == 0 and i >= 2:
                pe.wait_ge(S("att_out"), i - 1)
            for k in range(i + 1):
                last = mm(bank(6 + i % 2)[(h % 2) * 64:(h % 2) * 64 + 64, (h // 2) * P:(h // 2 + 1) * P],
                          kvtok[:, k, GW + h * DH:GW + (h + 1) * DH], mp_pt[:, j % 2, k * P:(k + 1) * P], k == 0, k == i)
            last.then_inc(S("att_pv"), 1)

        def moba_prompt_tensor(pe):
            kv_tensor(pe)
            pe.wait_ge(S("kv_out"), NT)
            mp_scores(pe, 0)
            mp_scores(pe, 1)
            for j in range(16):
                if j + 2 < 16:
                    mp_scores(pe, j + 2)
                mp_turn(pe, j)
                if j:
                    mp_pv(pe, j - 1)
            mp_pv(pe, 15)

        def moba_prompt_vector(v):
            kv_vector(v)
            v.wait_ge(S("mp_tables"), 1)

            def first_(j):
                i, h = divmod(j, H)
                nk = (i + 1) * P
                v.wait_ge(S("att_scores"), j + 1)
                if j >= 4:
                    v.wait_ge(S("att_turned"), j - 3)
                V.scalar_tensor_tensor(mp_s[:, j % 4, 0:nk], bank(j % 4)[:, 0:nk], SCALE, mp_bias[:, h, SEQ - nk:SEQ],
                                       ALU.mult, ALU.add).then_inc(S("mp_biased"), 1)
                v.wait_ge(S("mp_biased"), j + 1)
                V.tensor_reduce(mp_stat[:, 0, j:j + 1], mp_s[:, j % 4, 0:nk], AXX, ALU.max, negate=True)\
                    .then_inc(S("att_max"), 1)

            def second(j):
                nk = (j // H + 1) * P
                v.wait_ge(S("att_exp"), j + 1)
                link(V.reciprocal(mp_stat[:, 2, j:j + 1], mp_stat[:, 1, j:j + 1]))
                V.tensor_scalar(mp_s[:, j % 4, 0:nk], mp_s[:, j % 4, 0:nk], mp_stat[:, 2, j:j + 1], None, ALU.mult)\
                    .then_inc(S("att_probs"), 1)

            def out_(i):
                v.wait_ge(S("att_pv"), 4 * i + 4)
                V.tensor_copy(OM[:, 0:2, i * P:(i + 1) * P], bank(6 + i % 2)[:, 0:2 * P].rearrange("p (c t) -> p c t", t=P))\
                    .then_inc(S("att_out"), 1)

            first_(0)
            for j in range(16):
                if j + 1 < 16:
                    first_(j + 1)
                second(j)
                if j >= 4 and j % 4 == 1:
                    out_(j // 4 - 1)
            out_(3)

        def moba_prompt_scalar(s):
            def ex(j):
                nk = (j // H + 1) * P
                s.wait_ge(S("att_max"), j + 1)
                A.activation(mp_s[:, j % 4, 0:nk], mp_s[:, j % 4, 0:nk], ACT.Exp, bias=mp_stat[:, 0, j:j + 1],
                             accum_out=mp_stat[:, 1, j:j + 1]).then_inc(S("att_exp"), 1)

            ex(0)
            for j in range(16):
                if j + 1 < 16:
                    ex(j + 1)
                nk = (j // H + 1) * P
                s.wait_ge(S("att_turned"), j + 1)
                if j >= 2:
                    s.wait_ge(S("att_pv"), j - 1)
                A.activation(mp_pt[:, j % 2, 0:nk], bank(4 + j % 2)[:, 0:nk], ACT.Copy).then_inc(S("att_pt"), 1)

        def moba_sample_tensor(pe):
            def page_in(n):
                pe.wait_ge(S(f"pages{n % NPG}_in"), 64 * (n // NPG + 1))

            def turn(q):
                n, pp = divmod(q, 2)
                if pp == 0:
                    page_in(n)
                if q >= 2:
                    pe.wait_ge(S("keys_turned_s" if q % 2 == 0 else "keys_turned_v"), q // 2)
                for i in range(4):
                    last = tr(bank(q % 2)[:, i * P:(i + 1) * P], pages[:, n % NPG, 2 * pp + i // 2, (i % 2) * P:(i % 2 + 1) * P], P)
                last.then_inc(S("satt_turned"), 1)

            def score(q):
                b, pg = divmod(2 * q, NPAGE)
                pe.wait_ge(S("keys_turned_s" if q % 2 == 0 else "keys_turned_v"), q // 2 + 1)
                if pg == 0 and b >= 2:
                    pe.wait_ge(S("satt_st"), b - 1)
                for i in range(4):
                    last = mm(bank(2 + b % 2)[:, (pg + i // 2) * 16 + (i % 2) * 8:(pg + i // 2) * 16 + (i % 2) * 8 + 8],
                              ms_kt[:, q % 2, i * P:(i + 1) * P], ms_q[:, i % 2, b * 16 + (i % 2) * 8:b * 16 + (i % 2) * 8 + 8],
                              True, True)
                last.then_inc(S("satt_scored"), 1)

            pe.wait_ge(S("ms_q"), 1)
            turn(0)
            for q in range(1, 64):
                turn(q)
                score(q - 1)
            score(63)
            for c_ in range(2):
                last = mm(bank(0)[:, 0:NS], ms_q[:, c_, :], proj[:, C_MK + c_, SEQ:T], c_ == 0, c_ == 1)
            pe.wait_ge(S("satt_st"), NB)
            for i in range(NPAGE):
                last = tr(bank(4 + i // 4)[:, (i % 4) * P:(i % 4 + 1) * P], st_all[:, i, :], P)
            last.then_inc(S("satt_rows"), 1)
            pe.wait_ge(S("satt_probs"), 1)
            for i in range(NPAGE):
                last = tr(bank(i // 4)[:, (i % 4) * P:(i % 4 + 1) * P], ms_s[:, i * P:(i + 1) * P], P)
            last.then_inc(S("satt_pt"), 1)
            tr(bank(4)[0:NS, 0:P], ms_s[:, PAST:PAST + NS], P).then_inc(S("satt_pt"), 1)
            pe.wait_ge(S("satt_pt_out"), 2)
            for n in range(32, 64):
                b, qt = divmod(n - 32, 4)
                page_in(n)
                for i in range(4):
                    for c_ in range(2):
                        col = c_ * 64 + b * 8
                        last = mm(bank(5)[:, col:col + 8], pages[:, n % NPG, i, c_ * P:(c_ + 1) * P],
                           st_all[:, 4 * qt + i, b * 16 + c_ * 8:b * 16 + c_ * 8 + 8], n == 32 and i == 0 and c_ == 0, False)
                last.then_inc(S("ms_values_used"), 1)
            for c_ in range(2):
                last = mm(bank(5)[:, c_ * 64:(c_ + 1) * 64], kvs[0:NS, GW + c_ * P:GW + (c_ + 1) * P],
                          ms_pown[0:NS, :].rearrange("p (b c r) -> p c b r", c=2, r=8)[:, c_], False, c_ == 1)
            last.then_inc(S("satt_pv"), 1)

        def moba_sample_vector(v):
            v.wait_ge(S("ms_tables"), 1)
            sg = ms_grp
            link(V.reduce_sum(mr, sg[:, 32:64], AXX))
            link(V.reduce_sum(tr_, sg[:, 64:96], AXX))
            link(V.tensor_scalar(ms_bias[:, 0:PAST + NS], ms_bias[:, 0:PAST + NS], tr_, None, ALU.subtract))
            own = ms_bias[:, PAST:PAST + NS]
            ok = ms_s[:, 0:NS]
            link(V.tensor_scalar(ok, own, 0.0, None, ALU.is_le))
            link(tt(ok.rearrange("p (b t) -> p b t", t=TS), ok.rearrange("p (b t) -> p b t", t=TS),
                    bc(g8.rearrange("p (b t) -> p b t", t=1), (P, NB, TS)), ALU.mult))
            link(V.tensor_scalar(ok, ok, -1.0, -NEG, ALU.add, ALU.mult))
            link(V.tensor_scalar(ms_bias[:, 0:PAST + NS], ms_bias[:, 0:PAST + NS], mr, None, ALU.mult))
            link(tt(own, own, ok, ALU.add))
            link(V.memset(ms_q, 0.0))
            for h2 in range(2):
                for c_ in range(2):
                    r = slice(h2 * 64, h2 * 64 + 64)
                    dst = ms_q[r, c_, :].rearrange("p (b g t) -> p b g t", g=4, t=TS)[:, :, 2 * c_ + h2, :]
                    last = V.tensor_copy(dst, proj[r, C_MQ + c_, SEQ:T].rearrange("p (b t) -> p b t", t=TS))
            last.then_inc(S("ms_q"), 1)
            for b in range(NB):
                for q in range(8 * b, 8 * b + 8):
                    if q % 2:
                        v.wait_ge(S("satt_turned"), q + 1)
                        if q >= 2:
                            v.wait_ge(S("satt_scored"), q - 1)
                        V.tensor_copy(ms_kt[:, q % 2, :], bank(q % 2)).then_inc(S("keys_turned_v"), 1)
                if b:
                    ms_st_out(v, b - 1)
            ms_st_out(v, NB - 1)
            v.wait_ge(S("satt_rows"), 1)
            for i in range(4):
                link(V.tensor_reduce(ms_gate[:, 2 * i:2 * i + 2], bank(4 + i).rearrange("p (n k) -> p n k", k=MOBA_BLOCK), AXX, ALU.add))
            gm = bc(ms_gate.rearrange("p (o m) -> p o m", o=1), (P, 8, 8))
            gn = bc(ms_gate.rearrange("p (n o) -> p n o", o=1), (P, 8, 8))
            link(tt(ms_gt, gm, gn, ALU.is_gt))
            link(tt(ms_eq, gm, gn, ALU.is_equal))
            link(tt(ms_eq, ms_eq, ltm, ALU.mult))
            link(tt(ms_gt, ms_gt, ms_eq, ALU.add))
            link(V.tensor_reduce(ms_rank, ms_gt, AXX, ALU.add))
            link(V.tensor_scalar(ms_sel, ms_rank, 2.5, NEG, ALU.is_gt, ALU.mult))
            for i in range(4):
                sl = slice(i * 512, (i + 1) * 512)
                link(V.scalar_tensor_tensor(ms_s[:, sl], bank(4 + i), SCALE, ms_bias[:, sl], ALU.mult, ALU.add))
            s3 = ms_s[:, 0:PAST].rearrange("p (n k) -> p n k", k=MOBA_BLOCK)
            link(tt(s3, s3, bc(ms_sel.rearrange("p (n o) -> p n o", o=1), (P, 8, MOBA_BLOCK)), ALU.add))
            link(V.scalar_tensor_tensor(ms_s[:, PAST:PAST + NS], bank(0)[:, 0:NS], SCALE, ms_bias[:, PAST:PAST + NS], ALU.mult, ALU.add))
            V.tensor_reduce(ms_stat[:, 0:1], ms_s[:, :], AXX, ALU.max, negate=True).then_inc(S("satt_max"), 1)
            v.wait_ge(S("satt_exp"), 1)
            link(V.reciprocal(ms_stat[:, 2:3], ms_stat[:, 1:2]))
            V.tensor_scalar(ms_s[:, :], ms_s[:, :], ms_stat[:, 2:3], None, ALU.mult).then_inc(S("satt_probs"), 1)
            v.wait_ge(S("satt_pt"), 1)
            for i in range(2):
                link(V.tensor_copy(st_all[:, 4 * i:4 * i + 4, :], bank(i).rearrange("p (n k) -> p n k", k=P)))
            v.wait_ge(S("satt_pt"), 2)
            V.tensor_copy(ms_pown[0:NS, :], bank(4)[0:NS, 0:P]).then_inc(S("satt_pt_out"), 1)
            v.wait_ge(S("satt_pv"), 1)
            for h2 in range(2):
                r = slice(h2 * 64, h2 * 64 + 64)
                for c_ in range(2):
                    link(V.tensor_copy(OM[r, c_, SEQ:T].rearrange("p (b t) -> p b t", t=TS),
                                       bank(5)[r, c_ * 64:(c_ + 1) * 64].rearrange("p (b g t) -> p b g t", g=2, t=TS)[:, :, h2, :]))

        def ms_st_out(v, b):
            v.wait_ge(S("satt_scored"), 8 * b + 8)
            V.tensor_copy(st_all[:, :, b * 16:b * 16 + 16], bank(2 + b % 2)[:, 0:256].rearrange("p (n r) -> p n r", r=16))\
                .then_inc(S("satt_st"), 1)

        def moba_sample_scalar(s):
            for q in range(0, 64, 2):
                s.wait_ge(S("satt_turned"), q + 1)
                if q >= 2:
                    s.wait_ge(S("satt_scored"), q - 1)
                scopy(ms_kt[:, q % 2, :], bank(q % 2)).then_inc(S("keys_turned_s"), 1)
            s.wait_ge(S("satt_max"), 1)
            A.activation(ms_s[:, :], ms_s[:, :], ACT.Exp, bias=ms_stat[:, 0:1], accum_out=ms_stat[:, 1:2]).then_inc(S("satt_exp"), 1)
            s.wait_ge(S("satt_pt"), 1)
            link(scopy(st_all[:, 8:12, :], bank(2).rearrange("p (n k) -> p n k", k=P)), "s")
            scopy(st_all[:, 12:16, :], bank(3).rearrange("p (n k) -> p n k", k=P)).then_inc(S("satt_pt_out"), 1)

        tmp4 = SC[0:H, 0:16 * T].rearrange("p (c t) -> p c t", t=T)
        cw_in = carve(SC, 16 * T, 12, 27)
        cw_out = OM[0:27, 2:5, :].rearrange("p a b -> p (a b)")[:, 0:12 * P]

        def rows_vector(v):
            v.wait_ge(S("rates_exp"), 1)
            for i in (0, 2):
                link(V.tensor_scalar(head4[0:H, i + 4:i + 5], head4[0:H, i + 4:i + 5], -1.0, None, ALU.mult))
            x, e, u, d, l = (tmp4[:, 2 * i:2 * i + 2, :] for i in range(5))
            link(V.tensor_scalar(x[:, 0, :], raw[:, 0, :], head4[0:H, 1:2], None, ALU.add))
            link(V.tensor_scalar(x[:, 1, :], raw[:, 2, :], head4[0:H, 3:4], None, ALU.add))
            V.scalar_tensor_tensor(e, x, -1.0, x, ALU.mult, ALU.max).then_inc(S("rows_abs"), 1)
            v.wait_ge(S("rows_exp"), 1)
            link(V.tensor_scalar(u, e, 1.0, None, ALU.add))
            V.tensor_scalar(d, u, -1.0, None, ALU.add).then_inc(S("rows_u"), 1)
            v.wait_ge(S("rows_ln"), 1)
            link(tt(l, l, e, ALU.mult))
            link(V.tensor_scalar(u, d, 0.0, None, ALU.is_equal))
            link(tt(e, e, u, ALU.mult))
            link(V.tensor_scalar(d, d, 1e-30, None, ALU.max))
            link(V.reciprocal(d, d))
            link(tt(l, l, d, ALU.mult))
            link(tt(l, l, e, ALU.add))
            link(V.scalar_tensor_tensor(l, x, 0.0, l, ALU.max, ALU.add))
            link(V.tensor_copy(rows[:, 0, :], l[:, 0, :]))
            link(V.tensor_scalar(x[:, 0, :], l[:, 0, :], head4[0:H, 4:5], None, ALU.mult))
            link(V.tensor_scalar(x[:, 1, :], l[:, 1, :], head4[0:H, 6:7], None, ALU.mult))
            link(V.tensor_tensor_scan(rows[:, 1, :], keep[0:H, :], x[:, 0, :], 0.0, ALU.mult, ALU.add))
            link(V.tensor_tensor_scan(rows[:, 3, :], keep[0:H, :], x[:, 1, :], 0.0, ALU.mult, ALU.add))
            link(V.tensor_scalar(tmp4[:, 10, :], tmp4[:, 10, :], 1.0, None, ALU.add))
            link(V.reciprocal(rows[:, 2, :], tmp4[:, 10, :]))
            for m_ in range(2):
                c0 = C_XBC if m_ == 0 else C_GQKV
                dst = ups[:, 6 * m_:6 * m_ + 6, :, 3:7]
                link(V.tensor_copy(dst, proj[:, c0:c0 + 6, SEQ:T].rearrange("p c (b t) -> p c b t", t=TS)))
                link(V.tensor_copy(cw_in[:, 6 * m_:6 * m_ + 6, 0:3], proj[:, c0:c0 + 6, SEQ - 3:SEQ]))
            for c_ in range(12):
                last = V.tensor_copy(cw_in[:, c_, 3:27].rearrange("p (b w) -> p b w", w=3), ups[:, c_, :, 4:7])
            link(last)
            v.drain().then_inc(S("rows_made"), 1)
            v.wait_ge(S("rows_turned"), 1)
            link(V.tensor_copy(cumtok[:, 0:4, :], bank(6)[:, 0:32].rearrange("p (i h) -> p i h", h=8)))
            link(V.tensor_copy(cumtok[0:NS, 4, :], bank(6)[0:NS, 32:40]))
            v.wait_ge(S("conv_turned"), 1)
            for i in range(3):
                last = V.tensor_copy(cw_out[:, i * 512:(i + 1) * 512], bank(i)[0:27, :])
            link(last)
            v.drain().then_inc(S("conv_states_made"), 1)

        def rows_scalar(s):
            A.activation(head4[0:H, 4:5], head4[0:H, 0:1], ACT.Exp)
            A.activation(head4[0:H, 6:7], head4[0:H, 2:3], ACT.Exp).then_inc(S("rates_exp"), 1)
            A.activation(tmp4[:, 10, :], raw[:, 1, :], ACT.Exp, scale=-1.0)
            s.wait_ge(S("rows_abs"), 1)
            A.activation(tmp4[:, 2:4, :], tmp4[:, 2:4, :], ACT.Exp, scale=-1.0).then_inc(S("rows_exp"), 1)
            s.wait_ge(S("rows_u"), 1)
            A.activation(tmp4[:, 8:10, :], tmp4[:, 4:6, :], ACT.Ln).then_inc(S("rows_ln"), 1)
            for n in range(6):
                s.wait_ge(S("rows_spread"), n + 1)
                A.activation(halves(pb[:, n // 2, n % 2, :]), pair(n % 2), ACT.Copy).then_inc(S("rows_spread_out"), 1)

        def rows_tensor(pe):
            pe.wait_ge(S("rows_made"), 1)
            for i, (t0, w, _) in enumerate(TILES):
                for m_, kind in enumerate((1, 3)):
                    last = tr(bank(6)[0:w, i * 8 + 4 * m_:i * 8 + 4 * m_ + 4], rows[:, kind, t0:t0 + w], H)
            last.then_inc(S("rows_turned"), 1)
            for n in range(6):
                kind, hp = (0, 2, 3)[n // 2], n % 2
                if n >= 2:
                    pe.wait_ge(S("rows_spread_out"), n - 1)
                for j in range(2):
                    last = mm(PS[n % 2][:, j, 0:HT], pairsel[0:H, hp, :], rows[:, kind, j * HT:(j + 1) * HT], True, True)
                last.then_inc(S("rows_spread"), 1)
            pe.wait_ge(S("rows_spread_out"), 6)
            for c_ in range(12):
                last = tr(bank(c_ // 4)[0:27, (c_ % 4) * P:(c_ % 4 + 1) * P], cw_in[:, c_, :], P)
            last.then_inc(S("conv_turned"), 1)

        def conv_vector(v, c0, m_, wrow, brow):
            for c_ in range(6):
                src, dst = proj[:, c0 + c_, :], xc[:, c_, :]
                win_ = ups[:, 6 * m_ + c_, :, :]
                ds_ = dst[:, SEQ:T].rearrange("p (b t) -> p b t", t=TS)
                wt = [par(wrow + 6 * j + c_) for j in range(4)]
                b_ = par(brow + c_) if brow is not None else 0.0
                V.tensor_scalar(dst[:, 0:SEQ], src[:, 0:SEQ], wt[3], b_, ALU.mult, ALU.add)
                link(V.tensor_scalar(ds_, win_[:, :, 3:7], wt[3], b_, ALU.mult, ALU.add))
                for d in range(1, 4):
                    last = V.scalar_tensor_tensor(dst[:, d:SEQ], src[:, 0:SEQ - d], wt[3 - d], dst[:, d:SEQ], ALU.mult, ALU.add)
                    last = V.scalar_tensor_tensor(ds_, win_[:, :, 3 - d:7 - d], wt[3 - d], ds_, ALU.mult, ALU.add)
                    if d < 3:
                        link(last)
                last.then_inc(S("conv"), 1)

        def conv_scalar(s, m_):
            for c_ in range(6):
                s.wait_ge(S("conv"), 6 * m_ + c_ + 1)
                A.activation(xc[:, c_, :], xc[:, c_, :], ACT.Silu).then_inc(S("conv_silu"), 1)

        def dec_tensor(pe, b, kind, t0, w, np_):
            for h in range(H):
                last = mm(bank(b)[0:np_, h * w:(h + 1) * w], onehot[0:H, h, 0:np_], rows[:, kind, t0:t0 + w], True, True)
            return last

        def dec_vector(dst, b, col, i, w):
            c3 = cumtok[0:w, i, col:col + 4].rearrange("p (h o) -> p h o", o=1)
            msk = (negmask if w == P else negmask_s)[0:w, 0:w].rearrange("p (o l) -> p o l", o=1)
            link(tt(dst, bank(b)[0:w, 0:H * w].rearrange("p (h l) -> p h l", l=w), bc(c3, (w, H, w)), ALU.subtract))
            return tt(dst, dst, bc(msk, (w, H, w)), ALU.add)

        def hl(buf, w):
            flat = buf.rearrange("p a b -> p (a b)") if len(buf.shape) == 3 else buf
            return flat[0:w, 0:H * w].rearrange("p (h l) -> p h l", l=w)

        def ssm_tensor(pe):
            pe.wait_ge(S("ssm_xdt"), 1)
            pe.wait_ge(S("conv_silu"), 6)
            for i, (t0, w, _) in enumerate(TILES):
                sl = slice(t0, t0 + w)
                if i:
                    pe.wait_ge(S("ssm_tile_out"), i)
                for g in range(2):
                    mm(bank(0)[0:w, g * w:(g + 1) * w], xc[:, 2 + g, sl], xc[:, 4 + g, sl], True, True)
                dec_tensor(pe, 1, 1, t0, w, P)
                for k in range(4):
                    src = xdt[:, k, sl] if k < 2 else xc[:, k, sl]
                    last = tr(bank(2)[0:w, k * P:(k + 1) * P], src, P)
                last.then_inc(S("ssm_pre"), 1)
                if w == NS:
                    pe.wait_ge(S("state_in"), 16)
                    for n in range(16):
                        last = tr(bank(4 + n // 4)[:, (n % 4) * P:(n % 4 + 1) * P], s_h0[:, n // 2, n % 2, :], P)
                    last.then_inc(S("ssm_h0_turned"), 1)
                    pe.wait_ge(S("ssm_h0_out"), 1)
                pe.wait_ge(S("ssm_ready"), i + 1)
                for h in range(H):
                    r = slice((h % 2) * 64, (h % 2) * 64 + 64)
                    o_ = bank(3)[r, (h // 2) * w:(h // 2 + 1) * w]
                    alone = w == P and i == 0
                    last = mm(o_, s_tok[0:w, h * 64:(h + 1) * 64], hl(s_m, w)[:, h, :], True, alone)
                    if w == NS:
                        for b in range(NB):
                            last = mm(o_[:, b * TS:(b + 1) * TS], s_h0t[:, b, h * 64:(h + 1) * 64],
                                      sc_view(w)[:, h, b * TS:(b + 1) * TS], False, True)
                    elif i:
                        last = mm(o_, s_ht[:, h * 64:(h + 1) * 64], sc_view(w)[:, h, :], False, True)
                last.then_inc(S("ssm_y"), 1)
                if w == P:
                    for g in range(2):
                        last = mm(bank(4)[:, g * P:(g + 1) * P], s_tok[:, 256 + g * P:256 + (g + 1) * P], s_xd[:, g * P:(g + 1) * P], True, True)
                    last.then_inc(S("ssm_state"), 1)
                else:
                    for hp in range(2):
                        last = mm(bank(2)[:, hp * 8:hp * 8 + 8], pairsel[0:H, hp, :],
                                  rows[:, 1, SEQ:T].rearrange("p (b t) -> p b t", t=TS)[:, :, TS - 1], True, True)
                    last.then_inc(S("ssm_dec"), 1)
                    for g in range(2):
                        last = tr(bank(0)[:, g * P:(g + 1) * P], s_ht[:, g * P:(g + 1) * P], P)
                    last.then_inc(S("ssm_final"), 1)
                    pe.wait_ge(S("ssm_bm"), 1)
                    for g in range(2):
                        for q in range(2):
                            last = mm(bank(4 + 2 * g + q), s_xd[0:NS, g * P:(g + 1) * P],
                                      s_bm[0:NS, 4 * q:4 * q + 4, g, :], True, True)
                    last.then_inc(S("ssm_state"), 1)
            pe.wait_ge(S("tail_sq"), 1)
            for k in range(2):
                for j in range(2):
                    last = mm(PS[0][:, j, 0:HT], ones, xdt[:, k, j * HT:(j + 1) * HT], k == 0, k == 1)
            last.then_inc(S("tail_sum"), 1)

        def sc_view(w):
            return s_c.rearrange("p a b -> p (a b)")[:, 0:H * w].rearrange("p (h l) -> p h l", l=w)

        s_bm = xc[:, 2:6, :].rearrange("p a b -> p (a b)")[:, 0:NB * 256].rearrange("p (b g n) -> p b g n", g=2, n=P)
        s_fin = s_er.rearrange("p a b -> p (a b)")[:, 0:2 * P].rearrange("p (c n) -> p c n", n=P)

        def ssm_vector(v):
            conv_vector(v, C_XBC, 0, R_SCW, R_SCB)
            v.wait_ge(S("conv_silu"), 6)
            tt(xdt, xc[:, 0:2, :], pb[:, 0, :, :], ALU.mult).then_inc(S("ssm_xdt"), 1)
            for i, (t0, w, _) in enumerate(TILES):
                sl = slice(t0, t0 + w)
                M = hl(s_m, w)
                er = s_er.rearrange("p a b -> p (a b)")[:, 0:H * w].rearrange("p (h l) -> p h l", l=w)
                v.wait_ge(S("ssm_pre"), i + 1)
                dec_vector(M, 1, 0, i, w).then_inc(S("ssm_m"), 1)
                link(V.tensor_copy(s_tok[0:w, :], bank(2)[0:w, :]))
                v.wait_ge(S("ssm_exp"), i + 1)
                if w == P:
                    link(V.tensor_copy(s_dl[:, :], M[:, :, P - 1]))
                else:
                    link(V.tensor_reduce(s_dl[0:w, :], M.rearrange("p h (b t) -> p h b t", t=TS)[:, :, :, TS - 1], AXX, ALU.add))
                for g in range(2):
                    c4 = bc(xc[:, 4 + g, sl].rearrange("p (o l) -> p o l", o=1), (P, 2, w))
                    g4 = bc(bank(0)[0:w, g * w:(g + 1) * w].rearrange("p (o l) -> p o l", o=1), (w, 2, w))
                    tt(sc_view(w)[:, 2 * g:2 * g + 2, :], er[:, 2 * g:2 * g + 2, :], c4, ALU.mult)
                    link(tt(M[:, 2 * g:2 * g + 2, :], M[:, 2 * g:2 * g + 2, :], g4, ALU.mult))
                xd3 = s_xd[0:w, :].rearrange("p (h d) -> p h d", d=DH)
                tt(xd3, s_tok[0:w, 0:256].rearrange("p (h d) -> p h d", d=DH),
                   bc(s_dl[0:w, :].rearrange("p (h o) -> p h o", o=1), (w, H, DH)), ALU.mult).then_inc(S("ssm_ready"), 1)
                if w == NS:
                    v.wait_ge(S("ssm_h0_turned"), 1)
                    for n in range(4):
                        last = V.tensor_copy(s_h0t[:, 2 * n:2 * n + 2, :], bank(4 + n).rearrange("p (b n) -> p b n", n=256))
                    last.then_inc(S("ssm_h0_out"), 1)
                v.wait_ge(S("ssm_y"), i + 1)
                if i == 0:
                    v.wait_ge(S("conv_states_out"), 16 * 4)
                link(V.tensor_copy(OM[:, 2:4, sl], bank(3)[:, 0:2 * w].rearrange("p (c l) -> p c l", l=w)))
                if w == P:
                    v.wait_ge(S("ssm_state"), i + 1)
                    if i == 0:
                        link(V.tensor_copy(s_ht, bank(4)[:, 0:256]))
                    else:
                        h3 = s_ht.rearrange("p (h d) -> p h d", d=DH)
                        link(tt(h3, h3, bc(er[:, :, P - 1:P], (P, H, DH)), ALU.mult))
                        link(tt(s_ht, s_ht, bank(4)[:, 0:256], ALU.add))
                else:
                    tt(s_bm[0:NS].rearrange("p b g n -> p b (g n)"), bc(s_tok[0:NS, 256:512].rearrange("p (o n) -> p o n", o=1), (NS, NB, 256)),
                       bc(ind[0:NS].rearrange("p (b o) -> p b o", o=1), (NS, NB, 256)), ALU.mult).then_inc(S("ssm_bm"), 1)
                    v.wait_ge(S("ssm_final"), 1)
                    V.tensor_copy(s_fin, bank(0)[:, 0:256].rearrange("p (c n) -> p c n", n=P)).then_inc(S("fin_made"), 1)
                    v.wait_ge(S("ssm_dec_exp"), 1)
                    for hp in range(2):
                        link(tt(s_h0[:, :, hp, :], s_h0[:, :, hp, :], bc(s_dec[:, hp, :].rearrange("p (b o) -> p b o", o=1), (P, NB, P)), ALU.mult))
                    v.wait_ge(S("ssm_state"), 5)
                    for g in range(2):
                        for q in range(2):
                            last = tt(s_h0[:, 4 * q:4 * q + 4, g, :], s_h0[:, 4 * q:4 * q + 4, g, :],
                                      bank(4 + 2 * g + q).rearrange("p (b n) -> p b n", n=P), ALU.add)
                    last.then_inc(S("states_made"), 1)
                v.drain().then_inc(S("ssm_tile_out"), 1)
            Y = OM[:, 2:4, :]
            for c_ in range(2):
                link(V.scalar_tensor_tensor(Y[:, c_, :], xc[:, c_, :], par(R_SD + c_), Y[:, c_, :], ALU.mult, ALU.add))
            v.wait_ge(S("ssm_gate"), 2)
            link(tt(Y, Y, proj[:, C_Z:C_Z + 2, :], ALU.mult))
            tt(xdt, Y, Y, ALU.mult).then_inc(S("tail_sq"), 1)
            v.wait_ge(S("tail_root"), 1)
            link(V.reciprocal(rsq[:, :], rsq[:, :]))
            for c_ in range(2):
                last = V.scalar_tensor_tensor(Y[:, c_, :], Y[:, c_, :], par(R_SNORM + c_), rsq[:, :], ALU.mult, ALU.mult)
            link(last)

        def ssm_scalar(s):
            conv_scalar(s, 0)
            for c_ in range(2):
                A.activation(proj[:, C_Z + c_, :], proj[:, C_Z + c_, :], ACT.Silu).then_inc(S("ssm_gate"), 1)
            for i, (t0, w, _) in enumerate(TILES):
                M = hl(s_m, w)
                s.wait_ge(S("ssm_pre"), i + 1)
                if i:
                    s.wait_ge(S("ssm_tile_out"), i)
                s.wait_ge(S("ssm_m"), i + 1)
                A.activation(s_er.rearrange("p a b -> p (a b)")[:, 0:H * w], bank(1)[:, 0:H * w], ACT.Exp)
                A.activation(M, M, ACT.Exp).then_inc(S("ssm_exp"), 1)
            s.wait_ge(S("ssm_dec"), 1)
            A.activation(s_dec, bank(2)[:, 0:16].rearrange("p (c b) -> p c b", b=NB), ACT.Exp).then_inc(S("ssm_dec_exp"), 1)
            s.wait_ge(S("tail_sum"), 1)
            A.activation(halves(rsq[:, :]), pair(0), ACT.Sqrt, bias=eps, scale=1.0 / GW).then_inc(S("tail_root"), 1)

        def tail_prep_vector(v, run, b2, q, k, qe, kd, last_, e1):
            v.wait_ge(S("tail_eb"), run + 1)
            link(tt(qe, q, e1, ALU.mult))
            for c_ in range(2):
                for (lo, hi, step) in ((0, SEQ, P), (SEQ, T, TS)):
                    x3 = b2[:, c_, lo:hi].rearrange("p (n i) -> p n i", i=step)
                    o3 = e1[:, c_, lo:hi].rearrange("p (n i) -> p n i", i=step)
                    last = tt(o3, bc(x3[:, :, step - 1:step], (P, (hi - lo) // step, step)), x3, ALU.subtract)
            last.then_inc(S("tail_bd"), 1)
            v.wait_ge(S("tail_ebd"), run + 1)
            tt(kd, k, e1, ALU.mult).then_inc(S("tail_prep"), 1)

        def tail_prep_scalar(s, run, b2, e1):
            A.activation(e1, b2, ACT.Exp).then_inc(S("tail_eb"), 1)
            for c_ in range(2):
                A.activation(t_lastp[:, :, c_], b2[:, c_, 0:SEQ].rearrange("p (n i) -> p n i", i=P)[:, :, P - 1], ACT.Exp)
                A.activation(t_lasts[:, :, c_], b2[:, c_, SEQ:T].rearrange("p (n i) -> p n i", i=TS)[:, :, TS - 1], ACT.Exp)
            s.wait_ge(S("tail_bd"), run + 1)
            A.activation(e1, e1, ACT.Exp).then_inc(S("tail_ebd"), 1)

        t_lastp = sm(4, 2)
        t_lasts = sm(NB, 2)

        def tail_tensor(pe, run, att, kd, qe, vT, kbg, N):
            gdn = kbg is not None
            pe.wait_ge(S("tail_prep"), run + 1)
            for i, (t0, w, _) in enumerate(TILES):
                sl = slice(t0, t0 + w)
                if i:
                    pe.wait_ge(S("tail_tile_out"), 5 * run + i)
                sample = w == NS
                for k in range(2):
                    tr(bank(0)[0:w, k * P:(k + 1) * P], kd[:, k, sl], P)
                if not (sample and gdn):
                    for k in range(2):
                        last = tr(bank(0)[0:w, 256 + k * P:256 + (k + 1) * P], vT[:, k, sl], P)
                if sample:
                    pe.wait_ge(S("state_in"), 32 + 16 * run)
                if gdn and sample:
                    for h in range(H):
                        r = slice((h % 2) * 64, (h % 2) * 64 + 64)
                        for b in range(NB):
                            last = mm(bank(1)[r, (h // 2) * w + b * TS:(h // 2) * w + (b + 1) * TS], t_s0[r, b, h // 2, :],
                                      kbg[r, h // 2, t0 + b * TS:t0 + (b + 1) * TS], True, True)
                elif gdn and i:
                    for h in range(H):
                        r = slice((h % 2) * 64, (h % 2) * 64 + 64)
                        last = mm(bank(1 if h % 2 == 0 else 5)[0:w, (h // 2) * 64:(h // 2 + 1) * 64], kbg[r, h // 2, sl], t_st[r, h // 2, :], True, True)
                last.then_inc(S("tail_tok"), 1)
                if gdn and sample:
                    pe.wait_ge(S("tail_rt"), 1)
                    for k in range(2):
                        last = tr(bank(5)[0:w, k * P:(k + 1) * P], t_rt[:, k, :], P)
                    last.then_inc(S("tail_rt_turned"), 1)
                pe.wait_ge(S("tail_tok_out"), 5 * run + i + 1)
                if gdn:
                    for h in range(H):
                        last = mm(bank(2)[0:w, h * 64:(h + 1) * 64], N(i, w)[:, h, :], t_tok[0:w, 256 + h * 64:256 + (h + 1) * 64], True, True)
                    last.then_inc(S("tail_vn"), 1)
                    pe.wait_ge(S("tail_vn_out"), i + 1)
                for h in range(H):
                    r = slice((h % 2) * 64, (h % 2) * 64 + 64)
                    o_ = bank(3)[r, (h // 2) * w:(h // 2 + 1) * w]
                    last = mm(o_, t_vn[0:w, h * 64:(h + 1) * 64], att(i, w, h), True, i == 0)
                    if sample:
                        for b in range(NB):
                            last = mm(o_[:, b * TS:(b + 1) * TS], t_s0[r, b, h // 2, :], qe[r, h // 2, t0 + b * TS:t0 + (b + 1) * TS], False, True)
                    elif i:
                        last = mm(o_, t_st[r, h // 2, :], qe[r, h // 2, sl], False, True)
                last.then_inc(S("tail_o"), 1)
                if sample:
                    pe.wait_ge(S("tail_vm"), run + 1)
                for h in range(H):
                    r = slice((h % 2) * 64, (h % 2) * 64 + 64)
                    if sample:
                        last = mm(bank(6 + h // 2)[r, :], t_tok[0:w, h * 64:(h + 1) * 64], vm_of(run)[0:w, h * 512:(h + 1) * 512], True, True)
                    else:
                        last = mm(bank(4)[r, (h // 2) * DH:(h // 2 + 1) * DH], t_tok[0:w, h * 64:(h + 1) * 64], t_vn[0:w, h * 64:(h + 1) * 64], True, True)
                last.then_inc(S("tail_st"), 1)
            pe.wait_ge(S("tail_sq"), run + 2)
            for k in range(2):
                for j in range(2):
                    last = mm(PS[k][:, j, 0:HT], blk64, qe[:, k, j * HT:(j + 1) * HT], True, True)
            last.then_inc(S("tail_sum"), 1)

        t_rt = sm(2, NS)

        def vm_of(run):
            return h_vm_ if run == 0 else t_vm

        def tail_vector(v, run, gdn, vT, qe, c_out, c_gate, rnorm):
            for i, (t0, w, _) in enumerate(TILES):
                sl = slice(t0, t0 + w)
                sample = w == NS
                v.wait_ge(S("tail_tok"), 5 * run + i + 1)
                V.tensor_copy(t_tok[0:w, 0:256], bank(0)[0:w, 0:256])
                if gdn and sample:
                    tt(t_rt, vT[:, :, sl], bank(1)[:, 0:2 * w].rearrange("p (c l) -> p c l", l=w), ALU.subtract).then_inc(S("tail_rt"), 1)
                    v.wait_ge(S("tail_rt_turned"), 1)
                    V.tensor_copy(t_tok[0:w, 256:512], bank(5)[0:w, 0:256]).then_inc(S("tail_tok_out"), 1)
                elif gdn and i:
                    link(V.tensor_copy(t_tok[0:w, 256:512], bank(0)[0:w, 256:512]))
                    for e in range(2):
                        half = t_tok[0:w, 256:512].rearrange("p (c e d) -> p e c d", e=2, d=DH)[:, e]
                        last = tt(half, half, bank(1 if e == 0 else 5)[0:w, 0:P].rearrange("p (c d) -> p c d", d=DH), ALU.subtract)
                    last.then_inc(S("tail_tok_out"), 1)
                elif gdn:
                    V.tensor_copy(t_tok[0:w, 256:512], bank(0)[0:w, 256:512]).then_inc(S("tail_tok_out"), 1)
                else:
                    V.tensor_copy(t_vn[0:w, :], bank(0)[0:w, 256:512]).then_inc(S("tail_tok_out"), 1)
                if gdn:
                    v.wait_ge(S("tail_vn"), i + 1)
                    V.tensor_copy(t_vn[0:w, :], bank(2)[0:w, 0:256]).then_inc(S("tail_vn_out"), 1)
                if sample:
                    if gdn:
                        v.wait_ge(S("tail_vn_out"), i + 1)
                    else:
                        v.wait_ge(S("tail_tok_out"), i + 1)
                    vm4 = vm_of(run)[0:w, :].rearrange("p (h b d) -> p h b d", b=NB, d=DH)
                    for h in range(H):
                        last = tt(vm4[:, h], bc(t_vn[0:w, h * 64:(h + 1) * 64].rearrange("p (o d) -> p o d", o=1), (w, NB, DH)),
                                  bc(ind[0:w].rearrange("p (b o) -> p b o", o=1), (w, NB, DH)), ALU.mult)
                    last.then_inc(S("tail_vm"), 1)
                v.wait_ge(S("tail_o"), 5 * run + i + 1)
                link(V.tensor_copy(OM[:, c_out:c_out + 2, sl], bank(3)[:, 0:2 * w].rearrange("p (c l) -> p c l", l=w)))
                v.wait_ge(S("tail_st"), 5 * run + i + 1)
                if sample:
                    link(tt(t_s0.rearrange("p b c d -> p (b c) d"), t_s0.rearrange("p b c d -> p (b c) d"),
                            bc(t_lasts.rearrange("p b (c o) -> p (b c) o", o=1), (P, 2 * NB, DH)), ALU.mult))
                    for c_ in range(2):
                        last = tt(t_s0[:, :, c_, :], t_s0[:, :, c_, :], bank(6 + c_).rearrange("p (b d) -> p b d", d=DH), ALU.add)
                    last.then_inc(S("states_made"), 1)
                elif i == 0:
                    link(V.tensor_copy(t_st, bank(4)[:, 0:2 * DH].rearrange("p (c d) -> p c d", d=DH)))
                else:
                    link(tt(t_st, t_st, bc(t_lastp[:, i, :].rearrange("p (c o) -> p c o", o=1), (P, 2, DH)), ALU.mult))
                    last = tt(t_st, t_st, bank(4)[:, 0:2 * DH].rearrange("p (c d) -> p c d", d=DH), ALU.add)
                    link(last)
                if i == 3:
                    v.drain().then_inc(S("fin_made"), 1)
                v.drain().then_inc(S("tail_tile_out"), 1)
            Y = OM[:, c_out:c_out + 2, :]
            tt(qe, Y, Y, ALU.mult).then_inc(S("tail_sq"), 1)
            v.wait_ge(S("tail_root"), 1 + 2 * run + 2)
            link(V.reciprocal(qe, qe))
            for c_ in range(2):
                link(V.scalar_tensor_tensor(Y[:, c_, :], Y[:, c_, :], par(rnorm), qe[:, c_, :], ALU.mult, ALU.mult))
            link(tt(Y, Y, proj[:, c_gate:c_gate + 2, :], ALU.mult))

        def tail_scalar(s, run, qe, c_gate):
            s.wait_ge(S("tail_sum"), run + 2)
            for k in range(2):
                A.activation(halves(qe[:, k, :]), pair(k), ACT.Sqrt, bias=eps, scale=1.0 / DH).then_inc(S("tail_root"), 1)

        h_vm_ = carve(SC, 2 * T, NB * H * DH)
        hq, hk = proj[:, C_HQ:C_HQ + 2, :], h_k

        def lv_groups():
            return (((0, SEQ), 4, P, 8), ((SEQ, T), 2, NS, 3))

        def hgrn_vector(v):
            fx = proj[:, C_HF:C_HF + 2, :]
            v.wait_ge(S("states_out"), 32)
            V.scalar_tensor_tensor(h_d, fx, -1.0, fx, ALU.mult, ALU.max).then_inc(S("h_abs"), 1)
            v.wait_ge(S("h_ln"), 1)
            link(V.scalar_tensor_tensor(h_d, fx, 0.0, h_d, ALU.min, ALU.subtract))
            for c_ in range(2):
                link(V.tensor_tensor_scan(h_b[:, c_, :], keep[:, :], h_d[:, c_, :], 0.0, ALU.mult, ALU.add))
            link(V.tensor_scalar(h_k, h_k, 1.0, None, ALU.add))
            V.reciprocal(h_k, h_k).then_inc(S("h_k"), 1)
            v.wait_ge(S("h_k"), 1)
            n = 0
            m_ = 0
            for (lo, hi), nt, w, nl in lv_groups():
                def decays(j, n):
                    B = 1 << j
                    for c_ in range(2):
                        x3 = h_b[:, c_, lo:hi].rearrange("p (n i) -> p n i", i=B)
                        o3 = h_d[:, c_, lo:hi].rearrange("p (n i) -> p n i", i=B)
                        mid = bc(x3[:, :, B // 2 - 1:B // 2], (P, (hi - lo) // B, B // 2))
                        tt(o3[:, :, 0:B // 2], mid, x3[:, :, 0:B // 2], ALU.subtract)
                        last = tt(o3[:, :, B // 2:B], x3[:, :, B // 2:B], mid, ALU.subtract)
                    last.then_inc(S("h_diff"), 1)
                    v.wait_ge(S("h_dec"), n + 1)
                    if n >= 2:
                        v.wait_ge(S("h_lv_mm"), h_lvdone(n - 2))
                    tt(h_q1[:, n % 2, :, lo:hi], hq[:, :, lo:hi], h_d[:, :, lo:hi], ALU.mult)
                    tt(h_k1[:, n % 2, :, lo:hi], hk[:, :, lo:hi], h_d[:, :, lo:hi], ALU.mult).then_inc(S("h_qk"), 1)
                    v.wait_ge(S("h_qk"), n + 1)
                for j in range(nl):
                    if j + 1 < nl:
                        decays(j + 1, n)
                        n += 1
                    nm = 4 if w == P else 2
                    msk = bc(lev[0:w, j, 0:w].rearrange("p (o l) -> p o l", o=1), (w, nm, w))
                    for i in range(nt):
                        v.wait_ge(S("h_lv_mm"), m_ + 1)
                        src = bank(m_ % 8)[0:w, 0:nm * w].rearrange("p (h l) -> p h l", l=w)
                        if j == 0:
                            tt(h_store(i, w), src, msk, ALU.mult).then_inc(S("h_lv_out"), 1)
                        else:
                            v.wait_ge(S("h_added"), m_ - 3)
                            tt(h_job(h_msk, m_ % 4, w), src, msk, ALU.mult).then_inc(S("h_lv_out"), 1)
                        m_ += 1

        def h_lvdone(n):
            return 4 * (n + 2) if n < 7 else 32 + 2 * (n - 7 + 2)

        def h_job(buf, i, w):
            n = 4 if w == P else 2
            return buf[0:w, i * 512:i * 512 + n * w].rearrange("p (h l) -> p h l", l=w)

        def h_store(m_, w):
            if w == P:
                return h_job(h_att, m_, w)
            return h_att[0:w, 2048 + 64 * m_:2048 + 64 * (m_ + 1)].rearrange("p (h l) -> p h l", l=w)

        def h_att_of(i, w, h):
            if w == P:
                return h_store(2 * (i // 2) + h % 2, w)[:, 2 * (i % 2) + h // 2, :]
            return h_store(h % 2, w)[:, h // 2, :]

        def hgrn_gpsimd(g):
            m_, added = 0, 0
            for _, nt, w, nl in lv_groups():
                for j in range(nl):
                    for i in range(nt):
                        g.wait_ge(S("h_lv_out"), m_ + 1)
                        if j == 0:
                            g.drain().then_inc(S("h_added"), 1)
                        else:
                            at = h_store(i, w)
                            if j > 1:
                                g.wait_ge(S("h_added"), m_ - nt + 1)
                            G.tensor_tensor(at, at, h_job(h_msk, m_ % 4, w), ALU.add).then_inc(S("h_added"), 1)
                        m_ += 1

        def hgrn_tensor(pe):
            pe.wait_ge(S("h_k"), 1)
            m_, n = 0, 0
            for (lo, hi), nt, w, nl in lv_groups():
                for j in range(nl):
                    if j:
                        pe.wait_ge(S("h_qk"), n + 1)
                    for i in range(nt):
                        if m_ >= 8:
                            pe.wait_ge(S("h_lv_out"), m_ - 7)
                        r = slice((i % 2) * 64, (i % 2) * 64 + 64)
                        for n_ in range(4 if w == P else 2):
                            t_ = 2 * (i // 2) + n_ // 2 if w == P else 0
                            sl = slice(lo + t_ * w, lo + (t_ + 1) * w)
                            q_ = hq[r, n_ % 2, sl] if j == 0 else h_q1[r, n % 2, n_ % 2, sl]
                            k_ = hk[r, n_ % 2, sl] if j == 0 else h_k1[r, n % 2, n_ % 2, sl]
                            last = mm(bank(m_ % 8)[0:w, n_ * w:(n_ + 1) * w], k_, q_, True, True)
                        last.then_inc(S("h_lv_mm"), 1)
                        m_ += 1
                    if j:
                        n += 1
            tail_tensor(pe, 0, h_att_of, h_k1[:, 0], h_q1[:, 0], proj[:, C_HI:C_HI + 2, :], None, None)

        def hgrn_vector_tail(v):
            v.wait_ge(S("h_lv_mm"), 38)
            v.wait_ge(S("h_added"), 38)
            v.drain().then_inc(S("h_levels_done"), 1)
            tail_prep_vector(v, 0, h_b, hq, hk, h_q1[:, 0], h_k1[:, 0], None, h_d)
            tail_vector(v, 0, False, None, h_q1[:, 0], 4, C_HG, R_HNORM)

        def hgrn_scalar(s):
            s.wait_ge(S("h_abs"), 1)
            link(A.activation(h_d, h_d, ACT.Exp, scale=-1.0), "s")
            A.activation(h_k, proj[:, C_HF:C_HF + 2, :], ACT.Exp)
            A.activation(h_d, h_d, ACT.Ln, bias=ones[:, 0:1]).then_inc(S("h_ln"), 1)
            n = 0
            for (lo, hi), nt, w, nl in lv_groups():
                for j in range(1, nl):
                    s.wait_ge(S("h_diff"), n + 1)
                    A.activation(h_d[:, :, lo:hi], h_d[:, :, lo:hi], ACT.Exp).then_inc(S("h_dec"), 1)
                    n += 1
            s.wait_ge(S("h_levels_done"), 1)
            tail_prep_scalar(s, 0, h_b, h_d)
            for c_ in range(2):
                A.activation(proj[:, C_HG + c_, :], proj[:, C_HG + c_, :], ACT.Silu)
            tail_scalar(s, 0, h_q1[:, 0], C_HG)

        g_al = carve(XN, 4 * T, 2048)
        gq, gk, gv = xc[:, 0:2, :], xc[:, 2:4, :], xc[:, 4:6, :]
        g_e1 = carve(SC, 12 * T, 2, T)

        def gtile(buf, i, w):
            return buf[0:w, i * 512:i * 512 + H * w].rearrange("p (h l) -> p h l", l=w)

        def gdn_vector(v):
            conv_vector(v, C_GQKV, 1, R_GCW, None)
            v.wait_ge(S("conv_silu"), 12)
            tt(g_sq, xc[:, 0:4, :], xc[:, 0:4, :], ALU.mult).then_inc(S("g_sq"), 1)
            v.wait_ge(S("g_root"), 4)
            link(V.reciprocal(g_sq, g_sq))
            link(V.scalar_tensor_tensor(gq, gq, SCALE, g_sq[:, 0:2, :], ALU.mult, ALU.mult))
            link(tt(gk, gk, g_sq[:, 2:4, :], ALU.mult))
            link(tt(g_kb, gk, pb[:, 1, :, :], ALU.mult))
            tt(gv, gv, pb[:, 1, :, :], ALU.mult).then_inc(S("g_kb"), 1)
            v.wait_ge(S("g_kb"), 1)
            for i, (t0, w, _) in enumerate(TILES):
                ex = hl(g_p1[:, i % 4, :], w)
                v.wait_ge(S("g_mm"), i + 1)
                if i == 4:
                    v.wait_ge(S("g_al_free"), 1)
                dec_vector(ex, 4 * (i % 2) + 2, 4, i, w).then_inc(S("g_m"), 1)
                v.wait_ge(S("g_exp"), i + 1)
                for e in range(2):
                    src = bank(4 * (i % 2) + e)[0:w, 0:H * w].rearrange("p (h l) -> p h l", l=w)
                    par_ = lambda m_: m_.rearrange("p (c e) l -> p e c l", e=2)[:, e]
                    tt(par_(gtile(g_A, i, w)), par_(ex), src[:, 0:2, :], ALU.mult)
                    tt(par_(gtile(g_QK, i, w)), par_(ex), src[:, 2:4, :], ALU.mult)
                id3 = bc(ident[0:w, 0:w].rearrange("p (o l) -> p o l", o=1), (w, H, w))
                V.tensor_copy(gtile(g_T, i, w), id3)
                V.tensor_copy(gtile(g_N, i, w), id3).then_inc(S("g_mats"), 1)
            v.wait_ge(S("g_mats"), NT)
            v.wait_ge(S("states_out"), 64)
            done = 0
            for nt, i0, w, nl in ((4, 0, P, 7), (1, 4, NS, 2)):
                for j in range(1, nl + 1):
                    msk = bc(lev[0:w, j, 0:w].rearrange("p (o l) -> p o l", o=1), (w, H, w))
                    for i in range(nt):
                        if j > 1:
                            v.wait_ge(S("g_p1_mm"), done - nt + i + 1)
                        tt(gtile(g_al, i, w), gtile(g_A, i0 + i, w), msk, ALU.mult).then_inc(S("g_al"), 1)
                    for i in range(nt):
                        v.wait_ge(S("g_tn_mm"), done + 1)
                        b_ = 4 + 2 * (done % 2)
                        b3 = lambda q_: bank(q_)[0:w, 0:H * w].rearrange("p (h l) -> p h l", l=w)
                        tt(gtile(g_T, i0 + i, w), gtile(g_T, i0 + i, w), b3(b_), ALU.subtract)
                        tt(gtile(g_N, i0 + i, w), gtile(g_N, i0 + i, w), b3(b_ + 1), ALU.subtract).then_inc(S("g_tn"), 1)
                        done += 1
            v.wait_ge(S("g_tn"), done)
            v.drain().then_inc(S("g_inverted"), 1)
            tail_prep_vector(v, 1, pb[:, 2], gq, gk, g_qg, t_kd, None, g_e1)
            link(tt(g_kbg, g_kbg, g_kb, ALU.mult))
            v.drain().then_inc(S("g_kbg"), 1)
            tail_vector(v, 1, True, gv, g_qg, 6, C_GZ, R_GNORM)

        def gdn_scalar(s):
            conv_scalar(s, 1)
            for c_ in range(2):
                A.activation(proj[:, C_GZ + c_, :], proj[:, C_GZ + c_, :], ACT.Silu)
            s.wait_ge(S("g_sum"), 1)
            for k in range(4):
                A.activation(halves(g_sq[:, k, :]), pair(k), ACT.Sqrt, bias=eps).then_inc(S("g_root"), 1)
            for i, (t0, w, _) in enumerate(TILES):
                s.wait_ge(S("g_m"), i + 1)
                ex = hl(g_p1[:, i % 4, :], w)
                A.activation(ex, ex, ACT.Exp).then_inc(S("g_exp"), 1)
            A.activation(g_kbg, pb[:, 2], ACT.Exp)
            done = 0
            for nt, i0, w, nl in ((4, 0, P, 7), (1, 4, NS, 2)):
                for j in range(1, nl + 1):
                    for i in range(nt):
                        s.wait_ge(S("g_p1_mm"), done + 1)
                        A.activation(gtile(g_p1.rearrange("p a b -> p (a b)"), i, w), bank(i)[0:w, 0:H * w].rearrange("p (h l) -> p h l", l=w),
                                     ACT.Copy).then_inc(S("g_p1"), 1)
                        done += 1
            s.wait_ge(S("g_inverted"), 1)
            tail_prep_scalar(s, 1, pb[:, 2], g_e1)
            tail_scalar(s, 1, g_qg, C_GZ)

        def gdn_tensor(pe):
            pe.wait_ge(S("g_sq"), 1)
            for k in range(4):
                for j in range(2):
                    last = mm(PS[k][:, j, 0:HT], blk64, g_sq[:, k, j * HT:(j + 1) * HT], True, True)
            last.then_inc(S("g_sum"), 1)
            pe.wait_ge(S("g_kb"), 1)
            for i, (t0, w, _) in enumerate(TILES):
                sl = slice(t0, t0 + w)
                if i >= 2:
                    pe.wait_ge(S("g_mats"), i - 1)
                b_ = 4 * (i % 2)
                for h in range(H):
                    r = slice((h % 2) * 64, (h % 2) * 64 + 64)
                    for m_, rhs in enumerate((g_kb, gq)):
                        c0 = (2 * m_ + h // 2) * w
                        mm(bank(b_ + h % 2)[0:w, c0:c0 + w], gk[r, h // 2, sl], rhs[r, h // 2, sl], True, True)
                dec_tensor(pe, b_ + 2, 3, t0, w, w).then_inc(S("g_mm"), 1)
                if i == 3:
                    pe.drain().then_inc(S("g_al_free"), 1)
            pe.wait_ge(S("g_mats"), NT)
            done = 0
            for nt, i0, w, nl in ((4, 0, P, 7), (1, 4, NS, 2)):
                for j in range(1, nl + 1):
                    base_ = done
                    for i in range(nt):
                        pe.wait_ge(S("g_al"), base_ + i + 1)
                        if j > 1:
                            pe.wait_ge(S("g_tn"), base_ - nt + i + 1)
                        for h in range(H):
                            last = mm(bank(i)[0:w, h * w:(h + 1) * w], gtile(g_al, i, w)[:, h, :], gtile(g_T, i0 + i, w)[:, h, :], True, True)
                        last.then_inc(S("g_p1_mm"), 1)
                    for i in range(nt):
                        pe.wait_ge(S("g_p1"), done + 1)
                        if done >= 2:
                            pe.wait_ge(S("g_tn"), done - 1)
                        b_ = 4 + 2 * (done % 2)
                        p1 = gtile(g_p1.rearrange("p a b -> p (a b)"), i, w)
                        for h in range(H):
                            mm(bank(b_)[0:w, h * w:(h + 1) * w], gtile(g_N, i0 + i, w)[:, h, :], p1[:, h, :], True, True)
                        for h in range(H):
                            last = mm(bank(b_ + 1)[0:w, h * w:(h + 1) * w], p1[:, h, :], gtile(g_N, i0 + i, w)[:, h, :], True, True)
                        last.then_inc(S("g_tn_mm"), 1)
                        done += 1
            pe.wait_ge(S("g_kbg"), 1)
            tail_tensor(pe, 1, lambda i, w, h: gtile(g_QK, i, w)[:, h, :], t_kd, g_qg, gv, g_kbg, lambda i, w: gtile(g_N, i, w))
        def mem_tensor(pe):
            pe.wait_ge(S("mem_in"), 32)
            for q in range(4):
                i, hf = divmod(q, 2)
                for k in range(4):
                    last = tr(bank(q)[:, k * P:(k + 1) * P], mkv[:, i, (4 * hf + k) * P:(4 * hf + k + 1) * P], P)
                last.then_inc(S("mem_turned"), 1)
            norm_tensor(pe, "mem", memn, MEM)
            pe.wait_ge(S("mem_normed"), 1)
            for n in range(8):
                w = weights(pe, first["wkv"] + n)
                for mt in range(2):
                    job = 2 * n + mt
                    if job >= 4:
                        pe.wait_ge(S("kvm_out_s" if mt == 0 else "kvm_out_v"), (job - 4) // 2 + 1)
                    for k in range(KD):
                        last = mm(bank(job % 4)[:, 0:256], memn[:, k, mt * P:(mt + 1) * P], w[:, k, :], k == 0, k == KD - 1)
                    last.then_inc(S("kvm_mm"), 1)
            pe.wait_ge(S("kvm_out_s"), 8)
            pe.wait_ge(S("kvm_out_v"), 8)
            for q in range(4):
                mt, kq = divmod(q, 2)
                for k in range(4):
                    last = tr(bank(4 + q)[:, k * P:(k + 1) * P], mkv[:, mt, (4 * kq + k) * P:(4 * kq + k + 1) * P], P)
                last.then_inc(S("kt_turned"), 1)

        def mem_vector(v):
            for q in range(4):
                i, hf = divmod(q, 2)
                v.wait_ge(S("mem_turned"), q + 1)
                last = V.tensor_copy(memt[:, 4 * hf:4 * hf + 4, i * P:(i + 1) * P], bank(q).rearrange("p (k t) -> p k t", t=P))
            last.then_inc(S("mem_raw"), 1)
            v.wait_ge(S("mem_raw"), 1)
            norm_vector(v, memt, memn, MEM, R_MEM, memn)
            v.drain().then_inc(S("mem_normed"), 1)
            for n in range(8):
                v.wait_ge(S("kvm_mm"), 2 * n + 2)
                V.tensor_copy(mkv[:, 1, n * 256:(n + 1) * 256], bank((2 * n + 1) % 4)[:, 0:256]).then_inc(S("kvm_out_v"), 1)
            for q in range(4):
                mt, kq = divmod(q, 2)
                v.wait_ge(S("kt_turned"), q + 1)
                V.tensor_copy(mkt[:, 4 * kq:4 * kq + 4, mt * P:(mt + 1) * P], bank(4 + q).rearrange("p (k t) -> p k t", t=P))

        def mem_scalar(s):
            s.wait_ge(S("mem_raw"), 1)
            norm_scalar(s, memt, memn, MEM)
            for n in range(8):
                s.wait_ge(S("kvm_mm"), 2 * n + 1)
                scopy(mkv[:, 0, n * 256:(n + 1) * 256], bank((2 * n) % 4)[:, 0:256]).then_inc(S("kvm_out_s"), 1)

        def cross_prompt_tensor(pe):
            def scores(j):
                h, i = divmod(j, 4)
                if j >= 4:
                    pe.wait_ge(S("att_exp"), 16 + j - 3)
                for k in range(2):
                    last = mm(bank(j % 4)[:, 0:MEM], xq[:, 2 * h + k, i * P:(i + 1) * P], mkt[:, 2 * h + k, :], k == 0, k == 1)
                last.then_inc(S("att_scores"), 1)

            def turn(j):
                pe.wait_ge(S("att_probs"), 16 + j + 1)
                if j >= 2:
                    pe.wait_ge(S("att_pt"), 16 + j - 1)
                for k in range(2):
                    last = tr(bank(6 + j % 2)[:, k * P:(k + 1) * P], cx_s[:, j % 4, k * P:(k + 1) * P], P)
                last.then_inc(S("att_turned"), 1)

            def pv(h):
                pe.wait_ge(S("att_pt"), 16 + 4 * h + 4)
                if h:
                    pe.wait_ge(S("att_out"), 4 + 2 * h)
                for ft in range(2):
                    for k in range(2):
                        last = mm(bank(4 + ft), mkv[:, k, D + h * XDH + ft * P:D + h * XDH + (ft + 1) * P], cx_pt[:, h % 2, k, :], k == 0, k == 1)
                last.then_inc(S("att_pv"), 1)

            scores(0)
            scores(1)
            for j in range(16):
                if j + 2 < 16:
                    scores(j + 2)
                turn(j)
                if j >= 5 and j % 4 == 1:
                    pv(j // 4 - 1)
            pv(3)

        def cross_prompt_vector(v):
            def first_(j):
                v.wait_ge(S("att_scores"), 16 + j + 1)
                link(V.tensor_reduce(cx_stat[:, 0, j:j + 1], bank(j % 4)[:, 0:MEM], AXX, ALU.max, negate=True))
                V.tensor_scalar(cx_stat[:, 0, j:j + 1], cx_stat[:, 0, j:j + 1], XSCALE, None, ALU.mult).then_inc(S("att_max"), 1)

            def second(j):
                v.wait_ge(S("att_exp"), 16 + j + 1)
                link(V.reciprocal(cx_stat[:, 2, j:j + 1], cx_stat[:, 1, j:j + 1]))
                V.tensor_scalar(cx_s[:, j % 4, :], cx_s[:, j % 4, :], cx_stat[:, 2, j:j + 1], None, ALU.mult).then_inc(S("att_probs"), 1)

            def out_(h):
                v.wait_ge(S("att_pv"), 16 + h + 1)
                for ft in range(2):
                    V.tensor_copy(OM[:, 2 * h + ft, 0:SEQ], bank(4 + ft)).then_inc(S("att_out"), 1)

            first_(0)
            for j in range(16):
                if j + 1 < 16:
                    first_(j + 1)
                second(j)
                if j >= 6 and j % 4 == 2:
                    out_(j // 4 - 1)
            out_(3)

        def cross_prompt_scalar(s):
            def ex(j):
                s.wait_ge(S("att_max"), 16 + j + 1)
                if j >= 4:
                    s.wait_ge(S("att_turned"), 16 + j - 3)
                A.activation(cx_s[:, j % 4, :], bank(j % 4)[:, 0:MEM], ACT.Exp, bias=cx_stat[:, 0, j:j + 1], scale=XSCALE,
                             accum_out=cx_stat[:, 1, j:j + 1]).then_inc(S("att_exp"), 1)

            ex(0)
            for j in range(16):
                if j + 1 < 16:
                    ex(j + 1)
                h, i = divmod(j, 4)
                s.wait_ge(S("att_turned"), 16 + j + 1)
                if h >= 2 and i == 0:
                    s.wait_ge(S("att_pv"), 16 + h - 1)
                scopy(cx_pt[:, h % 2, :, i * P:(i + 1) * P], bank(6 + j % 2)[:, 0:2 * P].rearrange("p (k t) -> p k t", t=P))\
                    .then_inc(S("att_pt"), 1)

        def cross_sample_tensor(pe):
            def turn(q):
                b, x = divmod(q, 4)
                if x == 0:
                    pe.wait_ge(S(f"cx_ring{b % 2}_in"), 16 * (b // 2 + 1))
                if q >= 2:
                    pe.wait_ge(S("keys_turned_s" if q % 2 == 0 else "keys_turned_v"), 32 + q // 2)
                for kk in range(2):
                    for i in range(2):
                        last = tr(bank(q % 2)[:, (2 * kk + i) * P:(2 * kk + i + 1) * P],
                                  cx_ring[:, b % 2, i * D + (2 * x + kk) * P:i * D + (2 * x + kk + 1) * P], P)
                last.then_inc(S("satt_turned"), 1)

            def score(q):
                b, h = divmod(q, 4)
                pe.wait_ge(S("keys_turned_s" if q % 2 == 0 else "keys_turned_v"), 32 + q // 2 + 1)
                for i in range(2):
                    for kk in range(2):
                        last = mm(bank(4)[:, i * P + b * 16 + h * 4:i * P + b * 16 + h * 4 + 4],
                                  cx_kt[:, q % 2, (2 * kk + i) * P:(2 * kk + i + 1) * P],
                                  xq[:, 2 * h + kk, SEQ + b * TS:SEQ + (b + 1) * TS], kk == 0, kk == 1)
                last.then_inc(S("satt_scored"), 1)

            turn(0)
            for q in range(1, 32):
                turn(q)
                score(q - 1)
            score(31)
            pe.wait_ge(S("satt_st"), 8 + 1)
            for i in range(2):
                last = tr(bank(0)[:, i * P:(i + 1) * P], cx_st[:, i, :], P)
            last.then_inc(S("satt_rows"), 1)
            pe.wait_ge(S("satt_probs"), 1 + 1)
            for i in range(2):
                last = tr(bank(1)[:, i * P:(i + 1) * P], cx_ss[:, i * P:(i + 1) * P], P)
            last.then_inc(S("satt_pt"), 1)
            pe.wait_ge(S("satt_pt_out"), 2 + 1)
            for b in range(NB):
                pe.wait_ge(S(f"cx_ring{b % 2}_in"), 16 * (4 + b // 2 + 1))
                for k in range(KD):
                    for i in range(2):
                        last = mm(bank(5)[:, k * NS + b * TS:k * NS + (b + 1) * TS],
                                  cx_ring[:, b % 2, i * D + k * P:i * D + (k + 1) * P],
                                  cx_pts[:, i, b * 16 + (k // 2) * 4:b * 16 + (k // 2) * 4 + 4], i == 0, i == 1)
                last.then_inc(S("satt_pv"), 1)

        def cross_sample_vector(v):
            for q in range(1, 32, 2):
                v.wait_ge(S("satt_turned"), 64 + q + 1)
                if q >= 2:
                    v.wait_ge(S("satt_scored"), 64 + q - 1)
                V.tensor_copy(cx_kt[:, q % 2, 0:512], bank(q % 2)).then_inc(S("keys_turned_v"), 1)
            v.wait_ge(S("satt_scored"), 64 + 32)
            V.tensor_copy(cx_st, bank(4)[:, 0:256].rearrange("p (i r) -> p i r", r=P)).then_inc(S("satt_st"), 1)
            v.wait_ge(S("satt_rows"), 1 + 1)
            link(V.tensor_reduce(cx_stat[:, 0, 0:1], bank(0)[:, 0:MEM], AXX, ALU.max, negate=True))
            V.tensor_scalar(cx_stat[:, 0, 0:1], cx_stat[:, 0, 0:1], XSCALE, None, ALU.mult).then_inc(S("satt_max"), 1)
            v.wait_ge(S("satt_exp"), 1 + 1)
            link(V.reciprocal(cx_stat[:, 2, 0:1], cx_stat[:, 1, 0:1]))
            V.tensor_scalar(cx_ss, cx_ss, cx_stat[:, 2, 0:1], None, ALU.mult).then_inc(S("satt_probs"), 1)
            v.wait_ge(S("satt_pt"), 2 + 1)
            V.tensor_copy(cx_pts, bank(1)[:, 0:256].rearrange("p (i r) -> p i r", r=P)).then_inc(S("satt_pt_out"), 1)
            v.wait_ge(S("satt_pv"), 1 + NB)
            V.tensor_copy(OM[:, :, SEQ:T], bank(5)[:, 0:KD * NS].rearrange("p (k t) -> p k t", t=NS))

        def cross_sample_scalar(s):
            for q in range(0, 32, 2):
                s.wait_ge(S("satt_turned"), 64 + q + 1)
                if q >= 2:
                    s.wait_ge(S("satt_scored"), 64 + q - 1)
                scopy(cx_kt[:, q % 2, 0:512], bank(q % 2)).then_inc(S("keys_turned_s"), 1)
            s.wait_ge(S("satt_max"), 1 + 1)
            A.activation(cx_ss, bank(0)[:, 0:MEM], ACT.Exp, bias=cx_stat[:, 0, 0:1], scale=XSCALE,
                         accum_out=cx_stat[:, 1, 0:1]).then_inc(S("satt_exp"), 1)

        def ff_tensor(pe):
            for t in range(KF):
                for gu in range(2):
                    job = 2 * t + gu
                    if job >= 4:
                        pe.wait_ge(S("ff_out"), t - 1)
                    w = weights(pe, first["wgu"] + 2 * (t // 2) + gu)
                    for k in range(KD):
                        for j in range(2):
                            last = mm(PS[job % 4][:, j, 0:HT], w[:, k, (t % 2) * P:(t % 2) * P + P], xn[:, k, j * HT:(j + 1) * HT],
                                      k == 0, k == KD - 1)
                    last.then_inc(S("ff_mm"), 1)

        def ff_scalar(s):
            for t in range(KF):
                s.wait_ge(S("ff_mm"), 2 * t + 1)
                if t >= 4:
                    s.wait_ge(S("ff_out"), t - 3)
                A.activation(halves(f_g[:, t % 4, :]), pair((2 * t) % 4), ACT.Silu).then_inc(S("ff_silu"), 1)

        def ff_vector(v):
            for t in range(KF):
                v.wait_ge(S("ff_silu"), t + 1)
                v.wait_ge(S("ff_mm"), 2 * t + 2)
                tt(halves(hT[:, t, :]), halves(f_g[:, t % 4, :]), pair((2 * t + 1) % 4), ALU.mult).then_inc(S("ff_out"), 1)

        def result_tensor(pe):
            for job in range(10):
                i, hf = divmod(job, 2)
                t0, w, _ = TILES[i]
                if job >= 8:
                    pe.wait_ge(S("turned_out_v" if job % 2 == 0 else "turned_out_s"), (6 if job % 2 == 0 else 5) + 1)
                for k in range(4):
                    last = tr(bank(job % 8)[0:w, k * P:(k + 1) * P], XT[:, 4 * hf + k, t0:t0 + w], P)
                last.then_inc(S("turned"), 1)

        def result_evac(eng, copy, name, par_):
            for job in range(par_, 10, 2):
                i, hf = divmod(job, 2)
                w = TILES[i][1]
                eng.wait_ge(S("turned"), 11 + job + 1)
                copy(y_tok[0:w, i, hf * 512:(hf + 1) * 512], bank(job % 8)[0:w, :]).then_inc(S(name), 1)

        def stage(eng, name, *work):
            n = STAGES.index(name)
            if n:
                eng.wait_ge(S("stage_ended"), 3 * n)
            for f in work:
                f()
            eng.drain().then_inc(S("stage_ended"), 1)

        xkt = lambda k: xn[:, k, :]
        omt = lambda k: OM[:, k, :]
        win_dst = lambda i: proj[:, i, :]
        xn_dst = lambda i: xn[:, i, :]
        xq_dst = lambda i: xq[:, i, :]

        @block.tensor
        def _(pe):
            stage(pe, "inputs", lambda: inputs_tensor(pe))
            stage(pe, "mixpre", lambda: norm_tensor(pe, "mixpre", xn, T))
            stage(pe, "win", lambda: win_tensor(pe))
            stage(pe, "moba_prompt", lambda: moba_prompt_tensor(pe))
            stage(pe, "moba_sample", lambda: moba_sample_tensor(pe))
            stage(pe, "rows", lambda: rows_tensor(pe))
            stage(pe, "ssm", lambda: ssm_tensor(pe))
            stage(pe, "hgrn", lambda: hgrn_tensor(pe))
            stage(pe, "gdn", lambda: gdn_tensor(pe))
            stage(pe, "wout", lambda: gemm_tensor(pe, "wout", first["wout"], KD, omt))
            stage(pe, "mixpost", lambda: norm_tensor(pe, "mixpost", OM, T))
            stage(pe, "mem", lambda: mem_tensor(pe))
            stage(pe, "xpre", lambda: norm_tensor(pe, "xpre", xn, T))
            stage(pe, "xq", lambda: gemm_tensor(pe, "wxq", first["wxq"], KD, xkt))
            stage(pe, "cross_prompt", lambda: cross_prompt_tensor(pe))
            stage(pe, "cross_sample", lambda: cross_sample_tensor(pe))
            stage(pe, "wxo", lambda: gemm_tensor(pe, "wxo", first["wxo"], KD, omt))
            stage(pe, "xpost", lambda: norm_tensor(pe, "xpost", OM, T))
            stage(pe, "fpre", lambda: norm_tensor(pe, "fpre", xn, T))
            stage(pe, "ff", lambda: ff_tensor(pe))
            stage(pe, "wdn", lambda: gemm_tensor(pe, "wdn", first["wdn"], KD, lambda k: hT[:, k, :], 3))
            stage(pe, "fpost", lambda: norm_tensor(pe, "fpost", OM, T))
            stage(pe, "result", lambda: result_tensor(pe))

        @block.vector
        def _(v):
            stage(v, "inputs", lambda: inputs_evac("v", v, vcopy, "turned_out_v", 0))
            stage(v, "mixpre", lambda: norm_vector(v, XT, xn, T, R_MIXPRE, xn))
            stage(v, "win", lambda: gemm_vector(v, "win", NPROJ, win_dst), lambda: win_small_vector(v))
            stage(v, "moba_prompt", lambda: moba_prompt_vector(v))
            stage(v, "moba_sample", lambda: moba_sample_vector(v))
            stage(v, "rows", lambda: rows_vector(v))
            stage(v, "ssm", lambda: ssm_vector(v))
            stage(v, "hgrn", lambda: hgrn_vector(v), lambda: hgrn_vector_tail(v))
            stage(v, "gdn", lambda: gdn_vector(v))
            stage(v, "wout", lambda: v.wait_ge(S("states_out"), 96), lambda: gemm_vector(v, "wout", KD, xn_dst))
            stage(v, "mixpost", lambda: norm_vector(v, xn, OM, T, R_MIXPOST, xn, XT))
            stage(v, "mem", lambda: mem_vector(v))
            stage(v, "xpre", lambda: norm_vector(v, XT, xn, T, R_XPRE, xn))
            stage(v, "xq", lambda: gemm_vector(v, "wxq", KD, xq_dst))
            stage(v, "cross_prompt", lambda: cross_prompt_vector(v))
            stage(v, "cross_sample", lambda: cross_sample_vector(v))
            stage(v, "wxo", lambda: gemm_vector(v, "wxo", KD, xn_dst))
            stage(v, "xpost", lambda: norm_vector(v, xn, OM, T, R_XPOST, xn, XT))
            stage(v, "fpre", lambda: norm_vector(v, XT, xn, T, R_FPRE, xn))
            stage(v, "ff", lambda: v.wait_ge(S("mem_kv_out"), 64), lambda: ff_vector(v))
            stage(v, "wdn", lambda: gemm_vector(v, "wdn", KD, xn_dst))
            stage(v, "fpost", lambda: norm_vector(v, xn, OM, T, R_FPOST, xn, XT))
            stage(v, "result", lambda: result_evac(v, vcopy, "turned_out_v", 0))

        @block.scalar
        def _(s):
            stage(s, "inputs", lambda: inputs_evac("s", s, scopy, "turned_out_s", 1))
            stage(s, "mixpre", lambda: norm_scalar(s, XT, xn, T))
            stage(s, "win", lambda: gemm_scalar(s, "win", NPROJ, win_dst))
            stage(s, "moba_prompt", lambda: moba_prompt_scalar(s))
            stage(s, "moba_sample", lambda: moba_sample_scalar(s))
            stage(s, "rows", lambda: rows_scalar(s))
            stage(s, "ssm", lambda: ssm_scalar(s))
            stage(s, "hgrn", lambda: hgrn_scalar(s))
            stage(s, "gdn", lambda: gdn_scalar(s))
            stage(s, "wout", lambda: s.wait_ge(S("states_out"), 96), lambda: gemm_scalar(s, "wout", KD, xn_dst))
            stage(s, "mixpost", lambda: norm_scalar(s, xn, OM, T))
            stage(s, "mem", lambda: mem_scalar(s))
            stage(s, "xpre", lambda: norm_scalar(s, XT, xn, T))
            stage(s, "xq", lambda: gemm_scalar(s, "wxq", KD, xq_dst))
            stage(s, "cross_prompt", lambda: cross_prompt_scalar(s))
            stage(s, "cross_sample", lambda: cross_sample_scalar(s))
            stage(s, "wxo", lambda: gemm_scalar(s, "wxo", KD, xn_dst))
            stage(s, "xpost", lambda: norm_scalar(s, xn, OM, T))
            stage(s, "fpre", lambda: norm_scalar(s, XT, xn, T))
            stage(s, "ff", lambda: ff_scalar(s))
            stage(s, "wdn", lambda: gemm_scalar(s, "wdn", KD, xn_dst))
            stage(s, "fpost", lambda: norm_scalar(s, xn, OM, T))
            stage(s, "result", lambda: result_evac(s, scopy, "turned_out_s", 1))

        @block.gpsimd
        def _(g):
            def st(dst, src, name):
                g.dma_start(dst, src).then_inc(S(name), 16)

            g_constants(g)
            g_moba_prompt_table(g)
            g.wait_ge(S("kv_out"), NT)
            for kv in range(2):
                for i in range(4):
                    st(o["moba_kp" if kv == 0 else "moba_vp"][0, 0].rearrange("s h d -> s (h d)")[i * P:(i + 1) * P, :],
                       kvtok[:, i, kv * GW:(kv + 1) * GW], "moba_kv_out")
                st(o["moba_ks" if kv == 0 else "moba_vs"][0].rearrange("b t h d -> (b t) (h d)"),
                   kvs[0:NS, kv * GW:(kv + 1) * GW], "moba_kv_out")
            g_moba_sample_table(g)
            g.wait_ge(S("conv_states_made"), 1)
            for m_ in range(2):
                n_ = "ssm_conv" if m_ == 0 else "gdn_conv"
                st(o[n_ + "_p"][0, 0], cw_out[0:3, m_ * 768:(m_ + 1) * 768], "conv_states_out")
                st(o[n_ + "_s"][0].rearrange("b w c -> (b w) c"), cw_out[3:27, m_ * 768:(m_ + 1) * 768], "conv_states_out")
            g.wait_ge(S("fin_made"), 1)
            st(o["ssm_p"][0, 0].rearrange("(c e) q n -> (e q) c n", e=2), s_fin, "states_out")
            g.wait_ge(S("states_made"), 1)
            st(o["ssm_s"][0].rearrange("b (c e) q n -> (e q) b c n", e=2), s_h0, "states_out")
            hgrn_gpsimd(g)
            for run, n_ in enumerate(("hgrn", "gdn")):
                g.wait_ge(S("fin_made"), run + 2)
                st(o[n_ + "_p"][0, 0].rearrange("(c e) k v -> (e k) c v", e=2), t_st, "states_out")
                g.wait_ge(S("states_made"), run + 2)
                st(o[n_ + "_s"][0].rearrange("b (c e) k v -> (e k) b c v", e=2), t_s0, "states_out")
            for mt in range(2):
                g.wait_ge(S("kvm_out_s" if mt == 0 else "kvm_out_v"), 8)
                for kv in range(2):
                    st(o["mem_k" if kv == 0 else "mem_v"][0, 0].rearrange("m h d -> m (h d)")[mt * P:(mt + 1) * P, :],
                       mkv[:, mt, kv * D:(kv + 1) * D], "mem_kv_out")
            for i in range(4):
                g.wait_ge(S("turned_out_v"), 6 + i + 1)
                g.wait_ge(S("turned_out_s"), 5 + i + 1)
                st(o["y_p"][0, i * P:(i + 1) * P, :], y_tok[:, i, :], "y_stored")
            g.wait_ge(S("turned_out_v"), 6 + 5)
            g.wait_ge(S("turned_out_s"), 5 + 5)
            st(o["y_s"].rearrange("b t d -> (b t) d"), y_tok[0:NS, 4, :], "y_stored")
            g.wait_ge(S("moba_kv_out"), 16 * 10)
            g.wait_ge(S("conv_states_out"), 16 * 4)
            g.wait_ge(S("states_out"), 16 * 6)
            g.wait_ge(S("mem_kv_out"), 16 * 4)
            g.wait_ge(S("y_stored"), 16 * 5)


_INS = ['x_prompt', 'x_sample', 'mem_prompt', 'cache_moba_k', 'cache_moba_v', 'page_table', 'cache_mem_k',
        'cache_mem_v', 'state_ssm_conv', 'state_ssm', 'state_hgrn', 'state_gdn_conv', 'state_gdn', 'n_mix_pre',
        'n_mix_post', 'w_in', 'w_out', 'ssm_conv_w', 'ssm_conv_b', 'ssm_dt_bias', 'ssm_a_log', 'ssm_d', 'ssm_norm',
        'hgrn_norm', 'gdn_conv_w', 'gdn_a_log', 'gdn_dt_bias', 'gdn_norm', 'n_x_pre', 'n_x_post',
        'mem_norm', 'w_xq', 'w_xkv', 'w_xo', 'n_f_pre', 'n_f_post', 'w_gu', 'w_down']
_OUTS = [("y_p", (1, 512, 1024)), ("y_s", (8, 4, 1024)),
         ("moba_kp", (1, 1, 512, 4, 64)), ("moba_ks", (1, 8, 4, 4, 64)),
         ("moba_vp", (1, 1, 512, 4, 64)), ("moba_vs", (1, 8, 4, 4, 64)),
         ("mem_k", (1, 1, 256, 4, 256)), ("mem_v", (1, 1, 256, 4, 256)),
         ("ssm_conv_p", (1, 1, 3, 768)), ("ssm_conv_s", (1, 8, 3, 768)),
         ("ssm_p", (1, 1, 4, 64, 128)), ("ssm_s", (1, 8, 4, 64, 128)),
         ("hgrn_p", (1, 1, 4, 64, 64)), ("hgrn_s", (1, 8, 4, 64, 64)),
         ("gdn_conv_p", (1, 1, 3, 768)), ("gdn_conv_s", (1, 8, 3, 768)),
         ("gdn_p", (1, 1, 4, 64, 64)), ("gdn_s", (1, 8, 4, 64, 64))]


def kernel(**inputs):
    import numpy as _np
    import concourse.bacc as _bacc
    from concourse import mybir as _mybir
    from concourse.bass_utils import run_bass_kernel_spmd as _run

    nc = _bacc.Bacc("TRN2", target_bir_lowering=False, num_devices=1)
    arrays, ins, outs = {}, {}, {}
    for name in _INS:
        x = _np.ascontiguousarray(inputs[name])
        arrays[f"in_{name}"] = x
        ins[name] = nc.dram_tensor(f"in_{name}", x.shape, _mybir.dt.from_np(x.dtype), kind="ExternalInput").ap()
    for name, shape in _OUTS:
        outs[name] = nc.dram_tensor(f"out_{name}", shape, _mybir.dt.float32, kind="ExternalOutput").ap()
    build(nc, ins, outs)
    r = _run(nc, [arrays], core_ids=[0])
    return tuple(r.results[0][f"out_{name}"] for name, _ in _OUTS)
```

```python
from contextlib import ExitStack

import concourse.bass as bass
from concourse import mybir

F32 = mybir.dt.float32
F32R = mybir.dt.float32r
I32 = mybir.dt.int32
ALU = mybir.AluOpType
ACT = mybir.ActivationFunctionType
AXX = mybir.AxisListType.X

P = 128
D = 1024
KD = D // P
SEQ = 512
NB, TS = 8, 4
NS = NB * TS
T = SEQ + NS
HT = T // 2
GW = D // 4
H = 4
DH = GW // H
PAGE, NPAGE = 128, 16
MOBA_BLOCK = 256
NBLK = PAGE * NPAGE // MOBA_BLOCK
PAST = PAGE * NPAGE
MEM = 256
XDH = D // H
FF = 2816
KF = FF // P
NEG = -1.0e30
EPS = 1e-6
SCALE = DH ** -0.5
XSCALE = XDH ** -0.5
SLOPE = [2.0 ** (-8.0 * (h + 1) / H) for h in range(H)]

C_MQ, C_MK, C_MV, C_Z, C_XBC, C_HQ, C_HF, C_HI, C_HG, C_GQKV, C_GZ = 0, 2, 4, 6, 8, 14, 16, 18, 20, 22, 28
NPROJ = 30
WIN_COLS = [0, 256, 512, 768, 1024, 1280, 1536, 1796, 2052, 2308, 2564, 2820, 3076, 3332, 3588]
COL_DT, COL_B, COL_A = 1792, 3844, 3848

TILES = [(i * P, P, 7) for i in range(SEQ // P)] + [(SEQ, NS, 2)]
NT = len(TILES)

R_MIXPRE, R_MIXPOST, R_XPRE, R_XPOST, R_MEM, R_FPRE, R_FPOST = [8 * i for i in range(7)]
R_SCW, R_GCW, R_SCB, R_SNORM, R_HNORM, R_GNORM, R_SD = 56, 80, 104, 110, 112, 113, 114
NROWS = 116


def build(nc, a, o):
    ctx = ExitStack()
    sems = {}

    STAGES = ["inputs", "win", "moba_prompt", "moba_sample", "spread", "ssm", "hgrn", "gdn", "mem", "wout",
              "cross_prompt", "cross_sample", "wxo", "wdn", "result"]

    def S(name):
        if name not in sems:
            sems[name] = ctx.enter_context(nc.semaphore(name))
        return sems[name]

    with ctx:
        def sb(name, shape, dt=F32):
            return ctx.enter_context(nc.sbuf_tensor(name, shape, dt))

        def sb2(name, shape):
            at = (nc.sbuf_base + 31) // 32 * 32
            return sb(name, shape), nc.alloc_sbuf_tensor_at(name + "_parts", shape, F32R, offset=at)

        XT = sb("XT", [P, KD, T])
        XN, XN_R = sb2("XN", [P, KD * T])
        OM, OM_R = sb2("OM", [P, KD, T])
        PROJ, PROJ_R = sb2("PROJ", [P, NPROJ * T])
        NW, NH, WSZ = 3, 3, 8 * P
        W = sb("W", [P, NW, WSZ])
        W_HI = sb("W_HI", [P, NH, WSZ], F32R)
        W_LO = sb("W_LO", [P, NH, WSZ], F32R)
        SC, SC_R = sb2("SC", [P, 9200])
        CN = sb("CN", [P, 2900])
        SM = sb("SM", [P, 400])
        PTAB = sb("PTAB", [1, P], I32)
        PS = [ctx.enter_context(nc.psum_tensor(f"PS{i}", [P, 2, 512], F32)) for i in range(4)]

        def bank(i):
            return PS[i // 2][:, i % 2, :]

        def pair(i):
            return PS[i][:, :, 0:HT]

        def carve(buf, at, *shape):
            n = 1
            for s in shape:
                n *= s
            v = buf[:, at:at + n]
            if len(shape) == 2:
                v = v.rearrange("p (a b) -> p a b", b=shape[1])
            elif len(shape) == 3:
                v = v.rearrange("p (a b c) -> p a b c", b=shape[1], c=shape[2])
            return v

        class Carver:
            def __init__(self, buf, at=0, size=None):
                self.buf, self.at = buf, at

            def __call__(self, *shape):
                v = carve(self.buf, self.at, *shape)
                n = 1
                for s in shape:
                    n *= s
                self.at += n
                assert self.at <= self.buf.shape[1], (self.at, self.buf.shape)
                return v

        proj = PROJ[:, :].rearrange("p (c t) -> p c t", t=T)
        xn = XN[:, :].rearrange("p (c t) -> p c t", t=T)

        c = Carver(CN)
        ident = c(P)
        ones = c(P)
        blk64 = c(P)
        lev = c(8, P)
        negmask = c(P)
        negmask_s = c(NS)
        ind = c(NB)
        keep = c(T)
        onehot = c(H, P)
        pairsel = c(2, P)
        eps = c(1)
        prm = SM[:, 0:NROWS]
        sm = Carver(SM, NROWS)
        head4 = sm(8)

        def par(r):
            return prm[:, r:r + 1]

        chunks = []

        def add(w, k0, nk, c0, ncol, sem, count):
            chunks.append((w.rearrange("(k p) n -> p k n", p=P)[:, k0:k0 + nk, c0:c0 + ncol], nk, ncol, sem, count))

        win = a["w_in"][0]
        first = {}

        def section(name):
            first[name] = len(chunks)

        BEFORE = {"wout": NPROJ, "wkv": 0, "wxq": NPROJ + KD, "wxo": NPROJ + 2 * KD, "wdn": NPROJ + 3 * KD}
        section("win")
        for i in range(NPROJ):
            add(win, 0, 8, WIN_COLS[i // 2] + P * (i % 2), P, "gemm_mm", i + 1)
        section("wkv")
        for n in range(8):
            add(a["w_xkv"][0], 0, 4, 256 * n, 256, "kvm_part", n + 1)
            add(a["w_xkv"][0], 4, 4, 256 * n, 256, "kvm_mm", 2 * n + 2)
        for name, src in (("wout", a["w_out"][0]), ("wxq", a["w_xq"][0]), ("wxo", a["w_xo"][0])):
            section(name)
            for i in range(KD):
                add(src, 0, 8, P * i, P, "gemm_mm", BEFORE[name] + i + 1)
        section("wgu")
        for i in range(KF):
            add(a["w_gu"][0], 0, 8, P * i, P, "ff_mm", 2 * i + 1)
            add(a["w_gu"][0], 0, 8, FF + P * i, P, "ff_mm", 2 * i + 2)
        section("wdn")
        for i in range(KD):
            add(a["w_down"][0], 0, 8, P * i, P, "gemm_part", 2 * i + 1)
            add(a["w_down"][0], 8, 8, P * i, P, "gemm_part", 2 * i + 2)
            add(a["w_down"][0], 16, 6, P * i, P, "gemm_mm", BEFORE["wdn"] + i + 1)

        def load_chunks(eng, n0, n1):
            for n in range(n0, n1):
                src, nk, ncol, _, _ = chunks[n]
                if n >= NW:
                    eng.wait_ge(S("weights_split"), n - NW + 1)
                eng.dma_start(W[:, n % NW, 0:nk * ncol].rearrange("p (k n) -> p k n", n=ncol), src)\
                   .then_inc(S(f"weights_in{n % NW}"), 16)

        parts_made = {"hi": 0, "lo": 0}

        def split_hi(s, upto):
            for n in range(parts_made["hi"], min(upto, len(chunks))):
                _, nk, ncol, _, _ = chunks[n]
                s.wait_ge(S(f"weights_in{n % NW}"), 16 * (n // NW + 1))
                if n >= NH:
                    s.wait_ge(S(chunks[n - NH][3]), chunks[n - NH][4])
                nc.scalar.activation(W_HI[:, n % NH, 0:nk * ncol], W[:, n % NW, 0:nk * ncol], ACT.Copy)\
                    .then_inc(S("weights_hi"), 1)
                parts_made["hi"] = n + 1

        def split_lo(g, upto):
            for n in range(parts_made["lo"], min(upto, len(chunks))):
                _, nk, ncol, _, _ = chunks[n]
                g.wait_ge(S("weights_hi"), n + 1)
                nc.gpsimd.tensor_tensor(W_LO[:, n % NH, 0:nk * ncol], W[:, n % NW, 0:nk * ncol],
                                        W_HI[:, n % NH, 0:nk * ncol].bitcast(F32), ALU.subtract).then_inc(S("weights_split"), 1)
                parts_made["lo"] = n + 1

        def weights(pe, n):
            _, nk, ncol, _, _ = chunks[n]
            pe.wait_ge(S("weights_split"), n + 1)
            return [b[:, n % NH, 0:nk * ncol].rearrange("p (k n) -> p k n", n=ncol) for b in (W_HI, W_LO)]

        def mm3(out, l, r, start, stop):
            mm(out, l[0], r[0], start, False)
            mm(out, l[0], r[1], False, False)
            return mm(out, l[1], r[0], False, stop)

        def mm(out, lhsT, rhs, start, stop):
            return nc.tensor.matmul(out, lhsT, rhs, start=start, stop=stop, skip_group_check=True)

        def tr(out, in_, k):
            return nc.tensor.transpose(out, in_, ident[0:k, 0:k])

        links = {"v": 0, "s": 0, "g": 0}
        chain_eng = {"v": nc.vector, "s": nc.scalar, "g": nc.gpsimd}
        chain_name = {"v": "vector_chain", "s": "scalar_chain", "g": "gpsimd_chain"}

        def link(ins, e="v"):
            links[e] += 1
            ins.then_inc(S(chain_name[e]), 1)
            chain_eng[e].wait_ge(S(chain_name[e]), links[e])

        def after(eng, name):
            eng.wait_ge(S("stage_ended"), 3 * (STAGES.index(name) + 1))

        V, A, G = nc.vector, nc.scalar, nc.gpsimd

        cumtok = sm(NT, 8)
        rsq = sb("RSQ", [P, T])
        ups = sb("UPS", [P, 12, NB, 7])
        w_small = sb("WSMALL", [P, 3, KD, H])
        w_small_hi = sb("WSMALL_HI", [P, 3, KD, H], F32R)
        w_small_lo = sb("WSMALL_LO", [P, 3, KD, H], F32R)

        x_tok = carve(PROJ, 0, 4, D)
        xs_tok = carve(PROJ, 4 * D, D)
        rows_in = carve(PROJ, 5 * D, P)
        cs_tok = carve(PROJ, 6 * D, 2, 768)
        raw = OM[0:H, 0:2, :]
        rows_t = SC[0:H, 4 * T:8 * T].rearrange("p (c t) -> p c t", t=T)
        rows_d = OM[0:H, 2:4, :]
        rawc = carve(SC, 0, 4, T)
        cw_in = carve(SC, 16 * T, 12, 27)
        cw_out = OM[0:27, 0:3, :].rearrange("p a b -> p (a b)")[:, 0:12 * P]
        m = Carver(SC)
        kvs = m(2 * GW)
        kvtok = m(4, 2 * GW)
        mp_s = m(4, SEQ)
        mp_pt = OM[:, 2:4, 0:SEQ]
        mp_stat = m(3, 16)
        mp_bias = carve(XN, 0, H, SEQ)
        m = Carver(SC, 4680)
        NPG = 4
        pages = m(NPG, 4, 2 * P)
        ms_q = m(2, P)
        ms_pown = m(P)
        m = Carver(SC, 2 * GW)
        ms_kt = [m(512), m(512), OM[:, 2, 0:512], OM[:, 3, 0:512]]
        st_all = m(NPAGE, P)
        ms_qp = m(2, NB, 32)
        ms_gate = m(8)
        ms_gt = m(8, 8)
        ms_eq = m(8, 8)
        ms_rank = m(8)
        ms_sel = m(8)
        ms_stat = m(4)
        ms_s = carve(XN, 0, PAST + NS)
        ms_o = carve(XN, 0, 2, GW)
        ms_bias = carve(XN, PAST + NS, PAST + NS)
        ms_rowtmp = sm(NS)
        mr = sm(1)
        tr_ = sm(1)
        g8 = sm(NB)
        cr = sm(1)
        ltm = sm(8, 8)
        xc = proj[:, C_XBC:C_XBC + 6, :]
        pb = carve(PROJ, 0, 3, 2, T)
        rows = OM[0:H, 4:8, :]
        m = Carver(SC)
        xdt = m(2, T)
        s_m = m(H, P)
        s_er = m(H, P)
        s_c = m(H, P)
        s_tok = m(512)
        s_xd = m(2 * P)
        s_ht = m(2 * P)
        s_h0t = m(NB, 2 * P)
        s_dl = m(H)
        s_h0 = carve(XN, 4 * T, NB, 2, P)
        s_dec = sm(2, NB)
        m = Carver(SC)
        h_b = m(2, T)
        h_k = m(2, T)
        h_d = m(2, T)
        h_q1 = m(2, 2, T)
        h_k1 = m(2, 2, T)
        h_att = carve(PROJ, C_Z * T, 4 * 512 + H * NS)
        h_msk = carve(PROJ, C_Z * T + 2176, 4 * 512)
        m = Carver(SC)
        g_kb = m(2, T)
        g_kbg = m(2, T)
        g_qg = m(2, T)
        g_p1 = m(4, 512)
        t_kd = m(2, T)
        t_vm = m(H * NB * DH)
        base = C_Z * T
        g_T = carve(PROJ, base, 2176)
        g_N = carve(PROJ, base + 2176, 2176)
        g_A = carve(PROJ, base + 2 * 2176, 2176)
        g_QK = carve(PROJ, base + 3 * 2176, 2176)
        g_sq = carve(PROJ, C_HQ * T, 4, T)
        m = Carver(XN, 4 * T)
        t_tok = m(512)
        t_vn = m(2 * P)
        t_st = m(2, DH)
        t_last = m(2, NB)
        t_s0 = m(NB, 2, DH)
        memt = carve(SC, 0, KD, MEM)
        memn = carve(SC, KD * MEM, KD, MEM)
        mkv = carve(PROJ, 0, 2, 2 * D)
        mkt = carve(PROJ, 4 * D, KD, MEM)
        xq = carve(PROJ, 6 * D, KD, T)
        m = Carver(SC)
        cx_s = m(4, MEM)
        cx_pt = m(2, 2, SEQ)
        cx_stat = m(3, 16)
        cx_ss = m(MEM)
        cx_pts = m(2, P)
        cx_kt = m(4, 512)
        cx_o = carve(SC, 0, 2, D)
        cx_qp = carve(XN, 0, KD, NB, 32)
        cx_slots = [carve(PROJ, 6 * D + KD * T, 2 * D), carve(PROJ, 8 * D + KD * T, 2 * D), carve(SC, 9200 - 2 * D, 2 * D)]

        def cx_slot(n):
            return cx_slots[n % 3]

        hT = PROJ[:, 0:KF * T].rearrange("p (c t) -> p c t", t=T)
        f_g = carve(SC, 14 * T, 2, T)
        y_tok = carve(PROJ, 0, 5, D)

        block = ctx.enter_context(nc.Block())

        def load_pages(eng, par_):
            for n in range(par_, 64, 2):
                cache = a["cache_moba_k"] if n < 32 else a["cache_moba_v"]
                ids = [eng.value_load(PTAB[0:1, (n % 32) * 4 + i:(n % 32) * 4 + i + 1], min_val=0,
                                      max_val=a["cache_moba_k"].shape[1] - 1) for i in range(4)]
                m_ = n - NPG
                if 0 <= m_ < 32:
                    eng.wait_ge(S("satt_turned"), 2 * m_ + 2)
                elif m_ >= 32:
                    eng.wait_ge(S("ms_values_used"), m_ - 31)
                else:
                    after(eng, "win")
                for i in range(4):
                    eng.dma_start(pages[:, n % NPG, i, :],
                                  cache[0].rearrange("g p h d -> g p (h d)")[bass.ds(ids[i], 1)].rearrange("g p n -> (g p) n"))\
                       .then_inc(S(f"pages{n % NPG}_in"), 16)

        @block.sync
        def _(sp):
            def ld(dst, src, name):
                sp.dma_start(dst, src).then_inc(S(name), 16)

            for i in range(4):
                ld(x_tok[:, i, :], a["x_prompt"][0, i * P:(i + 1) * P, :], "x_in")
            ld(xs_tok[0:NS, :], a["x_sample"].rearrange("b t d -> (b t) d"), "params_in")
            for r, n in ((R_MIXPRE, "n_mix_pre"), (R_MIXPOST, "n_mix_post"), (R_XPRE, "n_x_pre"),
                         (R_XPOST, "n_x_post"), (R_MEM, "mem_norm"), (R_FPRE, "n_f_pre"), (R_FPOST, "n_f_post")):
                ld(rows_in[r:r + 8, :], a[n].rearrange("o (k p) -> (o k) p", p=P), "params_in")
            for w in range(4):
                ld(rows_in[R_SCW + 6 * w:R_SCW + 6 * w + 6, :], a["ssm_conv_w"][0, w].rearrange("(k p) -> k p", p=P), "params_in")
                ld(rows_in[R_GCW + 6 * w:R_GCW + 6 * w + 6, :], a["gdn_conv_w"][0, w].rearrange("(k p) -> k p", p=P), "params_in")
            ld(rows_in[R_SCB:R_SCB + 6, :], a["ssm_conv_b"].rearrange("o (k p) -> (o k) p", p=P), "params_in")
            ld(rows_in[R_SNORM:R_SNORM + 2, :], a["ssm_norm"].rearrange("o (k p) -> (o k) p", p=P), "params_in")
            for i in range(2):
                ld(rows_in[R_HNORM:R_HNORM + 1, i * DH:(i + 1) * DH], a["hgrn_norm"], "params_in")
                ld(rows_in[R_GNORM:R_GNORM + 1, i * DH:(i + 1) * DH], a["gdn_norm"], "params_in")
                for j in range(2):
                    ld(rows_in[R_SD + i:R_SD + i + 1, j * DH:(j + 1) * DH].rearrange("r (d o) -> r d o", o=1),
                       a["ssm_d"][:, 2 * i + j:2 * i + j + 1].rearrange("r (d o) -> r d o", o=1).to_broadcast((1, DH, 1)),
                       "params_in")
            for i, n in enumerate(("ssm_a_log", "ssm_dt_bias", "gdn_a_log", "gdn_dt_bias")):
                ld(head4[0:H, i:i + 1], a[n].rearrange("o h -> h o"), "params_in")
            ld(cs_tok[0:24, 0, :], a["state_ssm_conv"][0].rearrange("b w c -> (b w) c"), "params_in")
            ld(cs_tok[0:24, 1, :], a["state_gdn_conv"][0].rearrange("b w c -> (b w) c"), "params_in")
            ld(PTAB[0:1, :], a["page_table"].rearrange("b n -> (b n)").rearrange("(o n) -> o n", o=1), "pages_in")
            for i, c0 in enumerate((COL_DT, COL_B, COL_A)):
                ld(w_small[:, i, :, :], win.rearrange("(k p) n -> p k n", p=P)[:, :, c0:c0 + H], "params_in")
            load_chunks(sp, 0, first["wkv"] + NW)
            sp.wait_ge(S("pages_in"), 16)
            load_pages(sp, 0)
            load_chunks(sp, first["wkv"] + NW, first["wkv"] + 2 * NW)
            after(sp, "moba_sample")
            sp.dma_start(s_h0, a["state_ssm"][0].rearrange("b (c e) q n -> (e q) b c n", e=2)).then_inc(S("state_in"), 16)
            after(sp, "ssm")
            sp.wait_ge(S("states_out"), 32)
            sp.dma_start(t_s0, a["state_hgrn"][0].rearrange("b (c e) k v -> (e k) b c v", e=2)).then_inc(S("state_in"), 16)
            sp.wait_ge(S("g_inverted"), 1)
            sp.dma_start(t_s0, a["state_gdn"][0].rearrange("b (c e) k v -> (e k) b c v", e=2)).then_inc(S("state_in"), 16)
            after(sp, "gdn")
            for i in range(2):
                ld(mkv[:, i, 0:D], a["mem_prompt"][0, i * P:(i + 1) * P, :], "mem_in")
            load_chunks(sp, first["wkv"] + 2 * NW, first["wxo"] + NW)
            for n in range(16):
                src = a["cache_mem_k"] if n < 8 else a["cache_mem_v"]
                if n == 2:
                    after(sp, "wout")
                if n >= 3:
                    if n < 11:
                        sp.wait_ge(S("satt_turned"), 64 + 4 * (n - 2))
                    else:
                        sp.wait_ge(S("satt_pv"), 1 + n - 10)
                sp.dma_start(cx_slot(n).rearrange("p (i n) -> p i n", n=D),
                             src[0, n % 8].rearrange("(i p) h d -> p i (h d)", p=P)).then_inc(S(f"cx_ring{n % 3}_in"), 16)
            load_chunks(sp, first["wxo"] + NW, len(chunks))

        def fill(view, pattern, base, mult, op, fillv):
            return G.affine_select(out=view, in_=view, compare_op=op, fill=fillv, base=base, pattern=pattern,
                                   channel_multiplier=mult)

        def g_constants(g):
            L = lambda ins: link(ins, "g")
            L(G.memset(CN[:, :], 0.0))
            L(G.memset(ones, 1.0))
            L(G.memset(keep, 1.0))
            L(G.memset(eps, EPS))
            L(G.memset(blk64[0:64, 0:64], 1.0))
            L(G.memset(blk64[64:128, 64:128], 1.0))
            L(fill(ident, [[-1, P]], 0, 1, ALU.not_equal, 1.0))
            L(G.memset(lev[:, 0, :], 0.0))
            L(fill(lev[:, 0, :], [[-1, P]], 0, 1, ALU.not_equal, 1.0))
            for j in range(1, 8):
                B = 1 << j
                r = lev[:, j, :].rearrange("p (n i) -> p n i", i=B)[:, :, B // 2:B]
                L(G.memset(r, 1.0))
                L(fill(r, [[-B, P // B], [0, B // 2]], 0, 1, ALU.is_ge, 0.0))
                L(fill(r, [[B, P // B], [0, B // 2]], B // 2 - 1, -1, ALU.is_ge, 0.0))
            L(fill(negmask, [[1, P]], 0, -1, ALU.is_ge, NEG))
            L(fill(negmask_s[0:NS, :], [[1, NS]], 0, -1, ALU.is_ge, NEG))
            v = negmask_s[0:NS, :].rearrange("p (b t) -> p b t", t=TS)
            L(fill(v, [[-TS, NB], [0, TS]], 0, 1, ALU.is_ge, NEG))
            L(G.memset(ind, 1.0))
            L(fill(ind, [[-TS, NB]], 0, 1, ALU.is_ge, 0.0))
            L(fill(ind, [[TS, NB]], TS - 1, -1, ALU.is_ge, 0.0))
            L(G.memset(keep[:, 0:SEQ].rearrange("p (n i) -> p n i", i=P)[:, :, 0:1], 0.0))
            L(G.memset(keep[:, SEQ:T].rearrange("p (n i) -> p n i", i=TS)[:, :, 0:1], 0.0))
            L(G.memset(onehot, 1.0))
            L(fill(onehot, [[-1, H], [0, P]], 0, 1, ALU.is_equal, 0.0))
            ps = pairsel.rearrange("p c (e d) -> p c e d", e=2)
            L(G.memset(pairsel, 1.0))
            L(fill(ps, [[-2, 2], [-1, 2], [0, DH]], 0, 1, ALU.is_equal, 0.0))
            L(G.memset(g8, 1.0))
            L(fill(g8, [[-16, NB]], 0, 1, ALU.is_ge, 0.0))
            L(fill(g8, [[16, NB]], 15, -1, ALU.is_ge, 0.0))
            L(G.memset(ltm, 1.0))
            G.affine_select(out=ltm, in_=ltm, compare_op=ALU.is_gt, fill=0.0, base=0, pattern=[[1, 8], [-1, 8]],
                            channel_multiplier=0).then_inc(S("consts"), 1)
            g.wait_ge(S("consts"), 1)

        ms_grp = XN[:, 2 * (PAST + NS):2 * (PAST + NS) + 96]
        ms_int = XN[:, 2 * (PAST + NS) + 96:2 * (PAST + NS) + 128].bitcast(I32)

        def g_moba_tables(g):
            L = lambda ins: link(ins, "g")
            it = mp_s.rearrange("p a b -> p (a b)")[:, 0:SEQ].bitcast(I32)
            after(g, "win")
            L(G.iota(it, pattern=[[1, SEQ]], base=-384, channel_multiplier=-1))
            L(G.tensor_copy(mp_bias[:, 0, :], it))
            for h in range(H - 1, -1, -1):
                L(G.tensor_scalar(mp_bias[:, h, :], mp_bias[:, 0, :], SLOPE[h], None, ALU.mult))
            for h in range(H):
                last = fill(mp_bias[:, h, :], [[-1, SEQ]], 384, 1, ALU.is_ge, NEG)
            last.then_inc(S("mp_tables"), 1)
            grp, slope, gi = ms_grp[:, 0:32], ms_grp[:, 32:64], ms_grp[:, 64:96]
            L(G.memset(grp, 1.0))
            L(fill(grp, [[-4, 32]], 0, 1, ALU.is_ge, 0.0))
            L(fill(grp, [[4, 32]], 3, -1, ALU.is_ge, 0.0))
            for h in range(H):
                L(G.memset(slope.rearrange("p (b h) -> p b h", h=H)[:, :, h:h + 1], SLOPE[h]))
            L(G.iota(ms_int, pattern=[[-4, 32]], base=0, channel_multiplier=1))
            L(G.tensor_copy(gi, ms_int))
            L(G.tensor_tensor(slope, slope, grp, ALU.mult))
            L(G.tensor_tensor(gi, gi, grp, ALU.mult))
            L(G.iota(ms_bias[:, 0:PAST].bitcast(I32), pattern=[[1, PAST]], base=-PAST, channel_multiplier=0))
            L(G.tensor_copy(ms_bias[:, 0:PAST], ms_bias[:, 0:PAST].bitcast(I32)))
            L(G.iota(ms_bias[:, PAST:PAST + NS].bitcast(I32), pattern=[[0, NB], [1, TS]], base=0, channel_multiplier=0))
            G.tensor_copy(ms_bias[:, PAST:PAST + NS], ms_bias[:, PAST:PAST + NS].bitcast(I32)).then_inc(S("ms_tables"), 1)

        def tt(out, x, y, op):
            return V.tensor_tensor(out, x, y, op)

        def bc(ap, shape):
            return ap.to_broadcast(shape)

        SQ = {"s": 0, "v": 0}
        SUMS = {"pe": 0, "s": 0, "v": 0}

        def norm_tensor(pe, sq, n, all_scalar=False, after_gemm=None):
            if after_gemm:
                pe.wait_ge(S("gemm_out_s"), GEMM_OUT[after_gemm] + 3)
            for k in range(KD):
                e = "s" if all_scalar or k % 2 == 0 else "v"
                SQ[e] += 1
                pe.wait_ge(S("norm_sq_" + e), SQ[e])
                for j in range(2):
                    last = mm(bank(j)[:, 0:n // 2], ones, sq[:, k, j * n // 2:(j + 1) * n // 2], k == 0, k == KD - 1)
            last.then_inc(S("norm_sum"), 1)

        def squares_scalar(s, src, sq, ks=range(0, KD, 2), wait=None):
            for k in ks:
                if wait is not None:
                    s.wait_ge(S("residual"), wait + k + 1)
                A.activation(sq[:, k, :], src[:, k, :], ACT.Square).then_inc(S("norm_sq_s"), 1)

        def squares_vector(v, src, sq):
            for k in range(1, KD, 2):
                tt(sq[:, k, :], src[:, k, :], src[:, k, :], ALU.mult).then_inc(S("norm_sq_v"), 1)

        def root_scalar(s, n):
            SUMS["s"] += 1
            s.wait_ge(S("norm_sum"), SUMS["s"])
            A.activation(rsq[:, 0:n].rearrange("p (j t) -> p j t", j=2), PS[0][:, :, 0:n // 2], ACT.Sqrt,
                         bias=eps, scale=1.0 / D).then_inc(S("norm_root"), 1)

        def scale_vector(v, src, n, gain, dst, add=None, parts=None):
            SUMS["v"] += 1
            v.wait_ge(S("norm_root"), SUMS["v"])
            link(V.reciprocal(rsq[:, 0:n], rsq[:, 0:n]))
            for k in range(KD):
                last = V.scalar_tensor_tensor(dst[:, k, :], src[:, k, :], par(gain + k), rsq[:, 0:n], ALU.mult, ALU.mult)
                if parts is not None:
                    last.then_inc(S("normed"), 1)
                    if k:
                        part_lo(v, parts, k - 1)
                else:
                    link(last)
                    tt(add[:, k, :], add[:, k, :], dst[:, k, :], ALU.add).then_inc(S("residual"), 1)
            if parts is not None:
                part_lo(v, parts, KD - 1)

        IN_BEFORE = {"win": 0, "wkv": KD, "wout": 2 * KD, "wxq": 3 * KD, "wxo": 4 * KD, "wgu": 5 * KD, "wdn": 6 * KD}
        NORMED_BEFORE = {"win": 0, "wkv": KD, "wxq": 2 * KD, "wgu": 3 * KD}
        sc_hi = SC_R[:, KD * T:2 * KD * T].rearrange("p (k t) -> p k t", t=T)
        xn_lo = XN_R[:, :].rearrange("p (k t) -> p k t", t=T)
        tile_of = lambda b: (lambda k: b[:, k, :])
        proj_r = PROJ_R[:, :].rearrange("p (k t) -> p k t", t=T)
        sc_r = SC_R[:, 0:16 * T].rearrange("p (k t) -> p k t", t=T)
        INPUTS = {
            "win": (tile_of(xn), tile_of(sc_hi), tile_of(xn_lo)),
            "wkv": (tile_of(memn), lambda k: SC_R[:, k * MEM:(k + 1) * MEM], lambda k: SC_R[:, (KD + k) * MEM:(KD + k + 1) * MEM]),
            "wout": (tile_of(OM), tile_of(sc_hi), tile_of(OM_R)),
            "wxq": (tile_of(xn), tile_of(OM_R), tile_of(xn_lo)),
            "wxo": (tile_of(OM), tile_of(sc_hi), tile_of(OM_R)),
            "wgu": (tile_of(xn), tile_of(OM_R), tile_of(xn_lo)),
            "wdn": (tile_of(hT), lambda k: proj_r[:, KF + k, :] if k < 8 else sc_r[:, k - 8, :], tile_of(proj_r)),
        }

        def part_hi(s, name, k):
            x, hi, _ = INPUTS[name]
            if name in NORMED_BEFORE:
                s.wait_ge(S("normed"), NORMED_BEFORE[name] + k + 1)
            A.activation(hi(k), x(k), ACT.Copy).then_inc(S("part_hi"), 1)

        def part_lo(v, name, k):
            x, hi, lo = INPUTS[name]
            v.wait_ge(S("part_hi"), IN_BEFORE[name] + k + 1)
            tt(lo(k), x(k), hi(k).bitcast(F32), ALU.subtract).then_inc(S("part_lo"), 1)

        def parts_scalar(s, name):
            for k in range(KD):
                part_hi(s, name, k)

        def parts_vector(v, name):
            for k in range(KD):
                part_lo(v, name, k)

        def operand(name, k, cols):
            _, hi, lo = INPUTS[name]
            return hi(k)[:, cols], lo(k)[:, cols]

        GEMM_NAMES = ("win", "wout", "wxq", "wxo", "wdn")
        GEMM_MM = dict(zip(GEMM_NAMES, (0, NPROJ, NPROJ + KD, NPROJ + 2 * KD, NPROJ + 3 * KD)))
        GEMM_OUT = {n: (0 if n == "win" else (NPROJ + (GEMM_NAMES.index(n) - 1) * KD) // 2) for n in GEMM_NAMES}

        def gemm_tensor(pe, name, ntile, nparts=1):
            n0 = first[name]
            for i in range(ntile):
                k = 0
                for part in range(nparts):
                    wh, wl = weights(pe, n0 + i * nparts + part)
                    if i >= 4 and part == 0:
                        pe.wait_ge(S("gemm_out_s" if i % 2 == 0 else "gemm_out_v"), GEMM_OUT[name] + (i - 4) // 2 + 1)
                    nk = wh.shape[1]
                    for kk in range(nk):
                        if i == 0:
                            pe.wait_ge(S("part_lo"), IN_BEFORE[name] + k + 1)
                        for j in range(2):
                            last = mm3(PS[i % 4][:, j, 0:HT], (wh[:, kk, :], wl[:, kk, :]),
                                       operand(name, k, slice(j * HT, (j + 1) * HT)),
                                       k == 0, part == nparts - 1 and kk == nk - 1)
                        k += 1
                    last.then_inc(S("gemm_mm" if part == nparts - 1 else "gemm_part"), 1)

        def gemm_loop_scalar(s, name, ntile, even, nparts=1):
            for i in range(ntile):
                split_hi(s, first[name] + nparts * (i + 1) + NH - 1)
                s.wait_ge(S("gemm_mm"), GEMM_MM[name] + i + 1)
                if i % 2 == 0:
                    even(i)
                split_hi(s, first[name] + nparts * (i + 1) + NH)

        def gemm_sq_scalar(s, name, sq, nparts=1):
            def even(i):
                A.activation(halves(sq[:, i, :]), pair(i % 4), ACT.Square).then_inc(S("norm_sq_s"), 1)
                A.activation(halves(xn[:, i, :]), pair(i % 4), ACT.Copy).then_inc(S("gemm_out_s"), 1)
            gemm_loop_scalar(s, name, KD, even, nparts)

        def gemm_sq_vector(v, name, sq):
            for i in range(1, KD, 2):
                v.wait_ge(S("gemm_mm"), GEMM_MM[name] + i + 1)
                V.tensor_copy(halves(xn[:, i, :]), pair(i % 4)).then_inc(S("gemm_out_v"), 1)
                v.wait_ge(S("gemm_out_v"), GEMM_OUT[name] + i // 2 + 1)
                tt(sq[:, i, :], xn[:, i, :], xn[:, i, :], ALU.mult).then_inc(S("norm_sq_v"), 1)

        def halves(ap):
            return ap.rearrange("p (j t) -> p j t", j=2)

        def gemm_scalar(s, name, ntile, dst):
            def even(i):
                A.activation(halves(dst(i)), pair(i % 4), ACT.Copy).then_inc(S("gemm_out_s"), 1)
            gemm_loop_scalar(s, name, ntile, even)

        def gemm_vector(v, name, ntile, dst):
            for i in range(1, ntile, 2):
                v.wait_ge(S("gemm_mm"), GEMM_MM[name] + i + 1)
                V.tensor_copy(halves(dst(i)), pair(i % 4)).then_inc(S("gemm_out_v"), 1)

        def inputs_tensor(pe):
            pe.wait_ge(S("consts"), 1)
            pe.wait_ge(S("params_in"), 16 * 35)
            tr(bank(0)[:, 0:NROWS], rows_in[0:NROWS, :], NROWS).then_inc(S("turned"), 1)
            for i in range(12):
                last = tr(bank(1)[:, i * 24:(i + 1) * 24], cs_tok[0:24, i // 6, (i % 6) * P:(i % 6 + 1) * P], 24)
            last.then_inc(S("turned"), 1)
            for i in range(4):
                pe.wait_ge(S("x_in"), 64)
                for hf in range(2):
                    job = 2 + 2 * i + hf
                    if job >= 8:
                        pe.wait_ge(S("turned_out_v" if job % 2 == 0 else "turned_out_s"), 1)
                    for k in range(4):
                        last = tr(bank(job % 8)[:, k * P:(k + 1) * P], x_tok[:, i, (4 * hf + k) * P:(4 * hf + k + 1) * P], P)
                    last.then_inc(S("turned"), 1)
            pe.wait_ge(S("turned_out_v"), 2)
            for k in range(8):
                last = tr(bank(2)[:, k * NS:(k + 1) * NS], xs_tok[0:NS, k * P:(k + 1) * P], NS)
            last.then_inc(S("turned"), 1)

        def inputs_evac(e, eng, copy, name, par_):
            for job in range(par_, 11, 2):
                eng.wait_ge(S("turned"), job + 1)
                if job == 0:
                    i = copy(prm, bank(0)[:, 0:NROWS])
                elif job == 1:
                    i = copy(ups[:, :, :, 0:3], bank(1)[:, 0:288].rearrange("p (c b w) -> p c b w", b=NB, w=3))
                elif job < 10:
                    i, hf = divmod(job - 2, 2)
                    i = copy(XT[:, 4 * hf:4 * hf + 4, i * P:(i + 1) * P], bank(job % 8).rearrange("p (k t) -> p k t", t=P))
                else:
                    i = copy(XT[:, :, SEQ:T], bank(2)[:, 0:8 * NS].rearrange("p (k t) -> p k t", t=NS))
                i.then_inc(S(name), 1)

        def small_hi(s):
            s.wait_ge(S("params_in"), 16 * 35)
            A.activation(w_small_hi[:, :, :, :], w_small[:, :, :, :], ACT.Copy).then_inc(S("weights_and_rates"), 1)

        def small_lo(v):
            v.wait_ge(S("weights_and_rates"), 1)
            tt(w_small_lo[:, :, :, :], w_small[:, :, :, :], w_small_hi[:, :, :, :].bitcast(F32), ALU.subtract)

        def vcopy(o_, i_):
            return V.tensor_copy(o_, i_)

        def scopy(o_, i_):
            return A.activation(o_, i_, ACT.Copy)

        CONV_OF = {**{C_XBC + k: k for k in range(6)}, **{C_GQKV + k: 6 + k for k in range(6)}}

        def win_dst(i):
            return rawc[:, CONV_OF[i] % 4, :] if i in CONV_OF else proj[:, i, :]

        def win_tensor(pe):
            for i in range(3):
                for k in range(KD):
                    if i == 0:
                        pe.wait_ge(S("part_lo"), k + 1)
                    for j in range(2):
                        last = mm3(PS[i][0:H, j, 0:HT], (w_small_hi[:, i, k, :], w_small_lo[:, i, k, :]),
                                   operand("win", k, slice(j * HT, (j + 1) * HT)), k == 0, k == KD - 1)
                last.then_inc(S("raw_mm"), 1)
            pe.wait_ge(S("raw_out_v"), 2)
            pe.wait_ge(S("raw_out_s"), 1)
            gemm_tensor(pe, "win", NPROJ)
            rows_turn_tensor(pe)

        def win_vector(v):
            rows_vector(v)
            for i in range(1, NPROJ, 2):
                v.wait_ge(S("gemm_mm"), i + 1)
                V.tensor_copy(halves(win_dst(i)), pair(i % 4)).then_inc(S("gemm_out_v"), 1)
                if i in CONV_OF:
                    v.wait_ge(S("gemm_out_s"), i // 2 + 1)
                    conv_vector(v, CONV_OF[i] - 1)
                    v.wait_ge(S("gemm_out_v"), i // 2 + 1)
                    conv_vector(v, CONV_OF[i])
            rows_turn_vector(v)

        def win_scalar(s):
            rows_scalar(s)

            def even(i):
                if CONV_OF.get(i, 0) >= 4:
                    s.wait_ge(S("conv"), CONV_OF[i] - 3)
                A.activation(halves(win_dst(i)), pair(i % 4), ACT.Copy).then_inc(S("gemm_out_s"), 1)
                if i - 2 in CONV_OF:
                    silu_scalar(s, CONV_OF[i - 2])
                    silu_scalar(s, CONV_OF[i - 2] + 1)

            gemm_loop_scalar(s, "win", NPROJ, even)

        def kv_tensor(pe):
            for i, (t0, w, _) in enumerate(TILES):
                for k in range(4):
                    last = tr(bank(i)[0:w, k * P:(k + 1) * P], proj[:, C_MK + k, t0:t0 + w], P)
                last.then_inc(S("kv_turned"), 1)

        def kv_vector(v):
            for i, (t0, w, _) in enumerate(TILES):
                v.wait_ge(S("kv_turned"), i + 1)
                dst = kvtok[:, i, :] if i < 4 else kvs[0:NS, :]
                V.tensor_copy(dst, bank(i)[0:w, :]).then_inc(S("kv_out"), 1)

        def mp_scores(pe, j):
            i, h = divmod(j, H)
            if j >= 4:
                pe.wait_ge(S("mp_biased"), j - 3)
            r = slice((h % 2) * 64, (h % 2) * 64 + 64)
            nk = (i + 1) * P
            mm(bank(j % 4)[:, 0:nk], proj[r, C_MQ + h // 2, i * P:(i + 1) * P], proj[r, C_MK + h // 2, 0:nk], True, True)\
                .then_inc(S("att_scores"), 1)

        def mp_turn(pe, j):
            i = j // H
            pe.wait_ge(S("att_probs"), j + 1)
            if j >= 2:
                pe.wait_ge(S("att_pt"), j - 1)
            for k in range(i + 1):
                last = tr(bank(4 + j % 2)[:, k * P:(k + 1) * P], mp_s[:, j % 4, k * P:(k + 1) * P], P)
            last.then_inc(S("att_turned"), 1)

        def mp_pv(pe, j):
            i, h = divmod(j, H)
            pe.wait_ge(S("att_pt"), j + 1)
            if h == 0 and i >= 2:
                pe.wait_ge(S("att_out"), i - 1)
            for k in range(i + 1):
                last = mm(bank(6 + i % 2)[(h % 2) * 64:(h % 2) * 64 + 64, (h // 2) * P:(h // 2 + 1) * P],
                          kvtok[:, k, GW + h * DH:GW + (h + 1) * DH], mp_pt[:, j % 2, k * P:(k + 1) * P], k == 0, k == i)
            last.then_inc(S("att_pv"), 1)

        def moba_prompt_tensor(pe):
            kv_tensor(pe)
            pe.wait_ge(S("kv_out"), NT)
            mp_scores(pe, 0)
            mp_scores(pe, 1)
            for j in range(16):
                if j + 2 < 16:
                    mp_scores(pe, j + 2)
                mp_turn(pe, j)
                if j:
                    mp_pv(pe, j - 1)
            mp_pv(pe, 15)

        def moba_prompt_vector(v):
            kv_vector(v)
            v.wait_ge(S("mp_tables"), 1)

            def first_(j):
                i, h = divmod(j, H)
                nk = (i + 1) * P
                v.wait_ge(S("att_scores"), j + 1)
                if j >= 4:
                    v.wait_ge(S("att_turned"), j - 3)
                V.scalar_tensor_tensor(mp_s[:, j % 4, 0:nk], bank(j % 4)[:, 0:nk], SCALE, mp_bias[:, h, SEQ - nk:SEQ],
                                       ALU.mult, ALU.add).then_inc(S("mp_biased"), 1)
                v.wait_ge(S("mp_biased"), j + 1)
                V.tensor_reduce(mp_stat[:, 0, j:j + 1], mp_s[:, j % 4, 0:nk], AXX, ALU.max, negate=True)\
                    .then_inc(S("att_max"), 1)

            def second(j):
                nk = (j // H + 1) * P
                v.wait_ge(S("att_exp"), j + 1)
                link(V.reciprocal(mp_stat[:, 2, j:j + 1], mp_stat[:, 1, j:j + 1]))
                V.tensor_scalar(mp_s[:, j % 4, 0:nk], mp_s[:, j % 4, 0:nk], mp_stat[:, 2, j:j + 1], None, ALU.mult)\
                    .then_inc(S("att_probs"), 1)

            def out_(i):
                v.wait_ge(S("att_pv"), 4 * i + 4)
                V.tensor_copy(OM[:, 0:2, i * P:(i + 1) * P], bank(6 + i % 2)[:, 0:2 * P].rearrange("p (c t) -> p c t", t=P))\
                    .then_inc(S("att_out"), 1)

            v.wait_ge(S("conv_states_out"), 16 * 4)
            first_(0)
            for j in range(16):
                if j + 1 < 16:
                    first_(j + 1)
                second(j)
                if j >= 4 and j % 4 == 1:
                    out_(j // 4 - 1)
                if j == 7:
                    moba_rows_vector(v)
            out_(3)

        def moba_prompt_scalar(s):
            s.wait_ge(S("conv_states_out"), 16 * 4)

            def ex(j):
                nk = (j // H + 1) * P
                s.wait_ge(S("att_max"), j + 1)
                A.activation(mp_s[:, j % 4, 0:nk], mp_s[:, j % 4, 0:nk], ACT.Exp, bias=mp_stat[:, 0, j:j + 1],
                             accum_out=mp_stat[:, 1, j:j + 1]).then_inc(S("att_exp"), 1)

            ex(0)
            for j in range(16):
                if j + 1 < 16:
                    ex(j + 1)
                nk = (j // H + 1) * P
                s.wait_ge(S("att_turned"), j + 1)
                if j >= 2:
                    s.wait_ge(S("att_pv"), j - 1)
                A.activation(mp_pt[:, j % 2, 0:nk], bank(4 + j % 2)[:, 0:nk], ACT.Copy).then_inc(S("att_pt"), 1)

        def moba_sample_tensor(pe):
            def page_in(n):
                pe.wait_ge(S(f"pages{n % NPG}_in"), 64 * (n // NPG + 1))

            def turn(j):
                n, c_ = divmod(j, 2)
                if c_ == 0:
                    page_in(n)
                if j >= 4:
                    pe.wait_ge(S("keys_turned_s" if c_ == 0 else "keys_turned_v"), (j - 4) // 2 + 1)
                for i in range(4):
                    last = tr(bank(j % 4)[:, i * P:(i + 1) * P], pages[:, n % NPG, i, c_ * P:(c_ + 1) * P], P)
                last.then_inc(S("satt_turned"), 1)

            def score(j):
                n, c_ = divmod(j, 2)
                b, qt = divmod(n, 4)
                pe.wait_ge(S("keys_turned_s" if c_ == 0 else "keys_turned_v"), j // 2 + 1)
                r = slice(32 * (b // 2), 32 * (b // 2) + 32)
                mm(bank(4 + qt)[r, :], ms_qp[:, c_, b, :], ms_kt[j % 4], b % 2 == 0 and c_ == 0, b % 2 == 1 and c_ == 1)\
                    .then_inc(S("satt_scored"), 1)

            pe.wait_ge(S("ms_q"), 2)
            turn(0)
            turn(1)
            for j in range(2, 64):
                turn(j)
                score(j - 2)
            score(62)
            score(63)
            for c_ in range(2):
                last = mm(bank(0)[:, 0:NS], ms_q[:, c_, :], proj[:, C_MK + c_, SEQ:T], c_ == 0, c_ == 1)
            last.then_inc(S("satt_rows"), 1)
            pe.wait_ge(S("satt_probs"), 1)
            for i in range(NPAGE):
                last = tr(bank(i // 4)[:, (i % 4) * P:(i % 4 + 1) * P], ms_s[:, i * P:(i + 1) * P], P)
            last.then_inc(S("satt_pt"), 1)
            tr(bank(4)[0:NS, 0:P], ms_s[:, PAST:PAST + NS], P).then_inc(S("satt_pt"), 1)
            pe.wait_ge(S("satt_pt_out"), 2)
            for e in range(2):
                mm(bank(5 + e)[:, 0:GW], ms_pown[0:NS, :], kvs[0:NS, GW:2 * GW], True, False)
            for n in range(32, 64):
                b, qt = divmod(n - 32, 4)
                r = slice(32 * (b // 2), 32 * (b // 2) + 32)
                page_in(n)
                for i in range(4):
                    last = mm(bank(5 + b % 2)[r, 0:GW], st_all[:, 4 * qt + i, r], pages[:, n % NPG, i, :], False, qt == 3 and i == 3)
                last.then_inc(S("ms_values_used"), 1)
            pe.wait_ge(S("satt_o"), 1)
            pick = ident.rearrange("p (g e h t) -> p g e h t", e=2, h=H, t=TS)
            for e in range(2):
                for c_ in range(2):
                    for h2 in range(2):
                        last = mm(bank(7)[h2 * 64:h2 * 64 + 64, c_ * NS:(c_ + 1) * NS].rearrange("p (g e t) -> p g e t", e=2, t=TS)[:, :, e, :],
                                  ms_o[:, e, (2 * c_ + h2) * DH:(2 * c_ + h2 + 1) * DH], pick[:, :, e, 2 * c_ + h2, :], True, True)
            last.then_inc(S("satt_pv"), 1)

        def moba_rows_vector(v):
            v.wait_ge(S("ms_tables"), 1)
            sg = ms_grp
            link(V.reduce_sum(mr, sg[:, 32:64], AXX))
            link(V.reduce_sum(tr_, sg[:, 64:96], AXX))
            link(V.tensor_scalar(ms_bias[:, 0:PAST + NS], ms_bias[:, 0:PAST + NS], tr_, None, ALU.subtract))
            own = ms_bias[:, PAST:PAST + NS]
            ok = ms_rowtmp
            link(V.tensor_scalar(ok, own, 0.0, None, ALU.is_le))
            link(tt(ok.rearrange("p (b t) -> p b t", t=TS), ok.rearrange("p (b t) -> p b t", t=TS),
                    bc(g8.rearrange("p (b t) -> p b t", t=1), (P, NB, TS)), ALU.mult))
            link(V.tensor_scalar(ok, ok, -1.0, -NEG, ALU.add, ALU.mult))
            link(V.tensor_scalar(ms_bias[:, 0:PAST + NS], ms_bias[:, 0:PAST + NS], mr, None, ALU.mult))
            link(tt(own, own, ok, ALU.add))
            link(V.memset(ms_q, 0.0))
            for h2 in range(2):
                for c_ in range(2):
                    r = slice(h2 * 64, h2 * 64 + 64)
                    dst = ms_q[r, c_, :].rearrange("p (b g t) -> p b g t", g=4, t=TS)[:, :, 2 * c_ + h2, :]
                    last = V.tensor_copy(dst, proj[r, C_MQ + c_, SEQ:T].rearrange("p (b t) -> p b t", t=TS))
            last.then_inc(S("ms_q"), 1)

        def moba_sample_vector(v):
            v.wait_ge(S("moba_kv_out"), 16 * 10)
            link(V.memset(ms_qp, 0.0))
            for e in range(2):
                last = V.tensor_copy(ms_qp.rearrange("p c (g e) r -> p c g e r", e=2)[:, :, :, e, 16 * e:16 * e + 16],
                                     ms_q.rearrange("p c (g e r) -> p c g e r", e=2, r=16)[:, :, :, e, :])
            last.then_inc(S("ms_q"), 1)
            for j in range(1, 64, 2):
                v.wait_ge(S("satt_turned"), j + 1)
                if j >= 4:
                    v.wait_ge(S("satt_scored"), j - 3)
                V.tensor_copy(ms_kt[j % 4], bank(j % 4)).then_inc(S("keys_turned_v"), 1)
            v.wait_ge(S("satt_rows"), 1)
            for i in range(4):
                link(V.tensor_reduce(ms_gate[:, 2 * i:2 * i + 2], bank(4 + i).rearrange("p (n k) -> p n k", k=MOBA_BLOCK), AXX, ALU.add))
            gm = bc(ms_gate.rearrange("p (o m) -> p o m", o=1), (P, 8, 8))
            gn = bc(ms_gate.rearrange("p (n o) -> p n o", o=1), (P, 8, 8))
            link(tt(ms_gt, gm, gn, ALU.is_gt))
            link(tt(ms_eq, gm, gn, ALU.is_equal))
            link(tt(ms_eq, ms_eq, ltm, ALU.mult))
            link(tt(ms_gt, ms_gt, ms_eq, ALU.add))
            link(V.tensor_reduce(ms_rank, ms_gt, AXX, ALU.add))
            link(V.tensor_scalar(ms_sel, ms_rank, 2.5, NEG, ALU.is_gt, ALU.mult))
            for i in range(4):
                sl = slice(i * 512, (i + 1) * 512)
                link(V.scalar_tensor_tensor(ms_s[:, sl], bank(4 + i), SCALE, ms_bias[:, sl], ALU.mult, ALU.add))
            s3 = ms_s[:, 0:PAST].rearrange("p (n k) -> p n k", k=MOBA_BLOCK)
            link(tt(s3, s3, bc(ms_sel.rearrange("p (n o) -> p n o", o=1), (P, 8, MOBA_BLOCK)), ALU.add))
            link(V.scalar_tensor_tensor(ms_s[:, PAST:PAST + NS], bank(0)[:, 0:NS], SCALE, ms_bias[:, PAST:PAST + NS], ALU.mult, ALU.add))
            V.tensor_reduce(ms_stat[:, 0:1], ms_s[:, :], AXX, ALU.max, negate=True).then_inc(S("satt_max"), 1)
            v.wait_ge(S("satt_exp"), 1)
            link(V.reciprocal(ms_stat[:, 2:3], ms_stat[:, 1:2]))
            V.tensor_scalar(ms_s[:, :], ms_s[:, :], ms_stat[:, 2:3], None, ALU.mult).then_inc(S("satt_probs"), 1)
            v.wait_ge(S("satt_pt"), 1)
            for i in range(2):
                link(V.tensor_copy(st_all[:, 4 * i:4 * i + 4, :], bank(i).rearrange("p (n k) -> p n k", k=P)))
            v.wait_ge(S("satt_pt"), 2)
            V.tensor_copy(ms_pown[0:NS, :], bank(4)[0:NS, 0:P]).then_inc(S("satt_pt_out"), 1)
            v.wait_ge(S("ms_values_used"), 32)
            link(V.tensor_copy(ms_o[:, 0, :], bank(5)[:, 0:GW]))
            V.tensor_copy(ms_o[:, 1, :], bank(6)[:, 0:GW]).then_inc(S("satt_o"), 1)
            v.wait_ge(S("satt_pv"), 1)
            V.tensor_copy(OM[:, 0:2, SEQ:T], bank(7)[:, 0:2 * NS].rearrange("p (c t) -> p c t", t=NS))

        def moba_sample_scalar(s):
            s.wait_ge(S("moba_kv_out"), 16 * 10)
            for j in range(0, 64, 2):
                s.wait_ge(S("satt_turned"), j + 1)
                if j >= 4:
                    s.wait_ge(S("satt_scored"), j - 3)
                scopy(ms_kt[j % 4], bank(j % 4)).then_inc(S("keys_turned_s"), 1)
            s.wait_ge(S("satt_max"), 1)
            A.activation(ms_s[:, :], ms_s[:, :], ACT.Exp, bias=ms_stat[:, 0:1], accum_out=ms_stat[:, 1:2]).then_inc(S("satt_exp"), 1)
            s.wait_ge(S("satt_pt"), 1)
            link(scopy(st_all[:, 8:12, :], bank(2).rearrange("p (n k) -> p n k", k=P)), "s")
            scopy(st_all[:, 12:16, :], bank(3).rearrange("p (n k) -> p n k", k=P)).then_inc(S("satt_pt_out"), 1)

        def rows_vector(v):
            e, u, d = rows_t[:, 0:2, :], rows_t[:, 2:4, :], rows_d
            for i, (job, col) in enumerate(((0, 1), (2, 3))):
                v.wait_ge(S("raw_mm"), job + 1)
                V.tensor_scalar(halves(raw[:, i, :]), PS[job][0:H, :, 0:HT], head4[0:H, col:col + 1], None, ALU.add)\
                    .then_inc(S("raw_out_v"), 1)
            v.wait_ge(S("raw_out_v"), 2)
            V.scalar_tensor_tensor(e, raw, -1.0, raw, ALU.mult, ALU.max).then_inc(S("rows_abs"), 1)
            v.wait_ge(S("weights_and_rates"), 2)
            for i in (4, 6):
                link(V.tensor_scalar(head4[0:H, i:i + 1], head4[0:H, i:i + 1], -1.0, None, ALU.mult))
            v.wait_ge(S("rows_exp"), 1)
            link(V.tensor_scalar(u, e, 1.0, None, ALU.add))
            V.tensor_scalar(d, u, -1.0, None, ALU.add).then_inc(S("rows_u"), 1)
            link(V.tensor_scalar(rows[:, 2, :], rows[:, 2, :], 1.0, None, ALU.add))
            link(V.reciprocal(rows[:, 2, :], rows[:, 2, :]))
            v.wait_ge(S("rows_ln"), 1)
            link(tt(u, u, e, ALU.mult))
            link(V.scalar_tensor_tensor(e, d, 0.0, e, ALU.is_equal, ALU.mult))
            link(V.tensor_scalar(d, d, 1e-30, None, ALU.max))
            link(V.reciprocal(d, d))
            link(tt(u, u, d, ALU.mult))
            link(tt(u, u, e, ALU.add))
            link(V.scalar_tensor_tensor(u, raw, 0.0, u, ALU.max, ALU.add))
            link(V.tensor_copy(rows[:, 0, :], u[:, 0, :]))
            link(V.tensor_scalar(raw[:, 0, :], u[:, 0, :], head4[0:H, 4:5], None, ALU.mult))
            link(V.tensor_scalar(raw[:, 1, :], u[:, 1, :], head4[0:H, 6:7], None, ALU.mult))
            V.tensor_tensor_scan(rows[:, 1, :], keep[0:H, :], raw[:, 0, :], 0.0, ALU.mult, ALU.add)
            V.tensor_tensor_scan(rows[:, 3, :], keep[0:H, :], raw[:, 1, :], 0.0, ALU.mult, ALU.add).then_inc(S("rows_made"), 1)

        def rows_scalar(s):
            s.wait_ge(S("raw_mm"), 2)
            A.activation(halves(rows[:, 2, :]), PS[1][0:H, :, 0:HT], ACT.Exp, scale=-1.0).then_inc(S("raw_out_s"), 1)
            A.activation(head4[0:H, 4:5], head4[0:H, 0:1], ACT.Exp)
            A.activation(head4[0:H, 6:7], head4[0:H, 2:3], ACT.Exp).then_inc(S("weights_and_rates"), 1)
            s.wait_ge(S("rows_abs"), 1)
            A.activation(rows_t[:, 0:2, :], rows_t[:, 0:2, :], ACT.Exp, scale=-1.0).then_inc(S("rows_exp"), 1)
            s.wait_ge(S("rows_u"), 1)
            A.activation(rows_t[:, 2:4, :], rows_t[:, 2:4, :], ACT.Ln).then_inc(S("rows_ln"), 1)

        def rows_turn_vector(v):
            v.wait_ge(S("rows_turned"), 1)
            link(V.tensor_copy(cumtok[:, 0:4, :], bank(6)[:, 0:32].rearrange("p (i h) -> p i h", h=8)))
            link(V.tensor_copy(cumtok[0:NS, 4, :], bank(6)[0:NS, 32:40]))
            v.wait_ge(S("conv_turned"), 1)
            for i in range(3):
                last = V.tensor_copy(cw_out[:, i * 512:(i + 1) * 512], bank(i)[0:27, :])
            last.then_inc(S("conv_states_made"), 1)

        def rows_turn_tensor(pe):
            pe.wait_ge(S("conv"), 12)
            pe.wait_ge(S("rows_made"), 1)
            pe.wait_ge(S("gemm_out_s"), NPROJ // 2)
            pe.wait_ge(S("gemm_out_v"), NPROJ // 2)
            for i, (t0, w, _) in enumerate(TILES):
                for m_, kind in enumerate((1, 3)):
                    last = tr(bank(6)[0:w, i * 8 + 4 * m_:i * 8 + 4 * m_ + 4], rows[:, kind, t0:t0 + w], H)
            last.then_inc(S("rows_turned"), 1)
            for c_ in range(12):
                last = tr(bank(c_ // 4)[0:27, (c_ % 4) * P:(c_ % 4 + 1) * P], cw_in[:, c_, :], P)
            last.then_inc(S("conv_turned"), 1)

        def spread_scalar(s):
            for n in range(6):
                s.wait_ge(S("rows_spread"), n + 1)
                A.activation(halves(pb[:, n // 2, n % 2, :]), pair(n % 4), ACT.Copy).then_inc(S("rows_spread_out"), 1)

        def spread_tensor(pe):
            for n in range(6):
                kind, hp = (0, 2, 3)[n // 2], n % 2
                if n >= 4:
                    pe.wait_ge(S("rows_spread_out"), n - 3)
                for j in range(2):
                    last = mm(PS[n % 4][:, j, 0:HT], pairsel[0:H, hp, :], rows[:, kind, j * HT:(j + 1) * HT], True, True)
                last.then_inc(S("rows_spread"), 1)

        def conv_vector(v, c_):
            m_, k = divmod(c_, 6)
            wrow = R_SCW if m_ == 0 else R_GCW
            src, dst = rawc[:, c_ % 4, :], proj[:, (C_XBC if m_ == 0 else C_GQKV) + k, :]
            win_ = ups[:, c_, :, :]
            link(V.tensor_copy(win_[:, :, 3:7], src[:, SEQ:T].rearrange("p (b t) -> p b t", t=TS)))
            V.tensor_copy(cw_in[:, c_, 0:3], src[:, SEQ - 3:SEQ])
            V.tensor_copy(cw_in[:, c_, 3:27].rearrange("p (b w) -> p b w", w=3), win_[:, :, 4:7])
            ds_ = dst[:, SEQ:T].rearrange("p (b t) -> p b t", t=TS)
            wt = [par(wrow + 6 * j + k) for j in range(4)]
            b_ = par(R_SCB + k) if m_ == 0 else 0.0
            V.tensor_scalar(dst[:, 0:SEQ], src[:, 0:SEQ], wt[3], b_, ALU.mult, ALU.add)
            link(V.tensor_scalar(ds_, win_[:, :, 3:7], wt[3], b_, ALU.mult, ALU.add))
            for d in range(1, 4):
                V.scalar_tensor_tensor(dst[:, d:SEQ], src[:, 0:SEQ - d], wt[3 - d], dst[:, d:SEQ], ALU.mult, ALU.add)
                last = V.scalar_tensor_tensor(ds_, win_[:, :, 3 - d:7 - d], wt[3 - d], ds_, ALU.mult, ALU.add)
                if d < 3:
                    link(last)
            last.then_inc(S("conv"), 1)

        def silu_scalar(s, c_):
            t_ = (C_XBC if c_ < 6 else C_GQKV - 6) + c_
            s.wait_ge(S("conv"), c_ + 1)
            A.activation(proj[:, t_, :], proj[:, t_, :], ACT.Silu)

        def dec_tensor(pe, b, kind, t0, w, np_):
            for h in range(H):
                last = mm(bank(b)[0:np_, h * w:(h + 1) * w], onehot[0:H, h, 0:np_], rows[:, kind, t0:t0 + w], True, True)
            return last

        def dec_vector(dst, b, col, i, w):
            c3 = cumtok[0:w, i, col:col + 4].rearrange("p (h o) -> p h o", o=1)
            msk = (negmask if w == P else negmask_s)[0:w, 0:w].rearrange("p (o l) -> p o l", o=1)
            link(tt(dst, bank(b)[0:w, 0:H * w].rearrange("p (h l) -> p h l", l=w), bc(c3, (w, H, w)), ALU.subtract))
            return tt(dst, dst, bc(msk, (w, H, w)), ALU.add)

        def hl(buf, w):
            flat = buf.rearrange("p a b -> p (a b)") if len(buf.shape) == 3 else buf
            return flat[0:w, 0:H * w].rearrange("p (h l) -> p h l", l=w)

        def ssm_tensor(pe):
            pe.wait_ge(S("ssm_xdt"), 1)
            for i, (t0, w, _) in enumerate(TILES):
                sl = slice(t0, t0 + w)
                if i:
                    pe.wait_ge(S("ssm_tile_out"), i)
                for g in range(2):
                    mm(bank(0)[0:w, g * w:(g + 1) * w], xc[:, 2 + g, sl], xc[:, 4 + g, sl], True, True)
                dec_tensor(pe, 1, 1, t0, w, P)
                for k in range(4):
                    src = xdt[:, k, sl] if k < 2 else xc[:, k, sl]
                    last = tr(bank(2)[0:w, k * P:(k + 1) * P], src, P)
                last.then_inc(S("ssm_pre"), 1)
                if w == NS:
                    pe.wait_ge(S("state_in"), 16)
                    for n in range(16):
                        last = tr(bank(4 + n // 4)[:, (n % 4) * P:(n % 4 + 1) * P], s_h0[:, n // 2, n % 2, :], P)
                    last.then_inc(S("ssm_h0_turned"), 1)
                    pe.wait_ge(S("ssm_h0_out"), 1)
                pe.wait_ge(S("ssm_ready"), i + 1)
                for h in range(H):
                    r = slice((h % 2) * 64, (h % 2) * 64 + 64)
                    o_ = bank(3)[r, (h // 2) * w:(h // 2 + 1) * w]
                    alone = w == P and i == 0
                    last = mm(o_, s_tok[0:w, h * 64:(h + 1) * 64], hl(s_m, w)[:, h, :], True, alone)
                    if w == NS:
                        for b in range(NB):
                            last = mm(o_[:, b * TS:(b + 1) * TS], s_h0t[:, b, h * 64:(h + 1) * 64],
                                      sc_view(w)[:, h, b * TS:(b + 1) * TS], False, True)
                    elif i:
                        last = mm(o_, s_ht[:, h * 64:(h + 1) * 64], sc_view(w)[:, h, :], False, True)
                last.then_inc(S("ssm_y"), 1)
                if w == P:
                    for g in range(2):
                        last = mm(bank(4)[:, g * P:(g + 1) * P], s_tok[:, 256 + g * P:256 + (g + 1) * P], s_xd[:, g * P:(g + 1) * P], True, True)
                    last.then_inc(S("ssm_state"), 1)
                else:
                    for hp in range(2):
                        last = mm(bank(2)[:, hp * 8:hp * 8 + 8], pairsel[0:H, hp, :],
                                  rows[:, 1, SEQ:T].rearrange("p (b t) -> p b t", t=TS)[:, :, TS - 1], True, True)
                    last.then_inc(S("ssm_dec"), 1)
                    for g in range(2):
                        last = tr(bank(0)[:, g * P:(g + 1) * P], s_ht[:, g * P:(g + 1) * P], P)
                    last.then_inc(S("ssm_final"), 1)
                    pe.wait_ge(S("ssm_bm"), 1)
                    for g in range(2):
                        for q in range(2):
                            last = mm(bank(4 + 2 * g + q), s_xd[0:NS, g * P:(g + 1) * P],
                                      s_bm[0:NS, 4 * q:4 * q + 4, g, :], True, True)
                    last.then_inc(S("ssm_state"), 1)
            pe.wait_ge(S("tail_sq"), 1)
            for k in range(2):
                for j in range(2):
                    last = mm(PS[0][:, j, 0:HT], ones, xdt[:, k, j * HT:(j + 1) * HT], k == 0, k == 1)
            last.then_inc(S("tail_sum"), 1)

        def sc_view(w):
            return s_c.rearrange("p a b -> p (a b)")[:, 0:H * w].rearrange("p (h l) -> p h l", l=w)

        s_bm = xc[:, 2:6, :].rearrange("p a b -> p (a b)")[:, 0:NB * 256].rearrange("p (b g n) -> p b g n", g=2, n=P)
        s_fin = s_er.rearrange("p a b -> p (a b)")[:, 0:2 * P].rearrange("p (c n) -> p c n", n=P)

        def ssm_vector(v):
            tt(xdt, xc[:, 0:2, :], pb[:, 0, :, :], ALU.mult).then_inc(S("ssm_xdt"), 1)
            for i, (t0, w, _) in enumerate(TILES):
                sl = slice(t0, t0 + w)
                M = hl(s_m, w)
                er = s_er.rearrange("p a b -> p (a b)")[:, 0:H * w].rearrange("p (h l) -> p h l", l=w)
                v.wait_ge(S("ssm_pre"), i + 1)
                dec_vector(M, 1, 0, i, w).then_inc(S("ssm_m"), 1)
                link(V.tensor_copy(s_tok[0:w, :], bank(2)[0:w, :]))
                v.wait_ge(S("ssm_exp"), i + 1)
                if w == P:
                    link(V.tensor_copy(s_dl[:, :], M[:, :, P - 1]))
                else:
                    link(V.tensor_reduce(s_dl[0:w, :], M.rearrange("p h (b t) -> p h b t", t=TS)[:, :, :, TS - 1], AXX, ALU.add))
                for g in range(2):
                    c4 = bc(xc[:, 4 + g, sl].rearrange("p (o l) -> p o l", o=1), (P, 2, w))
                    g4 = bc(bank(0)[0:w, g * w:(g + 1) * w].rearrange("p (o l) -> p o l", o=1), (w, 2, w))
                    tt(sc_view(w)[:, 2 * g:2 * g + 2, :], er[:, 2 * g:2 * g + 2, :], c4, ALU.mult)
                    link(tt(M[:, 2 * g:2 * g + 2, :], M[:, 2 * g:2 * g + 2, :], g4, ALU.mult))
                xd3 = s_xd[0:w, :].rearrange("p (h d) -> p h d", d=DH)
                tt(xd3, s_tok[0:w, 0:256].rearrange("p (h d) -> p h d", d=DH),
                   bc(s_dl[0:w, :].rearrange("p (h o) -> p h o", o=1), (w, H, DH)), ALU.mult).then_inc(S("ssm_ready"), 1)
                if w == NS:
                    v.wait_ge(S("ssm_h0_turned"), 1)
                    for n in range(4):
                        last = V.tensor_copy(s_h0t[:, 2 * n:2 * n + 2, :], bank(4 + n).rearrange("p (b n) -> p b n", n=256))
                    last.then_inc(S("ssm_h0_out"), 1)
                v.wait_ge(S("ssm_y"), i + 1)
                link(V.tensor_copy(OM[:, 2:4, sl], bank(3)[:, 0:2 * w].rearrange("p (c l) -> p c l", l=w)))
                if w == P:
                    v.wait_ge(S("ssm_state"), i + 1)
                    if i == 0:
                        link(V.tensor_copy(s_ht, bank(4)[:, 0:256]))
                    else:
                        h3 = s_ht.rearrange("p (h d) -> p h d", d=DH)
                        link(tt(h3, h3, bc(er[:, :, P - 1:P], (P, H, DH)), ALU.mult))
                        link(tt(s_ht, s_ht, bank(4)[:, 0:256], ALU.add))
                else:
                    tt(s_bm[0:NS].rearrange("p b g n -> p b (g n)"), bc(s_tok[0:NS, 256:512].rearrange("p (o n) -> p o n", o=1), (NS, NB, 256)),
                       bc(ind[0:NS].rearrange("p (b o) -> p b o", o=1), (NS, NB, 256)), ALU.mult).then_inc(S("ssm_bm"), 1)
                    v.wait_ge(S("ssm_final"), 1)
                    V.tensor_copy(s_fin, bank(0)[:, 0:256].rearrange("p (c n) -> p c n", n=P)).then_inc(S("fin_made"), 1)
                    v.wait_ge(S("ssm_dec_exp"), 1)
                    for hp in range(2):
                        link(tt(s_h0[:, :, hp, :], s_h0[:, :, hp, :], bc(s_dec[:, hp, :].rearrange("p (b o) -> p b o", o=1), (P, NB, P)), ALU.mult))
                    v.wait_ge(S("ssm_state"), 5)
                    for g in range(2):
                        for q in range(2):
                            last = tt(s_h0[:, 4 * q:4 * q + 4, g, :], s_h0[:, 4 * q:4 * q + 4, g, :],
                                      bank(4 + 2 * g + q).rearrange("p (b n) -> p b n", n=P), ALU.add)
                    last.then_inc(S("states_made"), 1)
                v.drain().then_inc(S("ssm_tile_out"), 1)
            Y = OM[:, 2:4, :]
            for c_ in range(2):
                link(V.scalar_tensor_tensor(Y[:, c_, :], xc[:, c_, :], par(R_SD + c_), Y[:, c_, :], ALU.mult, ALU.add))
            v.wait_ge(S("ssm_gate"), 2)
            link(tt(Y, Y, proj[:, C_Z:C_Z + 2, :], ALU.mult))
            tt(xdt, Y, Y, ALU.mult).then_inc(S("tail_sq"), 1)
            v.wait_ge(S("tail_root"), 1)
            link(V.reciprocal(rsq[:, :], rsq[:, :]))
            for c_ in range(2):
                last = V.scalar_tensor_tensor(Y[:, c_, :], Y[:, c_, :], par(R_SNORM + c_), rsq[:, :], ALU.mult, ALU.mult)
            link(last)

        def ssm_scalar(s):
            for c_ in range(2):
                A.activation(proj[:, C_Z + c_, :], proj[:, C_Z + c_, :], ACT.Silu).then_inc(S("ssm_gate"), 1)
            for i, (t0, w, _) in enumerate(TILES):
                M = hl(s_m, w)
                s.wait_ge(S("ssm_pre"), i + 1)
                if i:
                    s.wait_ge(S("ssm_tile_out"), i)
                s.wait_ge(S("ssm_m"), i + 1)
                A.activation(s_er.rearrange("p a b -> p (a b)")[:, 0:H * w], bank(1)[:, 0:H * w], ACT.Exp)
                A.activation(M, M, ACT.Exp).then_inc(S("ssm_exp"), 1)
            s.wait_ge(S("ssm_dec"), 1)
            A.activation(s_dec, bank(2)[:, 0:16].rearrange("p (c b) -> p c b", b=NB), ACT.Exp).then_inc(S("ssm_dec_exp"), 1)
            s.wait_ge(S("tail_sum"), 1)
            A.activation(halves(rsq[:, :]), pair(0), ACT.Sqrt, bias=eps, scale=1.0 / GW).then_inc(S("tail_root"), 1)

        def tail_prep_vector(v, run, b2, q, k, qe, kd, last_, e1):
            v.wait_ge(S("tail_eb"), run + 1)
            link(tt(qe, q, e1, ALU.mult))
            for c_ in range(2):
                for (lo, hi, step) in ((0, SEQ, P), (SEQ, T, TS)):
                    x3 = b2[:, c_, lo:hi].rearrange("p (n i) -> p n i", i=step)
                    o3 = e1[:, c_, lo:hi].rearrange("p (n i) -> p n i", i=step)
                    last = tt(o3, bc(x3[:, :, step - 1:step], (P, (hi - lo) // step, step)), x3, ALU.subtract)
            last.then_inc(S("tail_bd"), 1)
            v.wait_ge(S("tail_ebd"), run + 1)
            tt(kd, k, e1, ALU.mult).then_inc(S("tail_prep"), 1)

        def tail_prep_scalar(s, run, b2, e1):
            A.activation(e1, b2, ACT.Exp).then_inc(S("tail_eb"), 1)
            for c_ in range(2):
                A.activation(t_lastp[:, :, c_], b2[:, c_, 0:SEQ].rearrange("p (n i) -> p n i", i=P)[:, :, P - 1], ACT.Exp)
                A.activation(t_lasts[:, :, c_], b2[:, c_, SEQ:T].rearrange("p (n i) -> p n i", i=TS)[:, :, TS - 1], ACT.Exp)
            s.wait_ge(S("tail_bd"), run + 1)
            A.activation(e1, e1, ACT.Exp).then_inc(S("tail_ebd"), 1)

        t_lastp = sm(4, 2)
        t_lasts = sm(NB, 2)

        def tail_tensor(pe, run, att, kd, qe, vT, kbg, N):
            gdn = kbg is not None
            pe.wait_ge(S("tail_prep"), run + 1)
            for i, (t0, w, _) in enumerate(TILES):
                sl = slice(t0, t0 + w)
                if i:
                    pe.wait_ge(S("tail_tile_out"), 5 * run + i)
                sample = w == NS
                for k in range(2):
                    tr(bank(0)[0:w, k * P:(k + 1) * P], kd[:, k, sl], P)
                if not (sample and gdn):
                    for k in range(2):
                        last = tr(bank(0)[0:w, 256 + k * P:256 + (k + 1) * P], vT[:, k, sl], P)
                if sample:
                    pe.wait_ge(S("state_in"), 32 + 16 * run)
                if gdn and sample:
                    for h in range(H):
                        r = slice((h % 2) * 64, (h % 2) * 64 + 64)
                        for b in range(NB):
                            last = mm(bank(1)[r, (h // 2) * w + b * TS:(h // 2) * w + (b + 1) * TS], t_s0[r, b, h // 2, :],
                                      kbg[r, h // 2, t0 + b * TS:t0 + (b + 1) * TS], True, True)
                elif gdn and i:
                    for h in range(H):
                        r = slice((h % 2) * 64, (h % 2) * 64 + 64)
                        last = mm(bank(1 if h % 2 == 0 else 5)[0:w, (h // 2) * 64:(h // 2 + 1) * 64], kbg[r, h // 2, sl], t_st[r, h // 2, :], True, True)
                last.then_inc(S("tail_tok"), 1)
                if gdn and sample:
                    pe.wait_ge(S("tail_rt"), 1)
                    for k in range(2):
                        last = tr(bank(5)[0:w, k * P:(k + 1) * P], t_rt[:, k, :], P)
                    last.then_inc(S("tail_rt_turned"), 1)
                pe.wait_ge(S("tail_tok_out"), 5 * run + i + 1)
                if gdn:
                    for h in range(H):
                        last = mm(bank(2)[0:w, h * 64:(h + 1) * 64], N(i, w)[:, h, :], t_tok[0:w, 256 + h * 64:256 + (h + 1) * 64], True, True)
                    last.then_inc(S("tail_vn"), 1)
                    pe.wait_ge(S("tail_vn_out"), i + 1)
                for h in range(H):
                    r = slice((h % 2) * 64, (h % 2) * 64 + 64)
                    o_ = bank(3)[r, (h // 2) * w:(h // 2 + 1) * w]
                    last = mm(o_, t_vn[0:w, h * 64:(h + 1) * 64], att(i, w, h), True, i == 0)
                    if sample:
                        for b in range(NB):
                            last = mm(o_[:, b * TS:(b + 1) * TS], t_s0[r, b, h // 2, :], qe[r, h // 2, t0 + b * TS:t0 + (b + 1) * TS], False, True)
                    elif i:
                        last = mm(o_, t_st[r, h // 2, :], qe[r, h // 2, sl], False, True)
                last.then_inc(S("tail_o"), 1)
                if sample:
                    pe.wait_ge(S("tail_vm"), run + 1)
                for h in range(H):
                    r = slice((h % 2) * 64, (h % 2) * 64 + 64)
                    if sample:
                        last = mm(bank(6 + h // 2)[r, :], t_tok[0:w, h * 64:(h + 1) * 64], vm_of(run)[0:w, h * 512:(h + 1) * 512], True, True)
                    else:
                        last = mm(bank(4)[r, (h // 2) * DH:(h // 2 + 1) * DH], t_tok[0:w, h * 64:(h + 1) * 64], t_vn[0:w, h * 64:(h + 1) * 64], True, True)
                last.then_inc(S("tail_st"), 1)
            pe.wait_ge(S("tail_sq"), run + 2)
            for k in range(2):
                for j in range(2):
                    last = mm(PS[k][:, j, 0:HT], blk64, qe[:, k, j * HT:(j + 1) * HT], True, True)
            last.then_inc(S("tail_sum"), 1)

        t_rt = sm(2, NS)

        def vm_of(run):
            return h_vm_ if run == 0 else t_vm

        def tail_vector(v, run, gdn, vT, qe, c_out, c_gate, rnorm):
            for i, (t0, w, _) in enumerate(TILES):
                sl = slice(t0, t0 + w)
                sample = w == NS
                v.wait_ge(S("tail_tok"), 5 * run + i + 1)
                V.tensor_copy(t_tok[0:w, 0:256], bank(0)[0:w, 0:256])
                if gdn and sample:
                    tt(t_rt, vT[:, :, sl], bank(1)[:, 0:2 * w].rearrange("p (c l) -> p c l", l=w), ALU.subtract).then_inc(S("tail_rt"), 1)
                    v.wait_ge(S("tail_rt_turned"), 1)
                    V.tensor_copy(t_tok[0:w, 256:512], bank(5)[0:w, 0:256]).then_inc(S("tail_tok_out"), 1)
                elif gdn and i:
                    link(V.tensor_copy(t_tok[0:w, 256:512], bank(0)[0:w, 256:512]))
                    for e in range(2):
                        half = t_tok[0:w, 256:512].rearrange("p (c e d) -> p e c d", e=2, d=DH)[:, e]
                        last = tt(half, half, bank(1 if e == 0 else 5)[0:w, 0:P].rearrange("p (c d) -> p c d", d=DH), ALU.subtract)
                    last.then_inc(S("tail_tok_out"), 1)
                elif gdn:
                    V.tensor_copy(t_tok[0:w, 256:512], bank(0)[0:w, 256:512]).then_inc(S("tail_tok_out"), 1)
                else:
                    V.tensor_copy(t_vn[0:w, :], bank(0)[0:w, 256:512]).then_inc(S("tail_tok_out"), 1)
                if gdn:
                    v.wait_ge(S("tail_vn"), i + 1)
                    V.tensor_copy(t_vn[0:w, :], bank(2)[0:w, 0:256]).then_inc(S("tail_vn_out"), 1)
                if sample:
                    if gdn:
                        v.wait_ge(S("tail_vn_out"), i + 1)
                    else:
                        v.wait_ge(S("tail_tok_out"), i + 1)
                    vm4 = vm_of(run)[0:w, :].rearrange("p (h b d) -> p h b d", b=NB, d=DH)
                    for h in range(H):
                        last = tt(vm4[:, h], bc(t_vn[0:w, h * 64:(h + 1) * 64].rearrange("p (o d) -> p o d", o=1), (w, NB, DH)),
                                  bc(ind[0:w].rearrange("p (b o) -> p b o", o=1), (w, NB, DH)), ALU.mult)
                    last.then_inc(S("tail_vm"), 1)
                v.wait_ge(S("tail_o"), 5 * run + i + 1)
                link(V.tensor_copy(OM[:, c_out:c_out + 2, sl], bank(3)[:, 0:2 * w].rearrange("p (c l) -> p c l", l=w)))
                v.wait_ge(S("tail_st"), 5 * run + i + 1)
                if sample:
                    link(tt(t_s0.rearrange("p b c d -> p (b c) d"), t_s0.rearrange("p b c d -> p (b c) d"),
                            bc(t_lasts.rearrange("p b (c o) -> p (b c) o", o=1), (P, 2 * NB, DH)), ALU.mult))
                    for c_ in range(2):
                        last = tt(t_s0[:, :, c_, :], t_s0[:, :, c_, :], bank(6 + c_).rearrange("p (b d) -> p b d", d=DH), ALU.add)
                    last.then_inc(S("states_made"), 1)
                elif i == 0:
                    link(V.tensor_copy(t_st, bank(4)[:, 0:2 * DH].rearrange("p (c d) -> p c d", d=DH)))
                else:
                    link(tt(t_st, t_st, bc(t_lastp[:, i, :].rearrange("p (c o) -> p c o", o=1), (P, 2, DH)), ALU.mult))
                    last = tt(t_st, t_st, bank(4)[:, 0:2 * DH].rearrange("p (c d) -> p c d", d=DH), ALU.add)
                    link(last)
                if i == 3:
                    v.drain().then_inc(S("fin_made"), 1)
                v.drain().then_inc(S("tail_tile_out"), 1)
            Y = OM[:, c_out:c_out + 2, :]
            tt(qe, Y, Y, ALU.mult).then_inc(S("tail_sq"), 1)
            v.wait_ge(S("tail_root"), 1 + 2 * run + 2)
            link(V.reciprocal(qe, qe))
            for c_ in range(2):
                link(V.scalar_tensor_tensor(Y[:, c_, :], Y[:, c_, :], par(rnorm), qe[:, c_, :], ALU.mult, ALU.mult))
            link(tt(Y, Y, proj[:, c_gate:c_gate + 2, :], ALU.mult))

        def tail_scalar(s, run, qe, c_gate):
            s.wait_ge(S("tail_sum"), run + 2)
            for k in range(2):
                A.activation(halves(qe[:, k, :]), pair(k), ACT.Sqrt, bias=eps, scale=1.0 / DH).then_inc(S("tail_root"), 1)

        h_vm_ = carve(SC, 2 * T, NB * H * DH)
        hq, hk = proj[:, C_HQ:C_HQ + 2, :], h_k

        def lv_groups():
            return (((0, SEQ), 4, P, 8), ((SEQ, T), 2, NS, 3))

        def hgrn_vector(v):
            fx = proj[:, C_HF:C_HF + 2, :]
            v.wait_ge(S("states_out"), 32)
            V.scalar_tensor_tensor(h_d, fx, -1.0, fx, ALU.mult, ALU.max).then_inc(S("h_abs"), 1)
            v.wait_ge(S("h_ln"), 1)
            link(V.scalar_tensor_tensor(h_d, fx, 0.0, h_d, ALU.min, ALU.subtract))
            for c_ in range(2):
                link(V.tensor_tensor_scan(h_b[:, c_, :], keep[:, :], h_d[:, c_, :], 0.0, ALU.mult, ALU.add))
            link(V.tensor_scalar(h_k, h_k, 1.0, None, ALU.add))
            V.reciprocal(h_k, h_k).then_inc(S("h_k"), 1)
            v.wait_ge(S("h_k"), 1)
            n = 0
            m_ = 0
            for (lo, hi), nt, w, nl in lv_groups():
                def decays(j, n):
                    B = 1 << j
                    for c_ in range(2):
                        x3 = h_b[:, c_, lo:hi].rearrange("p (n i) -> p n i", i=B)
                        o3 = h_d[:, c_, lo:hi].rearrange("p (n i) -> p n i", i=B)
                        mid = bc(x3[:, :, B // 2 - 1:B // 2], (P, (hi - lo) // B, B // 2))
                        tt(o3[:, :, 0:B // 2], mid, x3[:, :, 0:B // 2], ALU.subtract)
                        last = tt(o3[:, :, B // 2:B], x3[:, :, B // 2:B], mid, ALU.subtract)
                    last.then_inc(S("h_diff"), 1)
                    v.wait_ge(S("h_dec"), n + 1)
                    if n >= 2:
                        v.wait_ge(S("h_lv_mm"), h_lvdone(n - 2))
                    tt(h_q1[:, n % 2, :, lo:hi], hq[:, :, lo:hi], h_d[:, :, lo:hi], ALU.mult)
                    tt(h_k1[:, n % 2, :, lo:hi], hk[:, :, lo:hi], h_d[:, :, lo:hi], ALU.mult).then_inc(S("h_qk"), 1)
                    v.wait_ge(S("h_qk"), n + 1)
                for j in range(nl):
                    if j + 1 < nl:
                        decays(j + 1, n)
                        n += 1
                    nm = 4 if w == P else 2
                    msk = bc(lev[0:w, j, 0:w].rearrange("p (o l) -> p o l", o=1), (w, nm, w))
                    for i in range(nt):
                        v.wait_ge(S("h_lv_mm"), m_ + 1)
                        src = bank(m_ % 8)[0:w, 0:nm * w].rearrange("p (h l) -> p h l", l=w)
                        if j == 0:
                            tt(h_store(i, w), src, msk, ALU.mult).then_inc(S("h_lv_out"), 1)
                        else:
                            v.wait_ge(S("h_added"), m_ - 3)
                            tt(h_job(h_msk, m_ % 4, w), src, msk, ALU.mult).then_inc(S("h_lv_out"), 1)
                        m_ += 1

        def h_lvdone(n):
            return 4 * (n + 2) if n < 7 else 32 + 2 * (n - 7 + 2)

        def h_job(buf, i, w):
            n = 4 if w == P else 2
            return buf[0:w, i * 512:i * 512 + n * w].rearrange("p (h l) -> p h l", l=w)

        def h_store(m_, w):
            if w == P:
                return h_job(h_att, m_, w)
            return h_att[0:w, 2048 + 64 * m_:2048 + 64 * (m_ + 1)].rearrange("p (h l) -> p h l", l=w)

        def h_att_of(i, w, h):
            if w == P:
                return h_store(2 * (i // 2) + h % 2, w)[:, 2 * (i % 2) + h // 2, :]
            return h_store(h % 2, w)[:, h // 2, :]

        def hgrn_gpsimd(g):
            m_, added = 0, 0
            for _, nt, w, nl in lv_groups():
                for j in range(nl):
                    for i in range(nt):
                        g.wait_ge(S("h_lv_out"), m_ + 1)
                        if j == 0:
                            g.drain().then_inc(S("h_added"), 1)
                        else:
                            at = h_store(i, w)
                            if j > 1:
                                g.wait_ge(S("h_added"), m_ - nt + 1)
                            G.tensor_tensor(at, at, h_job(h_msk, m_ % 4, w), ALU.add).then_inc(S("h_added"), 1)
                        m_ += 1

        def hgrn_tensor(pe):
            pe.wait_ge(S("h_k"), 1)
            m_, n = 0, 0
            for (lo, hi), nt, w, nl in lv_groups():
                for j in range(nl):
                    if j:
                        pe.wait_ge(S("h_qk"), n + 1)
                    for i in range(nt):
                        if m_ >= 8:
                            pe.wait_ge(S("h_lv_out"), m_ - 7)
                        r = slice((i % 2) * 64, (i % 2) * 64 + 64)
                        for n_ in range(4 if w == P else 2):
                            t_ = 2 * (i // 2) + n_ // 2 if w == P else 0
                            sl = slice(lo + t_ * w, lo + (t_ + 1) * w)
                            q_ = hq[r, n_ % 2, sl] if j == 0 else h_q1[r, n % 2, n_ % 2, sl]
                            k_ = hk[r, n_ % 2, sl] if j == 0 else h_k1[r, n % 2, n_ % 2, sl]
                            last = mm(bank(m_ % 8)[0:w, n_ * w:(n_ + 1) * w], k_, q_, True, True)
                        last.then_inc(S("h_lv_mm"), 1)
                        m_ += 1
                    if j:
                        n += 1
            tail_tensor(pe, 0, h_att_of, h_k1[:, 0], h_q1[:, 0], proj[:, C_HI:C_HI + 2, :], None, None)

        def hgrn_vector_tail(v):
            v.wait_ge(S("h_lv_mm"), 38)
            v.wait_ge(S("h_added"), 38)
            v.drain().then_inc(S("h_levels_done"), 1)
            tail_prep_vector(v, 0, h_b, hq, hk, h_q1[:, 0], h_k1[:, 0], None, h_d)
            tail_vector(v, 0, False, None, h_q1[:, 0], 4, C_HG, R_HNORM)

        def hgrn_scalar(s):
            s.wait_ge(S("h_abs"), 1)
            link(A.activation(h_d, h_d, ACT.Exp, scale=-1.0), "s")
            A.activation(h_k, proj[:, C_HF:C_HF + 2, :], ACT.Exp)
            A.activation(h_d, h_d, ACT.Ln, bias=ones[:, 0:1]).then_inc(S("h_ln"), 1)
            n = 0
            for (lo, hi), nt, w, nl in lv_groups():
                for j in range(1, nl):
                    s.wait_ge(S("h_diff"), n + 1)
                    A.activation(h_d[:, :, lo:hi], h_d[:, :, lo:hi], ACT.Exp).then_inc(S("h_dec"), 1)
                    n += 1
            s.wait_ge(S("h_levels_done"), 1)
            tail_prep_scalar(s, 0, h_b, h_d)
            for c_ in range(2):
                A.activation(proj[:, C_HG + c_, :], proj[:, C_HG + c_, :], ACT.Silu)
            tail_scalar(s, 0, h_q1[:, 0], C_HG)

        g_al = carve(XN, 4 * T, 2048)
        gq, gk, gv = (proj[:, C_GQKV + 2 * i:C_GQKV + 2 * i + 2, :] for i in range(3))
        g_e1 = carve(SC, 6 * T, 2, T)

        def gtile(buf, i, w):
            return buf[0:w, i * 512:i * 512 + H * w].rearrange("p (h l) -> p h l", l=w)

        def gdn_vector(v):
            gqk = proj[:, C_GQKV:C_GQKV + 4, :]
            tt(g_sq, gqk, gqk, ALU.mult).then_inc(S("g_sq"), 1)
            v.wait_ge(S("g_root"), 4)
            link(V.reciprocal(g_sq, g_sq))
            link(V.scalar_tensor_tensor(gq, gq, SCALE, g_sq[:, 0:2, :], ALU.mult, ALU.mult))
            link(tt(gk, gk, g_sq[:, 2:4, :], ALU.mult))
            link(tt(g_kb, gk, pb[:, 1, :, :], ALU.mult))
            tt(gv, gv, pb[:, 1, :, :], ALU.mult).then_inc(S("g_kb"), 1)
            v.wait_ge(S("g_kb"), 1)
            for i, (t0, w, _) in enumerate(TILES):
                ex = hl(g_p1[:, i % 4, :], w)
                v.wait_ge(S("g_mm"), i + 1)
                if i == 4:
                    v.wait_ge(S("g_al_free"), 1)
                dec_vector(ex, 4 * (i % 2) + 2, 4, i, w).then_inc(S("g_m"), 1)
                v.wait_ge(S("g_exp"), i + 1)
                for e in range(2):
                    src = bank(4 * (i % 2) + e)[0:w, 0:H * w].rearrange("p (h l) -> p h l", l=w)
                    par_ = lambda m_: m_.rearrange("p (c e) l -> p e c l", e=2)[:, e]
                    tt(par_(gtile(g_A, i, w)), par_(ex), src[:, 0:2, :], ALU.mult)
                    tt(par_(gtile(g_QK, i, w)), par_(ex), src[:, 2:4, :], ALU.mult)
                id3 = bc(ident[0:w, 0:w].rearrange("p (o l) -> p o l", o=1), (w, H, w))
                V.tensor_copy(gtile(g_T, i, w), id3)
                V.tensor_copy(gtile(g_N, i, w), id3).then_inc(S("g_mats"), 1)
            v.wait_ge(S("g_mats"), NT)
            v.wait_ge(S("states_out"), 64)
            done = 0
            for nt, i0, w, nl in ((4, 0, P, 7), (1, 4, NS, 2)):
                for j in range(1, nl + 1):
                    msk = bc(lev[0:w, j, 0:w].rearrange("p (o l) -> p o l", o=1), (w, H, w))
                    for i in range(nt):
                        if j > 1:
                            v.wait_ge(S("g_p1_mm"), done - nt + i + 1)
                        tt(gtile(g_al, i, w), gtile(g_A, i0 + i, w), msk, ALU.mult).then_inc(S("g_al"), 1)
                    for i in range(nt):
                        v.wait_ge(S("g_tn_mm"), done + 1)
                        b_ = 4 + 2 * (done % 2)
                        b3 = lambda q_: bank(q_)[0:w, 0:H * w].rearrange("p (h l) -> p h l", l=w)
                        tt(gtile(g_T, i0 + i, w), gtile(g_T, i0 + i, w), b3(b_), ALU.subtract)
                        tt(gtile(g_N, i0 + i, w), gtile(g_N, i0 + i, w), b3(b_ + 1), ALU.subtract).then_inc(S("g_tn"), 1)
                        done += 1
            v.wait_ge(S("g_tn"), done)
            v.drain().then_inc(S("g_inverted"), 1)
            tail_prep_vector(v, 1, pb[:, 2], gq, gk, g_qg, t_kd, None, g_e1)
            link(tt(g_kbg, g_kbg, g_kb, ALU.mult))
            v.drain().then_inc(S("g_kbg"), 1)
            tail_vector(v, 1, True, gv, g_qg, 6, C_GZ, R_GNORM)

        def gdn_scalar(s):
            for c_ in range(2):
                A.activation(proj[:, C_GZ + c_, :], proj[:, C_GZ + c_, :], ACT.Silu)
            s.wait_ge(S("g_sum"), 1)
            for k in range(4):
                A.activation(halves(g_sq[:, k, :]), pair(k), ACT.Sqrt, bias=eps).then_inc(S("g_root"), 1)
            for i, (t0, w, _) in enumerate(TILES):
                s.wait_ge(S("g_m"), i + 1)
                ex = hl(g_p1[:, i % 4, :], w)
                A.activation(ex, ex, ACT.Exp).then_inc(S("g_exp"), 1)
            A.activation(g_kbg, pb[:, 2], ACT.Exp)
            done = 0
            for nt, i0, w, nl in ((4, 0, P, 7), (1, 4, NS, 2)):
                for j in range(1, nl + 1):
                    for i in range(nt):
                        s.wait_ge(S("g_p1_mm"), done + 1)
                        A.activation(gtile(g_p1.rearrange("p a b -> p (a b)"), i, w), bank(i)[0:w, 0:H * w].rearrange("p (h l) -> p h l", l=w),
                                     ACT.Copy).then_inc(S("g_p1"), 1)
                        done += 1
            s.wait_ge(S("g_inverted"), 1)
            tail_prep_scalar(s, 1, pb[:, 2], g_e1)
            tail_scalar(s, 1, g_qg, C_GZ)

        def gdn_tensor(pe):
            pe.wait_ge(S("g_sq"), 1)
            for k in range(4):
                for j in range(2):
                    last = mm(PS[k][:, j, 0:HT], blk64, g_sq[:, k, j * HT:(j + 1) * HT], True, True)
            last.then_inc(S("g_sum"), 1)
            pe.wait_ge(S("g_kb"), 1)
            for i, (t0, w, _) in enumerate(TILES):
                sl = slice(t0, t0 + w)
                if i >= 2:
                    pe.wait_ge(S("g_mats"), i - 1)
                b_ = 4 * (i % 2)
                for h in range(H):
                    r = slice((h % 2) * 64, (h % 2) * 64 + 64)
                    for m_, rhs in enumerate((g_kb, gq)):
                        c0 = (2 * m_ + h // 2) * w
                        mm(bank(b_ + h % 2)[0:w, c0:c0 + w], gk[r, h // 2, sl], rhs[r, h // 2, sl], True, True)
                dec_tensor(pe, b_ + 2, 3, t0, w, w).then_inc(S("g_mm"), 1)
                if i == 3:
                    pe.drain().then_inc(S("g_al_free"), 1)
            pe.wait_ge(S("g_mats"), NT)
            done = 0
            for nt, i0, w, nl in ((4, 0, P, 7), (1, 4, NS, 2)):
                for j in range(1, nl + 1):
                    base_ = done
                    for i in range(nt):
                        pe.wait_ge(S("g_al"), base_ + i + 1)
                        if j > 1:
                            pe.wait_ge(S("g_tn"), base_ - nt + i + 1)
                        for h in range(H):
                            last = mm(bank(i)[0:w, h * w:(h + 1) * w], gtile(g_al, i, w)[:, h, :], gtile(g_T, i0 + i, w)[:, h, :], True, True)
                        last.then_inc(S("g_p1_mm"), 1)
                    for i in range(nt):
                        pe.wait_ge(S("g_p1"), done + 1)
                        if done >= 2:
                            pe.wait_ge(S("g_tn"), done - 1)
                        b_ = 4 + 2 * (done % 2)
                        p1 = gtile(g_p1.rearrange("p a b -> p (a b)"), i, w)
                        for h in range(H):
                            mm(bank(b_)[0:w, h * w:(h + 1) * w], gtile(g_N, i0 + i, w)[:, h, :], p1[:, h, :], True, True)
                        for h in range(H):
                            last = mm(bank(b_ + 1)[0:w, h * w:(h + 1) * w], p1[:, h, :], gtile(g_N, i0 + i, w)[:, h, :], True, True)
                        last.then_inc(S("g_tn_mm"), 1)
                        done += 1
            pe.wait_ge(S("g_kbg"), 1)
            tail_tensor(pe, 1, lambda i, w, h: gtile(g_QK, i, w)[:, h, :], t_kd, g_qg, gv, g_kbg, lambda i, w: gtile(g_N, i, w))
        def mem_tensor(pe):
            pe.wait_ge(S("mem_in"), 32)
            for q in range(4):
                i, hf = divmod(q, 2)
                for k in range(4):
                    last = tr(bank(q)[:, k * P:(k + 1) * P], mkv[:, i, (4 * hf + k) * P:(4 * hf + k + 1) * P], P)
                last.then_inc(S("mem_turned"), 1)
            norm_tensor(pe, memn, MEM)
            pe.wait_ge(S("part_lo"), IN_BEFORE["wkv"] + KD)
            for n in range(8):
                for kh in range(2):
                    w = weights(pe, first["wkv"] + 2 * n + kh)
                    for mt in range(2):
                        job = 2 * n + mt
                        if job >= 4 and kh == 0:
                            pe.wait_ge(S("kvm_out_s" if mt == 0 else "kvm_out_v"), (job - 4) // 2 + 1)
                        for kk in range(4):
                            k = 4 * kh + kk
                            last = mm3(bank(job % 4)[:, 0:256], operand("wkv", k, slice(mt * P, (mt + 1) * P)),
                                       (w[0][:, kk, :], w[1][:, kk, :]), k == 0, k == KD - 1)
                        if kh:
                            last.then_inc(S("kvm_mm"), 1)
                    if kh == 0:
                        last.then_inc(S("kvm_part"), 1)
            pe.wait_ge(S("kvm_out_s"), 8)
            pe.wait_ge(S("kvm_out_v"), 8)
            for q in range(4):
                mt, kq = divmod(q, 2)
                for k in range(4):
                    last = tr(bank(4 + q)[:, k * P:(k + 1) * P], mkv[:, mt, (4 * kq + k) * P:(4 * kq + k + 1) * P], P)
                last.then_inc(S("kt_turned"), 1)

        def mem_vector(v):
            for q in range(4):
                i, hf = divmod(q, 2)
                v.wait_ge(S("mem_turned"), q + 1)
                last = V.tensor_copy(memt[:, 4 * hf:4 * hf + 4, i * P:(i + 1) * P], bank(q).rearrange("p (k t) -> p k t", t=P))
            last.then_inc(S("mem_raw"), 1)
            v.wait_ge(S("mem_raw"), 1)
            squares_vector(v, memt, memn)
            scale_vector(v, memt, MEM, R_MEM, memn, parts="wkv")
            for n in range(8):
                part_lo(v, "wout", n)
                v.wait_ge(S("kvm_mm"), 2 * n + 2)
                V.tensor_copy(mkv[:, 1, n * 256:(n + 1) * 256], bank((2 * n + 1) % 4)[:, 0:256]).then_inc(S("kvm_out_v"), 1)
            for q in range(4):
                mt, kq = divmod(q, 2)
                v.wait_ge(S("kt_turned"), q + 1)
                V.tensor_copy(mkt[:, 4 * kq:4 * kq + 4, mt * P:(mt + 1) * P], bank(4 + q).rearrange("p (k t) -> p k t", t=P))

        def mem_scalar(s):
            s.wait_ge(S("mem_raw"), 1)
            squares_scalar(s, memt, memn)
            root_scalar(s, MEM)
            parts_scalar(s, "wkv")
            for n in range(8):
                part_hi(s, "wout", n)
                split_hi(s, first["wkv"] + 2 * n + 1 + NH)
                s.wait_ge(S("kvm_mm"), 2 * n + 1)
                scopy(mkv[:, 0, n * 256:(n + 1) * 256], bank((2 * n) % 4)[:, 0:256]).then_inc(S("kvm_out_s"), 1)
                split_hi(s, first["wkv"] + 2 * n + 2 + NH)

        def cross_prompt_tensor(pe):
            def scores(j):
                h, i = divmod(j, 4)
                if j >= 4:
                    pe.wait_ge(S("att_exp"), 16 + j - 3)
                for k in range(2):
                    last = mm(bank(j % 4)[:, 0:MEM], xq[:, 2 * h + k, i * P:(i + 1) * P], mkt[:, 2 * h + k, :], k == 0, k == 1)
                last.then_inc(S("att_scores"), 1)

            def turn(j):
                pe.wait_ge(S("att_probs"), 16 + j + 1)
                if j >= 2:
                    pe.wait_ge(S("att_pt"), 16 + j - 1)
                for k in range(2):
                    last = tr(bank(6 + j % 2)[:, k * P:(k + 1) * P], cx_s[:, j % 4, k * P:(k + 1) * P], P)
                last.then_inc(S("att_turned"), 1)

            def pv(h):
                pe.wait_ge(S("att_pt"), 16 + 4 * h + 4)
                if h:
                    pe.wait_ge(S("att_out"), 4 + 2 * h)
                for ft in range(2):
                    for k in range(2):
                        last = mm(bank(4 + ft), mkv[:, k, D + h * XDH + ft * P:D + h * XDH + (ft + 1) * P], cx_pt[:, h % 2, k, :], k == 0, k == 1)
                last.then_inc(S("att_pv"), 1)

            scores(0)
            scores(1)
            for j in range(16):
                if j + 2 < 16:
                    scores(j + 2)
                turn(j)
                if j >= 5 and j % 4 == 1:
                    pv(j // 4 - 1)
            pv(3)

        def cross_prompt_vector(v):
            def first_(j):
                v.wait_ge(S("att_scores"), 16 + j + 1)
                link(V.tensor_reduce(cx_stat[:, 0, j:j + 1], bank(j % 4)[:, 0:MEM], AXX, ALU.max, negate=True))
                V.tensor_scalar(cx_stat[:, 0, j:j + 1], cx_stat[:, 0, j:j + 1], XSCALE, None, ALU.mult).then_inc(S("att_max"), 1)

            def second(j):
                v.wait_ge(S("att_exp"), 16 + j + 1)
                link(V.reciprocal(cx_stat[:, 2, j:j + 1], cx_stat[:, 1, j:j + 1]))
                V.tensor_scalar(cx_s[:, j % 4, :], cx_s[:, j % 4, :], cx_stat[:, 2, j:j + 1], None, ALU.mult).then_inc(S("att_probs"), 1)

            def out_(h):
                v.wait_ge(S("att_pv"), 16 + h + 1)
                for ft in range(2):
                    V.tensor_copy(OM[:, 2 * h + ft, 0:SEQ], bank(4 + ft)).then_inc(S("att_out"), 1)

            first_(0)
            for j in range(16):
                if j + 1 < 16:
                    first_(j + 1)
                second(j)
                if j >= 6 and j % 4 == 2:
                    out_(j // 4 - 1)
            out_(3)

        def cross_prompt_scalar(s):
            def ex(j):
                s.wait_ge(S("att_max"), 16 + j + 1)
                if j >= 4:
                    s.wait_ge(S("att_turned"), 16 + j - 3)
                A.activation(cx_s[:, j % 4, :], bank(j % 4)[:, 0:MEM], ACT.Exp, bias=cx_stat[:, 0, j:j + 1], scale=XSCALE,
                             accum_out=cx_stat[:, 1, j:j + 1]).then_inc(S("att_exp"), 1)

            ex(0)
            for j in range(16):
                if j + 1 < 16:
                    ex(j + 1)
                h, i = divmod(j, 4)
                s.wait_ge(S("att_turned"), 16 + j + 1)
                if h >= 2 and i == 0:
                    s.wait_ge(S("att_pv"), 16 + h - 1)
                scopy(cx_pt[:, h % 2, :, i * P:(i + 1) * P], bank(6 + j % 2)[:, 0:2 * P].rearrange("p (k t) -> p k t", t=P))\
                    .then_inc(S("att_pt"), 1)

        def cross_sample_tensor(pe):
            def turn(q):
                b, x = divmod(q, 4)
                if x == 0:
                    pe.wait_ge(S(f"cx_ring{b % 3}_in"), 16 * (b // 3 + 1))
                if q >= 4:
                    pe.wait_ge(S("keys_turned_s" if q % 2 == 0 else "keys_turned_v"), 32 + (q - 4) // 2 + 1)
                for kk in range(2):
                    for i in range(2):
                        last = tr(bank(q % 4)[:, (2 * kk + i) * P:(2 * kk + i + 1) * P],
                                  cx_slot(b)[:, i * D + (2 * x + kk) * P:i * D + (2 * x + kk + 1) * P], P)
                last.then_inc(S("satt_turned"), 1)

            def score(q):
                b, h = divmod(q, 4)
                pe.wait_ge(S("keys_turned_s" if q % 2 == 0 else "keys_turned_v"), 32 + q // 2 + 1)
                r = slice(32 * (b // 2), 32 * (b // 2) + 32)
                for kk in range(2):
                    last = mm(bank(4)[r, 0:MEM], cx_qp[:, 2 * h + kk, b, :], cx_kt[:, q % 4, kk * MEM:(kk + 1) * MEM],
                              b % 2 == 0 and h == 0 and kk == 0, b % 2 == 1 and h == 3 and kk == 1)
                last.then_inc(S("satt_scored"), 1)

            pe.wait_ge(S("cross_q"), 1)
            turn(0)
            turn(1)
            for q in range(2, 32):
                turn(q)
                score(q - 2)
            score(30)
            score(31)
            pe.wait_ge(S("satt_probs"), 1 + 1)
            for i in range(2):
                last = tr(bank(1)[:, i * P:(i + 1) * P], cx_ss[:, i * P:(i + 1) * P], P)
            last.then_inc(S("satt_pt"), 1)
            pe.wait_ge(S("satt_pt_out"), 2 + 1)
            for b in range(NB):
                pe.wait_ge(S(f"cx_ring{(8 + b) % 3}_in"), 16 * ((8 + b) // 3 + 1))
                r = slice(32 * (b // 2), 32 * (b // 2) + 32)
                for hf in range(2):
                    for i in range(2):
                        last = mm(bank((2 if b % 2 == 0 else 5) + hf)[r, :], cx_pts[:, i, r],
                                  cx_slot(8 + b)[:, i * D + hf * 512:i * D + (hf + 1) * 512], i == 0, i == 1)
                last.then_inc(S("satt_pv"), 1)
            pick = ident.rearrange("p (g e h t) -> p g e h t", e=2, h=H, t=TS)
            for e in range(2):
                pe.wait_ge(S("satt_o" if e == 0 else "satt_exp"), 2 if e == 0 else 3)
                for k in range(KD):
                    last = mm(bank(0)[:, k * NS:(k + 1) * NS].rearrange("p (g e t) -> p g e t", e=2, t=TS)[:, :, e, :],
                              cx_o[:, e, k * P:(k + 1) * P], pick[:, :, e, k // 2, :], True, True)
            last.then_inc(S("satt_pv"), 1)

        def cross_sample_vector(v):
            for q in range(1, 32, 2):
                v.wait_ge(S("satt_turned"), 64 + q + 1)
                if q >= 4:
                    v.wait_ge(S("satt_scored"), 64 + q - 3)
                V.tensor_copy(cx_kt[:, q % 4, :], bank(q % 4)).then_inc(S("keys_turned_v"), 1)
            v.wait_ge(S("satt_scored"), 64 + 32)
            link(V.tensor_reduce(cx_stat[:, 0, 0:1], bank(4)[:, 0:MEM], AXX, ALU.max, negate=True))
            V.tensor_scalar(cx_stat[:, 0, 0:1], cx_stat[:, 0, 0:1], XSCALE, None, ALU.mult).then_inc(S("satt_max"), 1)
            v.wait_ge(S("satt_exp"), 1 + 1)
            link(V.reciprocal(cx_stat[:, 2, 0:1], cx_stat[:, 1, 0:1]))
            V.tensor_scalar(cx_ss, cx_ss, cx_stat[:, 2, 0:1], None, ALU.mult).then_inc(S("satt_probs"), 1)
            v.wait_ge(S("satt_pt"), 2 + 1)
            V.tensor_copy(cx_pts, bank(1)[:, 0:256].rearrange("p (i r) -> p i r", r=P)).then_inc(S("satt_pt_out"), 1)
            v.wait_ge(S("satt_pv"), 1 + NB)
            V.tensor_copy(cx_o[:, 0, :].rearrange("p (j n) -> p j n", j=2), PS[1][:, :, :]).then_inc(S("satt_o"), 1)
            v.wait_ge(S("satt_pv"), 1 + NB + 1)
            V.tensor_copy(OM[:, :, SEQ:T], bank(0)[:, 0:KD * NS].rearrange("p (k t) -> p k t", t=NS))

        def cross_sample_scalar(s):
            for q in range(0, 32, 2):
                s.wait_ge(S("satt_turned"), 64 + q + 1)
                if q >= 4:
                    s.wait_ge(S("satt_scored"), 64 + q - 3)
                scopy(cx_kt[:, q % 4, :], bank(q % 4)).then_inc(S("keys_turned_s"), 1)
            s.wait_ge(S("satt_max"), 1 + 1)
            A.activation(cx_ss, bank(4)[:, 0:MEM], ACT.Exp, bias=cx_stat[:, 0, 0:1], scale=XSCALE,
                         accum_out=cx_stat[:, 1, 0:1]).then_inc(S("satt_exp"), 1)
            s.wait_ge(S("satt_pv"), 1 + NB)
            link(scopy(cx_o[:, 1, 0:512], bank(5)), "s")
            scopy(cx_o[:, 1, 512:1024], bank(6)).then_inc(S("satt_exp"), 1)

        def ff_tensor(pe):
            for t in range(KF):
                for gu in range(2):
                    job = 2 * t + gu
                    if job >= 4:
                        pe.wait_ge(S("ff_out"), t - 1)
                    wh, wl = weights(pe, first["wgu"] + job)
                    for k in range(KD):
                        if job == 0:
                            pe.wait_ge(S("part_lo"), IN_BEFORE["wgu"] + k + 1)
                        for j in range(2):
                            last = mm3(PS[job % 4][:, j, 0:HT], (wh[:, k, :], wl[:, k, :]),
                                       operand("wgu", k, slice(j * HT, (j + 1) * HT)), k == 0, k == KD - 1)
                    last.then_inc(S("ff_mm"), 1)

        def ff_scalar(s):
            for t in range(KF):
                s.wait_ge(S("ff_mm"), 2 * t + 1)
                if t >= 2:
                    s.wait_ge(S("ff_out"), t - 1)
                A.activation(halves(f_g[:, t % 2, :]), pair((2 * t) % 4), ACT.Silu).then_inc(S("ff_silu"), 1)
                split_hi(s, first["wgu"] + 2 * t + 1 + NH)
                if t:
                    s.wait_ge(S("ff_out"), t)
                    part_hi(s, "wdn", t - 1)
                split_hi(s, first["wgu"] + 2 * t + 2 + NH)
            s.wait_ge(S("ff_out"), KF)
            part_hi(s, "wdn", KF - 1)

        def ff_vector(v):
            for t in range(KF):
                v.wait_ge(S("ff_silu"), t + 1)
                v.wait_ge(S("ff_mm"), 2 * t + 2)
                tt(halves(hT[:, t, :]), halves(f_g[:, t % 2, :]), pair((2 * t + 1) % 4), ALU.mult).then_inc(S("ff_out"), 1)
                if t:
                    part_lo(v, "wdn", t - 1)
            part_lo(v, "wdn", KF - 1)

        def result_tensor(pe):
            for job in range(10):
                i, hf = divmod(job, 2)
                t0, w, _ = TILES[i]
                if job >= 8:
                    pe.wait_ge(S("turned_out_v" if job % 2 == 0 else "turned_out_s"), (6 if job % 2 == 0 else 5) + 1)
                for k in range(4):
                    last = tr(bank(job % 8)[0:w, k * P:(k + 1) * P], XT[:, 4 * hf + k, t0:t0 + w], P)
                last.then_inc(S("turned"), 1)

        def result_evac(eng, copy, name, par_):
            for job in range(par_, 10, 2):
                i, hf = divmod(job, 2)
                w = TILES[i][1]
                eng.wait_ge(S("turned"), 11 + job + 1)
                copy(y_tok[0:w, i, hf * 512:(hf + 1) * 512], bank(job % 8)[0:w, :]).then_inc(S(name), 1)

        def stage(eng, name, *work):
            n = STAGES.index(name)
            if n:
                eng.wait_ge(S("stage_ended"), 3 * n)
            for f in work:
                f()
            eng.drain().then_inc(S("stage_ended"), 1)

        xq_dst = lambda i: xq[:, i, :]
        nsq = carve(SC, 0, KD, T)

        @block.tensor
        def _(pe):
            stage(pe, "inputs", lambda: inputs_tensor(pe))
            stage(pe, "win", lambda: norm_tensor(pe, OM, T), lambda: win_tensor(pe))
            stage(pe, "moba_prompt", lambda: moba_prompt_tensor(pe))
            stage(pe, "moba_sample", lambda: moba_sample_tensor(pe))
            stage(pe, "spread", lambda: spread_tensor(pe))
            stage(pe, "ssm", lambda: ssm_tensor(pe))
            stage(pe, "hgrn", lambda: hgrn_tensor(pe))
            stage(pe, "gdn", lambda: gdn_tensor(pe))
            stage(pe, "mem", lambda: mem_tensor(pe))
            stage(pe, "wout",
                  lambda: gemm_tensor(pe, "wout", KD),
                  lambda: norm_tensor(pe, nsq, T, after_gemm="wout"),
                  lambda: norm_tensor(pe, nsq, T, True),
                  lambda: gemm_tensor(pe, "wxq", KD))
            stage(pe, "cross_prompt", lambda: cross_prompt_tensor(pe))
            stage(pe, "cross_sample", lambda: cross_sample_tensor(pe))
            stage(pe, "wxo",
                  lambda: gemm_tensor(pe, "wxo", KD),
                  lambda: norm_tensor(pe, nsq, T, after_gemm="wxo"),
                  lambda: norm_tensor(pe, nsq, T, True),
                  lambda: ff_tensor(pe))
            stage(pe, "wdn",
                  lambda: gemm_tensor(pe, "wdn", KD, 3),
                  lambda: norm_tensor(pe, OM, T, after_gemm="wdn"))
            stage(pe, "result", lambda: result_tensor(pe))

        @block.vector
        def _(v):
            stage(v, "inputs", lambda: inputs_evac("v", v, vcopy, "turned_out_v", 0), lambda: small_lo(v))
            stage(v, "win", lambda: squares_vector(v, XT, OM), lambda: scale_vector(v, XT, T, R_MIXPRE, xn, parts="win"),
                  lambda: win_vector(v))
            stage(v, "moba_prompt", lambda: moba_prompt_vector(v))
            stage(v, "moba_sample", lambda: moba_sample_vector(v))
            stage(v, "spread")
            stage(v, "ssm", lambda: ssm_vector(v))
            stage(v, "hgrn", lambda: hgrn_vector(v), lambda: hgrn_vector_tail(v))
            stage(v, "gdn", lambda: gdn_vector(v))
            stage(v, "mem", lambda: mem_vector(v))
            stage(v, "wout",
                  lambda: v.wait_ge(S("states_out"), 96),
                  lambda: gemm_sq_vector(v, "wout", nsq),
                  lambda: scale_vector(v, xn, T, R_MIXPOST, xn, XT),
                  lambda: scale_vector(v, XT, T, R_XPRE, xn, parts="wxq"),
                  lambda: gemm_vector(v, "wxq", KD, xq_dst))
            stage(v, "cross_prompt", lambda: cross_prompt_vector(v))
            stage(v, "cross_sample", lambda: cross_sample_vector(v))
            stage(v, "wxo",
                  lambda: parts_vector(v, "wxo"),
                  lambda: gemm_sq_vector(v, "wxo", nsq),
                  lambda: scale_vector(v, xn, T, R_XPOST, xn, XT),
                  lambda: scale_vector(v, XT, T, R_FPRE, xn, parts="wgu"),
                  lambda: v.wait_ge(S("mem_kv_out"), 64),
                  lambda: ff_vector(v))
            stage(v, "wdn", lambda: gemm_sq_vector(v, "wdn", OM), lambda: scale_vector(v, xn, T, R_FPOST, xn, XT))
            stage(v, "result", lambda: result_evac(v, vcopy, "turned_out_v", 0))

        @block.scalar
        def _(s):
            stage(s, "inputs", lambda: small_hi(s), lambda: inputs_evac("s", s, scopy, "turned_out_s", 1))
            stage(s, "win", lambda: squares_scalar(s, XT, OM), lambda: split_hi(s, NH), lambda: root_scalar(s, T),
                  lambda: parts_scalar(s, "win"), lambda: win_scalar(s))
            stage(s, "moba_prompt", lambda: moba_prompt_scalar(s))
            stage(s, "moba_sample", lambda: moba_sample_scalar(s))
            stage(s, "spread", lambda: spread_scalar(s))
            stage(s, "ssm", lambda: ssm_scalar(s))
            stage(s, "hgrn", lambda: hgrn_scalar(s))
            stage(s, "gdn", lambda: gdn_scalar(s))
            stage(s, "mem", lambda: mem_scalar(s))
            stage(s, "wout",
                  lambda: s.wait_ge(S("states_out"), 96),
                  lambda: gemm_sq_scalar(s, "wout", nsq),
                  lambda: root_scalar(s, T),
                  lambda: squares_scalar(s, XT, nsq, range(KD), 0),
                  lambda: root_scalar(s, T),
                  lambda: parts_scalar(s, "wxq"),
                  lambda: gemm_scalar(s, "wxq", KD, xq_dst))
            stage(s, "cross_prompt", lambda: cross_prompt_scalar(s))
            stage(s, "cross_sample", lambda: cross_sample_scalar(s))
            stage(s, "wxo",
                  lambda: parts_scalar(s, "wxo"),
                  lambda: gemm_sq_scalar(s, "wxo", nsq),
                  lambda: root_scalar(s, T),
                  lambda: squares_scalar(s, XT, nsq, range(KD), KD),
                  lambda: root_scalar(s, T),
                  lambda: parts_scalar(s, "wgu"),
                  lambda: ff_scalar(s))
            stage(s, "wdn", lambda: gemm_sq_scalar(s, "wdn", OM, 3), lambda: root_scalar(s, T))
            stage(s, "result", lambda: result_evac(s, scopy, "turned_out_s", 1))

        @block.gpsimd
        def _(g):
            def st(dst, src, name):
                g.dma_start(dst, src).then_inc(S(name), 16)

            g_constants(g)
            split_lo(g, first["wkv"] + NH)
            g.wait_ge(S("conv_states_made"), 1)
            for m_ in range(2):
                n_ = "ssm_conv" if m_ == 0 else "gdn_conv"
                st(o[n_ + "_p"][0, 0], cw_out[0:3, m_ * 768:(m_ + 1) * 768], "conv_states_out")
                st(o[n_ + "_s"][0].rearrange("b w c -> (b w) c"), cw_out[3:27, m_ * 768:(m_ + 1) * 768], "conv_states_out")
            g_moba_tables(g)
            g.wait_ge(S("pages_in"), 16)
            g.wait_ge(S("kv_out"), NT)
            for kv in range(2):
                for i in range(4):
                    st(o["moba_kp" if kv == 0 else "moba_vp"][0, 0].rearrange("s h d -> s (h d)")[i * P:(i + 1) * P, :],
                       kvtok[:, i, kv * GW:(kv + 1) * GW], "moba_kv_out")
                st(o["moba_ks" if kv == 0 else "moba_vs"][0].rearrange("b t h d -> (b t) (h d)"),
                   kvs[0:NS, kv * GW:(kv + 1) * GW], "moba_kv_out")
            load_pages(g, 1)
            g.wait_ge(S("fin_made"), 1)
            st(o["ssm_p"][0, 0].rearrange("(c e) q n -> (e q) c n", e=2), s_fin, "states_out")
            g.wait_ge(S("states_made"), 1)
            st(o["ssm_s"][0].rearrange("b (c e) q n -> (e q) b c n", e=2), s_h0, "states_out")
            hgrn_gpsimd(g)
            for run, n_ in enumerate(("hgrn", "gdn")):
                g.wait_ge(S("fin_made"), run + 2)
                st(o[n_ + "_p"][0, 0].rearrange("(c e) k v -> (e k) c v", e=2), t_st, "states_out")
                g.wait_ge(S("states_made"), run + 2)
                st(o[n_ + "_s"][0].rearrange("b (c e) k v -> (e k) b c v", e=2), t_s0, "states_out")
            split_lo(g, first["wout"] + NH)
            for mt in range(2):
                g.wait_ge(S("kvm_out_s" if mt == 0 else "kvm_out_v"), 8)
                for kv in range(2):
                    st(o["mem_k" if kv == 0 else "mem_v"][0, 0].rearrange("m h d -> m (h d)")[mt * P:(mt + 1) * P, :],
                       mkv[:, mt, kv * D:(kv + 1) * D], "mem_kv_out")
            split_lo(g, first["wxo"] + NH)
            after(g, "wout")
            link(G.memset(cx_qp, 0.0), "g")
            for k in range(KD):
                for e in range(2):
                    at = 16 * e + 4 * (k // 2)
                    last = G.tensor_copy(cx_qp[:, k, :, at:at + TS].rearrange("p (g e) t -> p g e t", e=2)[:, :, e, :],
                                         xq[:, k, SEQ:T].rearrange("p (g e t) -> p g e t", e=2, t=TS)[:, :, e, :])
            last.then_inc(S("cross_q"), 1)
            split_lo(g, len(chunks))
            for i in range(4):
                g.wait_ge(S("turned_out_v"), 6 + i + 1)
                g.wait_ge(S("turned_out_s"), 5 + i + 1)
                st(o["y_p"][0, i * P:(i + 1) * P, :], y_tok[:, i, :], "y_stored")
            g.wait_ge(S("turned_out_v"), 6 + 5)
            g.wait_ge(S("turned_out_s"), 5 + 5)
            st(o["y_s"].rearrange("b t d -> (b t) d"), y_tok[0:NS, 4, :], "y_stored")
            g.wait_ge(S("moba_kv_out"), 16 * 10)
            g.wait_ge(S("conv_states_out"), 16 * 4)
            g.wait_ge(S("states_out"), 16 * 6)
            g.wait_ge(S("mem_kv_out"), 16 * 4)
            g.wait_ge(S("y_stored"), 16 * 5)


_INS = ['x_prompt', 'x_sample', 'mem_prompt', 'cache_moba_k', 'cache_moba_v', 'page_table', 'cache_mem_k',
        'cache_mem_v', 'state_ssm_conv', 'state_ssm', 'state_hgrn', 'state_gdn_conv', 'state_gdn', 'n_mix_pre',
        'n_mix_post', 'w_in', 'w_out', 'ssm_conv_w', 'ssm_conv_b', 'ssm_dt_bias', 'ssm_a_log', 'ssm_d', 'ssm_norm',
        'hgrn_norm', 'gdn_conv_w', 'gdn_a_log', 'gdn_dt_bias', 'gdn_norm', 'n_x_pre', 'n_x_post',
        'mem_norm', 'w_xq', 'w_xkv', 'w_xo', 'n_f_pre', 'n_f_post', 'w_gu', 'w_down']
_OUTS = [("y_p", (1, 512, 1024)), ("y_s", (8, 4, 1024)),
         ("moba_kp", (1, 1, 512, 4, 64)), ("moba_ks", (1, 8, 4, 4, 64)),
         ("moba_vp", (1, 1, 512, 4, 64)), ("moba_vs", (1, 8, 4, 4, 64)),
         ("mem_k", (1, 1, 256, 4, 256)), ("mem_v", (1, 1, 256, 4, 256)),
         ("ssm_conv_p", (1, 1, 3, 768)), ("ssm_conv_s", (1, 8, 3, 768)),
         ("ssm_p", (1, 1, 4, 64, 128)), ("ssm_s", (1, 8, 4, 64, 128)),
         ("hgrn_p", (1, 1, 4, 64, 64)), ("hgrn_s", (1, 8, 4, 64, 64)),
         ("gdn_conv_p", (1, 1, 3, 768)), ("gdn_conv_s", (1, 8, 3, 768)),
         ("gdn_p", (1, 1, 4, 64, 64)), ("gdn_s", (1, 8, 4, 64, 64))]


def kernel(**inputs):
    import numpy as _np
    import concourse.bacc as _bacc
    from concourse import mybir as _mybir
    from concourse.bass_utils import run_bass_kernel_spmd as _run

    nc = _bacc.Bacc("TRN2", target_bir_lowering=False, num_devices=1)
    arrays, ins, outs = {}, {}, {}
    for name in _INS:
        x = _np.ascontiguousarray(inputs[name])
        arrays[f"in_{name}"] = x
        ins[name] = nc.dram_tensor(f"in_{name}", x.shape, _mybir.dt.from_np(x.dtype), kind="ExternalInput").ap()
    for name, shape in _OUTS:
        outs[name] = nc.dram_tensor(f"out_{name}", shape, _mybir.dt.float32, kind="ExternalOutput").ap()
    build(nc, ins, outs)
    r = _run(nc, [arrays], core_ids=[0])
    return tuple(r.results[0][f"out_{name}"] for name, _ in _OUTS)
```

```python
from contextlib import ExitStack

import concourse.bass as bass
from concourse import mybir

F32 = mybir.dt.float32
F32R = mybir.dt.float32r
I32 = mybir.dt.int32
ALU = mybir.AluOpType
ACT = mybir.ActivationFunctionType
AXX = mybir.AxisListType.X

P = 128
D = 1024
KD = D // P
SEQ = 512
NB, TS = 8, 4
NS = NB * TS
T = SEQ + NS
HT = T // 2
GW = D // 4
H = 4
DH = GW // H
PAGE, NPAGE = 128, 16
MOBA_BLOCK = 256
NBLK = PAGE * NPAGE // MOBA_BLOCK
PAST = PAGE * NPAGE
MEM = 256
XDH = D // H
FF = 2816
KF = FF // P
NEG = -1.0e30
EPS = 1e-6
SCALE = DH ** -0.5
XSCALE = XDH ** -0.5
SLOPE = [2.0 ** (-8.0 * (h + 1) / H) for h in range(H)]

C_MQ, C_MK, C_MV, C_Z, C_XBC, C_HQ, C_HF, C_HI, C_HG, C_GQKV, C_GZ = 0, 2, 4, 6, 8, 14, 16, 18, 20, 22, 28
NPROJ = 30
WIN_COLS = [0, 256, 512, 768, 1024, 1280, 1536, 1796, 2052, 2308, 2564, 2820, 3076, 3332, 3588]
COL_DT, COL_B, COL_A = 1792, 3844, 3848

TILES = [(i * P, P, 7) for i in range(SEQ // P)] + [(SEQ, NS, 2)]
NT = len(TILES)

R_MIXPRE, R_MIXPOST, R_XPRE, R_XPOST, R_MEM, R_FPRE, R_FPOST = [8 * i for i in range(7)]
R_SCW, R_GCW, R_SCB, R_SNORM, R_HNORM, R_GNORM, R_SD = 56, 80, 104, 110, 112, 113, 114
NROWS = 116


def build(nc, a, o):
    ctx = ExitStack()
    sems = {}

    STAGES = ["inputs", "win", "moba_prompt", "moba_sample", "ssm", "hgrn", "gdn", "mem", "wout",
              "cross_prompt", "cross_sample", "wxo", "wdn", "result"]

    def S(name):
        if name not in sems:
            sems[name] = ctx.enter_context(nc.semaphore(name))
        return sems[name]

    with ctx:
        def sb(name, shape, dt=F32):
            return ctx.enter_context(nc.sbuf_tensor(name, shape, dt))

        def sb2(name, shape):
            at = (nc.sbuf_base + 31) // 32 * 32
            return sb(name, shape), nc.alloc_sbuf_tensor_at(name + "_parts", shape, F32R, offset=at)

        XT = sb("XT", [P, KD, T])
        XN, XN_R = sb2("XN", [P, KD * T])
        OM, OM_R = sb2("OM", [P, KD, T])
        PROJ, PROJ_R = sb2("PROJ", [P, NPROJ * T])
        NW, NH, WSZ = 3, 3, 8 * P
        W = sb("W", [P, NW * WSZ])
        W_HI = sb("W_HI", [P, NH, WSZ], F32R)
        W_LO = sb("W_LO", [P, NH, WSZ], F32R)
        SC, SC_R = sb2("SC", [P, 9200])
        CN = sb("CN", [P, 2900])
        SM = sb("SM", [P, 400])
        PTAB = sb("PTAB", [1, P], I32)
        PS = [ctx.enter_context(nc.psum_tensor(f"PS{i}", [P, 2, 512], F32)) for i in range(4)]

        def bank(i):
            return PS[i // 2][:, i % 2, :]

        def pair(i):
            return PS[i][:, :, 0:HT]

        def carve(buf, at, *shape):
            n = 1
            for s in shape:
                n *= s
            v = buf[:, at:at + n]
            if len(shape) == 2:
                v = v.rearrange("p (a b) -> p a b", b=shape[1])
            elif len(shape) == 3:
                v = v.rearrange("p (a b c) -> p a b c", b=shape[1], c=shape[2])
            return v

        class Carver:
            def __init__(self, buf, at=0, size=None):
                self.buf, self.at = buf, at

            def __call__(self, *shape):
                v = carve(self.buf, self.at, *shape)
                n = 1
                for s in shape:
                    n *= s
                self.at += n
                assert self.at <= self.buf.shape[1], (self.at, self.buf.shape)
                return v

        proj = PROJ[:, :].rearrange("p (c t) -> p c t", t=T)
        xn = XN[:, :].rearrange("p (c t) -> p c t", t=T)

        c = Carver(CN)
        ident = c(P)
        ones = c(P)
        blk64 = c(P)
        lev = c(8, P)
        negmask = c(P)
        negmask_s = c(NS)
        ind = c(NB)
        keep = c(T)
        onehot = c(H, P)
        pairsel = c(2, P)
        CONSTS_END = c.at
        eps = c(1)
        prm = SM[:, 0:NROWS]
        sm = Carver(SM, NROWS)
        head4 = sm(8)

        def par(r):
            return prm[:, r:r + 1]

        chunks = []

        def add(w, k0, nk, c0, ncol, sem, count):
            chunks.append((w.rearrange("(k p) n -> p k n", p=P)[:, k0:k0 + nk, c0:c0 + ncol], nk, ncol, sem, count))

        win = a["w_in"][0]
        first = {}

        def section(name):
            first[name] = len(chunks)

        BEFORE = {"wout": NPROJ, "wkv": 0, "wxq": NPROJ + KD, "wxo": NPROJ + 2 * KD, "wdn": NPROJ + 3 * KD}
        section("win")
        for i in range(NPROJ):
            add(win, 0, 8, WIN_COLS[i // 2] + P * (i % 2), P, "gemm_mm", i + 1)
        section("wkv")
        for n in range(8):
            add(a["w_xkv"][0], 0, 4, 256 * n, 256, "kvm_part", n + 1)
            add(a["w_xkv"][0], 4, 4, 256 * n, 256, "kvm_mm", 2 * n + 2)
        for name, src in (("wout", a["w_out"][0]), ("wxq", a["w_xq"][0]), ("wxo", a["w_xo"][0])):
            section(name)
            for i in range(KD):
                add(src, 0, 8, P * i, P, "gemm_mm", BEFORE[name] + i + 1)
        section("wgu")
        for i in range(KF):
            add(a["w_gu"][0], 0, 8, P * i, P, "ff_mm", 2 * i + 1)
            add(a["w_gu"][0], 0, 8, FF + P * i, P, "ff_mm", 2 * i + 2)
        section("wdn")
        for i in range(KD):
            add(a["w_down"][0], 0, 8, P * i, P, "gemm_part", 2 * i + 1)
            add(a["w_down"][0], 8, 8, P * i, P, "gemm_part", 2 * i + 2)
            add(a["w_down"][0], 16, 6, P * i, P, "gemm_mm", BEFORE["wdn"] + i + 1)

        def raw_chunk(n):
            return W[:, n % NW * WSZ:n % NW * WSZ + chunks[n][1] * chunks[n][2]]

        def load_chunks(eng, n0, n1):
            for n in range(n0, n1):
                src, nk, ncol, _, _ = chunks[n]
                if n >= NW:
                    eng.wait_ge(S("weights_split"), n - NW + 1)
                eng.dma_start(raw_chunk(n).rearrange("p (k n) -> p k n", n=ncol), src)\
                   .then_inc(S(f"weights_in{n % NW}"), 16)

        parts_made = {"hi": 0, "lo": 0}

        def split_hi(s, upto):
            for n in range(parts_made["hi"], min(upto, len(chunks))):
                _, nk, ncol, _, _ = chunks[n]
                s.wait_ge(S(f"weights_in{n % NW}"), 16 * (n // NW + 1))
                if n >= NH:
                    s.wait_ge(S(chunks[n - NH][3]), chunks[n - NH][4])
                nc.scalar.activation(W_HI[:, n % NH, 0:nk * ncol], raw_chunk(n), ACT.Copy)\
                    .then_inc(S("weights_hi"), 1)
                parts_made["hi"] = n + 1

        def split_lo(g, upto):
            for n in range(parts_made["lo"], min(upto, len(chunks))):
                _, nk, ncol, _, _ = chunks[n]
                g.wait_ge(S("weights_hi"), n + 1)
                nc.gpsimd.tensor_tensor(W_LO[:, n % NH, 0:nk * ncol], raw_chunk(n),
                                        W_HI[:, n % NH, 0:nk * ncol].bitcast(F32), ALU.subtract).then_inc(S("weights_split"), 1)
                parts_made["lo"] = n + 1

        def weights(pe, n):
            _, nk, ncol, _, _ = chunks[n]
            pe.wait_ge(S("weights_split"), n + 1)
            return [b[:, n % NH, 0:nk * ncol].rearrange("p (k n) -> p k n", n=ncol) for b in (W_HI, W_LO)]

        def mm3(out, l, r, start, stop):
            mm(out, l[0], r[0], start, False)
            mm(out, l[0], r[1], False, False)
            return mm(out, l[1], r[0], False, stop)

        def mm(out, lhsT, rhs, start, stop):
            return nc.tensor.matmul(out, lhsT, rhs, start=start, stop=stop, skip_group_check=True)

        def tr(out, in_, k):
            return nc.tensor.transpose(out, in_, ident[0:k, 0:k])

        links = {"v": 0, "s": 0, "g": 0}
        chain_eng = {"v": nc.vector, "s": nc.scalar, "g": nc.gpsimd}
        chain_name = {"v": "vector_chain", "s": "scalar_chain", "g": "gpsimd_chain"}

        def link(ins, e="v"):
            links[e] += 1
            ins.then_inc(S(chain_name[e]), 1)
            chain_eng[e].wait_ge(S(chain_name[e]), links[e])

        def after(eng, name):
            eng.wait_ge(S("stage_ended"), 3 * (STAGES.index(name) + 1))

        V, A, G = nc.vector, nc.scalar, nc.gpsimd

        cumtok = sm(NT, 8)
        rsq = sb("RSQ", [P, T])
        mp_dist = rsq[:, 0:SEQ]
        ups = sb("UPS", [P, 12, NB, 7])
        w_small = sb("WSMALL", [P, 3, KD, H])
        w_small_hi = sb("WSMALL_HI", [P, 3, KD, H], F32R)
        w_small_lo = sb("WSMALL_LO", [P, 3, KD, H], F32R)

        x_tok = carve(PROJ, 0, 4, D)
        xs_tok = carve(PROJ, 4 * D, D)
        rows_in = carve(PROJ, 5 * D, P)
        cs_tok = carve(PROJ, 6 * D, 2, 768)
        raw = OM[0:H, 0:2, :]
        rows_t = SC[0:H, 4 * T:8 * T].rearrange("p (c t) -> p c t", t=T)
        rows_d = OM[0:H, 2:4, :]
        rawc = carve(SC, 0, 4, T)
        cw_in = carve(SC, 16 * T, 12, 27)
        cw_out = OM[0:27, 0:3, :].rearrange("p a b -> p (a b)")[:, 0:12 * P]
        m = Carver(SC)
        kvs = m(2 * GW)
        kvtok = m(4, 2 * GW)
        mp_s = m(4, SEQ)
        mp_pt = OM[:, 2:4, 0:SEQ]
        mp_stat = m(3, 16)
        m = Carver(SC, 4680)
        NPG = 4
        pages = m(NPG, 4, 2 * P)
        ms_q = m(2, P)
        ms_pown = m(P)
        m = Carver(SC, 2 * GW)
        ms_kt = [m(512), m(512), OM[:, 2, 0:512], OM[:, 3, 0:512]]
        st_all = m(NPAGE, P)
        ms_qp = m(2, NB, 32)
        ms_gate = m(8)
        ms_gt = m(8, 8)
        ms_eq = m(8, 8)
        ms_rank = m(8)
        ms_sel = m(8)
        ms_stat = m(4)
        ms_s = carve(XN, 0, PAST + NS)
        ms_o = carve(XN, 0, 2, GW)
        ms_bias = carve(XN, PAST + NS, PAST + NS)
        ms_rowtmp = sm(NS)
        mr = sm(1)
        tr_ = sm(1)
        g8 = sm(NB)
        cr = sm(1)
        ltm = sm(8, 8)
        xc = proj[:, C_XBC:C_XBC + 6, :]
        pb = carve(PROJ, 0, 3, 2, T)
        rows = OM[0:H, 4:8, :]
        m = Carver(SC)
        xdt = m(2, T)
        s_m = m(H, P), m(H, P)
        s_er = m(H, P), m(H, P)
        s_c = m(H, P), m(H, P)
        s_tok = m(512), m(512)
        s_xd = m(2 * P), m(2 * P)
        s_dl = m(H), m(H)
        s_ht = m(2 * P)
        s_h0t = m(NB, 2 * P)
        s_h0 = carve(XN, 4 * T, NB, 2, P)
        s_dec = sm(2, NB)
        m = Carver(SC)
        h_b = proj[:, C_HF:C_HF + 2, :]
        h_k = carve(W, 0, 2, T)
        h_d = carve(W, 2 * T, 2, T)
        m(6, T)
        h_q1 = m(2, 2, T)
        h_k1 = m(2, 2, T)
        h_att = carve(PROJ, C_Z * T, 4 * 512 + H * NS)
        h_msk = carve(PROJ, C_Z * T + 2176, 4 * 512)
        m = Carver(SC)
        g_kbg = m(2, T)
        g_qg = m(2, T)
        g_p1 = m(4, 512)
        t_kd = m(2, T)
        t_vm = m(H * NB * DH)
        base = C_Z * T
        g_T = carve(PROJ, base, 2176)
        g_N = carve(PROJ, base + 2176, 2176)
        g_A = carve(PROJ, base + 2 * 2176, 2176)
        g_QK = carve(PROJ, base + 3 * 2176, 2176)
        g_sq = carve(XN, 1024, 4, T)
        g_kb = carve(XN, 1024, 2, T)
        m = Carver(XN, 4 * T)
        t_tok = m(512)
        t_vn = m(2 * P)
        t_st = m(2, DH), carve(XN, 0, 2, DH)
        t_last = m(2, NB)
        t_s0 = m(NB, 2, DH)
        memt = carve(SC, 0, KD, MEM)
        memn = carve(SC, KD * MEM, KD, MEM)
        mem_raw = carve(PROJ, C_Z * T, 2, D)
        mkv = carve(PROJ, 0, 2, 2 * D)
        mkt = carve(PROJ, 4 * D, KD, MEM)
        xq = carve(PROJ, 6 * D, KD, T)
        m = Carver(SC)
        cx_s = m(4, MEM)
        cx_pt = m(2, 2, SEQ)
        cx_stat = m(3, 16)
        cx_ss = m(MEM)
        cx_pts = m(2, P)
        cx_kt = m(4, 512)
        cx_o = carve(SC, 0, 2, D)
        cx_qp = carve(XN, 0, KD, NB, 32)
        cx_slots = [carve(PROJ, 6 * D + KD * T, 2 * D), carve(PROJ, 8 * D + KD * T, 2 * D), carve(SC, 9200 - 2 * D, 2 * D),
                    carve(XN, KD * NB * 32, 2 * D)]

        def cx_slot(n):
            return cx_slots[n % 4]

        hT = PROJ[:, 0:KF * T].rearrange("p (c t) -> p c t", t=T)
        f_g = carve(SC, 14 * T, 2, T)
        y_tok = carve(PROJ, 0, 5, D)

        block = ctx.enter_context(nc.Block())

        def issuer(n):
            if n % 8 in (1, 4, 5):
                return "gpsimd"
            return "scalar" if n >= NPG and n % 4 == 3 else "sync"

        def pages_sem(n):
            pool = issuer(n) == "gpsimd"
            same = [m_ for m_ in range(n % NPG, n + 1, NPG) if (issuer(m_) == "gpsimd") == pool]
            return S(f"pages{n % NPG}_in" + ("_gpsimd" if pool else "")), 64 * len(same)

        def load_pages(eng, quarters):
            for n in quarters:
                cache = a["cache_moba_k"] if n < 32 else a["cache_moba_v"]
                ids = [eng.value_load(PTAB[0:1, (n % 32) * 4 + i:(n % 32) * 4 + i + 1], min_val=0,
                                      max_val=a["cache_moba_k"].shape[1] - 1) for i in range(4)]
                m_ = n - NPG
                if 0 <= m_ < 32:
                    eng.wait_ge(S("satt_turned"), 2 * m_ + 2)
                elif m_ >= 32:
                    eng.wait_ge(S("ms_values_used"), m_ - 31)
                else:
                    after(eng, "win")
                for i in range(4):
                    eng.dma_start(pages[:, n % NPG, i, :],
                                  cache[0].rearrange("g p h d -> g p (h d)")[bass.ds(ids[i], 1)].rearrange("g p n -> (g p) n"))\
                       .then_inc(pages_sem(n)[0], 16)

        @block.sync
        def _(sp):
            def ld(dst, src, name):
                sp.dma_start(dst, src).then_inc(S(name), 16)

            for i in range(4):
                ld(x_tok[:, i, :], a["x_prompt"][0, i * P:(i + 1) * P, :], "x_in")
            ld(xs_tok[0:NS, :], a["x_sample"].rearrange("b t d -> (b t) d"), "x_in")
            for r, n in ((R_MIXPRE, "n_mix_pre"), (R_MIXPOST, "n_mix_post"), (R_XPRE, "n_x_pre"),
                         (R_XPOST, "n_x_post"), (R_MEM, "mem_norm"), (R_FPRE, "n_f_pre"), (R_FPOST, "n_f_post")):
                ld(rows_in[r:r + 8, :], a[n].rearrange("o (k p) -> (o k) p", p=P), "params_in")
            for w in range(4):
                ld(rows_in[R_SCW + 6 * w:R_SCW + 6 * w + 6, :], a["ssm_conv_w"][0, w].rearrange("(k p) -> k p", p=P), "params_in")
                ld(rows_in[R_GCW + 6 * w:R_GCW + 6 * w + 6, :], a["gdn_conv_w"][0, w].rearrange("(k p) -> k p", p=P), "params_in")
            ld(rows_in[R_SCB:R_SCB + 6, :], a["ssm_conv_b"].rearrange("o (k p) -> (o k) p", p=P), "params_in")
            ld(rows_in[R_SNORM:R_SNORM + 2, :], a["ssm_norm"].rearrange("o (k p) -> (o k) p", p=P), "params_in")
            for i in range(2):
                ld(rows_in[R_HNORM:R_HNORM + 1, i * DH:(i + 1) * DH], a["hgrn_norm"], "params_in")
                ld(rows_in[R_GNORM:R_GNORM + 1, i * DH:(i + 1) * DH], a["gdn_norm"], "params_in")
                for j in range(2):
                    ld(rows_in[R_SD + i:R_SD + i + 1, j * DH:(j + 1) * DH].rearrange("r (d o) -> r d o", o=1),
                       a["ssm_d"][:, 2 * i + j:2 * i + j + 1].rearrange("r (d o) -> r d o", o=1).to_broadcast((1, DH, 1)),
                       "params_in")
            for i, n in enumerate(("ssm_a_log", "ssm_dt_bias", "gdn_a_log", "gdn_dt_bias")):
                ld(head4[0:H, i:i + 1], a[n].rearrange("o h -> h o"), "params_in")
            ld(cs_tok[0:24, 0, :], a["state_ssm_conv"][0].rearrange("b w c -> (b w) c"), "params_in")
            ld(cs_tok[0:24, 1, :], a["state_gdn_conv"][0].rearrange("b w c -> (b w) c"), "params_in")
            ld(PTAB[0:1, :], a["page_table"].rearrange("b n -> (b n)").rearrange("(o n) -> o n", o=1), "pages_in")
            for i, c0 in enumerate((COL_DT, COL_B, COL_A)):
                ld(w_small[:, i, :, :], win.rearrange("(k p) n -> p k n", p=P)[:, :, c0:c0 + H], "params_in")
            load_chunks(sp, 0, first["wkv"] + NW)
            sp.wait_ge(S("pages_in"), 16)
            load_pages(sp, [n for n in range(NPG) if issuer(n) == "sync"])
            sp.wait_ge(S("kv_out"), NT)
            for kv in range(2):
                for i in range(4):
                    ld(o["moba_kp" if kv == 0 else "moba_vp"][0, 0].rearrange("s h d -> s (h d)")[i * P:(i + 1) * P, :],
                       kvtok[:, i, kv * GW:(kv + 1) * GW], "moba_kv_out")
                ld(o["moba_ks" if kv == 0 else "moba_vs"][0].rearrange("b t h d -> (b t) (h d)"),
                   kvs[0:NS, kv * GW:(kv + 1) * GW], "moba_kv_out")
            load_pages(sp, [n for n in range(NPG, 64) if issuer(n) == "sync"])
            after(sp, "moba_sample")
            sp.dma_start(s_h0, a["state_ssm"][0].rearrange("b (c e) q n -> (e q) b c n", e=2)).then_inc(S("state_in"), 16)
            after(sp, "ssm")
            sp.wait_ge(S("states_out"), 32)
            sp.dma_start(t_s0, a["state_hgrn"][0].rearrange("b (c e) k v -> (e k) b c v", e=2)).then_inc(S("state_in"), 16)
            sp.wait_ge(S("g_inverted"), 1)
            sp.dma_start(t_s0, a["state_gdn"][0].rearrange("b (c e) k v -> (e k) b c v", e=2)).then_inc(S("state_in"), 16)
            load_chunks(sp, first["wkv"] + NW, first["wkv"] + 2 * NW)
            for i in range(2):
                ld(mem_raw[:, i, :], a["mem_prompt"][0, i * P:(i + 1) * P, :], "mem_in")
            load_chunks(sp, first["wkv"] + 2 * NW, first["wxo"] + NW)
            after(sp, "gdn")
            for n in range(16):
                src = a["cache_mem_k"] if n < 8 else a["cache_mem_v"]
                if n == 2:
                    after(sp, "wout")
                if n >= 4:
                    if n < 12:
                        sp.wait_ge(S("satt_turned"), 64 + 4 * (n - 3))
                    else:
                        sp.wait_ge(S("satt_pv"), 1 + n - 11)
                sp.dma_start(cx_slot(n).rearrange("p (i n) -> p i n", n=D),
                             src[0, n % 8].rearrange("(i p) h d -> p i (h d)", p=P)).then_inc(S(f"cx_ring{n % 4}_in"), 16)
            load_chunks(sp, first["wxo"] + NW, len(chunks))

        def fill(view, pattern, base, mult, op, fillv):
            return G.affine_select(out=view, in_=view, compare_op=op, fill=fillv, base=base, pattern=pattern,
                                   channel_multiplier=mult)

        def g_constants(g):
            L = lambda ins: link(ins, "g")
            L(G.memset(ident, 0.0))
            L(G.memset(ones, 1.0))
            L(G.memset(eps, EPS))
            fill(ident, [[-1, P]], 0, 1, ALU.not_equal, 1.0).then_inc(S("consts"), 1)
            L(G.memset(CN[:, 2 * P:CONSTS_END], 0.0))
            L(G.memset(keep, 1.0))
            L(G.memset(blk64[0:64, 0:64], 1.0))
            L(G.memset(blk64[64:128, 64:128], 1.0))
            L(G.memset(lev[:, 0, :], 0.0))
            L(fill(lev[:, 0, :], [[-1, P]], 0, 1, ALU.not_equal, 1.0))
            for j in range(1, 8):
                B = 1 << j
                r = lev[:, j, :].rearrange("p (n i) -> p n i", i=B)[:, :, B // 2:B]
                L(G.memset(r, 1.0))
                L(fill(r, [[-B, P // B], [0, B // 2]], 0, 1, ALU.is_ge, 0.0))
                L(fill(r, [[B, P // B], [0, B // 2]], B // 2 - 1, -1, ALU.is_ge, 0.0))
            L(fill(negmask, [[1, P]], 0, -1, ALU.is_ge, NEG))
            L(fill(negmask_s[0:NS, :], [[1, NS]], 0, -1, ALU.is_ge, NEG))
            v = negmask_s[0:NS, :].rearrange("p (b t) -> p b t", t=TS)
            L(fill(v, [[-TS, NB], [0, TS]], 0, 1, ALU.is_ge, NEG))
            L(G.memset(ind, 1.0))
            L(fill(ind, [[-TS, NB]], 0, 1, ALU.is_ge, 0.0))
            L(fill(ind, [[TS, NB]], TS - 1, -1, ALU.is_ge, 0.0))
            L(G.memset(keep[:, 0:SEQ].rearrange("p (n i) -> p n i", i=P)[:, :, 0:1], 0.0))
            L(G.memset(keep[:, SEQ:T].rearrange("p (n i) -> p n i", i=TS)[:, :, 0:1], 0.0))
            L(G.memset(onehot, 1.0))
            L(fill(onehot, [[-1, H], [0, P]], 0, 1, ALU.is_equal, 0.0))
            ps = pairsel.rearrange("p c (e d) -> p c e d", e=2)
            L(G.memset(pairsel, 1.0))
            L(fill(ps, [[-2, 2], [-1, 2], [0, DH]], 0, 1, ALU.is_equal, 0.0))
            L(G.memset(g8, 1.0))
            L(fill(g8, [[-16, NB]], 0, 1, ALU.is_ge, 0.0))
            L(fill(g8, [[16, NB]], 15, -1, ALU.is_ge, 0.0))
            L(G.memset(ltm, 1.0))
            G.affine_select(out=ltm, in_=ltm, compare_op=ALU.is_gt, fill=0.0, base=0, pattern=[[1, 8], [-1, 8]],
                            channel_multiplier=0).then_inc(S("consts"), 1)
            g.wait_ge(S("consts"), 2)

        ms_grp = XN[:, 2 * (PAST + NS):2 * (PAST + NS) + 96]
        ms_int = XN[:, 2 * (PAST + NS) + 96:2 * (PAST + NS) + 128].bitcast(I32)

        def g_prompt_table(g):
            L = lambda ins: link(ins, "g")
            g.wait_ge(S("normed"), KD)
            L(G.iota(mp_dist.bitcast(I32), pattern=[[1, SEQ]], base=-384, channel_multiplier=-1))
            L(G.tensor_copy(mp_dist, mp_dist.bitcast(I32)))
            fill(mp_dist, [[-1, SEQ]], 384, 1, ALU.is_ge, NEG).then_inc(S("mp_table"), 1)

        def g_moba_tables(g):
            L = lambda ins: link(ins, "g")
            after(g, "win")
            grp, slope, gi = ms_grp[:, 0:32], ms_grp[:, 32:64], ms_grp[:, 64:96]
            L(G.memset(grp, 1.0))
            L(fill(grp, [[-4, 32]], 0, 1, ALU.is_ge, 0.0))
            L(fill(grp, [[4, 32]], 3, -1, ALU.is_ge, 0.0))
            for h in range(H):
                L(G.memset(slope.rearrange("p (b h) -> p b h", h=H)[:, :, h:h + 1], SLOPE[h]))
            L(G.iota(ms_int, pattern=[[-4, 32]], base=0, channel_multiplier=1))
            L(G.tensor_copy(gi, ms_int))
            L(G.tensor_tensor(slope, slope, grp, ALU.mult))
            L(G.tensor_tensor(gi, gi, grp, ALU.mult))
            L(G.iota(ms_bias[:, 0:PAST].bitcast(I32), pattern=[[1, PAST]], base=-PAST, channel_multiplier=0))
            L(G.tensor_copy(ms_bias[:, 0:PAST], ms_bias[:, 0:PAST].bitcast(I32)))
            L(G.iota(ms_bias[:, PAST:PAST + NS].bitcast(I32), pattern=[[0, NB], [1, TS]], base=0, channel_multiplier=0))
            G.tensor_copy(ms_bias[:, PAST:PAST + NS], ms_bias[:, PAST:PAST + NS].bitcast(I32)).then_inc(S("ms_tables"), 1)

        def tt(out, x, y, op):
            return V.tensor_tensor(out, x, y, op)

        def bc(ap, shape):
            return ap.to_broadcast(shape)

        SQ = {"s": 0, "v": 0}
        SUMS = {"pe": 0, "s": 0, "v": 0}

        def norm_tensor(pe, sq, n, all_scalar=False, after_gemm=None):
            if after_gemm:
                pe.wait_ge(S("gemm_out_s"), GEMM_OUT[after_gemm] + 3)
            for k in range(KD):
                e = "s" if all_scalar or k % 2 == 0 else "v"
                SQ[e] += 1
                pe.wait_ge(S("norm_sq_" + e), SQ[e])
                for j in range(2):
                    last = mm(bank(j)[:, 0:n // 2], ones, sq[:, k, j * n // 2:(j + 1) * n // 2], k == 0, k == KD - 1)
            last.then_inc(S("norm_sum"), 1)

        def squares_scalar(s, src, sq, ks=range(0, KD, 2), wait=None):
            for k in ks:
                if wait is not None:
                    s.wait_ge(S("residual"), wait + k + 1)
                A.activation(sq[:, k, :], src[:, k, :], ACT.Square).then_inc(S("norm_sq_s"), 1)

        def squares_vector(v, src, sq):
            for k in range(1, KD, 2):
                tt(sq[:, k, :], src[:, k, :], src[:, k, :], ALU.mult).then_inc(S("norm_sq_v"), 1)

        def root_scalar(s, n):
            SUMS["s"] += 1
            s.wait_ge(S("norm_sum"), SUMS["s"])
            A.activation(rsq[:, 0:n].rearrange("p (j t) -> p j t", j=2), PS[0][:, :, 0:n // 2], ACT.Sqrt,
                         bias=eps, scale=1.0 / D).then_inc(S("norm_root"), 1)

        def scale_vector(v, src, n, gain, dst, add=None, parts=None):
            SUMS["v"] += 1
            v.wait_ge(S("norm_root"), SUMS["v"])
            link(V.reciprocal(rsq[:, 0:n], rsq[:, 0:n]))
            for k in range(KD):
                last = V.scalar_tensor_tensor(dst[:, k, :], src[:, k, :], par(gain + k), rsq[:, 0:n], ALU.mult, ALU.mult)
                if parts is not None:
                    last.then_inc(S("normed"), 1)
                    if k:
                        part_lo(v, parts, k - 1)
                else:
                    link(last)
                    tt(add[:, k, :], add[:, k, :], dst[:, k, :], ALU.add).then_inc(S("residual"), 1)
            if parts is not None:
                part_lo(v, parts, KD - 1)

        IN_BEFORE = {"win": 0, "wkv": KD, "wout": 2 * KD, "wxq": 3 * KD, "wxo": 4 * KD, "wgu": 5 * KD, "wdn": 6 * KD}
        NORMED_BEFORE = {"win": 0, "wkv": KD, "wxq": 2 * KD, "wgu": 3 * KD}
        sc_hi = SC_R[:, KD * T:2 * KD * T].rearrange("p (k t) -> p k t", t=T)
        xn_lo = XN_R[:, :].rearrange("p (k t) -> p k t", t=T)
        tile_of = lambda b: (lambda k: b[:, k, :])
        proj_r = PROJ_R[:, :].rearrange("p (k t) -> p k t", t=T)
        sc_r = SC_R[:, 0:16 * T].rearrange("p (k t) -> p k t", t=T)
        INPUTS = {
            "win": (tile_of(xn), tile_of(sc_hi), tile_of(xn_lo)),
            "wkv": (tile_of(memn), lambda k: SC_R[:, k * MEM:(k + 1) * MEM], lambda k: SC_R[:, (KD + k) * MEM:(KD + k + 1) * MEM]),
            "wout": (tile_of(OM), tile_of(sc_hi), tile_of(OM_R)),
            "wxq": (tile_of(xn), tile_of(OM_R), tile_of(xn_lo)),
            "wxo": (tile_of(OM), tile_of(sc_hi), tile_of(OM_R)),
            "wgu": (tile_of(xn), tile_of(OM_R), tile_of(xn_lo)),
            "wdn": (tile_of(hT), lambda k: proj_r[:, KF + k, :] if k < 8 else sc_r[:, k - 8, :], tile_of(proj_r)),
        }

        def part_hi(s, name, k):
            x, hi, _ = INPUTS[name]
            if name in NORMED_BEFORE:
                s.wait_ge(S("normed"), NORMED_BEFORE[name] + k + 1)
            A.activation(hi(k), x(k), ACT.Copy).then_inc(S("part_hi"), 1)

        def part_lo(v, name, k):
            x, hi, lo = INPUTS[name]
            v.wait_ge(S("part_hi"), IN_BEFORE[name] + k + 1)
            tt(lo(k), x(k), hi(k).bitcast(F32), ALU.subtract).then_inc(S("part_lo"), 1)

        def parts_scalar(s, name):
            for k in range(KD):
                part_hi(s, name, k)

        def parts_vector(v, name):
            for k in range(KD):
                part_lo(v, name, k)

        def operand(name, k, cols):
            _, hi, lo = INPUTS[name]
            return hi(k)[:, cols], lo(k)[:, cols]

        GEMM_NAMES = ("win", "wout", "wxq", "wxo", "wdn")
        GEMM_MM = dict(zip(GEMM_NAMES, (0, NPROJ, NPROJ + KD, NPROJ + 2 * KD, NPROJ + 3 * KD)))
        GEMM_OUT = {n: (0 if n == "win" else (NPROJ + (GEMM_NAMES.index(n) - 1) * KD) // 2) for n in GEMM_NAMES}

        def gemm_tensor(pe, name, ntile, nparts=1):
            n0 = first[name]
            for i in range(ntile):
                k = 0
                for part in range(nparts):
                    wh, wl = weights(pe, n0 + i * nparts + part)
                    if i >= 4 and part == 0:
                        pe.wait_ge(S("gemm_out_s" if i % 2 == 0 else "gemm_out_v"), GEMM_OUT[name] + (i - 4) // 2 + 1)
                    nk = wh.shape[1]
                    for kk in range(nk):
                        if i == 0:
                            pe.wait_ge(S("part_lo"), IN_BEFORE[name] + k + 1)
                        for j in range(2):
                            last = mm3(PS[i % 4][:, j, 0:HT], (wh[:, kk, :], wl[:, kk, :]),
                                       operand(name, k, slice(j * HT, (j + 1) * HT)),
                                       k == 0, part == nparts - 1 and kk == nk - 1)
                        k += 1
                    last.then_inc(S("gemm_mm" if part == nparts - 1 else "gemm_part"), 1)

        def gemm_loop_scalar(s, name, ntile, even, nparts=1):
            for i in range(ntile):
                split_hi(s, first[name] + nparts * (i + 1) + NH - 1)
                s.wait_ge(S("gemm_mm"), GEMM_MM[name] + i + 1)
                if i % 2 == 0:
                    even(i)
                split_hi(s, first[name] + nparts * (i + 1) + NH)

        def gemm_sq_scalar(s, name, sq, nparts=1):
            def even(i):
                A.activation(halves(sq[:, i, :]), pair(i % 4), ACT.Square).then_inc(S("norm_sq_s"), 1)
                A.activation(halves(xn[:, i, :]), pair(i % 4), ACT.Copy).then_inc(S("gemm_out_s"), 1)
            gemm_loop_scalar(s, name, KD, even, nparts)

        def gemm_sq_vector(v, name, sq):
            for i in range(1, KD, 2):
                v.wait_ge(S("gemm_mm"), GEMM_MM[name] + i + 1)
                V.tensor_copy(halves(xn[:, i, :]), pair(i % 4)).then_inc(S("gemm_out_v"), 1)
                v.wait_ge(S("gemm_out_v"), GEMM_OUT[name] + i // 2 + 1)
                tt(sq[:, i, :], xn[:, i, :], xn[:, i, :], ALU.mult).then_inc(S("norm_sq_v"), 1)

        def halves(ap):
            return ap.rearrange("p (j t) -> p j t", j=2)

        def gemm_scalar(s, name, ntile, dst):
            def even(i):
                A.activation(halves(dst(i)), pair(i % 4), ACT.Copy).then_inc(S("gemm_out_s"), 1)
            gemm_loop_scalar(s, name, ntile, even)

        def gemm_vector(v, name, ntile, dst):
            for i in range(1, ntile, 2):
                v.wait_ge(S("gemm_mm"), GEMM_MM[name] + i + 1)
                V.tensor_copy(halves(dst(i)), pair(i % 4)).then_inc(S("gemm_out_v"), 1)

        def inputs_tensor(pe):
            pe.wait_ge(S("consts"), 1)
            pe.wait_ge(S("x_in"), 80)
            for job in range(8):
                i, hf = divmod(job, 2)
                for k in range(4):
                    last = tr(bank(job)[:, k * P:(k + 1) * P], x_tok[:, i, (4 * hf + k) * P:(4 * hf + k + 1) * P], P)
                last.then_inc(S("turned"), 1)
            pe.wait_ge(S("turned_out_v"), 1)
            for k in range(8):
                last = tr(bank(0)[:, k * NS:(k + 1) * NS], xs_tok[0:NS, k * P:(k + 1) * P], NS)
            last.then_inc(S("turned"), 1)

        def params_tensor(pe):
            pe.wait_ge(S("params_in"), 16 * 34)
            tr(bank(2)[:, 0:NROWS], rows_in[0:NROWS, :], NROWS).then_inc(S("turned"), 1)
            for i in range(12):
                last = tr(bank(4)[:, i * 24:(i + 1) * 24], cs_tok[0:24, i // 6, (i % 6) * P:(i % 6 + 1) * P], 24)
            last.then_inc(S("turned"), 1)

        def inputs_evac(e, eng, copy, name, par_):
            for job in range(par_, 9, 2):
                eng.wait_ge(S("turned"), job + 1)
                if job < 8:
                    i, hf = divmod(job, 2)
                    i = copy(XT[:, 4 * hf:4 * hf + 4, i * P:(i + 1) * P], bank(job).rearrange("p (k t) -> p k t", t=P))
                else:
                    i = copy(XT[:, :, SEQ:T], bank(0)[:, 0:8 * NS].rearrange("p (k t) -> p k t", t=NS))
                i.then_inc(S(name), 1)

        def params_vector(v):
            v.wait_ge(S("turned"), 10)
            V.tensor_copy(prm, bank(2)[:, 0:NROWS]).then_inc(S("turned_out_v"), 1)
            v.wait_ge(S("turned_out_v"), 6)

        def params_scalar(s):
            s.wait_ge(S("turned"), 11)
            scopy(ups[:, :, :, 0:3], bank(4)[:, 0:288].rearrange("p (c b w) -> p c b w", b=NB, w=3)).then_inc(S("turned_out_s"), 1)

        def small_hi(s):
            s.wait_ge(S("params_in"), 16 * 34)
            A.activation(w_small_hi[:, :, :, :], w_small[:, :, :, :], ACT.Copy).then_inc(S("weights_and_rates"), 1)

        def small_lo(v):
            v.wait_ge(S("weights_and_rates"), 1)
            tt(w_small_lo[:, :, :, :], w_small[:, :, :, :], w_small_hi[:, :, :, :].bitcast(F32), ALU.subtract)

        def vcopy(o_, i_):
            return V.tensor_copy(o_, i_)

        def scopy(o_, i_):
            return A.activation(o_, i_, ACT.Copy)

        CONV_OF = {**{C_XBC + k: k for k in range(6)}, **{C_GQKV + k: 6 + k for k in range(6)}}

        def win_dst(i):
            return rawc[:, CONV_OF[i] % 4, :] if i in CONV_OF else proj[:, i, :]

        def win_tensor(pe):
            for i in range(3):
                for k in range(KD):
                    if i == 0:
                        pe.wait_ge(S("part_lo"), k + 1)
                    for j in range(2):
                        last = mm3(PS[i][0:H, j, 0:HT], (w_small_hi[:, i, k, :], w_small_lo[:, i, k, :]),
                                   operand("win", k, slice(j * HT, (j + 1) * HT)), k == 0, k == KD - 1)
                last.then_inc(S("raw_mm"), 1)
            pe.wait_ge(S("raw_out_v"), 2)
            pe.wait_ge(S("raw_out_s"), 1)
            pe.wait_ge(S("consts"), 2)
            gemm_tensor(pe, "win", NPROJ)
            rows_turn_tensor(pe)

        def win_vector(v):
            rows_vector(v)
            for i in range(1, NPROJ, 2):
                v.wait_ge(S("gemm_mm"), i + 1)
                V.tensor_copy(halves(win_dst(i)), pair(i % 4)).then_inc(S("gemm_out_v"), 1)
                if i in CONV_OF:
                    v.wait_ge(S("gemm_out_s"), i // 2 + 1)
                    conv_vector(v, CONV_OF[i] - 1)
                    v.wait_ge(S("gemm_out_v"), i // 2 + 1)
                    conv_vector(v, CONV_OF[i])
            rows_turn_vector(v)

        def win_scalar(s):
            rows_scalar(s)

            def even(i):
                if CONV_OF.get(i, 0) >= 4:
                    s.wait_ge(S("conv"), CONV_OF[i] - 3)
                A.activation(halves(win_dst(i)), pair(i % 4), ACT.Copy).then_inc(S("gemm_out_s"), 1)
                if i - 2 in CONV_OF:
                    silu_scalar(s, CONV_OF[i - 2])
                    silu_scalar(s, CONV_OF[i - 2] + 1)

            gemm_loop_scalar(s, "win", NPROJ, even)

        def kv_tensor(pe):
            for i, (t0, w, _) in enumerate(TILES):
                for k in range(4):
                    last = tr(bank(i)[0:w, k * P:(k + 1) * P], proj[:, C_MK + k, t0:t0 + w], P)
                last.then_inc(S("kv_turned"), 1)

        def kv_vector(v):
            for i, (t0, w, _) in enumerate(TILES):
                v.wait_ge(S("kv_turned"), i + 1)
                dst = kvtok[:, i, :] if i < 4 else kvs[0:NS, :]
                V.tensor_copy(dst, bank(i)[0:w, :]).then_inc(S("kv_out"), 1)

        def mp_scores(pe, j):
            i, h = divmod(j, H)
            if j >= 4:
                pe.wait_ge(S("mp_biased"), j - 3)
            r = slice((h % 2) * 64, (h % 2) * 64 + 64)
            nk = (i + 1) * P
            mm(bank(j % 4)[:, 0:nk], proj[r, C_MQ + h // 2, i * P:(i + 1) * P], proj[r, C_MK + h // 2, 0:nk], True, True)\
                .then_inc(S("att_scores"), 1)

        def mp_turn(pe, j):
            i = j // H
            pe.wait_ge(S("att_probs"), j + 1)
            if j >= 2:
                pe.wait_ge(S("att_pt"), j - 1)
            for k in range(i + 1):
                last = tr(bank(4 + j % 2)[:, k * P:(k + 1) * P], mp_s[:, j % 4, k * P:(k + 1) * P], P)
            last.then_inc(S("att_turned"), 1)

        def mp_pv(pe, j):
            i, h = divmod(j, H)
            pe.wait_ge(S("att_pt"), j + 1)
            if h == 0 and i >= 2:
                pe.wait_ge(S("att_out"), i - 1)
            for k in range(i + 1):
                last = mm(bank(6 + i % 2)[(h % 2) * 64:(h % 2) * 64 + 64, (h // 2) * P:(h // 2 + 1) * P],
                          kvtok[:, k, GW + h * DH:GW + (h + 1) * DH], mp_pt[:, j % 2, k * P:(k + 1) * P], k == 0, k == i)
            last.then_inc(S("att_pv"), 1)

        def moba_prompt_tensor(pe):
            kv_tensor(pe)
            pe.wait_ge(S("kv_out"), NT)
            mp_scores(pe, 0)
            mp_scores(pe, 1)
            for j in range(16):
                if j + 2 < 16:
                    mp_scores(pe, j + 2)
                mp_turn(pe, j)
                if j:
                    mp_pv(pe, j - 1)
            mp_pv(pe, 15)

        def moba_prompt_vector(v):
            kv_vector(v)
            v.wait_ge(S("mp_table"), 1)

            def first_(j):
                i, h = divmod(j, H)
                nk = (i + 1) * P
                v.wait_ge(S("att_scores"), j + 1)
                if j >= 4:
                    v.wait_ge(S("att_turned"), j - 3)
                V.scalar_tensor_tensor(mp_s[:, j % 4, 0:nk], bank(j % 4)[:, 0:nk], SCALE / SLOPE[h], mp_dist[:, SEQ - nk:SEQ],
                                       ALU.mult, ALU.add).then_inc(S("mp_biased"), 1)
                v.wait_ge(S("mp_biased"), j + 1)
                link(V.tensor_reduce(mp_stat[:, 0, j:j + 1], mp_s[:, j % 4, 0:nk], AXX, ALU.max, negate=True))
                V.tensor_scalar(mp_stat[:, 0, j:j + 1], mp_stat[:, 0, j:j + 1], SLOPE[h], None, ALU.mult).then_inc(S("att_max"), 1)

            def second(j):
                nk = (j // H + 1) * P
                v.wait_ge(S("att_exp"), j + 1)
                link(V.reciprocal(mp_stat[:, 2, j:j + 1], mp_stat[:, 1, j:j + 1]))
                V.tensor_scalar(mp_s[:, j % 4, 0:nk], mp_s[:, j % 4, 0:nk], mp_stat[:, 2, j:j + 1], None, ALU.mult)\
                    .then_inc(S("att_probs"), 1)

            def out_(i):
                v.wait_ge(S("att_pv"), 4 * i + 4)
                V.tensor_copy(OM[:, 0:2, i * P:(i + 1) * P], bank(6 + i % 2)[:, 0:2 * P].rearrange("p (c t) -> p c t", t=P))\
                    .then_inc(S("att_out"), 1)

            v.wait_ge(S("conv_states_out"), 16 * 4)
            first_(0)
            for j in range(16):
                if j + 1 < 16:
                    first_(j + 1)
                second(j)
                if j >= 4 and j % 4 == 1:
                    out_(j // 4 - 1)
                if j == 7:
                    moba_rows_vector(v)
            out_(3)

        def moba_prompt_scalar(s):
            s.wait_ge(S("conv_states_out"), 16 * 4)

            def ex(j):
                nk = (j // H + 1) * P
                s.wait_ge(S("att_max"), j + 1)
                A.activation(mp_s[:, j % 4, 0:nk], mp_s[:, j % 4, 0:nk], ACT.Exp, bias=mp_stat[:, 0, j:j + 1], scale=SLOPE[j % H],
                             accum_out=mp_stat[:, 1, j:j + 1]).then_inc(S("att_exp"), 1)

            ex(0)
            for j in range(16):
                if j + 1 < 16:
                    ex(j + 1)
                nk = (j // H + 1) * P
                s.wait_ge(S("att_turned"), j + 1)
                if j >= 2:
                    s.wait_ge(S("att_pv"), j - 1)
                A.activation(mp_pt[:, j % 2, 0:nk], bank(4 + j % 2)[:, 0:nk], ACT.Copy).then_inc(S("att_pt"), 1)

        def moba_sample_tensor(pe):
            def page_in(n):
                pe.wait_ge(*pages_sem(n))

            def turn(j):
                n, c_ = divmod(j, 2)
                if c_ == 0:
                    page_in(n)
                if j >= 4:
                    pe.wait_ge(S("keys_turned_s" if c_ == 0 else "keys_turned_v"), (j - 4) // 2 + 1)
                for i in range(4):
                    last = tr(bank(j % 4)[:, i * P:(i + 1) * P], pages[:, n % NPG, i, c_ * P:(c_ + 1) * P], P)
                last.then_inc(S("satt_turned"), 1)

            def score(j):
                n, c_ = divmod(j, 2)
                b, qt = divmod(n, 4)
                pe.wait_ge(S("keys_turned_s" if c_ == 0 else "keys_turned_v"), j // 2 + 1)
                r = slice(32 * (b // 2), 32 * (b // 2) + 32)
                mm(bank(4 + qt)[r, :], ms_qp[:, c_, b, :], ms_kt[j % 4], b % 2 == 0 and c_ == 0, b % 2 == 1 and c_ == 1)\
                    .then_inc(S("satt_scored"), 1)

            pe.wait_ge(S("ms_q"), 2)
            turn(0)
            turn(1)
            for j in range(2, 64):
                turn(j)
                score(j - 2)
            score(62)
            score(63)
            for c_ in range(2):
                last = mm(bank(0)[:, 0:NS], ms_q[:, c_, :], proj[:, C_MK + c_, SEQ:T], c_ == 0, c_ == 1)
            last.then_inc(S("satt_rows"), 1)
            spread_tensor(pe)
            pe.wait_ge(S("rows_spread_out"), 12)
            pe.wait_ge(S("satt_exp"), 1)
            for i in range(NPAGE):
                last = tr(bank(i // 4)[:, (i % 4) * P:(i % 4 + 1) * P], ms_s[:, i * P:(i + 1) * P], P)
            last.then_inc(S("satt_pt"), 1)
            tr(bank(4)[0:NS, 0:P], ms_s[:, PAST:PAST + NS], P).then_inc(S("satt_pt"), 1)
            pe.wait_ge(S("satt_pt_out"), 2)
            for e in range(2):
                mm(bank(5 + e)[:, 0:GW], ms_pown[0:NS, :], kvs[0:NS, GW:2 * GW], True, False)
            for n in range(32, 64):
                b, qt = divmod(n - 32, 4)
                r = slice(32 * (b // 2), 32 * (b // 2) + 32)
                if n == 36:
                    unit_tensor(pe, (0, 1))
                elif n == 38:
                    unit_tensor(pe, (2, 3))
                page_in(n)
                for i in range(4):
                    last = mm(bank(5 + b % 2)[r, 0:GW], st_all[:, 4 * qt + i, r], pages[:, n % NPG, i, :], False, qt == 3 and i == 3)
                last.then_inc(S("ms_values_used"), 1)
            pe.wait_ge(S("satt_o"), 1)
            pick = ident.rearrange("p (g e h t) -> p g e h t", e=2, h=H, t=TS)
            for e in range(2):
                for c_ in range(2):
                    for h2 in range(2):
                        last = mm(bank(7)[h2 * 64:h2 * 64 + 64, c_ * NS:(c_ + 1) * NS].rearrange("p (g e t) -> p g e t", e=2, t=TS)[:, :, e, :],
                                  ms_o[:, e, (2 * c_ + h2) * DH:(2 * c_ + h2 + 1) * DH], pick[:, :, e, 2 * c_ + h2, :], True, True)
            last.then_inc(S("satt_pv"), 1)

        def moba_rows_vector(v):
            v.wait_ge(S("ms_tables"), 1)
            sg = ms_grp
            link(V.reduce_sum(mr, sg[:, 32:64], AXX))
            link(V.reduce_sum(tr_, sg[:, 64:96], AXX))
            link(V.tensor_scalar(ms_bias[:, 0:PAST + NS], ms_bias[:, 0:PAST + NS], tr_, None, ALU.subtract))
            own = ms_bias[:, PAST:PAST + NS]
            ok = ms_rowtmp
            link(V.tensor_scalar(ok, own, 0.0, None, ALU.is_le))
            link(tt(ok.rearrange("p (b t) -> p b t", t=TS), ok.rearrange("p (b t) -> p b t", t=TS),
                    bc(g8.rearrange("p (b t) -> p b t", t=1), (P, NB, TS)), ALU.mult))
            link(V.tensor_scalar(ok, ok, -1.0, -NEG, ALU.add, ALU.mult))
            link(V.tensor_scalar(ms_bias[:, 0:PAST + NS], ms_bias[:, 0:PAST + NS], mr, None, ALU.mult))
            link(tt(own, own, ok, ALU.add))
            link(V.memset(ms_q, 0.0))
            for h2 in range(2):
                for c_ in range(2):
                    r = slice(h2 * 64, h2 * 64 + 64)
                    dst = ms_q[r, c_, :].rearrange("p (b g t) -> p b g t", g=4, t=TS)[:, :, 2 * c_ + h2, :]
                    last = V.tensor_copy(dst, proj[r, C_MQ + c_, SEQ:T].rearrange("p (b t) -> p b t", t=TS))
            last.then_inc(S("ms_q"), 1)

        def moba_sample_vector(v):
            v.wait_ge(S("moba_kv_out"), 16 * 10)
            link(V.memset(ms_qp, 0.0))
            for e in range(2):
                last = V.tensor_copy(ms_qp.rearrange("p c (g e) r -> p c g e r", e=2)[:, :, :, e, 16 * e:16 * e + 16],
                                     ms_q.rearrange("p c (g e r) -> p c g e r", e=2, r=16)[:, :, :, e, :])
            last.then_inc(S("ms_q"), 1)
            for j in range(1, 64, 2):
                v.wait_ge(S("satt_turned"), j + 1)
                if j >= 4:
                    v.wait_ge(S("satt_scored"), j - 3)
                V.tensor_copy(ms_kt[j % 4], bank(j % 4)).then_inc(S("keys_turned_v"), 1)
            v.wait_ge(S("satt_rows"), 1)
            for i in range(4):
                link(V.tensor_reduce(ms_gate[:, 2 * i:2 * i + 2], bank(4 + i).rearrange("p (n k) -> p n k", k=MOBA_BLOCK), AXX, ALU.add))
            gm = bc(ms_gate.rearrange("p (o m) -> p o m", o=1), (P, 8, 8))
            gn = bc(ms_gate.rearrange("p (n o) -> p n o", o=1), (P, 8, 8))
            link(tt(ms_gt, gm, gn, ALU.is_gt))
            link(tt(ms_eq, gm, gn, ALU.is_equal))
            link(tt(ms_eq, ms_eq, ltm, ALU.mult))
            link(tt(ms_gt, ms_gt, ms_eq, ALU.add))
            link(V.tensor_reduce(ms_rank, ms_gt, AXX, ALU.add))
            link(V.tensor_scalar(ms_sel, ms_rank, 2.5, NEG, ALU.is_gt, ALU.mult))
            for i in range(4):
                sl = slice(i * 512, (i + 1) * 512)
                link(V.scalar_tensor_tensor(ms_s[:, sl], bank(4 + i), SCALE, ms_bias[:, sl], ALU.mult, ALU.add))
            s3 = ms_s[:, 0:PAST].rearrange("p (n k) -> p n k", k=MOBA_BLOCK)
            link(tt(s3, s3, bc(ms_sel.rearrange("p (n o) -> p n o", o=1), (P, 8, MOBA_BLOCK)), ALU.add))
            link(V.scalar_tensor_tensor(ms_s[:, PAST:PAST + NS], bank(0)[:, 0:NS], SCALE, ms_bias[:, PAST:PAST + NS], ALU.mult, ALU.add))
            V.tensor_reduce(ms_stat[:, 0:1], ms_s[:, :], AXX, ALU.max, negate=True).then_inc(S("satt_max"), 1)
            v.wait_ge(S("satt_exp"), 1)
            link(V.reciprocal(ms_stat[:, 2:3], ms_stat[:, 1:2]))
            v.wait_ge(S("satt_pt"), 1)
            for i in range(2):
                link(V.tensor_copy(st_all[:, 4 * i:4 * i + 4, :], bank(i).rearrange("p (n k) -> p n k", k=P)))
            v.wait_ge(S("satt_pt"), 2)
            V.tensor_copy(ms_pown[0:NS, :], bank(4)[0:NS, 0:P]).then_inc(S("satt_pt_out"), 1)
            unit_squares_vector(v)
            unit_vector(v)
            v.wait_ge(S("ms_values_used"), 32)
            link(V.tensor_scalar(ms_o[:, 0, :], bank(5)[:, 0:GW], ms_stat[:, 2:3], None, ALU.mult))
            V.tensor_scalar(ms_o[:, 1, :], bank(6)[:, 0:GW], ms_stat[:, 2:3], None, ALU.mult).then_inc(S("satt_o"), 1)
            v.wait_ge(S("satt_pv"), 1)
            V.tensor_copy(OM[:, 0:2, SEQ:T], bank(7)[:, 0:2 * NS].rearrange("p (c t) -> p c t", t=NS))

        def moba_sample_scalar(s):
            s.wait_ge(S("moba_kv_out"), 16 * 10)
            s.wait_ge(S("pages_in"), 16)
            for j in range(0, 64, 2):
                s.wait_ge(S("satt_turned"), j + 1)
                if j >= 4:
                    s.wait_ge(S("satt_scored"), j - 3)
                scopy(ms_kt[j % 4], bank(j % 4)).then_inc(S("keys_turned_s"), 1)
                if issuer(j // 2 + NPG) == "scalar":
                    load_pages(s, [j // 2 + NPG])
            spread_scalar(s)
            s.wait_ge(S("satt_max"), 1)
            A.activation(ms_s[:, :], ms_s[:, :], ACT.Exp, bias=ms_stat[:, 0:1], accum_out=ms_stat[:, 1:2]).then_inc(S("satt_exp"), 1)
            s.wait_ge(S("satt_pt"), 1)
            link(scopy(st_all[:, 8:12, :], bank(2).rearrange("p (n k) -> p n k", k=P)), "s")
            scopy(st_all[:, 12:16, :], bank(3).rearrange("p (n k) -> p n k", k=P)).then_inc(S("satt_pt_out"), 1)
            unit_scalar(s)
            load_pages(s, [n for n in range(32 + NPG, 64) if issuer(n) == "scalar"])

        def rows_vector(v):
            v.wait_ge(S("consts"), 2)
            e, u, d = rows_t[:, 0:2, :], rows_t[:, 2:4, :], rows_d
            for i, (job, col) in enumerate(((0, 1), (2, 3))):
                v.wait_ge(S("raw_mm"), job + 1)
                V.tensor_scalar(halves(raw[:, i, :]), PS[job][0:H, :, 0:HT], head4[0:H, col:col + 1], None, ALU.add)\
                    .then_inc(S("raw_out_v"), 1)
            v.wait_ge(S("raw_out_v"), 2)
            V.scalar_tensor_tensor(e, raw, -1.0, raw, ALU.mult, ALU.max).then_inc(S("rows_abs"), 1)
            v.wait_ge(S("weights_and_rates"), 2)
            for i in (4, 6):
                link(V.tensor_scalar(head4[0:H, i:i + 1], head4[0:H, i:i + 1], -1.0, None, ALU.mult))
            v.wait_ge(S("rows_exp"), 1)
            link(V.tensor_scalar(u, e, 1.0, None, ALU.add))
            V.tensor_scalar(d, u, -1.0, None, ALU.add).then_inc(S("rows_u"), 1)
            link(V.tensor_scalar(rows[:, 2, :], rows[:, 2, :], 1.0, None, ALU.add))
            link(V.reciprocal(rows[:, 2, :], rows[:, 2, :]))
            v.wait_ge(S("rows_ln"), 1)
            link(tt(u, u, e, ALU.mult))
            link(V.scalar_tensor_tensor(e, d, 0.0, e, ALU.is_equal, ALU.mult))
            link(V.tensor_scalar(d, d, 1e-30, None, ALU.max))
            link(V.reciprocal(d, d))
            link(tt(u, u, d, ALU.mult))
            link(tt(u, u, e, ALU.add))
            link(V.scalar_tensor_tensor(u, raw, 0.0, u, ALU.max, ALU.add))
            link(V.tensor_copy(rows[:, 0, :], u[:, 0, :]))
            link(V.tensor_scalar(raw[:, 0, :], u[:, 0, :], head4[0:H, 4:5], None, ALU.mult))
            link(V.tensor_scalar(raw[:, 1, :], u[:, 1, :], head4[0:H, 6:7], None, ALU.mult))
            V.tensor_tensor_scan(rows[:, 1, :], keep[0:H, :], raw[:, 0, :], 0.0, ALU.mult, ALU.add)
            V.tensor_tensor_scan(rows[:, 3, :], keep[0:H, :], raw[:, 1, :], 0.0, ALU.mult, ALU.add).then_inc(S("rows_made"), 1)

        def rows_scalar(s):
            s.wait_ge(S("raw_mm"), 2)
            A.activation(halves(rows[:, 2, :]), PS[1][0:H, :, 0:HT], ACT.Exp, scale=-1.0).then_inc(S("raw_out_s"), 1)
            A.activation(head4[0:H, 4:5], head4[0:H, 0:1], ACT.Exp)
            A.activation(head4[0:H, 6:7], head4[0:H, 2:3], ACT.Exp).then_inc(S("weights_and_rates"), 1)
            s.wait_ge(S("rows_abs"), 1)
            A.activation(rows_t[:, 0:2, :], rows_t[:, 0:2, :], ACT.Exp, scale=-1.0).then_inc(S("rows_exp"), 1)
            s.wait_ge(S("rows_u"), 1)
            A.activation(rows_t[:, 2:4, :], rows_t[:, 2:4, :], ACT.Ln).then_inc(S("rows_ln"), 1)

        def rows_turn_vector(v):
            v.wait_ge(S("rows_turned"), 1)
            link(V.tensor_copy(cumtok[:, 0:4, :], bank(6)[:, 0:32].rearrange("p (i h) -> p i h", h=8)))
            link(V.tensor_copy(cumtok[0:NS, 4, :], bank(6)[0:NS, 32:40]))
            v.wait_ge(S("conv_turned"), 1)
            for i in range(3):
                last = V.tensor_copy(cw_out[:, i * 512:(i + 1) * 512], bank(i)[0:27, :])
            last.then_inc(S("conv_states_made"), 1)

        def rows_turn_tensor(pe):
            pe.wait_ge(S("conv"), 12)
            pe.wait_ge(S("rows_made"), 1)
            pe.wait_ge(S("gemm_out_s"), NPROJ // 2)
            pe.wait_ge(S("gemm_out_v"), NPROJ // 2)
            for i, (t0, w, _) in enumerate(TILES):
                for m_, kind in enumerate((1, 3)):
                    last = tr(bank(6)[0:w, i * 8 + 4 * m_:i * 8 + 4 * m_ + 4], rows[:, kind, t0:t0 + w], H)
            last.then_inc(S("rows_turned"), 1)
            for c_ in range(12):
                last = tr(bank(c_ // 4)[0:27, (c_ % 4) * P:(c_ % 4 + 1) * P], cw_in[:, c_, :], P)
            last.then_inc(S("conv_turned"), 1)

        def spread_scalar(s):
            for n in range(12):
                s.wait_ge(S("rows_spread"), n + 1)
                A.activation(pb[:, n // 4, n // 2 % 2, (n % 2) * HT:(n % 2 + 1) * HT], bank(1 + n % 3)[:, 0:HT], ACT.Copy)\
                    .then_inc(S("rows_spread_out"), 1)

        def spread_tensor(pe):
            for n in range(12):
                kind, hp, j = (0, 2, 3)[n // 4], n // 2 % 2, n % 2
                if n >= 3:
                    pe.wait_ge(S("rows_spread_out"), n - 2)
                mm(bank(1 + n % 3)[:, 0:HT], pairsel[0:H, hp, :], rows[:, kind, j * HT:(j + 1) * HT], True, True)\
                    .then_inc(S("rows_spread"), 1)

        def unit_tensor(pe, ks):
            for k in ks:
                pe.wait_ge(S("g_sq"), 1)
                if k >= 2:
                    pe.wait_ge(S("g_root"), k - 1)
                for j in range(2):
                    last = mm(PS[k % 2][:, j, 0:HT], blk64, g_sq[:, k, j * HT:(j + 1) * HT], True, True)
                last.then_inc(S("g_sum"), 1)

        def unit_scalar(s):
            for k in range(4):
                s.wait_ge(S("g_sum"), k + 1)
                A.activation(halves(g_sq[:, k, :]), pair(k % 2), ACT.Sqrt, bias=eps).then_inc(S("g_root"), 1)

        def unit_squares_vector(v):
            gqk = proj[:, C_GQKV:C_GQKV + 4, :]
            tt(g_sq, gqk, gqk, ALU.mult).then_inc(S("g_sq"), 1)

        def unit_vector(v):
            v.wait_ge(S("g_root"), 4)
            v.wait_ge(S("rows_spread_out"), 12)
            link(V.reciprocal(g_sq, g_sq))
            link(V.scalar_tensor_tensor(gq, gq, SCALE, g_sq[:, 0:2, :], ALU.mult, ALU.mult))
            link(tt(gk, gk, g_sq[:, 2:4, :], ALU.mult))
            tt(g_kb, gk, pb[:, 1, :, :], ALU.mult)
            tt(gv, gv, pb[:, 1, :, :], ALU.mult)

        def conv_vector(v, c_):
            m_, k = divmod(c_, 6)
            wrow = R_SCW if m_ == 0 else R_GCW
            src, dst = rawc[:, c_ % 4, :], proj[:, (C_XBC if m_ == 0 else C_GQKV) + k, :]
            win_ = ups[:, c_, :, :]
            link(V.tensor_copy(win_[:, :, 3:7], src[:, SEQ:T].rearrange("p (b t) -> p b t", t=TS)))
            V.tensor_copy(cw_in[:, c_, 0:3], src[:, SEQ - 3:SEQ])
            V.tensor_copy(cw_in[:, c_, 3:27].rearrange("p (b w) -> p b w", w=3), win_[:, :, 4:7])
            ds_ = dst[:, SEQ:T].rearrange("p (b t) -> p b t", t=TS)
            wt = [par(wrow + 6 * j + k) for j in range(4)]
            b_ = par(R_SCB + k) if m_ == 0 else 0.0
            V.tensor_scalar(dst[:, 0:SEQ], src[:, 0:SEQ], wt[3], b_, ALU.mult, ALU.add)
            link(V.tensor_scalar(ds_, win_[:, :, 3:7], wt[3], b_, ALU.mult, ALU.add))
            for d in range(1, 4):
                V.scalar_tensor_tensor(dst[:, d:SEQ], src[:, 0:SEQ - d], wt[3 - d], dst[:, d:SEQ], ALU.mult, ALU.add)
                last = V.scalar_tensor_tensor(ds_, win_[:, :, 3 - d:7 - d], wt[3 - d], ds_, ALU.mult, ALU.add)
                if d < 3:
                    link(last)
            last.then_inc(S("conv"), 1)

        def silu_scalar(s, c_):
            t_ = (C_XBC if c_ < 6 else C_GQKV - 6) + c_
            s.wait_ge(S("conv"), c_ + 1)
            A.activation(proj[:, t_, :], proj[:, t_, :], ACT.Silu)

        def dec_tensor(pe, b, kind, t0, w, np_):
            for h in range(H):
                last = mm(bank(b)[0:np_, h * w:(h + 1) * w], onehot[0:H, h, 0:np_], rows[:, kind, t0:t0 + w], True, True)
            return last

        def dec_vector(dst, b, col, i, w):
            c3 = cumtok[0:w, i, col:col + 4].rearrange("p (h o) -> p h o", o=1)
            msk = (negmask if w == P else negmask_s)[0:w, 0:w].rearrange("p (o l) -> p o l", o=1)
            link(tt(dst, bank(b)[0:w, 0:H * w].rearrange("p (h l) -> p h l", l=w), bc(c3, (w, H, w)), ALU.subtract))
            return tt(dst, dst, bc(msk, (w, H, w)), ALU.add)

        def hl(buf, w):
            flat = buf.rearrange("p a b -> p (a b)") if len(buf.shape) == 3 else buf
            return flat[0:w, 0:H * w].rearrange("p (h l) -> p h l", l=w)

        def ssm_banks(i):
            return (0, 1, 2) if i % 2 == 0 else (5, 6, 7)

        def ssm_tensor(pe):
            def pre(i):
                t0, w, _ = TILES[i]
                sl = slice(t0, t0 + w)
                if i >= 2:
                    pe.wait_ge(S("ssm_ready"), i - 1)
                bg, bd, bt = ssm_banks(i)
                for g in range(2):
                    mm(bank(bg)[0:w, g * w:(g + 1) * w], xc[:, 2 + g, sl], xc[:, 4 + g, sl], True, True)
                dec_tensor(pe, bd, 1, t0, w, P)
                for k in range(4):
                    src = xdt[:, k, sl] if k < 2 else xc[:, k, sl]
                    last = tr(bank(bt)[0:w, k * P:(k + 1) * P], src, P)
                last.then_inc(S("ssm_pre"), 1)

            pe.wait_ge(S("ssm_xdt"), 1)
            pre(0)
            pre(1)
            for i, (t0, w, _) in enumerate(TILES):
                q2 = i % 2
                pe.wait_ge(S("ssm_ready"), i + 1)
                if i:
                    pe.wait_ge(S("ssm_tile_out"), i)
                if w == NS:
                    pe.wait_ge(S("state_in"), 16)
                    for n in range(16):
                        last = tr(bank(4 + n // 4)[:, (n % 4) * P:(n % 4 + 1) * P], s_h0[:, n // 2, n % 2, :], P)
                    last.then_inc(S("ssm_h0_turned"), 1)
                    pe.wait_ge(S("ssm_h0_out"), 1)
                for h in range(H):
                    r = slice((h % 2) * 64, (h % 2) * 64 + 64)
                    o_ = bank(3)[r, (h // 2) * w:(h // 2 + 1) * w]
                    last = mm(o_, s_tok[q2][0:w, h * 64:(h + 1) * 64], hl(s_m[q2], w)[:, h, :], True, w == P and i == 0)
                    if w == NS:
                        for b in range(NB):
                            last = mm(o_[:, b * TS:(b + 1) * TS], s_h0t[:, b, h * 64:(h + 1) * 64],
                                      sc_view(i, w)[:, h, b * TS:(b + 1) * TS], False, True)
                    elif i:
                        last = mm(o_, s_ht[:, h * 64:(h + 1) * 64], sc_view(i, w)[:, h, :], False, True)
                last.then_inc(S("ssm_y"), 1)
                if w == P:
                    for g in range(2):
                        last = mm(bank(4)[:, g * P:(g + 1) * P], s_tok[q2][:, 256 + g * P:256 + (g + 1) * P],
                                  s_xd[q2][:, g * P:(g + 1) * P], True, True)
                    last.then_inc(S("ssm_state"), 1)
                    if i + 2 < NT:
                        pre(i + 2)
                else:
                    for hp in range(2):
                        last = mm(bank(2)[:, hp * 8:hp * 8 + 8], pairsel[0:H, hp, :],
                                  rows[:, 1, SEQ:T].rearrange("p (b t) -> p b t", t=TS)[:, :, TS - 1], True, True)
                    last.then_inc(S("ssm_dec"), 1)
                    for g in range(2):
                        last = tr(bank(0)[:, g * P:(g + 1) * P], s_ht[:, g * P:(g + 1) * P], P)
                    last.then_inc(S("ssm_final"), 1)
                    pe.wait_ge(S("ssm_bm"), 1)
                    for g in range(2):
                        for q in range(2):
                            last = mm(bank(4 + 2 * g + q), s_xd[q2][0:NS, g * P:(g + 1) * P],
                                      s_bm[0:NS, 4 * q:4 * q + 4, g, :], True, True)
                    last.then_inc(S("ssm_state"), 1)
            pe.wait_ge(S("tail_sq"), 1)
            for k in range(2):
                for j in range(2):
                    last = mm(PS[0][:, j, 0:HT], ones, xdt[:, k, j * HT:(j + 1) * HT], k == 0, k == 1)
            last.then_inc(S("tail_sum"), 1)

        def sc_view(i, w):
            return s_c[i % 2].rearrange("p a b -> p (a b)")[:, 0:H * w].rearrange("p (h l) -> p h l", l=w)

        def er_view(i, w):
            return s_er[i % 2].rearrange("p a b -> p (a b)")[:, 0:H * w].rearrange("p (h l) -> p h l", l=w)

        s_bm = xc[:, 2:6, :].rearrange("p a b -> p (a b)")[:, 0:NB * 256].rearrange("p (b g n) -> p b g n", g=2, n=P)
        s_fin = s_er[1].rearrange("p a b -> p (a b)")[:, 0:2 * P].rearrange("p (c n) -> p c n", n=P)

        def ssm_vector(v):
            def prep(i):
                t0, w, _ = TILES[i]
                sl = slice(t0, t0 + w)
                M, er, tok, dl, q2 = hl(s_m[i % 2], w), er_view(i, w), s_tok[i % 2], s_dl[i % 2], i % 2
                bg, bd, bt = ssm_banks(i)
                v.wait_ge(S("ssm_pre"), i + 1)
                dec_vector(M, bd, 0, i, w).then_inc(S("ssm_m"), 1)
                link(V.tensor_copy(tok[0:w, :], bank(bt)[0:w, :]))
                v.wait_ge(S("ssm_exp"), i + 1)
                if w == P:
                    link(V.tensor_copy(dl[:, :], M[:, :, P - 1]))
                else:
                    link(V.tensor_reduce(dl[0:w, :], M.rearrange("p h (b t) -> p h b t", t=TS)[:, :, :, TS - 1], AXX, ALU.add))
                for g in range(2):
                    c4 = bc(xc[:, 4 + g, sl].rearrange("p (o l) -> p o l", o=1), (P, 2, w))
                    g4 = bc(bank(bg)[0:w, g * w:(g + 1) * w].rearrange("p (o l) -> p o l", o=1), (w, 2, w))
                    tt(sc_view(i, w)[:, 2 * g:2 * g + 2, :], er[:, 2 * g:2 * g + 2, :], c4, ALU.mult)
                    link(tt(M[:, 2 * g:2 * g + 2, :], M[:, 2 * g:2 * g + 2, :], g4, ALU.mult))
                xd3 = s_xd[q2][0:w, :].rearrange("p (h d) -> p h d", d=DH)
                tt(xd3, tok[0:w, 0:256].rearrange("p (h d) -> p h d", d=DH),
                   bc(dl[0:w, :].rearrange("p (h o) -> p h o", o=1), (w, H, DH)), ALU.mult).then_inc(S("ssm_ready"), 1)

            tt(xdt, xc[:, 0:2, :], pb[:, 0, :, :], ALU.mult).then_inc(S("ssm_xdt"), 1)
            gate_vector(v, 0)
            prep(0)
            for i, (t0, w, _) in enumerate(TILES):
                sl = slice(t0, t0 + w)
                er, q2 = er_view(i, w), i % 2
                if i + 1 < NT:
                    prep(i + 1)
                if i in (0, 1):
                    gate_vector(v, i + 1)
                if w == NS:
                    v.wait_ge(S("ssm_h0_turned"), 1)
                    for n in range(4):
                        last = V.tensor_copy(s_h0t[:, 2 * n:2 * n + 2, :], bank(4 + n).rearrange("p (b n) -> p b n", n=256))
                    last.then_inc(S("ssm_h0_out"), 1)
                v.wait_ge(S("ssm_y"), i + 1)
                link(V.tensor_copy(OM[:, 2:4, sl], bank(3)[:, 0:2 * w].rearrange("p (c l) -> p c l", l=w)))
                if w == P:
                    v.wait_ge(S("ssm_state"), i + 1)
                    if i == 0:
                        link(V.tensor_copy(s_ht, bank(4)[:, 0:256]))
                    else:
                        h3 = s_ht.rearrange("p (h d) -> p h d", d=DH)
                        link(tt(h3, h3, bc(er[:, :, P - 1:P], (P, H, DH)), ALU.mult))
                        link(tt(s_ht, s_ht, bank(4)[:, 0:256], ALU.add))
                else:
                    tt(s_bm[0:NS].rearrange("p b g n -> p b (g n)"), bc(s_tok[q2][0:NS, 256:512].rearrange("p (o n) -> p o n", o=1), (NS, NB, 256)),
                       bc(ind[0:NS].rearrange("p (b o) -> p b o", o=1), (NS, NB, 256)), ALU.mult).then_inc(S("ssm_bm"), 1)
                    v.wait_ge(S("ssm_final"), 1)
                    V.tensor_copy(s_fin, bank(0)[:, 0:256].rearrange("p (c n) -> p c n", n=P)).then_inc(S("fin_made"), 1)
                    v.wait_ge(S("ssm_dec_exp"), 1)
                    for hp in range(2):
                        link(tt(s_h0[:, :, hp, :], s_h0[:, :, hp, :], bc(s_dec[:, hp, :].rearrange("p (b o) -> p b o", o=1), (P, NB, P)), ALU.mult))
                    v.wait_ge(S("ssm_state"), 5)
                    for g in range(2):
                        for q in range(2):
                            last = tt(s_h0[:, 4 * q:4 * q + 4, g, :], s_h0[:, 4 * q:4 * q + 4, g, :],
                                      bank(4 + 2 * g + q).rearrange("p (b n) -> p b n", n=P), ALU.add)
                    last.then_inc(S("states_made"), 1)
                v.drain().then_inc(S("ssm_tile_out"), 1)
            Y = OM[:, 2:4, :]
            for c_ in range(2):
                link(V.scalar_tensor_tensor(Y[:, c_, :], xc[:, c_, :], par(R_SD + c_), Y[:, c_, :], ALU.mult, ALU.add))
            v.wait_ge(S("ssm_gate"), 2)
            link(tt(Y, Y, proj[:, C_Z:C_Z + 2, :], ALU.mult))
            tt(xdt, Y, Y, ALU.mult).then_inc(S("tail_sq"), 1)
            v.wait_ge(S("tail_root"), 1)
            link(V.reciprocal(rsq[:, :], rsq[:, :]))
            for c_ in range(2):
                last = V.scalar_tensor_tensor(Y[:, c_, :], Y[:, c_, :], par(R_SNORM + c_), rsq[:, :], ALU.mult, ALU.mult)
            link(last)

        def ssm_scalar(s):
            for c_ in range(2):
                A.activation(proj[:, C_Z + c_, :], proj[:, C_Z + c_, :], ACT.Silu).then_inc(S("ssm_gate"), 1)
            gate_scalar(s)
            for i, (t0, w, _) in enumerate(TILES):
                M = hl(s_m[i % 2], w)
                s.wait_ge(S("ssm_pre"), i + 1)
                if i >= 2:
                    s.wait_ge(S("ssm_tile_out"), i - 1)
                s.wait_ge(S("ssm_m"), i + 1)
                A.activation(s_er[i % 2].rearrange("p a b -> p (a b)")[:, 0:H * w], bank(ssm_banks(i)[1])[:, 0:H * w], ACT.Exp)
                A.activation(M, M, ACT.Exp).then_inc(S("ssm_exp"), 1)
            s.wait_ge(S("ssm_dec"), 1)
            A.activation(s_dec, bank(2)[:, 0:16].rearrange("p (c b) -> p c b", b=NB), ACT.Exp).then_inc(S("ssm_dec_exp"), 1)
            s.wait_ge(S("tail_sum"), 1)
            A.activation(halves(rsq[:, :]), pair(0), ACT.Sqrt, bias=eps, scale=1.0 / GW).then_inc(S("tail_root"), 1)

        def tail_prep_vector(v, run, b2, q, k, qe, kd, last_, e1):
            v.wait_ge(S("tail_eb"), run + 1)
            link(tt(qe, q, e1, ALU.mult))
            for c_ in range(2):
                for (lo, hi, step) in ((0, SEQ, P), (SEQ, T, TS)):
                    x3 = b2[:, c_, lo:hi].rearrange("p (n i) -> p n i", i=step)
                    o3 = e1[:, c_, lo:hi].rearrange("p (n i) -> p n i", i=step)
                    last = tt(o3, bc(x3[:, :, step - 1:step], (P, (hi - lo) // step, step)), x3, ALU.subtract)
            last.then_inc(S("tail_bd"), 1)
            v.wait_ge(S("tail_ebd"), run + 1)
            tt(kd, k, e1, ALU.mult).then_inc(S("tail_prep"), 1)

        def tail_prep_scalar(s, run, b2, e1):
            A.activation(e1, b2, ACT.Exp).then_inc(S("tail_eb"), 1)
            for c_ in range(2):
                A.activation(t_lastp[:, :, c_], b2[:, c_, 0:SEQ].rearrange("p (n i) -> p n i", i=P)[:, :, P - 1], ACT.Exp)
                A.activation(t_lasts[:, :, c_], b2[:, c_, SEQ:T].rearrange("p (n i) -> p n i", i=TS)[:, :, TS - 1], ACT.Exp)
            s.wait_ge(S("tail_bd"), run + 1)
            A.activation(e1, e1, ACT.Exp).then_inc(S("tail_ebd"), 1)

        t_lastp = sm(4, 2)
        t_lasts = sm(NB, 2)

        def tail_tensor(pe, run, att, kd, qe, vT, kbg, N):
            gdn = kbg is not None

            def turn(i):
                t0, w, _ = TILES[i]
                sl = slice(t0, t0 + w)
                b_ = bank(0 if i % 2 == 0 else 7)
                for k in range(2):
                    last = tr(b_[0:w, k * P:(k + 1) * P], kd[:, k, sl], P)
                if not (w == NS and gdn):
                    for k in range(2):
                        last = tr(b_[0:w, 256 + k * P:256 + (k + 1) * P], vT[:, k, sl], P)
                last.then_inc(S("tail_tok"), 1)

            pe.wait_ge(S("tail_prep"), run + 1)
            turn(0)
            for i, (t0, w, _) in enumerate(TILES):
                sl = slice(t0, t0 + w)
                sample = w == NS
                state = t_st[i % 2]
                if i:
                    pe.wait_ge(S("tail_state"), 5 * run + i)
                if sample:
                    pe.wait_ge(S("state_in"), 32 + 16 * run)
                if gdn and sample:
                    for h in range(H):
                        r = slice((h % 2) * 64, (h % 2) * 64 + 64)
                        for b in range(NB):
                            last = mm(bank(1)[r, (h // 2) * w + b * TS:(h // 2) * w + (b + 1) * TS], t_s0[r, b, h // 2, :],
                                      kbg[r, h // 2, t0 + b * TS:t0 + (b + 1) * TS], True, True)
                    last.then_inc(S("tail_w"), 1)
                    pe.wait_ge(S("tail_rt"), 1)
                    for k in range(2):
                        last = tr(bank(5)[0:w, k * P:(k + 1) * P], t_rt[:, k, :], P)
                    last.then_inc(S("tail_rt_turned"), 1)
                elif gdn and i:
                    for h in range(H):
                        r = slice((h % 2) * 64, (h % 2) * 64 + 64)
                        last = mm(bank(1 if h % 2 == 0 else 5)[0:w, (h // 2) * 64:(h // 2 + 1) * 64], kbg[r, h // 2, sl], state[r, h // 2, :], True, True)
                    last.then_inc(S("tail_w"), 1)
                if i + 1 < NT:
                    turn(i + 1)
                pe.wait_ge(S("tail_tok_out"), 5 * run + i + 1)
                if gdn:
                    for h in range(H):
                        last = mm(bank(2)[0:w, h * 64:(h + 1) * 64], N(i, w)[:, h, :], t_tok[0:w, 256 + h * 64:256 + (h + 1) * 64], True, True)
                    last.then_inc(S("tail_vn"), 1)
                    pe.wait_ge(S("tail_vn_out"), i + 1)
                if not sample:
                    for h in range(H):
                        r = slice((h % 2) * 64, (h % 2) * 64 + 64)
                        last = mm(bank(4)[r, (h // 2) * DH:(h // 2 + 1) * DH], t_tok[0:w, h * 64:(h + 1) * 64], t_vn[0:w, h * 64:(h + 1) * 64], True, True)
                    last.then_inc(S("tail_st"), 1)
                for h in range(H):
                    r = slice((h % 2) * 64, (h % 2) * 64 + 64)
                    o_ = bank(3)[r, (h // 2) * w:(h // 2 + 1) * w]
                    last = mm(o_, t_vn[0:w, h * 64:(h + 1) * 64], att(i, w, h), True, i == 0)
                    if sample:
                        for b in range(NB):
                            last = mm(o_[:, b * TS:(b + 1) * TS], t_s0[r, b, h // 2, :], qe[r, h // 2, t0 + b * TS:t0 + (b + 1) * TS], False, True)
                    elif i:
                        last = mm(o_, state[r, h // 2, :], qe[r, h // 2, sl], False, True)
                last.then_inc(S("tail_o"), 1)
                if sample:
                    pe.wait_ge(S("tail_vm"), run + 1)
                    for h in range(H):
                        r = slice((h % 2) * 64, (h % 2) * 64 + 64)
                        last = mm(bank(6 + h // 2)[r, :], t_tok[0:w, h * 64:(h + 1) * 64], vm_of(run)[0:w, h * 512:(h + 1) * 512], True, True)
                    last.then_inc(S("tail_st"), 1)
            pe.wait_ge(S("tail_sq"), run + 2)
            for k in range(2):
                for j in range(2):
                    last = mm(PS[k][:, j, 0:HT], blk64, qe[:, k, j * HT:(j + 1) * HT], True, True)
            last.then_inc(S("tail_sum"), 1)

        t_rt = sm(2, NS)

        def vm_of(run):
            return h_vm_ if run == 0 else t_vm

        def tail_vector(v, run, gdn, vT, qe, c_out, c_gate, rnorm):
            for i, (t0, w, _) in enumerate(TILES):
                sl = slice(t0, t0 + w)
                sample = w == NS
                tokens = bank(0 if i % 2 == 0 else 7)
                v.wait_ge(S("tail_tok"), 5 * run + i + 1)
                V.tensor_copy(t_tok[0:w, 0:256], tokens[0:w, 0:256])
                if gdn and sample:
                    v.wait_ge(S("tail_w"), i)
                    tt(t_rt, vT[:, :, sl], bank(1)[:, 0:2 * w].rearrange("p (c l) -> p c l", l=w), ALU.subtract).then_inc(S("tail_rt"), 1)
                    v.wait_ge(S("tail_rt_turned"), 1)
                    V.tensor_copy(t_tok[0:w, 256:512], bank(5)[0:w, 0:256]).then_inc(S("tail_tok_out"), 1)
                elif gdn and i:
                    link(V.tensor_copy(t_tok[0:w, 256:512], tokens[0:w, 256:512]))
                    v.wait_ge(S("tail_w"), i)
                    for e in range(2):
                        half = t_tok[0:w, 256:512].rearrange("p (c e d) -> p e c d", e=2, d=DH)[:, e]
                        last = tt(half, half, bank(1 if e == 0 else 5)[0:w, 0:P].rearrange("p (c d) -> p c d", d=DH), ALU.subtract)
                    last.then_inc(S("tail_tok_out"), 1)
                elif gdn:
                    V.tensor_copy(t_tok[0:w, 256:512], tokens[0:w, 256:512]).then_inc(S("tail_tok_out"), 1)
                else:
                    V.tensor_copy(t_vn[0:w, :], tokens[0:w, 256:512]).then_inc(S("tail_tok_out"), 1)
                if gdn:
                    v.wait_ge(S("tail_vn"), i + 1)
                    V.tensor_copy(t_vn[0:w, :], bank(2)[0:w, 0:256]).then_inc(S("tail_vn_out"), 1)
                if sample:
                    if gdn:
                        v.wait_ge(S("tail_vn_out"), i + 1)
                    else:
                        v.wait_ge(S("tail_tok_out"), i + 1)
                    vm4 = vm_of(run)[0:w, :].rearrange("p (h b d) -> p h b d", b=NB, d=DH)
                    for h in range(H):
                        last = tt(vm4[:, h], bc(t_vn[0:w, h * 64:(h + 1) * 64].rearrange("p (o d) -> p o d", o=1), (w, NB, DH)),
                                  bc(ind[0:w].rearrange("p (b o) -> p b o", o=1), (w, NB, DH)), ALU.mult)
                    last.then_inc(S("tail_vm"), 1)
                def outputs():
                    v.wait_ge(S("tail_o"), 5 * run + i + 1)
                    link(V.tensor_copy(OM[:, c_out:c_out + 2, sl], bank(3)[:, 0:2 * w].rearrange("p (c l) -> p c l", l=w)))

                if sample:
                    outputs()
                v.wait_ge(S("tail_st"), 5 * run + i + 1)
                if sample:
                    link(tt(t_s0.rearrange("p b c d -> p (b c) d"), t_s0.rearrange("p b c d -> p (b c) d"),
                            bc(t_lasts.rearrange("p b (c o) -> p (b c) o", o=1), (P, 2 * NB, DH)), ALU.mult))
                    for c_ in range(2):
                        last = tt(t_s0[:, :, c_, :], t_s0[:, :, c_, :], bank(6 + c_).rearrange("p (b d) -> p b d", d=DH), ALU.add)
                    last.then_inc(S("states_made"), 1)
                    v.drain().then_inc(S("tail_state"), 1)
                else:
                    old, new = t_st[i % 2], t_st[(i + 1) % 2]
                    if i:
                        link(tt(new, old, bc(t_lastp[:, i, :].rearrange("p (c o) -> p c o", o=1), (P, 2, DH)), ALU.mult))
                        tt(new, new, bank(4)[:, 0:2 * DH].rearrange("p (c d) -> p c d", d=DH), ALU.add).then_inc(S("tail_state"), 1)
                    else:
                        V.tensor_copy(new, bank(4)[:, 0:2 * DH].rearrange("p (c d) -> p c d", d=DH)).then_inc(S("tail_state"), 1)
                    if i == 3:
                        v.drain().then_inc(S("fin_made"), 1)
                    v.wait_ge(S("tail_state"), 5 * run + i + 1)
                    outputs()
            Y = OM[:, c_out:c_out + 2, :]
            tt(qe, Y, Y, ALU.mult).then_inc(S("tail_sq"), 1)
            v.wait_ge(S("tail_root"), 1 + 2 * run + 2)
            link(V.reciprocal(qe, qe))
            for c_ in range(2):
                link(V.scalar_tensor_tensor(Y[:, c_, :], Y[:, c_, :], par(rnorm), qe[:, c_, :], ALU.mult, ALU.mult))
            link(tt(Y, Y, proj[:, c_gate:c_gate + 2, :], ALU.mult))

        def tail_scalar(s, run, qe, c_gate):
            s.wait_ge(S("tail_sum"), run + 2)
            for k in range(2):
                A.activation(halves(qe[:, k, :]), pair(k), ACT.Sqrt, bias=eps, scale=1.0 / DH).then_inc(S("tail_root"), 1)

        h_vm_ = carve(SC, 2 * T, NB * H * DH)
        hq, hk = proj[:, C_HQ:C_HQ + 2, :], h_k

        def lv_groups():
            return (((0, SEQ), 4, P, 8), ((SEQ, T), 2, NS, 3))

        fx = proj[:, C_HF:C_HF + 2, :]

        def gate_scalar(s):
            s.wait_ge(S("h_abs"), 1)
            link(A.activation(h_d, h_d, ACT.Exp, scale=-1.0), "s")
            A.activation(h_k, fx, ACT.Exp)
            A.activation(h_d, h_d, ACT.Ln, bias=ones[:, 0:1]).then_inc(S("h_ln"), 1)

        def gate_vector(v, step):
            if step == 0:
                V.scalar_tensor_tensor(h_d, fx, -1.0, fx, ALU.mult, ALU.max).then_inc(S("h_abs"), 1)
            elif step == 1:
                v.wait_ge(S("h_ln"), 1)
                link(V.scalar_tensor_tensor(h_d, fx, 0.0, h_d, ALU.min, ALU.subtract))
                for c_ in range(2):
                    last = V.tensor_tensor_scan(h_b[:, c_, :], keep[:, :], h_d[:, c_, :], 0.0, ALU.mult, ALU.add)
                link(last)
            else:
                link(V.tensor_scalar(h_k, h_k, 1.0, None, ALU.add))
                V.reciprocal(h_k, h_k).then_inc(S("h_k"), 1)

        def hgrn_vector(v):
            v.wait_ge(S("states_out"), 32)
            v.wait_ge(S("h_k"), 1)
            n = 0
            m_ = 0
            for (lo, hi), nt, w, nl in lv_groups():
                def decays(j, n):
                    B = 1 << j
                    for c_ in range(2):
                        x3 = h_b[:, c_, lo:hi].rearrange("p (n i) -> p n i", i=B)
                        o3 = h_d[:, c_, lo:hi].rearrange("p (n i) -> p n i", i=B)
                        mid = bc(x3[:, :, B // 2 - 1:B // 2], (P, (hi - lo) // B, B // 2))
                        tt(o3[:, :, 0:B // 2], mid, x3[:, :, 0:B // 2], ALU.subtract)
                        last = tt(o3[:, :, B // 2:B], x3[:, :, B // 2:B], mid, ALU.subtract)
                    last.then_inc(S("h_diff"), 1)
                    v.wait_ge(S("h_dec"), n + 1)
                    if n >= 2:
                        v.wait_ge(S("h_lv_mm"), h_lvdone(n - 2))
                    tt(h_q1[:, n % 2, :, lo:hi], hq[:, :, lo:hi], h_d[:, :, lo:hi], ALU.mult)
                    tt(h_k1[:, n % 2, :, lo:hi], hk[:, :, lo:hi], h_d[:, :, lo:hi], ALU.mult).then_inc(S("h_qk"), 1)
                    v.wait_ge(S("h_qk"), n + 1)
                for j in range(nl):
                    if j + 1 < nl:
                        decays(j + 1, n)
                        n += 1
                    nm = 4 if w == P else 2
                    msk = bc(lev[0:w, j, 0:w].rearrange("p (o l) -> p o l", o=1), (w, nm, w))
                    for i in range(nt):
                        v.wait_ge(S("h_lv_mm"), m_ + 1)
                        src = bank(m_ % 8)[0:w, 0:nm * w].rearrange("p (h l) -> p h l", l=w)
                        if j == 0:
                            tt(h_store(i, w), src, msk, ALU.mult).then_inc(S("h_lv_out"), 1)
                        else:
                            v.wait_ge(S("h_added"), m_ - 3)
                            tt(h_job(h_msk, m_ % 4, w), src, msk, ALU.mult).then_inc(S("h_lv_out"), 1)
                        m_ += 1

        def h_lvdone(n):
            return 4 * (n + 2) if n < 7 else 32 + 2 * (n - 7 + 2)

        def h_job(buf, i, w):
            n = 4 if w == P else 2
            return buf[0:w, i * 512:i * 512 + n * w].rearrange("p (h l) -> p h l", l=w)

        def h_store(m_, w):
            if w == P:
                return h_job(h_att, m_, w)
            return h_att[0:w, 2048 + 64 * m_:2048 + 64 * (m_ + 1)].rearrange("p (h l) -> p h l", l=w)

        def h_att_of(i, w, h):
            if w == P:
                return h_store(2 * (i // 2) + h % 2, w)[:, 2 * (i % 2) + h // 2, :]
            return h_store(h % 2, w)[:, h // 2, :]

        def hgrn_gpsimd(g):
            m_, added = 0, 0
            for _, nt, w, nl in lv_groups():
                for j in range(nl):
                    for i in range(nt):
                        g.wait_ge(S("h_lv_out"), m_ + 1)
                        if j == 0:
                            g.drain().then_inc(S("h_added"), 1)
                        else:
                            at = h_store(i, w)
                            if j > 1:
                                g.wait_ge(S("h_added"), m_ - nt + 1)
                            G.tensor_tensor(at, at, h_job(h_msk, m_ % 4, w), ALU.add).then_inc(S("h_added"), 1)
                        m_ += 1

        def hgrn_tensor(pe):
            pe.wait_ge(S("h_k"), 1)
            m_, n = 0, 0
            for (lo, hi), nt, w, nl in lv_groups():
                for j in range(nl):
                    if j:
                        pe.wait_ge(S("h_qk"), n + 1)
                    for i in range(nt):
                        if m_ >= 8:
                            pe.wait_ge(S("h_lv_out"), m_ - 7)
                        r = slice((i % 2) * 64, (i % 2) * 64 + 64)
                        for n_ in range(4 if w == P else 2):
                            t_ = 2 * (i // 2) + n_ // 2 if w == P else 0
                            sl = slice(lo + t_ * w, lo + (t_ + 1) * w)
                            q_ = hq[r, n_ % 2, sl] if j == 0 else h_q1[r, n % 2, n_ % 2, sl]
                            k_ = hk[r, n_ % 2, sl] if j == 0 else h_k1[r, n % 2, n_ % 2, sl]
                            last = mm(bank(m_ % 8)[0:w, n_ * w:(n_ + 1) * w], k_, q_, True, True)
                        last.then_inc(S("h_lv_mm"), 1)
                        m_ += 1
                    if j:
                        n += 1
            tail_tensor(pe, 0, h_att_of, h_k1[:, 0], h_q1[:, 0], proj[:, C_HI:C_HI + 2, :], None, None)

        def hgrn_vector_tail(v):
            v.wait_ge(S("h_lv_mm"), 38)
            v.wait_ge(S("h_added"), 38)
            v.drain().then_inc(S("h_levels_done"), 1)
            tail_prep_vector(v, 0, h_b, hq, hk, h_q1[:, 0], h_k1[:, 0], None, h_d)
            tail_vector(v, 0, False, None, h_q1[:, 0], 4, C_HG, R_HNORM)

        def hgrn_scalar(s):
            n = 0
            for (lo, hi), nt, w, nl in lv_groups():
                for j in range(1, nl):
                    s.wait_ge(S("h_diff"), n + 1)
                    A.activation(h_d[:, :, lo:hi], h_d[:, :, lo:hi], ACT.Exp).then_inc(S("h_dec"), 1)
                    n += 1
            s.wait_ge(S("h_levels_done"), 1)
            tail_prep_scalar(s, 0, h_b, h_d)
            for c_ in range(2):
                A.activation(proj[:, C_HG + c_, :], proj[:, C_HG + c_, :], ACT.Silu)
            tail_scalar(s, 0, h_q1[:, 0], C_HG)

        g_al = carve(XN, 4 * T, 2048)
        gq, gk, gv = (proj[:, C_GQKV + 2 * i:C_GQKV + 2 * i + 2, :] for i in range(3))
        g_e1 = carve(SC, 4 * T, 2, T)

        def gtile(buf, i, w):
            return buf[0:w, i * 512:i * 512 + H * w].rearrange("p (h l) -> p h l", l=w)

        def gdn_vector(v):
            for i, (t0, w, _) in enumerate(TILES):
                ex = hl(g_p1[:, i % 4, :], w)
                v.wait_ge(S("g_mm"), i + 1)
                if i == 4:
                    v.wait_ge(S("g_al_free"), 1)
                dec_vector(ex, 4 * (i % 2) + 2, 4, i, w).then_inc(S("g_m"), 1)
                v.wait_ge(S("g_exp"), i + 1)
                for e in range(2):
                    src = bank(4 * (i % 2) + e)[0:w, 0:H * w].rearrange("p (h l) -> p h l", l=w)
                    par_ = lambda m_: m_.rearrange("p (c e) l -> p e c l", e=2)[:, e]
                    tt(par_(gtile(g_A, i, w)), par_(ex), src[:, 0:2, :], ALU.mult)
                    last = tt(par_(gtile(g_QK, i, w)), par_(ex), src[:, 2:4, :], ALU.mult)
                last.then_inc(S("g_mats"), 1)
            v.wait_ge(S("g_mats"), NT)
            v.wait_ge(S("states_out"), 64)
            done, mults = 0, 0
            for nt, i0, w, nl in ((4, 0, P, 7), (1, 4, NS, 2)):
                id3 = bc(ident[0:w, 0:w].rearrange("p (o l) -> p o l", o=1), (w, H, w))
                b3 = lambda q_: bank(q_)[0:w, 0:H * w].rearrange("p (h l) -> p h l", l=w)
                for j in range(1, nl + 1):
                    msk = bc(lev[0:w, j, 0:w].rearrange("p (o l) -> p o l", o=1), (w, H, w))
                    for i in range(nt):
                        if j > 1:
                            v.wait_ge(S("g_p1_mm"), done - nt + i + 1)
                            if j == 2:
                                v.wait_ge(S("g_tn"), done - nt + i + 1)
                        last = tt(gtile(g_al, i, w), gtile(g_A, i0 + i, w), msk, ALU.mult)
                        last.then_inc(S("g_al"), 1)
                    for i in range(nt):
                        if j == 1:
                            v.wait_ge(S("g_al"), done + 1)
                            tt(gtile(g_N, i0 + i, w), id3, gtile(g_al, i, w), ALU.subtract)
                            v.wait_ge(S("g_p1_mm"), done + 1)
                            tt(gtile(g_T, i0 + i, w), id3, b3(i), ALU.subtract).then_inc(S("g_tn"), 1)
                        else:
                            v.wait_ge(S("g_tn_mm"), mults + 1)
                            b_ = 4 + 2 * (mults % 2)
                            if j < nl:
                                tt(gtile(g_T, i0 + i, w), gtile(g_T, i0 + i, w), b3(b_), ALU.subtract)
                            tt(gtile(g_N, i0 + i, w), gtile(g_N, i0 + i, w), b3(b_ + 1), ALU.subtract).then_inc(S("g_tn"), 1)
                            mults += 1
                        done += 1
            v.wait_ge(S("g_tn"), done)
            v.drain().then_inc(S("g_inverted"), 1)
            tail_prep_vector(v, 1, pb[:, 2], gq, gk, g_qg, t_kd, None, g_e1)
            link(tt(g_kbg, g_kbg, g_kb, ALU.mult))
            v.drain().then_inc(S("g_kbg"), 1)
            tail_vector(v, 1, True, gv, g_qg, 6, C_GZ, R_GNORM)

        def gdn_scalar(s):
            for c_ in range(2):
                A.activation(proj[:, C_GZ + c_, :], proj[:, C_GZ + c_, :], ACT.Silu)
            for i, (t0, w, _) in enumerate(TILES):
                s.wait_ge(S("g_m"), i + 1)
                ex = hl(g_p1[:, i % 4, :], w)
                A.activation(ex, ex, ACT.Exp).then_inc(S("g_exp"), 1)
            A.activation(g_kbg, pb[:, 2], ACT.Exp)
            done = 0
            for nt, i0, w, nl in ((4, 0, P, 7), (1, 4, NS, 2)):
                done += nt
                for j in range(2, nl + 1):
                    for i in range(nt):
                        s.wait_ge(S("g_p1_mm"), done + 1)
                        A.activation(gtile(g_p1.rearrange("p a b -> p (a b)"), i, w), bank(i)[0:w, 0:H * w].rearrange("p (h l) -> p h l", l=w),
                                     ACT.Copy).then_inc(S("g_p1"), 1)
                        done += 1
            s.wait_ge(S("g_inverted"), 1)
            tail_prep_scalar(s, 1, pb[:, 2], g_e1)
            tail_scalar(s, 1, g_qg, C_GZ)

        def gdn_tensor(pe):
            for i, (t0, w, _) in enumerate(TILES):
                sl = slice(t0, t0 + w)
                if i >= 2:
                    pe.wait_ge(S("g_mats"), i - 1)
                b_ = 4 * (i % 2)
                for h in range(H):
                    r = slice((h % 2) * 64, (h % 2) * 64 + 64)
                    for m_, rhs in enumerate((g_kb, gq)):
                        c0 = (2 * m_ + h // 2) * w
                        mm(bank(b_ + h % 2)[0:w, c0:c0 + w], gk[r, h // 2, sl], rhs[r, h // 2, sl], True, True)
                dec_tensor(pe, b_ + 2, 3, t0, w, w).then_inc(S("g_mm"), 1)
                if i == 3:
                    pe.drain().then_inc(S("g_al_free"), 1)
            pe.wait_ge(S("g_mats"), NT)
            done, mults = 0, 0
            for nt, i0, w, nl in ((4, 0, P, 7), (1, 4, NS, 2)):
                for j in range(1, nl + 1):
                    for i in range(nt):
                        pe.wait_ge(S("g_al"), done + i + 1)
                        if j > 1:
                            pe.wait_ge(S("g_tn"), done - nt + i + 1)
                        for h in range(H):
                            t_ = ident[0:w, 0:w] if j == 1 else gtile(g_T, i0 + i, w)[:, h, :]
                            last = mm(bank(i)[0:w, h * w:(h + 1) * w], gtile(g_al, i, w)[:, h, :], t_, True, True)
                        last.then_inc(S("g_p1_mm"), 1)
                    for i in range(nt if j > 1 else 0):
                        pe.wait_ge(S("g_p1"), mults + 1)
                        if mults >= 2:
                            pe.wait_ge(S("g_tn"), done + i - 1)
                        b_ = 4 + 2 * (mults % 2)
                        p1 = gtile(g_p1.rearrange("p a b -> p (a b)"), i, w)
                        if j < nl:
                            for h in range(H):
                                mm(bank(b_)[0:w, h * w:(h + 1) * w], gtile(g_N, i0 + i, w)[:, h, :], p1[:, h, :], True, True)
                        for h in range(H):
                            last = mm(bank(b_ + 1)[0:w, h * w:(h + 1) * w], p1[:, h, :], gtile(g_N, i0 + i, w)[:, h, :], True, True)
                        last.then_inc(S("g_tn_mm"), 1)
                        mults += 1
                    done += nt
            pe.wait_ge(S("g_kbg"), 1)
            tail_tensor(pe, 1, lambda i, w, h: gtile(g_QK, i, w)[:, h, :], t_kd, g_qg, gv, g_kbg, lambda i, w: gtile(g_N, i, w))
        def mem_turn_tensor(pe):
            pe.wait_ge(S("mem_in"), 32)
            for q in range(4):
                i, hf = divmod(q, 2)
                for k in range(4):
                    last = tr(bank(4 + q)[:, k * P:(k + 1) * P], mem_raw[:, i, (4 * hf + k) * P:(4 * hf + k + 1) * P], P)
                last.then_inc(S("mem_turned"), 1)

        def mem_tensor(pe):
            norm_tensor(pe, memn, MEM)
            pe.wait_ge(S("part_lo"), IN_BEFORE["wkv"] + KD)
            for n in range(8):
                for kh in range(2):
                    w = weights(pe, first["wkv"] + 2 * n + kh)
                    for mt in range(2):
                        job = 2 * n + mt
                        if job >= 4 and kh == 0:
                            pe.wait_ge(S("kvm_out_s" if mt == 0 else "kvm_out_v"), (job - 4) // 2 + 1)
                        for kk in range(4):
                            k = 4 * kh + kk
                            last = mm3(bank(job % 4)[:, 0:256], operand("wkv", k, slice(mt * P, (mt + 1) * P)),
                                       (w[0][:, kk, :], w[1][:, kk, :]), k == 0, k == KD - 1)
                        if kh:
                            last.then_inc(S("kvm_mm"), 1)
                    if kh == 0:
                        last.then_inc(S("kvm_part"), 1)
            pe.wait_ge(S("kvm_out_s"), 8)
            pe.wait_ge(S("kvm_out_v"), 8)
            for q in range(4):
                mt, kq = divmod(q, 2)
                for k in range(4):
                    last = tr(bank(4 + q)[:, k * P:(k + 1) * P], mkv[:, mt, (4 * kq + k) * P:(4 * kq + k + 1) * P], P)
                last.then_inc(S("kt_turned"), 1)

        def mem_vector(v):
            for q in range(4):
                i, hf = divmod(q, 2)
                v.wait_ge(S("mem_turned"), q + 1)
                last = V.tensor_copy(memt[:, 4 * hf:4 * hf + 4, i * P:(i + 1) * P], bank(4 + q).rearrange("p (k t) -> p k t", t=P))
            last.then_inc(S("mem_raw"), 1)
            v.wait_ge(S("mem_raw"), 1)
            squares_vector(v, memt, memn)
            scale_vector(v, memt, MEM, R_MEM, memn, parts="wkv")
            for n in range(8):
                part_lo(v, "wout", n)
                v.wait_ge(S("kvm_mm"), 2 * n + 2)
                V.tensor_copy(mkv[:, 1, n * 256:(n + 1) * 256], bank((2 * n + 1) % 4)[:, 0:256]).then_inc(S("kvm_out_v"), 1)
            for q in range(4):
                mt, kq = divmod(q, 2)
                v.wait_ge(S("kt_turned"), q + 1)
                V.tensor_copy(mkt[:, 4 * kq:4 * kq + 4, mt * P:(mt + 1) * P], bank(4 + q).rearrange("p (k t) -> p k t", t=P))

        def mem_scalar(s):
            s.wait_ge(S("mem_raw"), 1)
            squares_scalar(s, memt, memn)
            root_scalar(s, MEM)
            parts_scalar(s, "wkv")
            for n in range(8):
                part_hi(s, "wout", n)
                split_hi(s, first["wkv"] + 2 * n + 1 + NH)
                s.wait_ge(S("kvm_mm"), 2 * n + 1)
                scopy(mkv[:, 0, n * 256:(n + 1) * 256], bank((2 * n) % 4)[:, 0:256]).then_inc(S("kvm_out_s"), 1)
                split_hi(s, first["wkv"] + 2 * n + 2 + NH)

        def cross_prompt_tensor(pe):
            def scores(j):
                h, i = divmod(j, 4)
                if j >= 4:
                    pe.wait_ge(S("att_exp"), 16 + j - 3)
                for k in range(2):
                    last = mm(bank(j % 4)[:, 0:MEM], xq[:, 2 * h + k, i * P:(i + 1) * P], mkt[:, 2 * h + k, :], k == 0, k == 1)
                last.then_inc(S("att_scores"), 1)

            def turn(j):
                pe.wait_ge(S("att_probs"), 16 + j + 1)
                if j >= 2:
                    pe.wait_ge(S("att_pt"), 16 + j - 1)
                for k in range(2):
                    last = tr(bank(6 + j % 2)[:, k * P:(k + 1) * P], cx_s[:, j % 4, k * P:(k + 1) * P], P)
                last.then_inc(S("att_turned"), 1)

            def pv(h):
                pe.wait_ge(S("att_pt"), 16 + 4 * h + 4)
                if h:
                    pe.wait_ge(S("att_out"), 4 + 2 * h)
                for ft in range(2):
                    for k in range(2):
                        last = mm(bank(4 + ft), mkv[:, k, D + h * XDH + ft * P:D + h * XDH + (ft + 1) * P], cx_pt[:, h % 2, k, :], k == 0, k == 1)
                last.then_inc(S("att_pv"), 1)

            scores(0)
            scores(1)
            for j in range(16):
                if j + 2 < 16:
                    scores(j + 2)
                turn(j)
                if j >= 5 and j % 4 == 1:
                    pv(j // 4 - 1)
            pv(3)

        def cross_prompt_vector(v):
            def first_(j):
                v.wait_ge(S("att_scores"), 16 + j + 1)
                link(V.tensor_reduce(cx_stat[:, 0, j:j + 1], bank(j % 4)[:, 0:MEM], AXX, ALU.max, negate=True))
                V.tensor_scalar(cx_stat[:, 0, j:j + 1], cx_stat[:, 0, j:j + 1], XSCALE, None, ALU.mult).then_inc(S("att_max"), 1)

            def second(j):
                v.wait_ge(S("att_exp"), 16 + j + 1)
                link(V.reciprocal(cx_stat[:, 2, j:j + 1], cx_stat[:, 1, j:j + 1]))
                V.tensor_scalar(cx_s[:, j % 4, :], cx_s[:, j % 4, :], cx_stat[:, 2, j:j + 1], None, ALU.mult).then_inc(S("att_probs"), 1)

            def out_(h):
                v.wait_ge(S("att_pv"), 16 + h + 1)
                for ft in range(2):
                    V.tensor_copy(OM[:, 2 * h + ft, 0:SEQ], bank(4 + ft)).then_inc(S("att_out"), 1)

            first_(0)
            for j in range(16):
                if j + 1 < 16:
                    first_(j + 1)
                second(j)
                if j >= 6 and j % 4 == 2:
                    out_(j // 4 - 1)
            out_(3)

        def cross_prompt_scalar(s):
            def ex(j):
                s.wait_ge(S("att_max"), 16 + j + 1)
                if j >= 4:
                    s.wait_ge(S("att_turned"), 16 + j - 3)
                A.activation(cx_s[:, j % 4, :], bank(j % 4)[:, 0:MEM], ACT.Exp, bias=cx_stat[:, 0, j:j + 1], scale=XSCALE,
                             accum_out=cx_stat[:, 1, j:j + 1]).then_inc(S("att_exp"), 1)

            ex(0)
            for j in range(16):
                if j + 1 < 16:
                    ex(j + 1)
                h, i = divmod(j, 4)
                s.wait_ge(S("att_turned"), 16 + j + 1)
                if h >= 2 and i == 0:
                    s.wait_ge(S("att_pv"), 16 + h - 1)
                scopy(cx_pt[:, h % 2, :, i * P:(i + 1) * P], bank(6 + j % 2)[:, 0:2 * P].rearrange("p (k t) -> p k t", t=P))\
                    .then_inc(S("att_pt"), 1)

        def cross_sample_tensor(pe):
            def turn(q):
                b, x = divmod(q, 4)
                if x == 0:
                    pe.wait_ge(S(f"cx_ring{b % 4}_in"), 16 * (b // 4 + 1))
                if q >= 4:
                    pe.wait_ge(S("keys_turned_s" if q % 2 == 0 else "keys_turned_v"), 32 + (q - 4) // 2 + 1)
                for kk in range(2):
                    for i in range(2):
                        last = tr(bank(q % 4)[:, (2 * kk + i) * P:(2 * kk + i + 1) * P],
                                  cx_slot(b)[:, i * D + (2 * x + kk) * P:i * D + (2 * x + kk + 1) * P], P)
                last.then_inc(S("satt_turned"), 1)

            def score(q):
                b, h = divmod(q, 4)
                pe.wait_ge(S("keys_turned_s" if q % 2 == 0 else "keys_turned_v"), 32 + q // 2 + 1)
                r = slice(32 * (b // 2), 32 * (b // 2) + 32)
                for kk in range(2):
                    last = mm(bank(4)[r, 0:MEM], cx_qp[:, 2 * h + kk, b, :], cx_kt[:, q % 4, kk * MEM:(kk + 1) * MEM],
                              b % 2 == 0 and h == 0 and kk == 0, b % 2 == 1 and h == 3 and kk == 1)
                last.then_inc(S("satt_scored"), 1)

            pe.wait_ge(S("cross_q"), 1)
            turn(0)
            turn(1)
            for q in range(2, 32):
                turn(q)
                score(q - 2)
            score(30)
            score(31)
            pe.wait_ge(S("satt_probs"), 1)
            for i in range(2):
                last = tr(bank(1)[:, i * P:(i + 1) * P], cx_ss[:, i * P:(i + 1) * P], P)
            last.then_inc(S("satt_pt"), 1)
            pe.wait_ge(S("satt_pt_out"), 2 + 1)
            for b in range(NB):
                pe.wait_ge(S(f"cx_ring{(8 + b) % 4}_in"), 16 * ((8 + b) // 4 + 1))
                r = slice(32 * (b // 2), 32 * (b // 2) + 32)
                for hf in range(2):
                    for i in range(2):
                        last = mm(bank((2 if b % 2 == 0 else 5) + hf)[r, :], cx_pts[:, i, r],
                                  cx_slot(8 + b)[:, i * D + hf * 512:i * D + (hf + 1) * 512], i == 0, i == 1)
                last.then_inc(S("satt_pv"), 1)
            pick = ident.rearrange("p (g e h t) -> p g e h t", e=2, h=H, t=TS)
            for e in range(2):
                pe.wait_ge(S("satt_o" if e == 0 else "satt_exp"), 2 if e == 0 else 3)
                for k in range(KD):
                    last = mm(bank(0)[:, k * NS:(k + 1) * NS].rearrange("p (g e t) -> p g e t", e=2, t=TS)[:, :, e, :],
                              cx_o[:, e, k * P:(k + 1) * P], pick[:, :, e, k // 2, :], True, True)
            last.then_inc(S("satt_pv"), 1)

        def cross_sample_vector(v):
            for q in range(1, 32, 2):
                v.wait_ge(S("satt_turned"), 64 + q + 1)
                if q >= 4:
                    v.wait_ge(S("satt_scored"), 64 + q - 3)
                V.tensor_copy(cx_kt[:, q % 4, :], bank(q % 4)).then_inc(S("keys_turned_v"), 1)
            v.wait_ge(S("satt_scored"), 64 + 32)
            link(V.tensor_reduce(cx_stat[:, 0, 0:1], bank(4)[:, 0:MEM], AXX, ALU.max, negate=True))
            V.tensor_scalar(cx_stat[:, 0, 0:1], cx_stat[:, 0, 0:1], XSCALE, None, ALU.mult).then_inc(S("satt_max"), 1)
            v.wait_ge(S("satt_exp"), 1 + 1)
            link(V.reciprocal(cx_stat[:, 2, 0:1], cx_stat[:, 1, 0:1]))
            V.tensor_scalar(cx_ss, cx_ss, cx_stat[:, 2, 0:1], None, ALU.mult).then_inc(S("satt_probs"), 1)
            v.wait_ge(S("satt_pt"), 2 + 1)
            V.tensor_copy(cx_pts, bank(1)[:, 0:256].rearrange("p (i r) -> p i r", r=P)).then_inc(S("satt_pt_out"), 1)
            v.wait_ge(S("satt_pv"), 1 + NB)
            V.tensor_copy(cx_o[:, 0, :].rearrange("p (j n) -> p j n", j=2), PS[1][:, :, :]).then_inc(S("satt_o"), 1)
            v.wait_ge(S("satt_pv"), 1 + NB + 1)
            V.tensor_copy(OM[:, :, SEQ:T], bank(0)[:, 0:KD * NS].rearrange("p (k t) -> p k t", t=NS))

        def cross_sample_scalar(s):
            for q in range(0, 32, 2):
                s.wait_ge(S("satt_turned"), 64 + q + 1)
                if q >= 4:
                    s.wait_ge(S("satt_scored"), 64 + q - 3)
                scopy(cx_kt[:, q % 4, :], bank(q % 4)).then_inc(S("keys_turned_s"), 1)
            s.wait_ge(S("satt_max"), 1 + 1)
            A.activation(cx_ss, bank(4)[:, 0:MEM], ACT.Exp, bias=cx_stat[:, 0, 0:1], scale=XSCALE,
                         accum_out=cx_stat[:, 1, 0:1]).then_inc(S("satt_exp"), 1)
            s.wait_ge(S("satt_pv"), 1 + NB)
            link(scopy(cx_o[:, 1, 0:512], bank(5)), "s")
            scopy(cx_o[:, 1, 512:1024], bank(6)).then_inc(S("satt_exp"), 1)

        def ff_tensor(pe):
            for t in range(KF):
                for gu in range(2):
                    job = 2 * t + gu
                    if job >= 4:
                        pe.wait_ge(S("ff_out"), t - 1)
                    wh, wl = weights(pe, first["wgu"] + job)
                    for k in range(KD):
                        if job == 0:
                            pe.wait_ge(S("part_lo"), IN_BEFORE["wgu"] + k + 1)
                        for j in range(2):
                            last = mm3(PS[job % 4][:, j, 0:HT], (wh[:, k, :], wl[:, k, :]),
                                       operand("wgu", k, slice(j * HT, (j + 1) * HT)), k == 0, k == KD - 1)
                    last.then_inc(S("ff_mm"), 1)

        def ff_scalar(s):
            for t in range(KF):
                s.wait_ge(S("ff_mm"), 2 * t + 1)
                if t >= 2:
                    s.wait_ge(S("ff_out"), t - 1)
                A.activation(halves(f_g[:, t % 2, :]), pair((2 * t) % 4), ACT.Silu).then_inc(S("ff_silu"), 1)
                split_hi(s, first["wgu"] + 2 * t + 1 + NH)
                if t:
                    s.wait_ge(S("ff_out"), t)
                    part_hi(s, "wdn", t - 1)
                split_hi(s, first["wgu"] + 2 * t + 2 + NH)
            s.wait_ge(S("ff_out"), KF)
            part_hi(s, "wdn", KF - 1)

        def ff_vector(v):
            for t in range(KF):
                v.wait_ge(S("ff_silu"), t + 1)
                v.wait_ge(S("ff_mm"), 2 * t + 2)
                tt(halves(hT[:, t, :]), halves(f_g[:, t % 2, :]), pair((2 * t + 1) % 4), ALU.mult).then_inc(S("ff_out"), 1)
                if t:
                    part_lo(v, "wdn", t - 1)
            part_lo(v, "wdn", KF - 1)

        def result_tensor(pe):
            for job in range(10):
                i, hf = divmod(job, 2)
                t0, w, _ = TILES[i]
                if job >= 8:
                    pe.wait_ge(S("turned_out_v" if job % 2 == 0 else "turned_out_s"), (6 if job % 2 == 0 else 5) + 1)
                for k in range(4):
                    last = tr(bank(job % 8)[0:w, k * P:(k + 1) * P], XT[:, 4 * hf + k, t0:t0 + w], P)
                last.then_inc(S("turned"), 1)

        def result_evac(eng, copy, name, par_):
            for job in range(par_, 10, 2):
                i, hf = divmod(job, 2)
                w = TILES[i][1]
                eng.wait_ge(S("turned"), 11 + job + 1)
                copy(y_tok[0:w, i, hf * 512:(hf + 1) * 512], bank(job % 8)[0:w, :]).then_inc(S(name), 1)

        def stage(eng, name, *work):
            n = STAGES.index(name)
            if n:
                eng.wait_ge(S("stage_ended"), 3 * n)
            for f in work:
                f()
            eng.drain().then_inc(S("stage_ended"), 1)

        xq_dst = lambda i: xq[:, i, :]
        nsq = carve(SC, 0, KD, T)

        @block.tensor
        def _(pe):
            stage(pe, "inputs", lambda: inputs_tensor(pe))
            stage(pe, "win", lambda: norm_tensor(pe, OM, T), lambda: params_tensor(pe), lambda: win_tensor(pe))
            stage(pe, "moba_prompt", lambda: moba_prompt_tensor(pe))
            stage(pe, "moba_sample", lambda: moba_sample_tensor(pe))
            stage(pe, "ssm", lambda: ssm_tensor(pe))
            stage(pe, "hgrn", lambda: hgrn_tensor(pe))
            stage(pe, "gdn", lambda: gdn_tensor(pe), lambda: mem_turn_tensor(pe))
            stage(pe, "mem", lambda: mem_tensor(pe))
            stage(pe, "wout",
                  lambda: gemm_tensor(pe, "wout", KD),
                  lambda: norm_tensor(pe, nsq, T, after_gemm="wout"),
                  lambda: norm_tensor(pe, nsq, T, True),
                  lambda: gemm_tensor(pe, "wxq", KD))
            stage(pe, "cross_prompt", lambda: cross_prompt_tensor(pe))
            stage(pe, "cross_sample", lambda: cross_sample_tensor(pe))
            stage(pe, "wxo",
                  lambda: gemm_tensor(pe, "wxo", KD),
                  lambda: norm_tensor(pe, nsq, T, after_gemm="wxo"),
                  lambda: norm_tensor(pe, nsq, T, True),
                  lambda: ff_tensor(pe))
            stage(pe, "wdn",
                  lambda: gemm_tensor(pe, "wdn", KD, 3),
                  lambda: norm_tensor(pe, OM, T, after_gemm="wdn"))
            stage(pe, "result", lambda: result_tensor(pe))

        @block.vector
        def _(v):
            stage(v, "inputs", lambda: inputs_evac("v", v, vcopy, "turned_out_v", 0))
            stage(v, "win", lambda: squares_vector(v, XT, OM), lambda: params_vector(v), lambda: small_lo(v),
                  lambda: scale_vector(v, XT, T, R_MIXPRE, xn, parts="win"),
                  lambda: win_vector(v))
            stage(v, "moba_prompt", lambda: moba_prompt_vector(v))
            stage(v, "moba_sample", lambda: moba_sample_vector(v))
            stage(v, "ssm", lambda: ssm_vector(v))
            stage(v, "hgrn", lambda: hgrn_vector(v), lambda: hgrn_vector_tail(v))
            stage(v, "gdn", lambda: gdn_vector(v))
            stage(v, "mem", lambda: mem_vector(v))
            stage(v, "wout",
                  lambda: v.wait_ge(S("states_out"), 96),
                  lambda: gemm_sq_vector(v, "wout", nsq),
                  lambda: scale_vector(v, xn, T, R_MIXPOST, xn, XT),
                  lambda: scale_vector(v, XT, T, R_XPRE, xn, parts="wxq"),
                  lambda: gemm_vector(v, "wxq", KD, xq_dst))
            stage(v, "cross_prompt", lambda: cross_prompt_vector(v))
            stage(v, "cross_sample", lambda: cross_sample_vector(v))
            stage(v, "wxo",
                  lambda: parts_vector(v, "wxo"),
                  lambda: gemm_sq_vector(v, "wxo", nsq),
                  lambda: scale_vector(v, xn, T, R_XPOST, xn, XT),
                  lambda: scale_vector(v, XT, T, R_FPRE, xn, parts="wgu"),
                  lambda: v.wait_ge(S("mem_kv_out"), 64),
                  lambda: ff_vector(v))
            stage(v, "wdn", lambda: gemm_sq_vector(v, "wdn", OM), lambda: scale_vector(v, xn, T, R_FPOST, xn, XT))
            stage(v, "result", lambda: result_evac(v, vcopy, "turned_out_v", 0))

        @block.scalar
        def _(s):
            stage(s, "inputs", lambda: inputs_evac("s", s, scopy, "turned_out_s", 1))
            stage(s, "win", lambda: squares_scalar(s, XT, OM), lambda: root_scalar(s, T),
                  lambda: small_hi(s), lambda: params_scalar(s), lambda: split_hi(s, 1),
                  lambda: parts_scalar(s, "win"), lambda: split_hi(s, NH), lambda: win_scalar(s))
            stage(s, "moba_prompt", lambda: moba_prompt_scalar(s))
            stage(s, "moba_sample", lambda: moba_sample_scalar(s))
            stage(s, "ssm", lambda: ssm_scalar(s))
            stage(s, "hgrn", lambda: hgrn_scalar(s))
            stage(s, "gdn", lambda: gdn_scalar(s))
            stage(s, "mem", lambda: mem_scalar(s))
            stage(s, "wout",
                  lambda: s.wait_ge(S("states_out"), 96),
                  lambda: gemm_sq_scalar(s, "wout", nsq),
                  lambda: root_scalar(s, T),
                  lambda: squares_scalar(s, XT, nsq, range(KD), 0),
                  lambda: root_scalar(s, T),
                  lambda: parts_scalar(s, "wxq"),
                  lambda: gemm_scalar(s, "wxq", KD, xq_dst))
            stage(s, "cross_prompt", lambda: cross_prompt_scalar(s))
            stage(s, "cross_sample", lambda: cross_sample_scalar(s))
            stage(s, "wxo",
                  lambda: parts_scalar(s, "wxo"),
                  lambda: gemm_sq_scalar(s, "wxo", nsq),
                  lambda: root_scalar(s, T),
                  lambda: squares_scalar(s, XT, nsq, range(KD), KD),
                  lambda: root_scalar(s, T),
                  lambda: parts_scalar(s, "wgu"),
                  lambda: ff_scalar(s))
            stage(s, "wdn", lambda: gemm_sq_scalar(s, "wdn", OM, 3), lambda: root_scalar(s, T))
            stage(s, "result", lambda: result_evac(s, scopy, "turned_out_s", 1))

        @block.gpsimd
        def _(g):
            def st(dst, src, name):
                g.dma_start(dst, src).then_inc(S(name), 16)

            g_constants(g)
            split_lo(g, 4)
            g_prompt_table(g)
            split_lo(g, first["wkv"] + NH)
            g.wait_ge(S("conv_states_made"), 1)
            for m_ in range(2):
                n_ = "ssm_conv" if m_ == 0 else "gdn_conv"
                st(o[n_ + "_p"][0, 0], cw_out[0:3, m_ * 768:(m_ + 1) * 768], "conv_states_out")
                st(o[n_ + "_s"][0].rearrange("b w c -> (b w) c"), cw_out[3:27, m_ * 768:(m_ + 1) * 768], "conv_states_out")
            g.wait_ge(S("pages_in"), 16)
            load_pages(g, [n for n in range(NPG) if issuer(n) == "gpsimd"])
            g_moba_tables(g)
            load_pages(g, [n for n in range(NPG, 64) if issuer(n) == "gpsimd"])
            g.wait_ge(S("fin_made"), 1)
            st(o["ssm_p"][0, 0].rearrange("(c e) q n -> (e q) c n", e=2), s_fin, "states_out")
            g.wait_ge(S("states_made"), 1)
            st(o["ssm_s"][0].rearrange("b (c e) q n -> (e q) b c n", e=2), s_h0, "states_out")
            hgrn_gpsimd(g)
            for run, n_ in enumerate(("hgrn", "gdn")):
                g.wait_ge(S("fin_made"), run + 2)
                st(o[n_ + "_p"][0, 0].rearrange("(c e) k v -> (e k) c v", e=2), t_st[0], "states_out")
                g.wait_ge(S("states_made"), run + 2)
                st(o[n_ + "_s"][0].rearrange("b (c e) k v -> (e k) b c v", e=2), t_s0, "states_out")
            split_lo(g, first["wout"] + NH)
            for mt in range(2):
                g.wait_ge(S("kvm_out_s" if mt == 0 else "kvm_out_v"), 8)
                for kv in range(2):
                    st(o["mem_k" if kv == 0 else "mem_v"][0, 0].rearrange("m h d -> m (h d)")[mt * P:(mt + 1) * P, :],
                       mkv[:, mt, kv * D:(kv + 1) * D], "mem_kv_out")
            split_lo(g, first["wxo"] + NH)
            after(g, "wout")
            link(G.memset(cx_qp, 0.0), "g")
            for k in range(KD):
                for e in range(2):
                    at = 16 * e + 4 * (k // 2)
                    last = G.tensor_copy(cx_qp[:, k, :, at:at + TS].rearrange("p (g e) t -> p g e t", e=2)[:, :, e, :],
                                         xq[:, k, SEQ:T].rearrange("p (g e t) -> p g e t", e=2, t=TS)[:, :, e, :])
            last.then_inc(S("cross_q"), 1)
            split_lo(g, len(chunks))
            for i in range(4):
                g.wait_ge(S("turned_out_v"), 6 + i + 1)
                g.wait_ge(S("turned_out_s"), 5 + i + 1)
                st(o["y_p"][0, i * P:(i + 1) * P, :], y_tok[:, i, :], "y_stored")
            g.wait_ge(S("turned_out_v"), 6 + 5)
            g.wait_ge(S("turned_out_s"), 5 + 5)
            st(o["y_s"].rearrange("b t d -> (b t) d"), y_tok[0:NS, 4, :], "y_stored")
            g.wait_ge(S("moba_kv_out"), 16 * 10)
            g.wait_ge(S("conv_states_out"), 16 * 4)
            g.wait_ge(S("states_out"), 16 * 6)
            g.wait_ge(S("mem_kv_out"), 16 * 4)
            g.wait_ge(S("y_stored"), 16 * 5)


_INS = ['x_prompt', 'x_sample', 'mem_prompt', 'cache_moba_k', 'cache_moba_v', 'page_table', 'cache_mem_k',
        'cache_mem_v', 'state_ssm_conv', 'state_ssm', 'state_hgrn', 'state_gdn_conv', 'state_gdn', 'n_mix_pre',
        'n_mix_post', 'w_in', 'w_out', 'ssm_conv_w', 'ssm_conv_b', 'ssm_dt_bias', 'ssm_a_log', 'ssm_d', 'ssm_norm',
        'hgrn_norm', 'gdn_conv_w', 'gdn_a_log', 'gdn_dt_bias', 'gdn_norm', 'n_x_pre', 'n_x_post',
        'mem_norm', 'w_xq', 'w_xkv', 'w_xo', 'n_f_pre', 'n_f_post', 'w_gu', 'w_down']
_OUTS = [("y_p", (1, 512, 1024)), ("y_s", (8, 4, 1024)),
         ("moba_kp", (1, 1, 512, 4, 64)), ("moba_ks", (1, 8, 4, 4, 64)),
         ("moba_vp", (1, 1, 512, 4, 64)), ("moba_vs", (1, 8, 4, 4, 64)),
         ("mem_k", (1, 1, 256, 4, 256)), ("mem_v", (1, 1, 256, 4, 256)),
         ("ssm_conv_p", (1, 1, 3, 768)), ("ssm_conv_s", (1, 8, 3, 768)),
         ("ssm_p", (1, 1, 4, 64, 128)), ("ssm_s", (1, 8, 4, 64, 128)),
         ("hgrn_p", (1, 1, 4, 64, 64)), ("hgrn_s", (1, 8, 4, 64, 64)),
         ("gdn_conv_p", (1, 1, 3, 768)), ("gdn_conv_s", (1, 8, 3, 768)),
         ("gdn_p", (1, 1, 4, 64, 64)), ("gdn_s", (1, 8, 4, 64, 64))]


def kernel(**inputs):
    import numpy as _np
    import concourse.bacc as _bacc
    from concourse import mybir as _mybir
    from concourse.bass_utils import run_bass_kernel_spmd as _run

    nc = _bacc.Bacc("TRN2", target_bir_lowering=False, num_devices=1)
    arrays, ins, outs = {}, {}, {}
    for name in _INS:
        x = _np.ascontiguousarray(inputs[name])
        arrays[f"in_{name}"] = x
        ins[name] = nc.dram_tensor(f"in_{name}", x.shape, _mybir.dt.from_np(x.dtype), kind="ExternalInput").ap()
    for name, shape in _OUTS:
        outs[name] = nc.dram_tensor(f"out_{name}", shape, _mybir.dt.float32, kind="ExternalOutput").ap()
    build(nc, ins, outs)
    r = _run(nc, [arrays], core_ids=[0])
    return tuple(r.results[0][f"out_{name}"] for name, _ in _OUTS)
```
